# Optimizing a Trainium2 kernel written in Bass

```python
import math
import jax
import jax.numpy as jnp
from jax import lax
import numpy as np
import jax, jax.numpy as jnp

D_MODEL = 1024
BATCH = 1
SEQ = 512
DEPTH = 1

GRID_W = 64
CTX_LEN = 256

DN_HEADS = 4
DN_DK = 128
DN_DV = 128
DN_QK = DN_HEADS * DN_DK
DN_WIDTH = DN_HEADS * DN_DV
DN_CONV_DIM = 2 * DN_QK + DN_WIDTH
SHORT_CONV = 7
CHUNK = 64

CF_CH = 512
CF_K = 31

D_MIX = DN_WIDTH + CF_CH
OFF_Z = DN_CONV_DIM
OFF_BA = OFF_Z + DN_WIDTH
OFF_CF = OFF_BA + 4 * DN_HEADS
D_IN = OFF_CF + 2 * CF_CH

N_EXPERTS = 64
TOP_K = 6
N_GROUPS = 8
TOPK_GROUPS = 4
D_EXPERT = 256
D_SHARED = 256
ROUTED_SCALE = 2.5
MOE_BLOCK = 128

EPS = 1e-6


def rmsnorm(x, g):
    xf = x.astype(jnp.float32)
    y = xf * lax.rsqrt(jnp.mean(xf * xf, axis=-1, keepdims=True) + EPS)
    return (y * g.astype(jnp.float32)).astype(x.dtype)

def layernorm(x, g, b):
    xf = x.astype(jnp.float32)
    mu = jnp.mean(xf, axis=-1, keepdims=True)
    var = jnp.mean(jnp.square(xf - mu), axis=-1, keepdims=True)
    y = (xf - mu) * lax.rsqrt(var + EPS) * g.astype(jnp.float32) + b.astype(jnp.float32)
    return y.astype(x.dtype)

def l2norm(x):
    return x * lax.rsqrt(jnp.sum(x * x, axis=-1, keepdims=True) + EPS)

def modulate(h, shift, scale):
    return h * (1 + scale) + shift

def depthwise_conv_seq(x, w):
    k, ch = w.shape
    return lax.conv_general_dilated(x, w[:, None, :].astype(x.dtype), (1,), [(k // 2, k // 2)],
                                    dimension_numbers=('NWC', 'WIO', 'NWC'), feature_group_count=ch)

def depthwise_conv_grid_columns(x, w):
    bsz, n, ch = x.shape
    rows = n // GRID_W
    k = w.shape[0]
    y = lax.conv_general_dilated(x.reshape(bsz, rows, GRID_W, ch), w[:, None, None, :].astype(x.dtype),
                                 (1, 1), [(k // 2, k // 2), (0, 0)],
                                 dimension_numbers=('NHWC', 'HWIO', 'NHWC'), feature_group_count=ch)
    return y.reshape(bsz, n, ch)

def split_mixer_inputs(u):
    return u[..., :OFF_Z], u[..., OFF_Z:OFF_BA], u[..., OFF_BA:OFF_CF], u[..., OFF_CF:]

def delta_inputs(qkv, ba, conv_w, a_log, dt_bias):
    bsz, n, _ = qkv.shape
    qkv = jax.nn.silu(depthwise_conv_seq(qkv, conv_w)).astype(jnp.float32)
    q = l2norm(qkv[..., :DN_QK].reshape(bsz, n, DN_HEADS, DN_DK)) * (DN_DK ** -0.5)
    k = l2norm(qkv[..., DN_QK:2 * DN_QK].reshape(bsz, n, DN_HEADS, DN_DK))
    v = qkv[..., 2 * DN_QK:].reshape(bsz, n, DN_HEADS, DN_DV)
    ba = ba.astype(jnp.float32).reshape(bsz, n, 2, 2, DN_HEADS)
    beta = jax.nn.sigmoid(ba[:, :, :, 0])
    g = -jnp.exp(a_log.astype(jnp.float32)) * jax.nn.softplus(ba[:, :, :, 1] + dt_bias.astype(jnp.float32))
    return q, k, v, beta, g

def gated_delta_chunked(q, k, v, g, beta, s0):
    bsz, n, heads, dk = q.shape
    dv = v.shape[-1]
    nc = n // CHUNK

    def blocks(t):
        t = t.reshape(bsz, nc, CHUNK, heads, *t.shape[3:])
        return jnp.moveaxis(t, (1, 3), (0, 2))

    qc, kc, vc, bc = blocks(q), blocks(k), blocks(v), blocks(beta)
    gc = jnp.cumsum(blocks(g), axis=-1)
    tri_incl = jnp.tril(jnp.ones((CHUNK, CHUNK), dtype=bool))
    tri_strict = jnp.tril(jnp.ones((CHUNK, CHUNK), dtype=bool), -1)
    decay = jnp.exp(jnp.where(tri_incl, gc[..., :, None] - gc[..., None, :], -jnp.inf))
    kb = kc * bc[..., None]
    lmat = jnp.where(tri_strict, jnp.einsum('nbhik,nbhjk->nbhij', kb, kc) * decay, 0.0)
    eye = jnp.eye(CHUNK, dtype=lmat.dtype)
    tinv = lax.linalg.triangular_solve(eye + lmat, jnp.broadcast_to(eye, lmat.shape),
                                       left_side=True, lower=True, unit_diagonal=True)
    u = jnp.einsum('nbhij,nbhjv->nbhiv', tinv, vc * bc[..., None])
    w = jnp.einsum('nbhij,nbhjk->nbhik', tinv, kb * jnp.exp(gc)[..., None])
    intra = jnp.einsum('nbhik,nbhjk->nbhij', qc, kc) * decay
    qd = qc * jnp.exp(gc)[..., None]
    kd = kc * jnp.exp(gc[..., -1:] - gc)[..., None]
    glast = jnp.exp(gc[..., -1])

    def step(s, inp):
        u_i, w_i, a_i, qd_i, kd_i, gl_i = inp
        v_new = u_i - jnp.einsum('bhck,bhkv->bhcv', w_i, s)
        o = jnp.einsum('bhck,bhkv->bhcv', qd_i, s) + jnp.einsum('bhij,bhjv->bhiv', a_i, v_new)
        s = s * gl_i[..., None, None] + jnp.einsum('bhck,bhcv->bhkv', kd_i, v_new)
        return s, o

    s_fin, o = lax.scan(step, s0, (u, w, intra, qd, kd, glast))
    o = jnp.moveaxis(o, (0, 2), (1, 3)).reshape(bsz, n, heads, dv)
    return o, s_fin

def bidir_gated_delta(q, k, v, beta, g, s0_fwd, s0_bwd):
    o_f, s_f = gated_delta_chunked(q, k, v, g[:, :, 0], beta[:, :, 0], s0_fwd)
    fl = lambda t: jnp.flip(t, axis=1)
    o_b, s_b = gated_delta_chunked(fl(q), fl(k), fl(v), fl(g[:, :, 1]), fl(beta[:, :, 1]), s0_bwd)
    return o_f + fl(o_b), s_f, s_b

def gated_head_norm(o, z, norm_g):
    bsz, n = z.shape[0], z.shape[1]
    on = o * lax.rsqrt(jnp.mean(o * o, axis=-1, keepdims=True) + EPS) * norm_g.astype(jnp.float32)
    gate = jax.nn.silu(z.astype(jnp.float32)).reshape(bsz, n, DN_HEADS, DN_DV)
    return (on * gate).reshape(bsz, n, DN_WIDTH).astype(z.dtype)

def conformer_module(cf_in, conv_fn, dw_w, dw_b, ln_g, ln_b):
    y = cf_in[..., :CF_CH] * jax.nn.sigmoid(cf_in[..., CF_CH:])
    y = conv_fn(y, dw_w) + dw_b
    return jax.nn.silu(layernorm(y, ln_g, ln_b))

def swiglu(h, wg, wu, wd):
    return (jax.nn.silu(h @ wg) * (h @ wu)) @ wd

def moe_ffn(h, router_w, router_bias, w_gate, w_up, w_down, s_gate, s_up, s_down):
    bsz, n, d = h.shape
    t = bsz * n
    hf = h.reshape(t, d)
    scores = jax.nn.sigmoid((hf @ router_w).astype(jnp.float32))
    sel = scores + router_bias.astype(jnp.float32)
    grp_score = lax.top_k(sel.reshape(t, N_GROUPS, N_EXPERTS // N_GROUPS), 2)[0].sum(-1)
    _, grp_idx = lax.top_k(grp_score, TOPK_GROUPS)
    grp_keep = jnp.any(grp_idx[..., None] == jnp.arange(N_GROUPS), axis=-2)
    exp_keep = jnp.repeat(grp_keep, N_EXPERTS // N_GROUPS, axis=-1)
    _, top_idx = lax.top_k(jnp.where(exp_keep, sel, -jnp.inf), TOP_K)
    top_w = jnp.take_along_axis(scores, top_idx, axis=-1)
    top_w = top_w / jnp.sum(top_w, axis=-1, keepdims=True) * ROUTED_SCALE
    tk = t * TOP_K
    flat_e = top_idx.reshape(tk)
    order = jnp.argsort(flat_e, stable=True)
    sorted_e = flat_e[order]
    sorted_tok = (order // TOP_K).astype(jnp.int32)
    sorted_w = top_w.reshape(tk)[order]
    counts = jnp.bincount(flat_e, length=N_EXPERTS)
    padded = (counts + MOE_BLOCK - 1) // MOE_BLOCK * MOE_BLOCK
    start = jnp.cumsum(counts) - counts
    pad_end = jnp.cumsum(padded)
    pad_start = pad_end - padded
    dest = pad_start[sorted_e] + jnp.arange(tk) - start[sorted_e]
    n_blocks = -(-tk // MOE_BLOCK) + N_EXPERTS
    n_slots = n_blocks * MOE_BLOCK
    slot_tok = jnp.full((n_slots,), t, jnp.int32).at[dest].set(sorted_tok)
    slot_w = jnp.zeros((n_slots,), jnp.float32).at[dest].set(sorted_w)
    block_exp = jnp.minimum(jnp.searchsorted(pad_end, jnp.arange(n_blocks) * MOE_BLOCK, side='right'),
                            N_EXPERTS - 1)
    h_pad = jnp.concatenate([hf, jnp.zeros((1, d), hf.dtype)], axis=0)

    def expert_block(args):
        tok, e = args
        return swiglu(h_pad[tok], w_gate[e], w_up[e], w_down[e])

    out = lax.map(expert_block, (slot_tok.reshape(n_blocks, MOE_BLOCK), block_exp))
    weighted = (out.reshape(n_slots, d) * slot_w[:, None]).astype(h.dtype)
    routed = jnp.zeros((t + 1, d), h.dtype).at[slot_tok].add(weighted)[:t]
    return (routed + swiglu(hf, s_gate, s_up, s_down)).reshape(bsz, n, d)

def first_inputs(seed: int = 0) -> dict:
    key = jax.random.key(seed)
    ks = jax.random.split(key, 32)
    f32 = jnp.float32
    L = DEPTH

    def nrm(k, shape, s):
        return jax.random.normal(k, shape, f32) * s

    dt = jnp.exp(jax.random.uniform(ks[11], (L, 2, DN_HEADS), f32, math.log(1e-3), math.log(1e-1)))
    return {
        'x': nrm(ks[0], (BATCH, SEQ, D_MODEL), 1.0),
        'c': nrm(ks[1], (BATCH, D_MODEL), 1.0),
        'ctx': nrm(ks[2], (BATCH, CTX_LEN, D_MODEL), 1.0),
        'c_ctx': nrm(ks[3], (D_MODEL,), 1.0),
        'w_mod': nrm(ks[4], (L, D_MODEL, 6 * D_MODEL), 0.5 * D_MODEL ** -0.5),
        'b_mod': nrm(ks[5], (L, 6 * D_MODEL), 0.02),
        'g_mix': 1.0 + nrm(ks[6], (L, D_MODEL), 0.02),
        'g_ffn': 1.0 + nrm(ks[7], (L, D_MODEL), 0.02),
        'w_in': nrm(ks[8], (L, D_MODEL, D_IN), D_MODEL ** -0.5),
        'w_out': nrm(ks[9], (L, D_MIX, D_MODEL), D_MIX ** -0.5),
        'dn_conv_w': nrm(ks[10], (L, SHORT_CONV, DN_CONV_DIM), SHORT_CONV ** -0.5),
        'dn_a_log': jnp.log(jax.random.uniform(ks[12], (L, 2, DN_HEADS), f32, 1.0, 16.0)),
        'dn_dt_bias': dt + jnp.log(-jnp.expm1(-dt)),
        'dn_norm_g': 1.0 + nrm(ks[13], (L, DN_DV), 0.02),
        'cf_dw_w': nrm(ks[14], (L, CF_K, CF_CH), CF_K ** -0.5),
        'cf_dw_b': nrm(ks[15], (L, CF_CH), 0.02),
        'cf_ln_g': 1.0 + nrm(ks[16], (L, CF_CH), 0.02),
        'cf_ln_b': nrm(ks[17], (L, CF_CH), 0.02),
        'router_w': nrm(ks[18], (L, D_MODEL, N_EXPERTS), D_MODEL ** -0.5),
        'router_bias': nrm(ks[19], (L, N_EXPERTS), 0.01),
        'exp_w_gate': nrm(ks[20], (L, N_EXPERTS, D_MODEL, D_EXPERT), D_MODEL ** -0.5),
        'exp_w_up': nrm(ks[21], (L, N_EXPERTS, D_MODEL, D_EXPERT), D_MODEL ** -0.5),
        'exp_w_down': nrm(ks[22], (L, N_EXPERTS, D_EXPERT, D_MODEL), D_EXPERT ** -0.5),
        'sh_w_gate': nrm(ks[23], (L, D_MODEL, D_SHARED), D_MODEL ** -0.5),
        'sh_w_up': nrm(ks[24], (L, D_MODEL, D_SHARED), D_MODEL ** -0.5),
        'sh_w_down': nrm(ks[25], (L, D_SHARED, D_MODEL), D_SHARED ** -0.5),
        'g_final': 1.0 + nrm(ks[26], (D_MODEL,), 0.02),
    }

def first_block(x, c, ctx, c_ctx, w_mod, b_mod, g_mix, g_ffn, w_in, w_out, dn_conv_w, dn_a_log, dn_dt_bias,
              dn_norm_g, cf_dw_w, cf_dw_b, cf_ln_g, cf_ln_b, router_w, router_bias, exp_w_gate, exp_w_up,
              exp_w_down, sh_w_gate, sh_w_up, sh_w_down, g_final):
    bsz = x.shape[0]
    for l in range(DEPTH):
        sh1, sc1, gt1, sh2, sc2, gt2 = jnp.split((jax.nn.silu(c) @ w_mod[l] + b_mod[l])[:, None, :], 6, axis=-1)
        csh1, csc1, cgt1, csh2, csc2, cgt2 = jnp.split(jax.nn.silu(c_ctx) @ w_mod[l] + b_mod[l], 6, axis=-1)

        qkv_c, z_c, ba_c, cf_c = split_mixer_inputs(modulate(rmsnorm(ctx, g_mix[l]), csh1, csc1) @ w_in[l])
        s0 = jnp.zeros((bsz, DN_HEADS, DN_DK, DN_DV), jnp.float32)
        o_c, s_fwd, s_bwd = bidir_gated_delta(
            *delta_inputs(qkv_c, ba_c, dn_conv_w[l], dn_a_log[l], dn_dt_bias[l]), s0, s0)

        qkv_x, z_x, ba_x, cf_x = split_mixer_inputs(modulate(rmsnorm(x, g_mix[l]), sh1, sc1) @ w_in[l])
        o_x, _, _ = bidir_gated_delta(
            *delta_inputs(qkv_x, ba_x, dn_conv_w[l], dn_a_log[l], dn_dt_bias[l]), s_fwd, s_bwd)
        heads_x = jnp.concatenate([
            gated_head_norm(o_x, z_x, dn_norm_g[l]),
            conformer_module(cf_x, depthwise_conv_grid_columns, cf_dw_w[l], cf_dw_b[l], cf_ln_g[l], cf_ln_b[l]),
        ], axis=-1)
        x = x + gt1 * (heads_x @ w_out[l])
        x = x + gt2 * moe_ffn(modulate(rmsnorm(x, g_ffn[l]), sh2, sc2), router_w[l], router_bias[l],
                              exp_w_gate[l], exp_w_up[l], exp_w_down[l], sh_w_gate[l], sh_w_up[l], sh_w_down[l])

        if l + 1 < DEPTH:
            heads_c = jnp.concatenate([
                gated_head_norm(o_c, z_c, dn_norm_g[l]),
                conformer_module(cf_c, depthwise_conv_seq, cf_dw_w[l], cf_dw_b[l], cf_ln_g[l], cf_ln_b[l]),
            ], axis=-1)
            ctx = ctx + cgt1 * (heads_c @ w_out[l])
            ctx = ctx + cgt2 * moe_ffn(modulate(rmsnorm(ctx, g_ffn[l]), csh2, csc2), router_w[l], router_bias[l],
                                       exp_w_gate[l], exp_w_up[l], exp_w_down[l],
                                       sh_w_gate[l], sh_w_up[l], sh_w_down[l])
    return rmsnorm(x, g_final)


DEPTH_2 = 2

N_MIXERS = 2
N_RWKV = (DEPTH_2 + N_MIXERS - 1) // N_MIXERS
N_MLA = DEPTH_2 // N_MIXERS
NORM_EPS = 1e-6
RWKV_HEAD = 64
RWKV_HEADS = D_MODEL // RWKV_HEAD
DECAY_LORA = 64
ICLR_LORA = 64
GN_EPS = 64e-5
N_DIR = 2
MLA_HEADS = 16
QK_NOPE = 64
QK_ROPE = 32
V_HEAD = 64
Q_LORA = 384
KV_LORA = 256
MLA_GATE = MLA_HEADS * V_HEAD
MLA_IN = Q_LORA + KV_LORA + QK_ROPE + MLA_GATE
ROPE_THETA = 10000.0
Q_BLOCK = 128


def rmsnorm_2(x, g, eps=NORM_EPS):
    xf = x.astype(jnp.float32)
    y = xf * lax.rsqrt(jnp.mean(xf * xf, axis=-1, keepdims=True) + eps)
    return (y * g.astype(jnp.float32)).astype(x.dtype)

def centred_shift(h):
    prev = jnp.pad(h[:, :-1], ((0, 0), (1, 0), (0, 0)))
    nxt = jnp.pad(h[:, 1:], ((0, 0), (0, 1), (0, 0)))
    return 0.5 * (prev + nxt) - h

def rwkv_prepare(h, mu, w_in, w0, w1, w2, a0, a1, a2, k_k, k_a):
    B, T, D = h.shape
    xx = centred_shift(h)
    lerp = lambda j: h + xx * mu[j]
    heads = lambda t: t.reshape(t.shape[:-1] + (RWKV_HEADS, RWKV_HEAD))
    r = heads(lerp(0) @ w_in[0])
    k = heads(lerp(1) @ w_in[1])
    v = heads(lerp(2) @ w_in[2])
    gate = lerp(3) @ w_in[3]
    xw, xa = lerp(4), lerp(5)
    wpre = w0[:, None, None, :] + jnp.einsum('nbtr,nrd->nbtd', jnp.tanh(jnp.einsum('btd,ndr->nbtr', xw, w1)), w2)
    wpre = wpre.astype(jnp.float32)
    logw = heads(-jnp.exp(-jax.nn.softplus(-wpre) - 0.5))
    a = heads(jax.nn.sigmoid(a0[:, None, None, :] + jnp.einsum('nbtr,nrd->nbtd', jnp.einsum('btd,ndr->nbtr', xa, a1), a2)))
    kkf = (k * k_k.reshape(RWKV_HEADS, RWKV_HEAD)).astype(jnp.float32)
    kk = (kkf / jnp.maximum(jnp.linalg.norm(kkf, axis=-1, keepdims=True), 1e-12)).astype(h.dtype)
    k_dir = k[None] * (1.0 + (a - 1.0) * k_a.reshape(RWKV_HEADS, RWKV_HEAD))
    b = kk[None] * a
    return r, logw, k_dir, v, -kk, b, gate

def orient_shared(t):
    return jnp.stack([t, jnp.flip(t, 1)])

def orient_dir(t):
    return jnp.stack([t[0], jnp.flip(t[1], 1)])

def wkv_scan(r, logw, k, v, a, b, s0):
    tm = lambda t: jnp.moveaxis(t.astype(jnp.float32), 2, 0)

    def step(s, inp):
        r_t, lw_t, k_t, v_t, a_t, b_t = inp
        sa = jnp.einsum('dbhij,dbhj->dbhi', s, a_t)
        s = s * jnp.exp(lw_t)[..., None, :] + sa[..., None] * b_t[..., None, :] + v_t[..., None] * k_t[..., None, :]
        return s, jnp.einsum('dbhij,dbhj->dbhi', s, r_t)

    s_fin, y = lax.scan(step, s0, (tm(r), tm(logw), tm(k), tm(v), tm(a), tm(b)))
    return jnp.moveaxis(y, 0, 2), s_fin

def rwkv_run(prep, s0):
    r, logw, k_dir, v, a_vec, b, gate = prep
    return wkv_scan(orient_shared(r), orient_dir(logw), orient_dir(k_dir), orient_shared(v),
                    orient_shared(a_vec), orient_dir(b), s0)

def rwkv_readout(y, prep, r_k, lnx_g, lnx_b, w_out):
    r, logw, k_dir, v, a_vec, b, gate = prep
    B, T, D = gate.shape
    yf = y[0] + jnp.flip(y[1], 1)
    mean = jnp.mean(yf, axis=-1, keepdims=True)
    var = jnp.mean(jnp.square(yf - mean), axis=-1, keepdims=True)
    yn = ((yf - mean) * lax.rsqrt(var + GN_EPS)).reshape(B, T, D).astype(gate.dtype) * lnx_g + lnx_b
    bonus = jnp.sum(r[None] * k_dir * r_k, axis=(0, -1))[..., None] * v
    o = (yn + bonus.reshape(B, T, D)) * jax.nn.silu(gate)
    return o @ w_out

def rwkv_mixer(h_x, h_c, mu, w_in, w0, w1, w2, a0, a1, a2, k_k, k_a, r_k, lnx_g, lnx_b, w_out, need_ctx):
    B = h_x.shape[0]
    p_c = rwkv_prepare(h_c, mu, w_in, w0, w1, w2, a0, a1, a2, k_k, k_a)
    p_x = rwkv_prepare(h_x, mu, w_in, w0, w1, w2, a0, a1, a2, k_k, k_a)
    s0 = jnp.zeros((N_DIR, B, RWKV_HEADS, RWKV_HEAD, RWKV_HEAD), jnp.float32)
    y_c, s_c = rwkv_run(p_c, s0)
    y_x, _ = rwkv_run(p_x, s_c)
    d_x = rwkv_readout(y_x, p_x, r_k, lnx_g, lnx_b, w_out)
    d_c = rwkv_readout(y_c, p_c, r_k, lnx_g, lnx_b, w_out) if need_ctx else None
    return d_x, d_c

def axial_rope_angles(T, rows):
    row = jnp.broadcast_to(jnp.arange(rows)[:, None], (rows, GRID_W)).reshape(T).astype(jnp.float32)
    col = jnp.broadcast_to(jnp.arange(GRID_W)[None, :], (rows, GRID_W)).reshape(T).astype(jnp.float32)
    n_axis = QK_ROPE // 2
    inv = 1.0 / (ROPE_THETA ** (jnp.arange(0, n_axis, 2, dtype=jnp.float32) / n_axis))
    ang = jnp.concatenate([row[:, None] * inv, col[:, None] * inv], axis=-1)
    return jnp.cos(ang), jnp.sin(ang)

def apply_rope(x, cos, sin):
    half = QK_ROPE // 2
    x1, x2 = x[..., :half], x[..., half:]
    c = cos[:, None, :].astype(x.dtype)
    s = sin[:, None, :].astype(x.dtype)
    return jnp.concatenate([x1 * c - x2 * s, x1 * s + x2 * c], axis=-1)

def mla_project(h, w_in, q_norm_g, w_qb, kv_norm_g, w_kvb, cos=None, sin=None):
    B, T, D = h.shape
    p = h @ w_in
    q_c, kv_c, k_pe, gate = jnp.split(p, [Q_LORA, Q_LORA + KV_LORA, Q_LORA + KV_LORA + QK_ROPE], axis=-1)
    q = (rmsnorm_2(q_c, q_norm_g) @ w_qb).reshape(B, T, MLA_HEADS, QK_NOPE + QK_ROPE)
    kv = (rmsnorm_2(kv_c, kv_norm_g) @ w_kvb).reshape(B, T, MLA_HEADS, QK_NOPE + V_HEAD)
    q_nope, q_pe = q[..., :QK_NOPE], q[..., QK_NOPE:]
    k_nope, v = kv[..., :QK_NOPE], kv[..., QK_NOPE:]
    k_pe = k_pe[:, :, None, :]
    if cos is not None:
        q_pe = apply_rope(q_pe, cos, sin)
        k_pe = apply_rope(k_pe, cos, sin)
    q = jnp.concatenate([q_nope, q_pe], axis=-1)
    k = jnp.concatenate([k_nope, jnp.broadcast_to(k_pe, (B, T, MLA_HEADS, QK_ROPE))], axis=-1)
    return q, k, v, gate

def attend(q, k, v):
    s = jnp.einsum('bqhd,bkhd->bhqk', q, k, preferred_element_type=jnp.float32) * (1.0 / math.sqrt(QK_NOPE + QK_ROPE))
    p = jax.nn.softmax(s, axis=-1).astype(v.dtype)
    return jnp.einsum('bhqk,bkhd->bqhd', p, v, preferred_element_type=jnp.float32).astype(q.dtype)

def mla_mixer(h_x, h_c, cos, sin, w_in, q_norm_g, w_qb, kv_norm_g, w_kvb, w_out, need_ctx):
    B, T, D = h_x.shape
    L = h_c.shape[1]
    q_x, k_x, v_x, g_x = mla_project(h_x, w_in, q_norm_g, w_qb, kv_norm_g, w_kvb, cos, sin)
    q_c, k_c, v_c, g_c = mla_project(h_c, w_in, q_norm_g, w_qb, kv_norm_g, w_kvb)
    k_all = jnp.concatenate([k_x, k_c], axis=1)
    v_all = jnp.concatenate([v_x, v_c], axis=1)
    qb = q_x.reshape(B, T // Q_BLOCK, Q_BLOCK, MLA_HEADS, QK_NOPE + QK_ROPE).swapaxes(0, 1)
    o = lax.map(lambda qblk: attend(qblk, k_all, v_all), qb)
    o = o.swapaxes(0, 1).reshape(B, T, MLA_GATE)
    d_x = (o * jax.nn.silu(g_x)) @ w_out
    d_c = None
    if need_ctx:
        o_c = attend(q_c, k_c, v_c).reshape(B, L, MLA_GATE)
        d_c = (o_c * jax.nn.silu(g_c)) @ w_out
    return d_x, d_c

def second_inputs(seed: int = 0) -> dict:
    key = jax.random.key(seed)
    ks = iter(jax.random.split(key, 40))
    nrm = lambda shape, scale: scale * jax.random.normal(next(ks), shape, jnp.float32)
    D, NR, NM = D_MODEL, N_RWKV, N_MLA
    return {
        'x': nrm((BATCH, SEQ, D), 1.0),
        'c': nrm((BATCH, D), 1.0),
        'ctx': nrm((BATCH, CTX_LEN, D), 1.0),
        'c_ctx': nrm((D,), 1.0),
        'norm_g': 1.0 + nrm((DEPTH_2, D), 0.05),
        'mod_w': nrm((DEPTH_2, D, 3 * D), 0.5 * D ** -0.5),
        'mod_b': nrm((DEPTH_2, 3 * D), 0.05),
        'rwkv_mu': jax.random.uniform(next(ks), (NR, 6, D), jnp.float32),
        'rwkv_w_in': nrm((NR, 4, D, D), D ** -0.5),
        'rwkv_w0': jax.random.uniform(next(ks), (NR, N_DIR, D), jnp.float32, -6.0, -1.0),
        'rwkv_w1': nrm((NR, N_DIR, D, DECAY_LORA), D ** -0.5),
        'rwkv_w2': nrm((NR, N_DIR, DECAY_LORA, D), 0.5 * DECAY_LORA ** -0.5),
        'rwkv_a0': nrm((NR, N_DIR, D), 0.1),
        'rwkv_a1': nrm((NR, N_DIR, D, ICLR_LORA), D ** -0.5),
        'rwkv_a2': nrm((NR, N_DIR, ICLR_LORA, D), 0.5 * ICLR_LORA ** -0.5),
        'rwkv_k_k': 0.85 + nrm((NR, D), 0.05),
        'rwkv_k_a': 1.0 + nrm((NR, D), 0.05),
        'rwkv_r_k': nrm((NR, RWKV_HEADS, RWKV_HEAD), 0.1),
        'rwkv_lnx_g': 1.0 + nrm((NR, D), 0.05),
        'rwkv_lnx_b': nrm((NR, D), 0.02),
        'rwkv_w_out': nrm((NR, D, D), D ** -0.5),
        'mla_w_in': nrm((NM, D, MLA_IN), D ** -0.5),
        'mla_q_norm_g': 1.0 + nrm((NM, Q_LORA), 0.05),
        'mla_w_qb': nrm((NM, Q_LORA, MLA_HEADS * (QK_NOPE + QK_ROPE)), Q_LORA ** -0.5),
        'mla_kv_norm_g': 1.0 + nrm((NM, KV_LORA), 0.05),
        'mla_w_kvb': nrm((NM, KV_LORA, MLA_HEADS * (QK_NOPE + V_HEAD)), KV_LORA ** -0.5),
        'mla_w_out': nrm((NM, MLA_GATE, D), MLA_GATE ** -0.5),
        'final_g': 1.0 + nrm((D,), 0.05),
    }

def second_block(x, c, ctx, c_ctx, norm_g, mod_w, mod_b, rwkv_mu, rwkv_w_in, rwkv_w0, rwkv_w1, rwkv_w2,
              rwkv_a0, rwkv_a1, rwkv_a2, rwkv_k_k, rwkv_k_a, rwkv_r_k, rwkv_lnx_g, rwkv_lnx_b, rwkv_w_out,
              mla_w_in, mla_q_norm_g, mla_w_qb, mla_kv_norm_g, mla_w_kvb, mla_w_out, final_g):
    T = x.shape[1]
    ROWS = T // GRID_W
    cos, sin = axial_rope_angles(T, ROWS)
    for i in range(DEPTH_2):
        last = i == DEPTH_2 - 1
        mod_x = jax.nn.silu(c) @ mod_w[i] + mod_b[i]
        mod_c = jax.nn.silu(c_ctx) @ mod_w[i] + mod_b[i]
        sh_x, sc_x, g_x = jnp.split(mod_x[:, None, :], 3, axis=-1)
        sh_c, sc_c, g_c = jnp.split(mod_c, 3, axis=-1)
        h_x = rmsnorm_2(x, norm_g[i]) * (1.0 + sc_x) + sh_x
        h_c = rmsnorm_2(ctx, norm_g[i]) * (1.0 + sc_c) + sh_c
        j = i // N_MIXERS
        if i % N_MIXERS == 0:
            d_x, d_c = rwkv_mixer(h_x, h_c, rwkv_mu[j], rwkv_w_in[j], rwkv_w0[j], rwkv_w1[j], rwkv_w2[j],
                                  rwkv_a0[j], rwkv_a1[j], rwkv_a2[j], rwkv_k_k[j], rwkv_k_a[j], rwkv_r_k[j],
                                  rwkv_lnx_g[j], rwkv_lnx_b[j], rwkv_w_out[j], not last)
        else:
            d_x, d_c = mla_mixer(h_x, h_c, cos, sin, mla_w_in[j], mla_q_norm_g[j], mla_w_qb[j],
                                 mla_kv_norm_g[j], mla_w_kvb[j], mla_w_out[j], not last)
        x = x + g_x * d_x
        if not last:
            ctx = ctx + g_c * d_c
    return rmsnorm_2(x, final_g)


def setup_inputs(seed=0):
    out = dict(first_inputs(seed))
    for name, value in second_inputs(seed + 1).items():
        if name != "x":
            out[name + "_2"] = value
    return out


def reference(
    x, c, ctx, c_ctx, w_mod, b_mod, g_mix, g_ffn, w_in, w_out, dn_conv_w, dn_a_log, dn_dt_bias,
    dn_norm_g, cf_dw_w, cf_dw_b, cf_ln_g, cf_ln_b, router_w, router_bias, exp_w_gate, exp_w_up,
    exp_w_down, sh_w_gate, sh_w_up, sh_w_down, g_final, c_2, ctx_2, c_ctx_2, norm_g_2, mod_w_2,
    mod_b_2, rwkv_mu_2, rwkv_w_in_2, rwkv_w0_2, rwkv_w1_2, rwkv_w2_2, rwkv_a0_2, rwkv_a1_2,
    rwkv_a2_2, rwkv_k_k_2, rwkv_k_a_2, rwkv_r_k_2, rwkv_lnx_g_2, rwkv_lnx_b_2, rwkv_w_out_2,
    mla_w_in_2, mla_q_norm_g_2, mla_w_qb_2, mla_kv_norm_g_2, mla_w_kvb_2, mla_w_out_2,
    final_g_2,
):
    x = first_block(
        x, c, ctx, c_ctx, w_mod, b_mod, g_mix, g_ffn, w_in, w_out, dn_conv_w, dn_a_log,
        dn_dt_bias, dn_norm_g, cf_dw_w, cf_dw_b, cf_ln_g, cf_ln_b, router_w, router_bias,
        exp_w_gate, exp_w_up, exp_w_down, sh_w_gate, sh_w_up, sh_w_down, g_final,
    )
    return second_block(
        x, c_2, ctx_2, c_ctx_2, norm_g_2, mod_w_2, mod_b_2, rwkv_mu_2, rwkv_w_in_2, rwkv_w0_2,
        rwkv_w1_2, rwkv_w2_2, rwkv_a0_2, rwkv_a1_2, rwkv_a2_2, rwkv_k_k_2, rwkv_k_a_2,
        rwkv_r_k_2, rwkv_lnx_g_2, rwkv_lnx_b_2, rwkv_w_out_2, mla_w_in_2, mla_q_norm_g_2,
        mla_w_qb_2, mla_kv_norm_g_2, mla_w_kvb_2, mla_w_out_2, final_g_2,
    )


_drawn_inputs = setup_inputs


def setup_inputs(seed=0):
    import zlib

    import numpy as np

    out = dict(_drawn_inputs(seed))
    spreads = {}
    factors = {'ctx': 3.147,
     'c_ctx': 4.871,
     'g_mix': 3.051,
     'dn_norm_g': 3.258,
     'cf_ln_g': 3.809,
     'cf_ln_b': 4.56,
     'g_final': 2.72,
     'norm_g_2': 3.564,
     'rwkv_w1_2': 8.0,
     'rwkv_w2_2': 8.0,
     'rwkv_a0_2': 8.0,
     'rwkv_k_k_2': 3.235,
     'rwkv_k_a_2': 3.672,
     'rwkv_lnx_g_2': 7.849,
     'rwkv_lnx_b_2': 8.0,
     'mla_q_norm_g_2': 8.0,
     'mla_w_qb_2': 3.534,
     'mla_kv_norm_g_2': 8.0}
    for name, (base, spread) in spreads.items():
        noise = np.random.default_rng([zlib.crc32(name.encode()), seed]).standard_normal(out[name].shape)
        drawn = base * np.exp(spread * noise) if base else spread * noise
        out[name] = jnp.asarray(drawn.astype(out[name].dtype))
    for name, factor in factors.items():
        out[name] = (out[name] * factor).astype(out[name].dtype)
    return out
```

```python
from contextlib import ExitStack, contextmanager

import concourse.bass as bass
from concourse import mybir

F32 = mybir.dt.float32
ALU = mybir.AluOpType
ACT = mybir.ActivationFunctionType
AX = mybir.AxisListType

P = 128
D = 1024
KD = D // P
TC, TX = 256, 512
NT = (TC + TX) // P
JC = TC // P
JX = TX // P
TT = TC + TX
H1, DK = 4, 128
QKV = 3 * H1 * DK
NQKV = QKV // P
CFC = 512
NCF = CFC // P
TAPS = 7
GRID_W = 64
ROWS = TX // GRID_W
EPS = 1e-6
LEVELS = 7
NE = 64
GROUPS = 8
DE = 256
H2 = 16
HD = 64
LORA = 64


USED = {}


def sbuf(nc, name, shape, dtype):
    USED[name] = USED.get(name, 0) + 1
    return nc.sbuf_tensor(f"{name}_{USED[name]}", shape, dtype)


@contextmanager
def phase(nc, names):
    with ExitStack() as held:
        by_name = {n: held.enter_context(nc.semaphore(n)) for n in names.split()}
        handles = list(by_name.values())
        signals = by_name
        with nc.Block(no_gpsimd_drain=True) as block:
            yield block, signals
        with nc.Block(no_gpsimd_drain=True) as clearing:
            @clearing.sync
            def _(sp):
                nums = sorted(h.num for h in handles)
                if nums[-1] - nums[0] + 1 == len(nums):
                    sp.sem_clear(range(nums[0], nums[-1] + 1))
                else:
                    for h in handles:
                        sp.sem_clear(h)


class Chain:

    def __init__(self, eng, sem):
        self.eng, self.sem, self.n = eng, sem, 0

    def __call__(self, ins):
        self.put(ins)
        self.wait()

    def put(self, ins):
        self.n += 1
        ins.then_inc(self.sem, 1)

    def wait(self, back=0):
        if self.n - back > 0:
            self.eng.wait_ge(self.sem, self.n - back)


class Kernel:
    pass



MASK_NAMES = ["ident", "ones", "strF", "incF", "strB", "incB", "cumF", "cumB"]
ROPE_COL = len(MASK_NAMES) * P
CROSS_COL = ROPE_COL + 2 * TX
MIX_COL = CROSS_COL + 2 * LEVELS * P
CONST_COLS = MIX_COL + 4 + P


def constants():
    import numpy as np

    t = np.arange(P)
    s_, t_ = t[:, None], t[None, :]
    out = np.zeros((P, CONST_COLS), np.float32)

    def put(n, m):
        out[:, n * P:(n + 1) * P] = m

    put(0, s_ == t_)
    put(1, 1)
    put(2, s_ < t_)
    put(3, s_ <= t_)
    put(4, s_ > t_)
    put(5, s_ >= t_)
    put(6, (s_ <= t_).astype(np.float32) - (s_ < P // 2))
    put(7, (s_ >= t_).astype(np.float32) - (s_ >= P // 2))
    out[:, MIX_COL + 0] = t < P // 2
    out[:, MIX_COL + 1] = t >= P // 2
    out[:, MIX_COL + 2] = t >= P // 2
    out[:, MIX_COL + 3] = t < P // 2
    out[:, MIX_COL + 4:] = (s_ // HD == t_ // HD)
    for d in range(2):
        for level in range(LEVELS):
            b = 1 << level
            m = (s_ // b == t_ // b + 1) & (s_ // (2 * b) == t_ // (2 * b))
            if d:
                m = m.T
            at = CROSS_COL + (d * LEVELS + level) * P
            out[:, at:at + P] = -1.0 * m
    half = 16
    pos = np.arange(TX)
    inv = 1.0 / (10000.0 ** (np.arange(0, half, 2, dtype=np.float32) / half))
    ang = np.concatenate([(pos // GRID_W)[:, None] * inv, (pos % GRID_W)[:, None] * inv], -1)
    cos, sin = np.cos(ang.astype(np.float32)).T, np.sin(ang.astype(np.float32)).T
    out[64:96, ROPE_COL:ROPE_COL + TX] = np.concatenate([cos, cos])
    out[64:96, ROPE_COL + TX:ROPE_COL + 2 * TX] = np.concatenate([-sin, sin])
    return out


def rows_of(spec):
    at, where = 0, {}
    for name, n in spec:
        where[name] = at
        at += n
    return where, at


HALO = ROWS - 1
CF_USED = 2 * HALO + 1
SPEC_A = [("g_mix", KD), ("g_ffn", KD), ("norm_g_2", 2 * KD), ("cf_dw_b", NCF), ("cf_ln_g", NCF),
          ("cf_ln_b", NCF), ("dn_norm_g", 1), ("cf_dw_w", CF_USED * NCF)]
SPEC_B = [("dn_conv_w", TAPS * NQKV), ("q_norm", 3), ("kv_norm", 2)]
WHERE_A, N_A = rows_of(SPEC_A)
WHERE_B, N_B = rows_of(SPEC_B)
N_C = 6 * KD


def load_parameters(K, I):
    nc = K.nc
    cf_used = I["cf_dw_w"][0][15 - HALO:15 + HALO + 1, :].rearrange("j (f p) -> (j f) p", p=P)
    rows_a = {
        "g_mix": I["g_mix"][0].rearrange("(k p) -> k p", p=P),
        "g_ffn": I["g_ffn"][0].rearrange("(k p) -> k p", p=P),
        "norm_g_2": I["norm_g_2"].rearrange("l (k p) -> (l k) p", p=P),
        "cf_dw_b": I["cf_dw_b"][0].rearrange("(k p) -> k p", p=P),
        "cf_ln_g": I["cf_ln_g"][0].rearrange("(k p) -> k p", p=P),
        "cf_ln_b": I["cf_ln_b"][0].rearrange("(k p) -> k p", p=P),
        "dn_norm_g": I["dn_norm_g"],
        "cf_dw_w": cf_used,
    }
    rows_b = {
        "dn_conv_w": I["dn_conv_w"][0].rearrange("j (f p) -> (j f) p", p=P),
        "q_norm": I["mla_q_norm_g_2"][0].rearrange("(k p) -> k p", p=P),
        "kv_norm": I["mla_kv_norm_g_2"][0].rearrange("(k p) -> k p", p=P),
    }
    with ExitStack() as c, phase(nc, "consts_in rows_in turned cols_done x_in eps_set") as (block, S):
        ra = c.enter_context(sbuf(nc, "param_rows_a", [N_A, P], F32))
        rb = c.enter_context(sbuf(nc, "param_rows_b", [N_B, P], F32))
        rc = c.enter_context(sbuf(nc, "param_rows_c", [N_C, P], F32))

        @block.sync
        def _(sp):
            sp.dma_start(K.const[:, :], I["consts"]).then_inc(S["consts_in"], 16)
            sp.dma_start(rc[:, :], I["rwkv_mu_2"][0].rearrange("j (k p) -> (j k) p", p=P)).then_inc(S["rows_in"], 16)
            n = 1
            for where, rows, dst in ((WHERE_A, rows_a, ra), (WHERE_B, rows_b, rb)):
                for name, src in rows.items():
                    sp.dma_start(dst[where[name]:where[name] + src.shape[0], :], src).then_inc(S["rows_in"], 16)
                    n += 1
            sp.dma_start(K.X[:, 0:JC, :], I["ctx"][0].rearrange("(j p) n -> p j n", p=P)).then_inc(S["x_in"], 16)
            sp.dma_start(K.X[:, JC:NT, :], I["x"][0].rearrange("(j p) n -> p j n", p=P)).then_inc(S["x_in"], 16)
            sp.wait_ge(S["x_in"], 32)
            sp.wait_ge(S["rows_in"], 16 * n)

        @block.tensor
        def _(pe):
            pe.wait_ge(S["consts_in"], 16)
            pe.wait_ge(S["rows_in"], 16 * (1 + len(rows_a) + len(rows_b)))
            pe.transpose(K.bank[0][:, 0:N_A], ra[:, :], K.ident[0:N_A, 0:N_A])
            pe.transpose(K.bank[2][:, 0:N_C], rc[:, :], K.ident[0:N_C, 0:N_C])
            pe.transpose(K.bank[1][:, 0:N_B], rb[:, :], K.ident[0:N_B, 0:N_B]).then_inc(S["turned"], 1)

        @block.vector
        def _(dve):
            dve.memset(K.eps[:, :], EPS).then_inc(S["eps_set"], 1)
            dve.memset(K.one[:, :], 1.0).then_inc(S["eps_set"], 1)
            dve.memset(K.gneps[:, :], 64e-5).then_inc(S["eps_set"], 1)
            dve.wait_ge(S["turned"], 1)
            dve.tensor_copy(K.colA[:, :], K.bank[0][:, 0:N_A]).then_inc(S["cols_done"], 1)
            dve.tensor_copy(K.colB[:, :], K.bank[1][:, 0:N_B]).then_inc(S["cols_done"], 1)
            dve.tensor_copy(K.colC[:, :], K.bank[2][:, 0:N_C]).then_inc(S["cols_done"], 1)



WCH = 512
RING = 3


def modulation(K, vectors, w, b, N, row, rows_needed=None):
    nc = K.nc
    n_chunks = N // WCH
    names = "vec_in bias_in silu_done mm_done sum_done " + " ".join(f"w_in{i}" for i in range(RING))
    with ExitStack() as c, phase(nc, names) as (block, S):
        vec = c.enter_context(sbuf(nc, "mod_vec", [P, 2, KD], F32))
        act_vec = c.enter_context(sbuf(nc, "mod_silu", [P, 2, KD], F32))
        w_in = (S["w_in0"], S["w_in1"], S["w_in2"])
        w_rows = w.rearrange("(p k) n -> p k n", k=KD)

        @block.sync
        def _(sp):
            for r in range(2):
                sp.dma_start(vec[:, r, :], vectors[r].rearrange("(p k) -> p k", k=KD)).then_inc(S["vec_in"], 16)
                sp.dma_start(row[r:r + 1, 0:N], b.rearrange("(a n) -> a n", a=1)).then_inc(S["bias_in"], 16)
            for n in range(n_chunks):
                if n >= RING:
                    sp.wait_ge(S["mm_done"], n - RING + 1)
                sp.dma_start(K.wring[:, n % RING, :, :], w_rows[:, :, n * WCH:(n + 1) * WCH])\
                    .then_inc(w_in[n % RING], 16)

        @block.scalar
        def _(act):
            act.wait_ge(S["vec_in"], 32)
            act.activation(act_vec[:, :, :], vec[:, :, :], ACT.Silu).then_inc(S["silu_done"], 1)

        @block.tensor
        def _(pe):
            pe.wait_ge(S["silu_done"], 1)
            for n in range(n_chunks):
                pe.wait_ge(w_in[n % RING], 16 * (n // RING + 1))
                if n >= 2:
                    pe.wait_ge(S["sum_done"], n - 1)
                for k in range(KD):
                    mm = pe.matmul(K.bank[n % 2][0:2, :], act_vec[:, :, k], K.wring[:, n % RING, k, :],
                                   start=(k == 0), stop=(k == KD - 1))
                mm.then_inc(S["mm_done"], 1)

        @block.vector
        def _(dve):
            dve.wait_ge(S["bias_in"], 32)
            for n in range(n_chunks):
                part = row[0:2, n * WCH:(n + 1) * WCH]
                dve.wait_ge(S["mm_done"], n + 1)
                dve.tensor_tensor(part, K.bank[n % 2][0:2, :], part, ALU.add).then_inc(S["sum_done"], 1)


def spread(K, row, columns, broadcasts):
    nc = K.nc
    with ExitStack() as c, phase(nc, "sel_a sel_set turned cols_done spread_done copied") as (block, S):
        sel = c.enter_context(sbuf(nc, "row_selector", [2, 2, P], F32))

        @block.gpsimd
        def _(pool):
            pool.memset(sel[:, :, :], 1.0).then_inc(S["sel_a"], 1)
            pool.wait_ge(S["sel_a"], 1)
            pool.affine_select(out=sel[:, :, :], in_=sel[:, :, :], compare_op=ALU.is_equal, fill=0.0, base=0,
                               pattern=[[-1, 2], [0, P]], channel_multiplier=1).then_inc(S["sel_set"], 1)

        @block.tensor
        def _(pe):
            for n, (off, _, _) in enumerate(columns):
                for k in range(KD):
                    mm = pe.matmul(K.bank[0][:, (n * KD + k) * 2:(n * KD + k) * 2 + 2],
                                   row[0:2, off + k * P:off + (k + 1) * P], K.ident[0:2, 0:2],
                                   start=True, stop=True)
            mm.then_inc(S["turned"], 1)
            pe.wait_ge(S["sel_set"], 1)
            m = 0
            for r, off, _ in broadcasts:
                for h in range(D // 512):
                    if m >= 2:
                        pe.wait_ge(S["copied"], m - 1)
                    pe.matmul(K.bank[1 + m % 2][:, :], sel[:, r, :], row[0:2, off + h * 512:off + (h + 1) * 512],
                              start=True, stop=True).then_inc(S["spread_done"], 1)
                    m += 1

        @block.vector
        def _(dve):
            dve.wait_ge(S["turned"], 1)
            for n, (_, gain, dst) in enumerate(columns):
                src = K.bank[0][:, n * KD * 2:(n + 1) * KD * 2].rearrange("p (k r) -> p k r", r=2)
                if gain is None:
                    dve.tensor_copy(dst, src).then_inc(S["cols_done"], 1)
                else:
                    for r in range(2):
                        dve.scalar_tensor_tensor(out=dst[:, :, r], in0=src[:, :, r], scalar=1.0, in1=gain,
                                                 op0=ALU.add, op1=ALU.mult).then_inc(S["cols_done"], 1)

        @block.scalar
        def _(act):
            m = 0
            for _, _, dst in broadcasts:
                for h in range(D // 512):
                    act.wait_ge(S["spread_done"], m + 1)
                    act.activation(dst[:, h * 512:(h + 1) * 512], K.bank[1 + m % 2][:, :], ACT.Copy)\
                        .then_inc(S["copied"], 1)
                    m += 1



def norm_turn(K, tiles, gain, shift, zero_gain_cols=None):
    nc = K.nc
    names = "sq_done rms_done inv_done xn_done turned evac_a evac_b"
    with ExitStack() as c, phase(nc, names) as (block, S):
        junk = c.enter_context(sbuf(nc, "norm_junk", [P, D], F32))
        ssq = c.enter_context(sbuf(nc, "norm_ssq", [P, NT], F32))
        rms = c.enter_context(sbuf(nc, "norm_rms", [P, NT], F32))
        inv = c.enter_context(sbuf(nc, "norm_inv", [P, NT], F32))
        xn = c.enter_context(sbuf(nc, "norm_xn", [P, 2, D], F32))
        N = len(tiles)

        def bank(n, half):
            return K.bank[2 * (n % 2) + half]

        @block.scalar
        def _(act):
            for n, j in enumerate(tiles):
                if n:
                    act.wait_ge(S["sq_done"], n)
                act.activation(junk[:, :], K.X[:, j, :], ACT.Square, accum_out=ssq[:, n:n + 1]).then_inc(S["sq_done"], 1)
            act.wait_ge(S["sq_done"], N)
            act.activation(rms[:, 0:N], ssq[:, 0:N], ACT.Sqrt, bias=K.eps[:, :], scale=1.0 / D).then_inc(S["rms_done"], 1)
            for n, j in enumerate(tiles):
                r = int(j < JC)
                act.wait_ge(S["turned"], n + 1)
                for k in range(KD // 2):
                    last = act.activation(K.hT[:, k, j * P:(j + 1) * P], bank(n, 0)[:, k * P:(k + 1) * P],
                                          ACT.Identity, bias=shift[:, k, r:r + 1], scale=gain[:, k, r:r + 1])
                last.then_inc(S["evac_a"], 1)

        @block.vector
        def _(dve):
            dve.wait_ge(S["rms_done"], 1)
            dve.reciprocal(inv[:, 0:N], rms[:, 0:N]).then_inc(S["inv_done"], 1)
            dve.wait_ge(S["inv_done"], 1)

            def scale(n):
                if n >= 2:
                    dve.wait_ge(S["turned"], n - 1)
                dve.tensor_scalar(xn[:, n % 2, :], K.X[:, tiles[n], :], inv[:, n:n + 1], None, ALU.mult)\
                    .then_inc(S["xn_done"], 1)

            scale(0)
            for n, j in enumerate(tiles):
                if n + 1 < N:
                    scale(n + 1)
                r = int(j < JC)
                dve.wait_ge(S["turned"], n + 1)
                for k in range(KD // 2, KD):
                    q = k - KD // 2
                    last = dve.tensor_scalar(K.hT[:, k, j * P:(j + 1) * P], bank(n, 1)[:, q * P:(q + 1) * P],
                                             gain[:, k, r:r + 1], shift[:, k, r:r + 1], ALU.mult, ALU.add)
                last.then_inc(S["evac_b"], 1)

        @block.tensor
        def _(pe):
            for n in range(N):
                pe.wait_ge(S["xn_done"], n + 1)
                if n >= 2:
                    pe.wait_ge(S["evac_a"], n - 1)
                    pe.wait_ge(S["evac_b"], n - 1)
                for k in range(KD):
                    half, q = divmod(k, KD // 2)
                    tr = pe.transpose(bank(n, half)[:, q * P:(q + 1) * P], xn[:, n % 2, k * P:(k + 1) * P], K.ident)
                tr.then_inc(S["turned"], 1)



UC, UX = TC + 2 * (TAPS // 2), TX + 2 * (TAPS // 2)


def mixer_inputs(K, I, C, zT, cfa, cfs, ba):
    nc = K.nc
    w = I["w_in"][0].rearrange("(k p) n -> p k n", p=P)
    off_z, off_ba = QKV, QKV + H1 * DK
    off_cf = off_ba + 16
    loads = [(0, 512), (512, 512), (1024, 512), (off_z, 512), (off_cf, 512), (off_cf + 512, 512), (off_ba, 16)]
    names = ("pads mm_x mm_c qkv_out conv_x conv_c silu_done plain_out ba_turned ba_out "
             + " ".join(f"w_in{i}" for i in range(RING)) + " tap_c tap_x")
    NU = 3
    with ExitStack() as c, phase(nc, names) as (block, S):
        w_in = (S["w_in0"], S["w_in1"], S["w_in2"])
        U = c.enter_context(sbuf(nc, "conv_in", [P, NU, UC + UX], F32))
        baT = c.enter_context(sbuf(nc, "baT", [16, TT], F32))
        PAD = TAPS // 2
        n_plain = NCF * 3

        @block.sync
        def _(sp):
            for n, (off, cols) in enumerate(loads):
                if n >= RING:
                    sp.wait_ge(S["mm_x"], 4 * (n - RING + 1))
                sp.dma_start(K.wring[:, n % RING, :, 0:cols], w[:, :, off:off + cols]).then_inc(w_in[n % RING], 16)

        @block.tensor
        def _(pe):
            for f in range(NQKV + n_plain):
                n, m = divmod(f, 4)
                if m == 0:
                    pe.wait_ge(w_in[n % RING], 16 * (n // RING + 1))
                if f >= 4:
                    if f - 4 < NQKV:
                        pe.wait_ge(S["qkv_out"], f - 3)
                    else:
                        pe.wait_ge(S["plain_out"], f - 3 - NQKV)
                if f < NQKV:
                    for k in range(KD):
                        mm = pe.matmul(K.bank[2 * (f % 4) + 1][:, 0:TC], K.wring[:, n % RING, k, m * P:(m + 1) * P],
                                       K.hT[:, k, 0:TC], start=(k == 0), stop=(k == KD - 1))
                    mm.then_inc(S["mm_c"], 1)
                for k in range(KD):
                    mm = pe.matmul(K.bank[2 * (f % 4)][:, :], K.wring[:, n % RING, k, m * P:(m + 1) * P],
                                   K.hT[:, k, TC:TT], start=(k == 0), stop=(k == KD - 1))
                mm.then_inc(S["mm_x"], 1)
            n = len(loads) - 1
            pe.wait_ge(w_in[n % RING], 16 * (n // RING + 1))
            pe.wait_ge(S["plain_out"], n_plain)
            for b0, t0, t1 in ((0, 0, TC), (1, TC, TT)):
                for k in range(KD):
                    mm = pe.matmul(K.bank[b0][0:16, 0:t1 - t0], K.wring[:, n % RING, k, 0:16], K.hT[:, k, t0:t1],
                                   start=(k == 0), stop=(k == KD - 1))
            mm.then_inc(S["mm_x"], 1)
            pe.wait_ge(S["plain_out"], n_plain + 2)
            for j in range(NT):
                tr = pe.transpose(K.bank[2][:, j * 16:(j + 1) * 16], baT[:, j * P:(j + 1) * P], K.ident[0:16, 0:16])
            tr.then_inc(S["ba_turned"], 1)

        @block.gpsimd
        def _(pool):
            for a, b in ((0, PAD), (PAD + TC, UC), (UC, UC + PAD), (UC + PAD + TX, UC + UX)):
                pool.memset(U[:, :, a:b], 0.0).then_inc(S["pads"], 1)

        @block.scalar
        def _(act):
            def silu(f):
                act.wait_ge(S["conv_c"], f + 1)
                act.wait_ge(S["conv_x"], f + 1)
                act.activation(C[:, f, :], C[:, f, :], ACT.Silu).then_inc(S["silu_done"], 1)

            for f in range(NQKV):
                if f >= NU:
                    act.wait_ge(S["conv_c"], f - NU + 1)
                    act.wait_ge(S["conv_x"], f - NU + 1)
                act.wait_ge(S["mm_c"], f + 1)
                act.wait_ge(S["mm_x"], f + 1)
                act.activation(U[:, f % NU, PAD:PAD + TC], K.bank[2 * (f % 4) + 1][:, 0:TC], ACT.Copy)
                act.activation(U[:, f % NU, UC + PAD:UC + PAD + TX], K.bank[2 * (f % 4)][:, :], ACT.Copy)\
                    .then_inc(S["qkv_out"], 1)
                if f >= 2:
                    silu(f - 2)
            for f in range(NQKV - 2, NQKV):
                silu(f)
            for m in range(n_plain):
                f = NQKV + m
                act.wait_ge(S["mm_x"], f + 1)
                which, q = divmod(m, NCF)
                dst, func = ((zT, ACT.Silu), (cfa, ACT.Copy), (cfs, ACT.Sigmoid))[which]
                act.activation(dst[:, q, :], K.bank[2 * (f % 4)][:, :], func).then_inc(S["plain_out"], 1)
            act.wait_ge(S["mm_x"], NQKV + n_plain + 1)
            act.activation(baT[:, 0:TC], K.bank[0][0:16, 0:TC], ACT.Copy).then_inc(S["plain_out"], 1)
            act.activation(baT[:, TC:TT], K.bank[1][0:16, :], ACT.Copy).then_inc(S["plain_out"], 1)

        @block.vector
        def _(dve):
            dve.wait_ge(S["pads"], 4)
            tap_done = (S["tap_c"], S["tap_x"])
            for f in range(NQKV):
                dve.wait_ge(S["qkv_out"], f + 1)
                for tap in range(TAPS):
                    col = WHERE_B["dn_conv_w"] + tap * NQKV + f
                    wt = K.colB[:, col:col + 1]
                    for seg, (u0, c0, n, done) in enumerate(((0, 0, TC, S["conv_c"]), (UC, TC, TX, S["conv_x"]))):
                        src, dst = U[:, f % NU, u0 + tap:u0 + tap + n], C[:, f, c0:c0 + n]
                        if tap == 0:
                            ins = dve.tensor_scalar(dst, src, wt, None, ALU.mult)
                        else:
                            dve.wait_ge(tap_done[seg], f * (TAPS - 1) + tap)
                            ins = dve.scalar_tensor_tensor(out=dst, in0=src, scalar=wt, in1=dst,
                                                           op0=ALU.mult, op1=ALU.add)
                        ins.then_inc(done if tap == TAPS - 1 else tap_done[seg], 1)
            dve.wait_ge(S["ba_turned"], 1)
            dve.tensor_copy(ba, K.bank[2][:, 0:NT * 16].rearrange("p (j n) -> p j n", n=16)).then_inc(S["ba_out"], 1)

def qk_norm(K, C):
    nc = K.nc
    N = 2 * H1
    with ExitStack() as c, phase(nc, "sq_done sum_done len_done inv_done scaled") as (block, S):
        sq = c.enter_context(sbuf(nc, "qk_sq", [P, 2, TT], F32))
        ln = c.enter_context(sbuf(nc, "qk_len", [P, 2, TT], F32))
        inv = c.enter_context(sbuf(nc, "qk_inv", [P, 2, TT], F32))
        parts = ((0, 0, 512), (1, 512, TT))

        @block.scalar
        def _(act):
            def square(f):
                if f >= 2:
                    act.wait_ge(S["sum_done"], f - 1)
                act.activation(sq[:, f % 2, :], C[:, f, :], ACT.Square).then_inc(S["sq_done"], 1)

            square(0)
            for f in range(N):
                if f + 1 < N:
                    square(f + 1)
                act.wait_ge(S["sum_done"], f + 1)
                if f >= 2:
                    act.wait_ge(S["inv_done"], f - 1)
                for b, t0, t1 in parts:
                    last = act.activation(ln[:, f % 2, t0:t1], K.bank[2 * (f % 2) + b][:, 0:t1 - t0], ACT.Sqrt,
                                          bias=K.eps[:, :])
                last.then_inc(S["len_done"], 1)

        @block.tensor
        def _(pe):
            for f in range(N):
                pe.wait_ge(S["sq_done"], f + 1)
                if f >= 2:
                    pe.wait_ge(S["len_done"], f - 1)
                for b, t0, t1 in parts:
                    mm = pe.matmul(K.bank[2 * (f % 2) + b][:, 0:t1 - t0], K.ones, sq[:, f % 2, t0:t1],
                                   start=True, stop=True)
                mm.then_inc(S["sum_done"], 1)

        @block.vector
        def _(dve):
            for f in range(N):
                dve.wait_ge(S["len_done"], f + 1)
                if f >= 2:
                    dve.wait_ge(S["scaled"], f - 1)
                dve.reciprocal(inv[:, f % 2, :], ln[:, f % 2, :]).then_inc(S["inv_done"], 1)
                dve.wait_ge(S["inv_done"], f + 1)
                dve.scalar_tensor_tensor(out=C[:, f, :], in0=inv[:, f % 2, :],
                                         scalar=DK ** -0.5 if f < H1 else 1.0, in1=C[:, f, :],
                                         op0=ALU.mult, op1=ALU.mult).then_inc(S["scaled"], 1)


def turn_back(K, sources, destinations):
    nc = K.nc
    with phase(nc, "turned_a turned_b out_a out_b") as (block, S):
        @block.tensor
        def _(pe):
            for n, src in enumerate(sources):
                for lo, hi, b, turned, out in ((0, 4, 0, S["turned_a"], S["out_a"]), (4, NT, 1, S["turned_b"], S["out_b"])):
                    if n >= 2:
                        pe.wait_ge(out, n - 1)
                    for j in range(lo, hi):
                        tr = pe.transpose(K.bank[2 * (n % 2) + b][:, (j - lo) * P:(j - lo + 1) * P],
                                          src[:, j * P:(j + 1) * P], K.ident)
                    tr.then_inc(turned, 1)

        @block.scalar
        def _(act):
            for n, dst in enumerate(destinations):
                act.wait_ge(S["turned_a"], n + 1)
                act.activation(dst[:, 0:4, :], K.bank[2 * (n % 2)][:, :].rearrange("p (j n) -> p j n", n=P),
                               ACT.Copy).then_inc(S["out_a"], 1)

        @block.vector
        def _(dve):
            for n, dst in enumerate(destinations):
                dve.wait_ge(S["turned_b"], n + 1)
                dve.tensor_copy(dst[:, 4:NT, :], K.bank[2 * (n % 2) + 1][:, 0:(NT - 4) * P]
                                .rearrange("p (j n) -> p j n", n=P)).then_inc(S["out_b"], 1)


def conformer(K, cfa, cfs, cfT):
    nc = K.nc
    names = "glu tap conv_done sum1 centred sq_done sum2 rms_done inv_done normed out_done"
    with ExitStack() as c, phase(nc, names) as (block, S):
        y = c.enter_context(sbuf(nc, "cf_glu", [P, NCF, TX], F32))
        z = c.enter_context(sbuf(nc, "cf_conv", [P, NCF, TX], F32))
        rms = c.enter_context(sbuf(nc, "cf_rms", [P, TX], F32))
        inv = c.enter_context(sbuf(nc, "cf_inv", [P, TX], F32))

        def col(name, n):
            return K.colA[:, WHERE_A[name] + n:WHERE_A[name] + n + 1]

        @block.vector
        def _(dve):
            step = Chain(dve, S["tap"])
            for m in range(NCF):
                dve.tensor_tensor(y[:, m, :], cfa[:, m, :], cfs[:, m, :], ALU.mult).then_inc(S["glu"], 1)
                dve.wait_ge(S["glu"], m + 1)
                step(dve.tensor_scalar(z[:, m, :], y[:, m, :], col("cf_dw_w", HALO * NCF + m), col("cf_dw_b", m),
                                       ALU.mult, ALU.add))
                for d in range(-HALO, HALO + 1):
                    if d == 0:
                        continue
                    lo, hi = max(0, -d) * GRID_W, (ROWS - max(0, d)) * GRID_W
                    ins = dve.scalar_tensor_tensor(
                        out=z[:, m, lo:hi], in0=y[:, m, lo + d * GRID_W:hi + d * GRID_W],
                        scalar=col("cf_dw_w", (HALO + d) * NCF + m), in1=z[:, m, lo:hi], op0=ALU.mult, op1=ALU.add)
                    if d == HALO:
                        ins.then_inc(S["conv_done"], 1)
                    else:
                        step(ins)
            dve.wait_ge(S["conv_done"], NCF)
            dve.wait_ge(S["sum1"], 1)
            for m in range(NCF):
                dve.scalar_tensor_tensor(out=z[:, m, :], in0=K.bank[0][:, :], scalar=-1.0 / CFC, in1=z[:, m, :],
                                         op0=ALU.mult, op1=ALU.add).then_inc(S["centred"], 1)
            dve.wait_ge(S["rms_done"], 1)
            dve.reciprocal(inv[:, :], rms[:, :]).then_inc(S["inv_done"], 1)
            dve.wait_ge(S["inv_done"], 1)
            for m in range(NCF):
                dve.tensor_tensor(z[:, m, :], z[:, m, :], inv[:, :], ALU.mult).then_inc(S["normed"], 1)

        @block.tensor
        def _(pe):
            for m in range(NCF):
                pe.wait_ge(S["conv_done"], m + 1)
                mm = pe.matmul(K.bank[0][:, :], K.ones, z[:, m, :], start=(m == 0), stop=(m == NCF - 1))
            mm.then_inc(S["sum1"], 1)
            for m in range(NCF):
                pe.wait_ge(S["sq_done"], m + 1)
                mm = pe.matmul(K.bank[1][:, :], K.ones, y[:, m, :], start=(m == 0), stop=(m == NCF - 1))
            mm.then_inc(S["sum2"], 1)

        @block.scalar
        def _(act):
            for m in range(NCF):
                act.wait_ge(S["centred"], m + 1)
                act.activation(y[:, m, :], z[:, m, :], ACT.Square).then_inc(S["sq_done"], 1)
            act.wait_ge(S["sum2"], 1)
            act.activation(rms[:, :], K.bank[1][:, :], ACT.Sqrt, bias=K.eps[:, :], scale=1.0 / CFC)\
                .then_inc(S["rms_done"], 1)
            for m in range(NCF):
                act.wait_ge(S["normed"], m + 1)
                act.activation(cfT[:, m, :], z[:, m, :], ACT.Silu, bias=col("cf_ln_b", m), scale=col("cf_ln_g", m))\
                    .then_inc(S["out_done"], 1)



def delta_gates(K, I, ba, G):
    nc = K.nc
    with ExitStack() as c, phase(nc, "par_in a_step d_step sums gl_out") as (block, S):
        def buf(name):
            return c.enter_context(sbuf(nc, name, [P, 2, NT, H1], F32))

        par = c.enter_context(sbuf(nc, "gate_par", [P, 2, 2, H1], F32))
        ea = c.enter_context(sbuf(nc, "gate_ea", [P, 2, H1], F32))
        a, b, r, g, gl, t = (buf("gate_" + n) for n in ("a", "b", "r", "g", "gl", "t"))
        W = NT * H1

        @block.sync
        def _(sp):
            for n, src in enumerate((I["dn_a_log"], I["dn_dt_bias"])):
                sp.dma_start(par[:, n, :, :], src[0].partition_broadcast(P)).then_inc(S["par_in"], 16)
            sp.wait_ge(S["par_in"], 32)

        @block.vector
        def _(dve):
            step = Chain(dve, S["d_step"])
            dve.wait_ge(S["par_in"], 32)
            for d in range(2):
                dt = par[:, 1, d:d + 1, :].broadcast_to([P, NT, H1])
                ins = dve.tensor_tensor(a[:, d, :, :], ba[:, :, d * 8 + 4:d * 8 + 8], dt, ALU.add)
                step(ins)
            step(dve.tensor_scalar(b[:, :, :, :], a[:, :, :, :], 0.0, None, ALU.max))
            dve.wait_ge(S["a_step"], 5)
            step(dve.tensor_tensor(b[:, :, :, :], b[:, :, :, :], r[:, :, :, :], ALU.add))
            for d in range(2):
                e = ea[:, d:d + 1, :].broadcast_to([P, NT, H1])
                step(dve.scalar_tensor_tensor(out=g[:, d, :, :], in0=b[:, d, :, :], scalar=-1.0, in1=e,
                                              op0=ALU.mult, op1=ALU.mult))
            dve.wait_ge(S["sums"], 1)
            for d in range(2):
                step(dve.tensor_copy(G["cumg"][:, d, :, :], K.bank[0][:, d * W:(d + 1) * W]
                                     .rearrange("p (j h) -> p j h", h=H1)))
            step(dve.tensor_copy(gl[:, :, :, :], K.bank[1][:, 0:2 * W]
                                 .rearrange("p (d j h) -> p d j h", d=2, h=H1)))
            step(dve.tensor_tensor(t[:, :, :, :], gl[:, :, :, :], G["cumg"][:, :, :, :], ALU.subtract))

        @block.scalar
        def _(act):
            step = Chain(act, S["a_step"])
            act.wait_ge(S["par_in"], 32)
            step(act.activation(ea[:, :, :], par[:, 0, :, :], ACT.Exp))
            act.wait_ge(S["d_step"], 2)
            step(act.activation(r[:, :, :, :], a[:, :, :, :], ACT.Abs))
            step(act.activation(r[:, :, :, :], r[:, :, :, :], ACT.Exp, scale=-1.0))
            step(act.activation(t[:, :, :, :], r[:, :, :, :], ACT.Ln, bias=K.one[:, :]))
            step(act.activation(r[:, :, :, :], t[:, :, :, :], ACT.Copy))
            act.wait_ge(S["d_step"], 9)
            step(act.activation(G["egc"][:, :, :, :], G["cumg"][:, :, :, :], ACT.Exp))
            step(act.activation(G["egl"][:, :, :, :], gl[:, :, :, :], ACT.Exp))
            act.wait_ge(S["d_step"], 10)
            step(act.activation(G["ekd"][:, :, :, :], t[:, :, :, :], ACT.Exp))
            for d in range(2):
                step(act.activation(G["beta"][:, d, :, :], ba[:, :, d * 8:d * 8 + 4], ACT.Sigmoid))

        @block.tensor
        def _(pe):
            pe.wait_ge(S["d_step"], 6)
            for d in range(2):
                gd = g[:, d, :, :].rearrange("p j h -> p (j h)")
                pe.matmul(K.bank[0][:, d * W:(d + 1) * W], K.inc[d], gd, start=True, stop=True)
                mm = pe.matmul(K.bank[1][:, d * W:(d + 1) * W], K.ones, gd, start=True, stop=True)
            mm.then_inc(S["sums"], 1)


class Inverse:

    @staticmethod
    def buffers(K, c, d):
        def buf(name):
            return c.enter_context(sbuf(K.nc, f"inv_{name}{d}", [P, 4, P], F32))
        return buf("X"), buf("Z"), buf("Y")

    MM_COUNT = 1 + 3 * (LEVELS - 2) + 2
    STEP_COUNT = 3 + 3 * (LEVELS - 2) + 2


def tensor_inverses(pe, K, As, bufs, banks, steps, base, mms):
    dirs = range(len(As))
    for d in dirs:
        pe.wait_ge(steps[d], base + 2)
        for h in range(4):
            tr = pe.transpose(banks[d][0][:, h * P:(h + 1) * P], bufs[d][1][:, h, :], K.ident)
        tr.then_inc(mms[d], 1)
    n = base + 3
    for level in range(1, LEVELS):
        for d in dirs:
            pe.wait_ge(steps[d], n)
            for h in range(4):
                m = pe.matmul(banks[d][0][:, h * P:(h + 1) * P], As[d](h), bufs[d][0][:, h, :], start=True, stop=True)
            m.then_inc(mms[d], 1)
        for d in dirs:
            _, Z, Y = bufs[d]
            pe.wait_ge(steps[d], n + 1)
            if level < LEVELS - 1:
                for h in range(4):
                    m = pe.matmul(banks[d][1][:, h * P:(h + 1) * P], Z[:, h, :], Y[:, h, :], start=True, stop=True)
                m.then_inc(mms[d], 1)
            for h in range(4):
                m = pe.matmul(banks[d][2][:, h * P:(h + 1) * P], Y[:, h, :], Z[:, h, :], start=True, stop=True)
            m.then_inc(mms[d], 1)
        n += 3


def vector_inverses(dve, K, As, bufs, banks, steps, mms, before):
    dirs = range(len(As))

    def four(bank):
        return bank[:, :].rearrange("p (h t) -> p h t", h=4)

    for d in dirs:
        steps[d].put(dve.tensor_tensor(bufs[d][1][:, :, :], As[d], K.cross[1 - d][0], ALU.mult))
    for d in dirs:
        Z = bufs[d][1]
        steps[d].wait()
        steps[d].put(dve.tensor_tensor(Z[:, :, :], Z[:, :, :], K.ident4, ALU.add))
    n = before + 1
    for d in dirs:
        dve.wait_ge(mms[d], n)
        steps[d].put(dve.tensor_copy(bufs[d][0][:, :, :], four(banks[d][0])))
    for level in range(1, LEVELS):
        last = level == LEVELS - 1
        for d in dirs:
            dve.wait_ge(mms[d], n + 1)
            steps[d].put(dve.tensor_tensor(bufs[d][2][:, :, :], four(banks[d][0]), K.cross[d][level], ALU.mult))
        for d in dirs:
            X, Z, _ = bufs[d]
            if not last:
                dve.wait_ge(mms[d], n + 2)
                steps[d].put(dve.tensor_tensor(X[:, :, :], four(banks[d][1]), X[:, :, :], ALU.add))
            dve.wait_ge(mms[d], n + (2 if last else 3))
            steps[d].put(dve.tensor_tensor(Z[:, :, :], four(banks[d][2]), Z[:, :, :], ALU.add))
        n += 3
    for d in dirs:
        steps[d].wait()


def delta_step(K, C, Ktok, Vtok, G, O, St, tile_of, with_output):
    nc = K.nc
    names = "st_f st_b mm_f mm_b v_f v_b a_f a_b p_f p_b"
    with ExitStack() as c, phase(nc, names) as (block, S):
        def buf(name, d):
            return c.enter_context(sbuf(nc, f"{name}{d}", [P, 4, P], F32))

        dirs = (0, 1)
        kT, qT, Kd, Bv, Kb = ([buf(n, d) for d in dirs] for n in ("kT", "qT", "kd", "bv", "kb"))
        Dg, Db, Em, BE, QE, LT, IT = ([buf(n, d) for d in dirs] for n in
                                      ("diag_g", "diag_b", "decay", "bdecay", "qdecay", "LT", "intra"))
        inv = [Inverse.buffers(K, c, d) for d in dirs]
        nW, Vn = Dg, Db
        gcj = [c.enter_context(sbuf(nc, f"gates{d}", [P, 5, H1], F32)) for d in dirs]
        bank = [K.bank[4 * d:4 * d + 4] for d in dirs]
        mm = (S["mm_f"], S["mm_b"])
        vs = (S["v_f"], S["v_b"])
        as_ = (S["a_f"], S["a_b"])
        ps = (S["p_f"], S["p_b"])
        GC, BETA, EGC, EKD, EGL = range(5)
        four = lambda b: b[:, :].rearrange("p (h t) -> p h t", h=4)
        wide = lambda d, q: gcj[d][:, q, :].unsqueeze(2).broadcast_to([P, H1, P])

        @block.gpsimd
        def _(pool):
            for d in dirs:
                j = tile_of[d]
                step = Chain(pool, ps[d])
                for q, src in ((GC, G["cumg"]), (BETA, G["beta"]), (EGC, G["egc"]), (EKD, G["ekd"]), (EGL, G["egl"])):
                    step.put(pool.tensor_copy(gcj[d][:, q, :], src[:, d, bass.ds(j, 1), :]
                                              .rearrange("p o h -> p (o h)")))
            for d in dirs:
                pool.wait_ge(ps[d], 5)
                pool.tensor_tensor(Dg[d][:, :, :], K.ident4, wide(d, GC), ALU.mult).then_inc(ps[d], 1)
                pool.tensor_tensor(Db[d][:, :, :], K.ident4, wide(d, BETA), ALU.mult).then_inc(ps[d], 1)
            for d in dirs:
                j = tile_of[d]
                kt = Ktok[:, :, bass.ds(j, 1), :].rearrange("p h o n -> p (h o) n")
                vt = Vtok[:, :, bass.ds(j, 1), :].rearrange("p h o n -> p (h o) n")
                pool.tensor_tensor(Kb[d][:, :, :], kt, wide(d, BETA), ALU.mult).then_inc(ps[d], 1)
                pool.tensor_tensor(Bv[d][:, :, :], vt, wide(d, BETA), ALU.mult).then_inc(ps[d], 1)
                pool.tensor_tensor(Kd[d][:, :, :], kt, wide(d, EKD), ALU.mult).then_inc(ps[d], 1)
                pool.wait_ge(ps[d], 8)
                pool.tensor_tensor(Kb[d][:, :, :], Kb[d][:, :, :], wide(d, EGC), ALU.mult).then_inc(ps[d], 1)
            if with_output:
                for d in dirs:
                    pool.wait_ge(as_[d], 4)
                    pool.tensor_tensor(QE[d][:, :, :], QE[d][:, :, :], qT[d][:, :, :], ALU.mult).then_inc(ps[d], 1)

        @block.scalar
        def _(act):
            for d in dirs:
                j = tile_of[d]
                ts = bass.ds(j * P, P)
                act.activation(kT[d][:, :, :], C[:, H1:2 * H1, ts], ACT.Copy).then_inc(as_[d], 1)
                act.activation(qT[d][:, :, :], C[:, 0:H1, ts], ACT.Copy).then_inc(as_[d], 1)
            for d in dirs:
                act.wait_ge(vs[d], 1)
                act.activation(Em[d][:, :, :], Em[d][:, :, :], ACT.Exp).then_inc(as_[d], 1)
                act.activation(QE[d][:, :, :], four(bank[d][0]), ACT.Exp).then_inc(as_[d], 1)
            for d in dirs:
                act.wait_ge(mm[d], 3 + Inverse.MM_COUNT + 1)
                act.activation(nW[d][:, :, :], four(bank[d][3]), ACT.Copy, scale=-1.0).then_inc(as_[d], 1)

        @block.tensor
        def _(pe):
            for d in dirs:
                pe.wait_ge(ps[d], 7)
                pe.matmul(bank[d][0][:, :], K.ones, Dg[d][:, :, :], start=True, stop=True).then_inc(mm[d], 1)
                pe.matmul(bank[d][1][:, :], K.ones, Db[d][:, :, :], start=True, stop=True).then_inc(mm[d], 1)
                pe.wait_ge(as_[d], 2)
                for h in range(H1):
                    pe.matmul(bank[d][2][:, h * P:(h + 1) * P], kT[d][:, h, :], kT[d][:, h, :], start=True, stop=True)
                for h in range(H1):
                    m = pe.matmul(bank[d][3][:, h * P:(h + 1) * P], kT[d][:, h, :], qT[d][:, h, :],
                                  start=True, stop=True)
                m.then_inc(mm[d], 1)
            for d in dirs:
                pe.wait_ge(as_[d], 4)
            tensor_inverses(pe, K, [lambda h, d=d: LT[d][:, h, :] for d in dirs], inv, bank, vs, 6, mm)
            n = 6 + Inverse.STEP_COUNT
            for d in dirs:
                Z = inv[d][1]
                pe.wait_ge(ps[d], 11)
                pe.wait_ge(vs[d], n)
                for h in range(H1):
                    m = pe.matmul(bank[d][3][:, h * P:(h + 1) * P], Kb[d][:, h, :], Z[:, h, :], start=True, stop=True)
                m.then_inc(mm[d], 1)
                pe.wait_ge(as_[d], 5)
                for h in range(H1):
                    sl = bank[d][0][:, h * P:(h + 1) * P]
                    pe.matmul(sl, Z[:, h, :], Bv[d][:, h, :], start=True, stop=False)
                    m = pe.matmul(sl, nW[d][:, h, :], St[d][:, h, :], start=False, stop=True)
                m.then_inc(mm[d], 1)
                pe.wait_ge(vs[d], n + 1)
                for h in range(H1):
                    m = pe.matmul(bank[d][2][:, h * P:(h + 1) * P], Kd[d][:, h, :], Vn[d][:, h, :],
                                  start=True, stop=True)
                m.then_inc(mm[d], 1)
                if with_output:
                    pe.wait_ge(ps[d], 12)
                    for h in range(H1):
                        sl = bank[d][1][:, h * P:(h + 1) * P]
                        pe.matmul(sl, QE[d][:, h, :], St[d][:, h, :], start=True, stop=False)
                        m = pe.matmul(sl, IT[d][:, h, :], Vn[d][:, h, :], start=False, stop=True)
                    m.then_inc(mm[d], 1)

        @block.vector
        def _(dve):
            steps = [Chain(dve, vs[d]) for d in dirs]
            for d in dirs:
                dve.wait_ge(mm[d], 1)
                dve.wait_ge(ps[d], 5)
                for h in range(H1):
                    ins = dve.tensor_scalar(Em[d][:, h, :], bank[d][0][:, h * P:(h + 1) * P],
                                            gcj[d][:, GC, h:h + 1], 0.0, ALU.subtract, ALU.min)
                steps[d].put(ins)
            for d in dirs:
                step = steps[d]
                dve.wait_ge(as_[d], 4)
                step(dve.tensor_tensor(Em[d][:, :, :], Em[d][:, :, :], K.incl4[d], ALU.mult))
                dve.wait_ge(mm[d], 3)
                step(dve.tensor_tensor(IT[d][:, :, :], four(bank[d][3]), Em[d][:, :, :], ALU.mult))
                step(dve.tensor_tensor(BE[d][:, :, :], four(bank[d][1]), Em[d][:, :, :], ALU.mult))
                step(dve.tensor_tensor(BE[d][:, :, :], BE[d][:, :, :], K.strict4[d], ALU.mult))
                step(dve.tensor_tensor(LT[d][:, :, :], four(bank[d][2]), BE[d][:, :, :], ALU.mult))
            vector_inverses(dve, K, [LT[d][:, :, :] for d in dirs], inv, bank, steps, mm, 3)
            n = 3 + Inverse.MM_COUNT
            for d in dirs:
                step = steps[d]
                dve.wait_ge(mm[d], n + 2)
                step.put(dve.tensor_copy(Vn[d][:, :, :], four(bank[d][0])))
                dve.wait_ge(mm[d], n + 3 + with_output)
                for h in range(H1):
                    ins = dve.scalar_tensor_tensor(out=St[d][:, h, :], in0=St[d][:, h, :],
                                                   scalar=gcj[d][:, EGL, h:h + 1],
                                                   in1=bank[d][2][:, h * P:(h + 1) * P], op0=ALU.mult, op1=ALU.add)
                if with_output:
                    j = tile_of[d] - JC
                    o = O[:, bass.ds(j, 1), :].rearrange("p o n -> p (o n)")
                    ins = dve.tensor_tensor(o, bank[d][1][:, :], o, ALU.add)
                step.put(ins)

def delta_readout(K, O, headsT):
    nc = K.nc
    with ExitStack() as c, phase(nc, "sq_done v_step rms_done turned gated") as (block, S):
        sq = c.enter_context(sbuf(nc, "dr_sq", [P, JX, H1 * DK], F32))
        st = c.enter_context(sbuf(nc, "dr_stats", [P, 3, JX * H1], F32))

        @block.scalar
        def _(act):
            act.activation(sq[:, :, :], O[:, :, :], ACT.Square).then_inc(S["sq_done"], 1)
            act.wait_ge(S["v_step"], 1)
            act.activation(st[:, 1, :], st[:, 0, :], ACT.Sqrt, bias=K.eps[:, :], scale=1.0 / DK).then_inc(S["rms_done"], 1)

        @block.vector
        def _(dve):
            step = Chain(dve, S["v_step"])
            heads = lambda t: t[:, :, :].rearrange("p j (h n) -> p (j h) n", n=DK)
            dve.wait_ge(S["sq_done"], 1)
            step.put(dve.tensor_reduce(st[:, 0, :], heads(sq), AX.X, ALU.add))
            dve.wait_ge(S["rms_done"], 1)
            step(dve.reciprocal(st[:, 2, :], st[:, 1, :]))
            step.put(dve.tensor_tensor(heads(O), heads(O),
                                       st[:, 2, :].unsqueeze(2).broadcast_to([P, JX * H1, DK]), ALU.mult))
            g = K.colA[:, WHERE_A["dn_norm_g"]:WHERE_A["dn_norm_g"] + 1]
            for h in range(H1):
                dve.wait_ge(S["turned"], h + 1)
                dve.scalar_tensor_tensor(out=headsT[:, h, :], in0=K.bank[h][:, :], scalar=g, in1=headsT[:, h, :],
                                         op0=ALU.mult, op1=ALU.mult).then_inc(S["gated"], 1)

        @block.tensor
        def _(pe):
            pe.wait_ge(S["v_step"], 3)
            for h in range(H1):
                for j in range(JX):
                    tr = pe.transpose(K.bank[h][:, j * P:(j + 1) * P], O[:, j, h * DK:(h + 1) * DK], K.ident)
                tr.then_inc(S["turned"], 1)


def output_projection(K, srcT, w, gates, tiles, first_col):
    nc = K.nc
    with ExitStack() as c, phase(nc, "w_in0 w_in1 mm_done gated added") as (block, S):
        wb = c.enter_context(sbuf(nc, "wo", [P, 2, KD, 512], F32))
        t = c.enter_context(sbuf(nc, "wo_gated", [P, 2, 512], F32))
        w_in = (S["w_in0"], S["w_in1"])
        units = [(n, j) for n in range(2) for j in tiles]

        @block.sync
        def _(sp):
            for n in range(2):
                sp.dma_start(wb[:, n, :, :], w.rearrange("(k p) n -> p k n", p=P)[:, :, n * 512:(n + 1) * 512])\
                    .then_inc(w_in[n], 16)

        @block.tensor
        def _(pe):
            for u, (n, j) in enumerate(units):
                pe.wait_ge(w_in[n], 16)
                if u >= 4:
                    pe.wait_ge(S["gated"], u - 3)
                for k in range(KD):
                    mm = pe.matmul(K.bank[u % 4][:, :], srcT[:, k, (j - first_col) * P:(j - first_col + 1) * P],
                                   wb[:, n, k, :], start=(k == 0), stop=(k == KD - 1))
                mm.then_inc(S["mm_done"], 1)

        @block.vector
        def _(dve):
            for u, (n, j) in enumerate(units):
                dve.wait_ge(S["mm_done"], u + 1)
                if u >= 2:
                    dve.wait_ge(S["added"], u - 1)
                x = K.X[:, j, n * 512:(n + 1) * 512]
                dve.tensor_tensor(t[:, u % 2, :], K.bank[u % 4][:, :], gates(j)[:, n * 512:(n + 1) * 512], ALU.mult)\
                    .then_inc(S["gated"], 1)
                dve.wait_ge(S["gated"], u + 1)
                dve.tensor_tensor(x, x, t[:, u % 2, :], ALU.add).then_inc(S["added"], 1)


def final_norm(K, g, tiles, out=None):
    nc = K.nc
    N = len(tiles)
    with ExitStack() as c, phase(nc, "g_in sq_done rms_done v_step normed stored") as (block, S):
        gb = c.enter_context(sbuf(nc, "fn_gain", [P, D], F32))
        junk = c.enter_context(sbuf(nc, "fn_junk", [P, D], F32))
        st = c.enter_context(sbuf(nc, "fn_stats", [P, 3, NT], F32))

        @block.sync
        def _(sp):
            sp.dma_start(gb[:, :], g.partition_broadcast(P)).then_inc(S["g_in"], 16)
            sp.wait_ge(S["g_in"], 16)
            if out is not None:
                for n, j in enumerate(tiles):
                    sp.wait_ge(S["normed"], n + 1)
                    sp.dma_start(out[n * P:(n + 1) * P, :], K.X[:, j, :]).then_inc(S["stored"], 16)
                sp.wait_ge(S["stored"], 16 * N)

        @block.scalar
        def _(act):
            for n, j in enumerate(tiles):
                if n:
                    act.wait_ge(S["sq_done"], n)
                act.activation(junk[:, :], K.X[:, j, :], ACT.Square, accum_out=st[:, 0, n:n + 1]).then_inc(S["sq_done"], 1)
            act.wait_ge(S["sq_done"], N)
            act.activation(st[:, 1, 0:N], st[:, 0, 0:N], ACT.Sqrt, bias=K.eps[:, :], scale=1.0 / D)\
                .then_inc(S["rms_done"], 1)

        @block.vector
        def _(dve):
            step = Chain(dve, S["v_step"])
            dve.wait_ge(S["rms_done"], 1)
            step(dve.reciprocal(st[:, 2, 0:N], st[:, 1, 0:N]))
            dve.wait_ge(S["g_in"], 16)
            for n, j in enumerate(tiles):
                dve.scalar_tensor_tensor(out=K.X[:, j, :], in0=K.X[:, j, :], scalar=st[:, 2, n:n + 1],
                                         in1=gb[:, :], op0=ALU.mult, op1=ALU.mult).then_inc(S["normed"], 1)



def pick(dve, step, values, keep, k, n, bufs):
    top, eq, cnt, run, zero = bufs
    bc = lambda ap: ap.broadcast_to([P, JX, n])
    for j in range(JX):
        step.put(dve.max(top[:, j, :], values[:, j, :]))
    step.wait()
    least = bc(top[:, :, k - 1:k])
    step.put(dve.tensor_tensor(keep, values, least, ALU.is_gt))
    step(dve.tensor_tensor(eq, values, least, ALU.is_equal))
    step.put(dve.tensor_reduce(cnt[:, :], keep, AX.X, ALU.add))
    for j in range(JX):
        step.put(dve.tensor_tensor_scan(run[:, j, :], eq[:, j, :], zero[:, 0:n], 0.0, ALU.add, ALU.add))
    step.wait()
    step(dve.tensor_tensor(run, run, cnt[:, :].unsqueeze(2).broadcast_to([P, JX, n]), ALU.add))
    step(dve.scalar_tensor_tensor(out=eq, in0=run, scalar=k + 0.5, in1=eq, op0=ALU.is_le, op1=ALU.mult))
    step(dve.tensor_tensor(keep, keep, eq, ALU.add))


def router(K, I, wt):
    nc = K.nc
    with ExitStack() as c, phase(nc, "in_done mm_done sig_done v_step") as (block, S):
        buf = lambda name, shape: c.enter_context(sbuf(nc, "rt_" + name, shape, F32))
        rw = buf("w", [P, KD, NE])
        bias = buf("bias", [P, NE])
        sc, sel, kp, eq, run = (buf(n, [P, JX, NE]) for n in ("scores", "sel", "keep", "eq", "run"))
        top2, top = buf("top2", [P, JX * GROUPS, 8]), buf("top", [P, JX, 8])
        gs, gk, geq, grun = (buf(n, [P, JX, GROUPS]) for n in ("gs", "gk", "geq", "grun"))
        cnt, zero, tot = buf("cnt", [P, JX]), buf("zero", [P, NE]), buf("tot", [P, 2, JX])

        @block.sync
        def _(sp):
            sp.dma_start(rw[:, :, :], I["router_w"][0].rearrange("(k p) n -> p k n", p=P)).then_inc(S["in_done"], 16)
            sp.dma_start(bias[:, :], I["router_bias"][0].partition_broadcast(P)).then_inc(S["in_done"], 16)
            sp.wait_ge(S["in_done"], 32)

        @block.tensor
        def _(pe):
            pe.wait_ge(S["in_done"], 32)
            for j in range(JX):
                for k in range(KD):
                    mm = pe.matmul(K.bank[0][:, j * NE:(j + 1) * NE], K.hT[:, k, TC + j * P:TC + (j + 1) * P],
                                   rw[:, k, :], start=(k == 0), stop=(k == KD - 1))
            mm.then_inc(S["mm_done"], 1)

        @block.scalar
        def _(act):
            act.wait_ge(S["mm_done"], 1)
            act.activation(sc[:, :, :], K.bank[0][:, 0:JX * NE].rearrange("p (j e) -> p j e", e=NE), ACT.Sigmoid)\
                .then_inc(S["sig_done"], 1)

        @block.vector
        def _(dve):
            step = Chain(dve, S["v_step"])
            step.put(dve.memset(zero[:, :], 0.0))
            dve.wait_ge(S["sig_done"], 1)
            dve.wait_ge(S["in_done"], 32)
            step(dve.tensor_tensor(sel[:, :, :], sc[:, :, :], bias[:, :].unsqueeze(1).broadcast_to([P, JX, NE]), ALU.add))
            n = NE // GROUPS
            for j in range(JX):
                for g in range(GROUPS):
                    step.put(dve.max(top2[:, j * GROUPS + g, :], sel[:, j, g * n:(g + 1) * n]))
            step.wait()
            t2 = top2[:, :, :].rearrange("p (j g) e -> p j g e", g=GROUPS)
            step(dve.tensor_tensor(gs[:, :, :], t2[:, :, :, 0], t2[:, :, :, 1], ALU.add))
            pick(dve, step, gs[:, :, :], gk[:, :, :], 4, GROUPS, (top, geq[:, :, :], cnt, grun[:, :, :], zero))
            step(dve.tensor_scalar(geq[:, :, :], gk[:, :, :], 1e30, -1e30, ALU.mult, ALU.add))
            for g in range(GROUPS):
                part = sel[:, :, g * n:(g + 1) * n]
                step.put(dve.tensor_tensor(part, part, geq[:, :, g:g + 1].broadcast_to([P, JX, n]), ALU.add))
            step.wait()
            pick(dve, step, sel[:, :, :], kp[:, :, :], 6, NE, (top, eq[:, :, :], cnt, run[:, :, :], zero))
            step(dve.tensor_tensor(sc[:, :, :], sc[:, :, :], kp[:, :, :], ALU.mult))
            step(dve.tensor_reduce(tot[:, 0, :], sc[:, :, :], AX.X, ALU.add))
            step(dve.reciprocal(tot[:, 1, :], tot[:, 0, :]))
            step(dve.scalar_tensor_tensor(out=wt[:, :, :], in0=sc[:, :, :], scalar=2.5,
                                          in1=tot[:, 1, :].unsqueeze(2).broadcast_to([P, JX, NE]),
                                          op0=ALU.mult, op1=ALU.mult))


def load_expert(eng, Wb, s, srcs, sem):
    gate, up, down = srcs
    eng.dma_start(Wb[:, s, 0, :].rearrange("p (k n) -> p k n", n=DE), gate.rearrange("(k p) n -> p k n", p=P))\
        .then_inc(sem, 16)
    eng.dma_start(Wb[:, s, 1, :].rearrange("p (k n) -> p k n", n=DE), up.rearrange("(k p) n -> p k n", p=P))\
        .then_inc(sem, 16)
    eng.dma_start(Wb[:, s, 2, :].rearrange("p (k n) -> p k n", n=D), down.rearrange("(k p) n -> p k n", p=P))\
        .then_inc(sem, 16)


def experts(K, Wb, acc, weights, following):
    nc = K.nc
    N = len(weights)
    names = "in0 in1 up_done silu_done act_done down_done acc_done"
    with ExitStack() as c, phase(nc, names) as (block, S):
        sg = c.enter_context(sbuf(nc, "ex_silu", [P, 2, TX], F32))
        aT = c.enter_context(sbuf(nc, "ex_act", [P, 2, 2, TX], F32))

        @block.sync
        def _(sp):
            if N > 1:
                load_expert(sp, Wb, 1, following[1], S["in1"])
            if following[0] is not None:
                sp.wait_ge(S["down_done"], 8)
                load_expert(sp, Wb, 0, following[0], S["in0"])
                sp.wait_ge(S["in0"], 48)
            if N > 1:
                sp.wait_ge(S["in1"], 48)

        @block.tensor
        def _(pe):
            for s in range(N):
                if s:
                    pe.wait_ge(S["in1"], 48)
                for m in range(2):
                    for which in range(2):
                        if s:
                            pe.wait_ge(S["act_done"], 2 * (s - 1) + m + 1)
                        for k in range(KD):
                            mm = pe.matmul(K.bank[2 * m + which][:, :],
                                           Wb[:, s, which, k * DE + m * P:k * DE + (m + 1) * P],
                                           K.hT[:, k, TC:TT], start=(k == 0), stop=(k == KD - 1))
                        mm.then_inc(S["up_done"], 1)
            for s in range(N):
                pe.wait_ge(S["act_done"], 2 * s + 2)
                for j in range(JX):
                    for n in range(2):
                        u = 8 * s + 2 * j + n
                        if u >= 4:
                            pe.wait_ge(S["acc_done"], u - 3)
                        for m in range(2):
                            mm = pe.matmul(K.bank[4 + u % 4][:, :], aT[:, s, m, j * P:(j + 1) * P],
                                           Wb[:, s, 2, m * D + n * 512:m * D + (n + 1) * 512],
                                           start=(m == 0), stop=(m == 1))
                        mm.then_inc(S["down_done"], 1)

        @block.scalar
        def _(act):
            for s in range(N):
                for m in range(2):
                    if s:
                        act.wait_ge(S["act_done"], 2 * (s - 1) + m + 1)
                    act.wait_ge(S["up_done"], 4 * s + 2 * m + 1)
                    act.activation(sg[:, m, :], K.bank[2 * m][:, :], ACT.Silu).then_inc(S["silu_done"], 1)

        @block.vector
        def _(dve):
            def gated(s):
                for m in range(2):
                    dve.wait_ge(S["silu_done"], 2 * s + m + 1)
                    dve.wait_ge(S["up_done"], 4 * s + 2 * m + 2)
                    dve.tensor_tensor(aT[:, s, m, :], sg[:, m, :], K.bank[2 * m + 1][:, :], ALU.mult)\
                        .then_inc(S["act_done"], 1)

            for s in range(N):
                gated(s)
            for s in range(N):
                for j in range(JX):
                    for n in range(2):
                        u = 8 * s + 2 * j + n
                        if s:
                            dve.wait_ge(S["acc_done"], u - 7)
                        dve.wait_ge(S["down_done"], u + 1)
                        part = acc[:, j, n * 512:(n + 1) * 512]
                        dve.scalar_tensor_tensor(out=part, in0=K.bank[4 + u % 4][:, :], scalar=weights[s](j),
                                                 in1=part, op0=ALU.mult, op1=ALU.add).then_inc(S["acc_done"], 1)


def experts_start(K, I, Wb, acc):
    with phase(K.nc, "in0 zeroed") as (block, S):
        @block.sync
        def _(sp):
            load_expert(sp, Wb, 0, (I["exp_w_gate"][0, 0], I["exp_w_up"][0, 0], I["exp_w_down"][0, 0]), S["in0"])
            sp.wait_ge(S["in0"], 48)

        @block.vector
        def _(dve):
            dve.memset(acc[:, :, :], 0.0).then_inc(S["zeroed"], 1)


def add_experts(K, acc, gate):
    nc = K.nc
    with phase(nc, "gated added") as (block, S):
        @block.vector
        def _(dve):
            for j in range(JX):
                dve.tensor_tensor(acc[:, j, :], acc[:, j, :], gate, ALU.mult).then_inc(S["gated"], 1)
            for j in range(JX):
                dve.wait_ge(S["gated"], j + 1)
                dve.tensor_tensor(K.X[:, JC + j, :], K.X[:, JC + j, :], acc[:, j, :], ALU.add).then_inc(S["added"], 1)


def mixture(K, I):
    nc = K.nc
    with ExitStack() as c:
        sb = lambda name, shape: c.enter_context(sbuf(nc, name, shape, F32))
        wt = sb("expert_weights", [P, JX, NE])
        router(K, I, wt)
        Wb = sb("ex_w", [P, 2, 3, KD * DE])
        acc = sb("ex_acc", [P, JX, D])
        experts_start(K, I, Wb, acc)
        src = lambda e: tuple(a[0][bass.ds(e, 1)].rearrange("o k n -> (o k) n")
                              for a in (I["exp_w_gate"], I["exp_w_up"], I["exp_w_down"]))
        col = lambda e: (lambda j: wt[:, j, bass.ds(e, 1)])
        with nc.Fori(0, NE - 2, 2) as e:
            experts(K, Wb, acc, (col(e), col(e + 1)), (src(e + 2), src(e + 1)))
        shared = (I["sh_w_gate"][0], I["sh_w_up"][0], I["sh_w_down"][0])
        experts(K, Wb, acc, (col(NE - 2), col(NE - 1)), (shared, src(NE - 1)))
        experts(K, Wb, acc, ((lambda j: K.one[:, :]),), (None,))
        add_experts(K, acc, K.gate[:, 1, :])

(R_, V_, KK_, K_, GATE_, BONUS_, KD_, B_, LW_) = (0, 1, 2, 3, 4, 5, 6, 8, 10)
N_RW = 12
DECAY = float(2.718281828459045 ** -0.5)


def rwkv_projections(K, I, rw, tw, ta):
    nc = K.nc
    names = ("edges xx_sum xx_done lerped w_in0 w_in1 w1_in mm_done lora_done evac lora_out "
             "st0 st1 st2 st3")
    dest = (R_, K_, V_, GATE_)
    with ExitStack() as c, phase(nc, names) as (block, S):
        xx = c.enter_context(sbuf(nc, "rp_xx", [P, KD, TT], F32))
        lerp = c.enter_context(sbuf(nc, "rp_lerp", [P, 2, KD, TT], F32))
        wb = c.enter_context(sbuf(nc, "rp_w", [P, 2, KD, 512], F32))
        w1 = c.enter_context(sbuf(nc, "rp_w1", [P, 2, KD, 2 * LORA], F32))
        stage = c.enter_context(sbuf(nc, "rp_stage", [P, 4, 512], F32))
        w_in = (S["w_in0"], S["w_in1"])
        st = (S["st0"], S["st1"], S["st2"], S["st3"])
        units = [(n, half, j) for n in range(4) for half in range(2) for j in range(NT)]

        @block.sync
        def _(sp):
            for a, w in enumerate((I["rwkv_w1_2"], I["rwkv_a1_2"])):
                for d in range(2):
                    sp.dma_start(w1[:, a, :, d * LORA:(d + 1) * LORA], w[0, d].rearrange("(k p) r -> p k r", p=P))\
                        .then_inc(S["w1_in"], 16)
            for u in range(8):
                if u >= 2:
                    sp.wait_ge(S["mm_done"], NT * (u - 1))
                n, half = divmod(u, 2)
                w = I["rwkv_w_in_2"][0, n].rearrange("(k p) n -> p k n", p=P)
                sp.dma_start(wb[:, u % 2, :, :], w[:, :, half * 512:(half + 1) * 512]).then_inc(w_in[u % 2], 16)

        @block.vector
        def _(dve):
            h = K.hT
            for t0, t1 in ((0, TC), (TC, TT)):
                dve.tensor_tensor(xx[:, :, t0 + 1:t1 - 1], h[:, :, t0:t1 - 2], h[:, :, t0 + 2:t1], ALU.add)
                dve.tensor_copy(xx[:, :, t0:t0 + 1], h[:, :, t0 + 1:t0 + 2])
                dve.tensor_copy(xx[:, :, t1 - 1:t1], h[:, :, t1 - 2:t1 - 1]).then_inc(S["xx_sum"], 1)
            dve.wait_ge(S["xx_sum"], 2)
            dve.scalar_tensor_tensor(out=xx[:, :, :], in0=xx[:, :, :], scalar=0.5, in1=h[:, :, :],
                                     op0=ALU.mult, op1=ALU.subtract).then_inc(S["xx_done"], 1)
            dve.wait_ge(S["xx_done"], 1)
            for n in range(6):
                if n in (2, 3, 4):
                    dve.wait_ge(S["mm_done"], 2 * NT * (n - 1))
                if n == 5:
                    dve.wait_ge(S["mm_done"], 2 * NT * 4)
                for k in range(KD):
                    ins = dve.scalar_tensor_tensor(out=lerp[:, n % 2, k, :], in0=xx[:, k, :],
                                                   scalar=K.colC[:, n * KD + k:n * KD + k + 1], in1=h[:, k, :],
                                                   op0=ALU.mult, op1=ALU.add)
                ins.then_inc(S["lerped"], 1)

        @block.tensor
        def _(pe):
            for u, (n, half, j) in enumerate(units):
                if j == 0:
                    pe.wait_ge(S["lerped"], n + 1)
                    pe.wait_ge(w_in[half], 16 * (n + 1))
                if u >= 4:
                    pe.wait_ge(S["evac"], u - 3)
                for k in range(KD):
                    mm = pe.matmul(K.bank[u % 4][:, :], lerp[:, n % 2, k, j * P:(j + 1) * P], wb[:, half, k, :],
                                   start=(k == 0), stop=(k == KD - 1))
                mm.then_inc(S["mm_done"], 1)
            pe.wait_ge(S["w1_in"], 64)
            for a in range(2):
                pe.wait_ge(S["lerped"], 5 + a)
                for b, (t0, t1) in enumerate(((0, TC), (TC, TT))):
                    for k in range(KD):
                        mm = pe.matmul(K.bank[4 + 2 * a + b][:, 0:t1 - t0], w1[:, a, k, :], lerp[:, a, k, t0:t1],
                                       start=(k == 0), stop=(k == KD - 1))
                    mm.then_inc(S["lora_done"], 1)

        @block.scalar
        def _(act):
            def store(u):
                n, half, j = units[u]
                act.wait_ge(S["evac"], u + 1)
                act.dma_start(rw[dest[n], j * P:(j + 1) * P, half * 512:(half + 1) * 512], stage[:, u % 4, :])\
                    .then_inc(st[u % 4], 16)

            for u, (n, half, j) in enumerate(units):
                act.wait_ge(S["mm_done"], u + 1)
                if u >= 4:
                    act.wait_ge(st[u % 4], 16 * (u // 4))
                act.activation(stage[:, u % 4, :], K.bank[u % 4][:, :], ACT.Silu if n == 3 else ACT.Copy)\
                    .then_inc(S["evac"], 1)
                if u:
                    store(u - 1)
            store(len(units) - 1)
            for a in range(2):
                for b, (t0, t1) in enumerate(((0, TC), (TC, TT))):
                    act.wait_ge(S["lora_done"], 2 * a + b + 1)
                    act.activation((tw, ta)[a][:, t0:t1], K.bank[4 + 2 * a + b][:, 0:t1 - t0],
                                   (ACT.Tanh, ACT.Copy)[a]).then_inc(S["lora_out"], 1)
            for q in range(4):
                act.wait_ge(st[q], 16 * (len(units) // 4))


def rwkv_prepare(K, I, rw, tw, ta):
    nc = K.nc
    with ExitStack() as c0:
        sb = lambda name, shape, c: c.enter_context(sbuf(nc, "rq_" + name, shape, F32))
        w0, a0, w2 = sb("w0", [P, 2, D], c0), sb("a0", [P, 2, D], c0), sb("w2", [P, 2, D], c0)
        kk_p, ka_p, rk_p = sb("k_k", [P, D], c0), sb("k_a", [P, D], c0), sb("r_k", [P, D], c0)
        with phase(nc, "in_done") as (block, S):
            @block.sync
            def _(sp):
                for d in range(2):
                    sp.dma_start(w0[:, d, :], I["rwkv_w0_2"][0, d].partition_broadcast(P)).then_inc(S["in_done"], 16)
                    sp.dma_start(a0[:, d, :], I["rwkv_a0_2"][0, d].partition_broadcast(P)).then_inc(S["in_done"], 16)
                sp.dma_start(w2[:, 0, :], I["rwkv_w2_2"][0].rearrange("d r n -> (d r) n")).then_inc(S["in_done"], 16)
                sp.dma_start(w2[:, 1, :], I["rwkv_a2_2"][0].rearrange("d r n -> (d r) n")).then_inc(S["in_done"], 16)
                sp.dma_start(kk_p[:, :], I["rwkv_k_k_2"][0].partition_broadcast(P)).then_inc(S["in_done"], 16)
                sp.dma_start(ka_p[:, :], I["rwkv_k_a_2"][0].partition_broadcast(P)).then_inc(S["in_done"], 16)
                sp.dma_start(rk_p[:, :], I["rwkv_r_k_2"][0].rearrange("h n -> (h n)").partition_broadcast(P))\
                    .then_inc(S["in_done"], 16)
                sp.wait_ge(S["in_done"], 16 * 9)
        kin, rin, vin = sb("k", [P, D], c0), sb("r", [P, D], c0), sb("v", [P, D], c0)
        kk, sq, bon = sb("kk", [P, D], c0), sb("sq", [P, D], c0), sb("bonus", [P, D], c0)
        lw, aa, kd, bb = (sb(n, [P, 2, D], c0) for n in ("lw", "a", "kd", "b"))
        st = sb("stats", [P, 4, H2], c0)
        low = sb("low", [P, 2, P], c0)
        heads = lambda t: t.rearrange("p (h n) -> p h n", n=HD)
        wide = lambda ap: ap.unsqueeze(2).broadcast_to([P, H2, HD])
        with nc.Fori(0, NT) as j:
            with phase(nc, "in_k in_r in_v lowered mm_done v_step a_step p_step stored") as (block, S):
                rows = bass.ds(j * P, P)

                @block.sync
                def _(sp):
                    sp.dma_start(kin[:, :], rw[K_, rows, :]).then_inc(S["in_k"], 16)
                    sp.dma_start(rin[:, :], rw[R_, rows, :]).then_inc(S["in_r"], 16)
                    sp.dma_start(vin[:, :], rw[V_, rows, :]).then_inc(S["in_v"], 16)
                    sp.wait_ge(S["v_step"], 13)
                    sp.dma_start(rw[KK_, rows, :], kk[:, :]).then_inc(S["stored"], 16)
                    for d in range(2):
                        sp.dma_start(rw[LW_ + d, rows, :], lw[:, d, :]).then_inc(S["stored"], 16)
                        sp.dma_start(rw[KD_ + d, rows, :], kd[:, d, :]).then_inc(S["stored"], 16)
                    sp.wait_ge(S["p_step"], 2)
                    for d in range(2):
                        sp.dma_start(rw[B_ + d, rows, :], bb[:, d, :]).then_inc(S["stored"], 16)
                    sp.wait_ge(S["v_step"], 18)
                    sp.dma_start(rw[BONUS_, rows, :], bon[:, :]).then_inc(S["stored"], 16)
                    sp.wait_ge(S["stored"], 16 * 8)

                @block.tensor
                def _(pe):
                    pe.wait_ge(S["lowered"], 2)
                    for a in range(2):
                        for d in range(2):
                            for half in range(2):
                                pe.matmul(K.bank[4 * a + 2 * d + half][:, :], low[d * LORA:(d + 1) * LORA, a, :],
                                          w2[d * LORA:(d + 1) * LORA, a, half * 512:(half + 1) * 512],
                                          start=True, stop=True).then_inc(S["mm_done"], 1)

                @block.scalar
                def _(act):
                    act.activation(low[:, 0, :], tw[:, rows], ACT.Copy).then_inc(S["lowered"], 1)
                    act.activation(low[:, 1, :], ta[:, rows], ACT.Copy).then_inc(S["lowered"], 1)
                    step = Chain(act, S["a_step"])
                    act.wait_ge(S["v_step"], 1)
                    step.put(act.activation(sq[:, :], kk[:, :], ACT.Square))
                    act.wait_ge(S["v_step"], 2)
                    step.put(act.activation(st[:, 1, :], st[:, 0, :], ACT.Sqrt))
                    act.wait_ge(S["v_step"], 4)
                    step.put(act.activation(lw[:, :, :], lw[:, :, :], ACT.Sigmoid))
                    act.wait_ge(S["v_step"], 5)
                    step.put(act.activation(aa[:, :, :], aa[:, :, :], ACT.Sigmoid))

                @block.gpsimd
                def _(pool):
                    for d in range(2):
                        pool.wait_ge(S["v_step"], 8)
                        pool.wait_ge(S["a_step"], 4)
                        pool.tensor_tensor(bb[:, d, :], kk[:, :], aa[:, d, :], ALU.mult).then_inc(S["p_step"], 1)

                @block.vector
                def _(dve):
                    step = Chain(dve, S["v_step"])
                    dve.wait_ge(S["in_k"], 16)
                    step.put(dve.tensor_tensor(kk[:, :], kin[:, :], kk_p[:, :], ALU.mult))
                    dve.wait_ge(S["a_step"], 1)
                    step.put(dve.tensor_reduce(st[:, 0, :], heads(sq[:, :]), AX.X, ALU.add))
                    for a, (dst, base) in enumerate(((lw, w0), (aa, a0))):
                        dve.wait_ge(S["mm_done"], 4 * a + 4)
                        for d in range(2):
                            for half in range(2):
                                part = slice(half * 512, (half + 1) * 512)
                                ins = dve.tensor_tensor(dst[:, d, part], K.bank[4 * a + 2 * d + half][:, :],
                                                        base[:, d, part], ALU.add)
                        step.put(ins)
                        if a == 0:
                            step.put(dve.memset(st[:, 3, :], 0.0))
                    dve.wait_ge(S["a_step"], 2)
                    step(dve.tensor_scalar(st[:, 1, :], st[:, 1, :], 1e-12, None, ALU.max))
                    step(dve.reciprocal(st[:, 2, :], st[:, 1, :]))
                    step.put(dve.tensor_tensor(heads(kk[:, :]), heads(kk[:, :]), wide(st[:, 2, :]), ALU.mult))
                    dve.wait_ge(S["a_step"], 4)
                    step.put(dve.tensor_scalar(lw[:, :, :], lw[:, :, :], -DECAY, None, ALU.mult))
                    for d in range(2):
                        step(dve.scalar_tensor_tensor(out=kd[:, d, :], in0=aa[:, d, :], scalar=1.0, in1=ka_p[:, :],
                                                      op0=ALU.subtract, op1=ALU.mult))
                        step(dve.scalar_tensor_tensor(out=kd[:, d, :], in0=kd[:, d, :], scalar=1.0, in1=kin[:, :],
                                                      op0=ALU.add, op1=ALU.mult))
                    dve.wait_ge(S["in_r"], 16)
                    step(dve.tensor_tensor(bon[:, :], kd[:, 0, :], kd[:, 1, :], ALU.add))
                    step(dve.tensor_tensor(bon[:, :], bon[:, :], rin[:, :], ALU.mult))
                    step(dve.tensor_tensor(bon[:, :], bon[:, :], rk_p[:, :], ALU.mult))
                    step(dve.tensor_reduce(st[:, 3, :], heads(bon[:, :]), AX.X, ALU.add))
                    dve.wait_ge(S["in_v"], 16)
                    step.put(dve.tensor_tensor(heads(bon[:, :]), heads(vin[:, :]), wide(st[:, 3, :]), ALU.mult))


def rwkv_step(K, rw, Y, St, group, tile_of):
    nc = K.nc
    names = "in_f in_b mm_f mm_b v_f v_b a_f a_b p_f p_b st_f st_b"
    W = 4 * HD
    with ExitStack() as c, phase(nc, names) as (block, S):
        dirs = (0, 1)

        def buf(name, shape):
            return [c.enter_context(sbuf(nc, f"rs_{name}", shape, F32)) for _ in dirs]

        IN = buf("in", [P, 6, W])
        E = buf("exps", [P, 3, W])
        TM = buf("tokens", [P, 4, W])
        FM = buf("features", [P, 2, 4, P])
        SC = buf("scores", [P, 4, 4, P])
        em = buf("em", [P, 2, 2])
        S0, Mm = buf("s0", [P, 2, P]), buf("m", [P, 2, P])
        RH, SA, yb = buf("rhs", [P, W]), buf("sa", [P, W]), buf("y", [P, W])
        inv = [Inverse.buffers(K, c, d) for d in dirs]
        bank = [K.bank[4 * d:4 * d + 4] for d in dirs]
        ins_, mm, vs, as_, ps = (S["in_f"], S["in_b"]), (S["mm_f"], S["mm_b"]), (S["v_f"], S["v_b"]), (S["a_f"], S["a_b"]), (S["p_f"], S["p_b"])
        sts = (S["st_f"], S["st_b"])
        M0 = 4 + Inverse.MM_COUNT
        V0 = 8 + Inverse.STEP_COUNT
        pairs = lambda t: t.rearrange("p (q n) -> p q n", q=2)

        @block.sync
        def _(sp):
            for d in dirs:
                rows, cols = bass.ds(tile_of[d] * P, P), bass.ds(group * W, W)
                for n, src in enumerate((R_, V_, KK_, KD_ + d, B_ + d, LW_ + d)):
                    sp.dma_start(IN[d][:, n, :], rw[src, rows, cols]).then_inc(ins_[d], 16)
            for d in dirs:
                sp.wait_ge(as_[d], 8)
                sp.dma_start(Y[d, bass.ds(tile_of[d] * P, P), bass.ds(group * W, W)], yb[d][:, :]).then_inc(sts[d], 16)
            for d in dirs:
                sp.wait_ge(sts[d], 16)

        @block.scalar
        def _(act):
            for d in dirs:
                act.wait_ge(mm[d], 1)
                act.activation(E[d][:, 0, :], bank[d][0][:, 0:W], ACT.Exp).then_inc(as_[d], 1)
                act.activation(E[d][:, 1, :], bank[d][0][:, 0:W], ACT.Exp, scale=-1.0).then_inc(as_[d], 1)
                act.activation(em[d][:, :, :], bank[d][0][:, W:W + 4].rearrange("p (q n) -> p q n", q=2), ACT.Exp)\
                    .then_inc(as_[d], 1)
            for d in dirs:
                act.wait_ge(vs[d], 1)
                act.activation(E[d][:, 2, :], E[d][:, 2, :], ACT.Exp).then_inc(as_[d], 1)
            for d in dirs:
                act.wait_ge(mm[d], 2)
                act.activation(FM[d][:, 0, :, :], bank[d][1][:, :].rearrange("p (a t) -> p a t", a=4), ACT.Copy)\
                    .then_inc(as_[d], 1)
            for d in dirs:
                act.wait_ge(mm[d], 4)
                act.activation(RH[d][:, :], bank[d][3][:, 0:W], ACT.Copy).then_inc(as_[d], 1)
            for d in dirs:
                act.wait_ge(mm[d], M0 + 1)
                act.activation(SA[d][:, :], bank[d][0][:, 0:W], ACT.Copy, scale=-1.0).then_inc(as_[d], 1)
            for d in dirs:
                act.wait_ge(mm[d], M0 + 3)
                act.activation(yb[d][:, :], bank[d][1][:, 0:W], ACT.Copy).then_inc(as_[d], 1)

        @block.gpsimd
        def _(pool):
            for d in dirs:
                pool.wait_ge(ins_[d], 96)
                pool.wait_ge(as_[d], 2)
                for dst, src, e in ((0, 4, 1), (1, 3, 1), (3, 0, 0)):
                    pool.tensor_tensor(TM[d][:, dst, :], IN[d][:, src, :], E[d][:, e, :], ALU.mult).then_inc(ps[d], 1)

        @block.tensor
        def _(pe):
            for d in dirs:
                pe.wait_ge(ins_[d], 96)
                lw = IN[d][:, 5, :]
                pe.matmul(bank[d][0][:, 0:W], K.cum[d], lw, start=True, stop=True)
                for p in range(2):
                    m = pe.matmul(bank[d][0][:, W + 2 * p:W + 2 * p + 2], lw[:, p * P:(p + 1) * P],
                                  K.const[:, MIX_COL + 2 * d:MIX_COL + 2 * d + 2], start=True, stop=True)
                m.then_inc(mm[d], 1)
            for d in dirs:
                pe.wait_ge(ps[d], 3)
                pe.wait_ge(vs[d], 3)
                for p in range(2):
                    for a in range(4):
                        t = pe.transpose(bank[d][1 + p][:, a * P:(a + 1) * P], TM[d][:, a, p * P:(p + 1) * P], K.ident)
                t.then_inc(mm[d], 1)
            for d in dirs:
                pe.wait_ge(as_[d], 5)
                pe.wait_ge(vs[d], 4)
                for h in range(4):
                    p, q = divmod(h, 2)
                    rows = slice(q * HD, (q + 1) * HD)
                    for a in range(2):
                        m = pe.matmul(bank[d][h][:, a * 2 * P:(a + 1) * 2 * P], FM[d][rows, p, a, :],
                                      FM[d][rows, p, 2:4, :], start=True, stop=True)
                m.then_inc(mm[d], 1)
            for d in dirs:
                V = IN[d][:, 1, :]
                pe.wait_ge(vs[d], 8)
                for p in range(2):
                    pe.matmul(bank[d][3][:, p * P:(p + 1) * P], FM[d][:, p, 2, :], S0[d][:, p, :],
                              start=True, stop=False, skip_group_check=True)
                    for h in (2 * p, 2 * p + 1):
                        m = pe.matmul(bank[d][3][:, h * HD:(h + 1) * HD], SC[d][:, h, 2, :], V[:, h * HD:(h + 1) * HD],
                                      start=False, stop=True, skip_group_check=True)
                m.then_inc(mm[d], 1)
            tensor_inverses(pe, K, [lambda h, d=d: SC[d][:, h, 0, :] for d in dirs], inv, bank, vs, 8, mm)
            for d in dirs:
                Z, V = inv[d][1], IN[d][:, 1, :]
                pe.wait_ge(vs[d], V0)
                pe.wait_ge(as_[d], 6)
                for h in range(4):
                    m = pe.matmul(bank[d][0][:, h * HD:(h + 1) * HD], Z[:, h, :], RH[d][:, h * HD:(h + 1) * HD],
                                  start=True, stop=True)
                m.then_inc(mm[d], 1)
            for d in dirs:
                V = IN[d][:, 1, :]
                pe.wait_ge(as_[d], 7)
                for p in range(2):
                    cols = slice(p * P, (p + 1) * P)
                    pe.matmul(bank[d][2][:, cols], TM[d][:, 1, cols], V[:, cols], start=True, stop=False)
                    m = pe.matmul(bank[d][2][:, cols], TM[d][:, 0, cols], SA[d][:, cols], start=False, stop=True)
                m.then_inc(mm[d], 1)
                for p in range(2):
                    pe.matmul(bank[d][1][:, p * P:(p + 1) * P], FM[d][:, p, 3, :], S0[d][:, p, :],
                              start=True, stop=False, skip_group_check=True)
                    for h in (2 * p, 2 * p + 1):
                        hc = slice(h * HD, (h + 1) * HD)
                        pe.matmul(bank[d][1][:, hc], SC[d][:, h, 3, :], V[:, hc],
                                  start=False, stop=False, skip_group_check=True)
                        m = pe.matmul(bank[d][1][:, hc], SC[d][:, h, 1, :], SA[d][:, hc],
                                      start=False, stop=True, skip_group_check=True)
                m.then_inc(mm[d], 1)

        @block.vector
        def _(dve):
            steps = [Chain(dve, vs[d]) for d in dirs]
            for d in dirs:
                step = steps[d]
                dve.wait_ge(ins_[d], 96)
                dve.wait_ge(as_[d], 3)
                step.put(dve.tensor_tensor(E[d][:, 2, :], bank[d][0][:, 0:W], IN[d][:, 5, :], ALU.subtract))
                for p in range(2):
                    ins = dve.tensor_scalar(S0[d][:, p, :], St[d][:, p, :], em[d][:, p, 0:1], None, ALU.mult)
                step.put(ins)
            for d in dirs:
                dve.wait_ge(as_[d], 4)
                steps[d].put(dve.tensor_tensor(TM[d][:, 2, :], IN[d][:, 2, :], E[d][:, 2, :], ALU.mult))
            for d in dirs:
                dve.wait_ge(mm[d], 2)
                steps[d].put(dve.tensor_copy(FM[d][:, 1, :, :], bank[d][2][:, :]
                                             .rearrange("p (a t) -> p a t", a=4)))
            for d in dirs:
                dve.wait_ge(mm[d], 3)
                for h in range(4):
                    steps[d].put(dve.tensor_tensor(
                        SC[d][:, h, :, :].rearrange("p (a b) t -> p a b t", a=2),
                        bank[d][h][:, :].rearrange("p (a b t) -> p a b t", a=2, b=2),
                        K.mask2[d].unsqueeze(1).broadcast_to([P, 2, 2, P]), ALU.mult))
            for d in dirs:
                steps[d].wait()
            vector_inverses(dve, K, [SC[d][:, :, 0, :] for d in dirs], inv, bank, steps, mm, 4)
            for d in dirs:
                step = steps[d]
                dve.wait_ge(mm[d], M0 + 2)
                step(dve.tensor_tensor(Mm[d][:, :, :], pairs(bank[d][2][:, 0:W]), K.same_head, ALU.mult))
                step(dve.tensor_tensor(Mm[d][:, :, :], Mm[d][:, :, :], S0[d][:, :, :], ALU.add))
                for p in range(2):
                    ins = dve.tensor_scalar(St[d][:, p, :], Mm[d][:, p, :], em[d][:, p, 1:2], None, ALU.mult)
                step.put(ins)


def rwkv_readout(K, I, rw, Y, oT):
    nc = K.nc
    with ExitStack() as c0:
        sb = lambda name, shape: c0.enter_context(sbuf(nc, "ro_" + name, shape, F32))
        g, b = sb("g", [P, D]), sb("b", [P, D])
        with phase(nc, "in_done") as (block, S):
            @block.sync
            def _(sp):
                sp.dma_start(g[:, :], I["rwkv_lnx_g_2"][0].partition_broadcast(P)).then_inc(S["in_done"], 16)
                sp.dma_start(b[:, :], I["rwkv_lnx_b_2"][0].partition_broadcast(P)).then_inc(S["in_done"], 16)
                sp.wait_ge(S["in_done"], 32)
        y, y2, bon, gate, sq = (sb(n, [P, D]) for n in ("y", "y2", "bonus", "gate", "sq"))
        st = sb("stats", [P, 4, H2])
        heads = lambda t: t[:, :].rearrange("p (h n) -> p h n", n=HD)
        wide = lambda ap: ap.unsqueeze(2).broadcast_to([P, H2, HD])
        with nc.Fori(0, NT) as j:
            with phase(nc, "in_y in_bonus in_gate v_step sq_done rms_done turned out_a out_b") as (block, S):
                rows = bass.ds(j * P, P)

                @block.sync
                def _(sp):
                    sp.dma_start(y[:, :], Y[0, rows, :]).then_inc(S["in_y"], 16)
                    sp.dma_start(y2[:, :], Y[1, rows, :]).then_inc(S["in_y"], 16)
                    sp.dma_start(bon[:, :], rw[BONUS_, rows, :]).then_inc(S["in_bonus"], 16)
                    sp.dma_start(gate[:, :], rw[GATE_, rows, :]).then_inc(S["in_gate"], 16)
                    sp.wait_ge(S["in_gate"], 16)

                @block.vector
                def _(dve):
                    step = Chain(dve, S["v_step"])
                    dve.wait_ge(S["in_y"], 32)
                    step(dve.tensor_tensor(y[:, :], y[:, :], y2[:, :], ALU.add))
                    step(dve.tensor_reduce(st[:, 0, :], heads(y), AX.X, ALU.add))
                    step(dve.tensor_scalar(st[:, 0, :], st[:, 0, :], 1.0 / HD, None, ALU.mult))
                    step.put(dve.tensor_tensor(heads(y), heads(y), wide(st[:, 0, :]), ALU.subtract))
                    dve.wait_ge(S["sq_done"], 1)
                    step.put(dve.tensor_reduce(st[:, 1, :], heads(sq), AX.X, ALU.add))
                    dve.wait_ge(S["rms_done"], 1)
                    step(dve.reciprocal(st[:, 3, :], st[:, 2, :]))
                    step(dve.tensor_tensor(heads(y), heads(y), wide(st[:, 3, :]), ALU.mult))
                    step(dve.tensor_tensor(y[:, :], y[:, :], g[:, :], ALU.mult))
                    step(dve.tensor_tensor(y[:, :], y[:, :], b[:, :], ALU.add))
                    dve.wait_ge(S["in_bonus"], 16)
                    step(dve.tensor_tensor(y[:, :], y[:, :], bon[:, :], ALU.add))
                    dve.wait_ge(S["in_gate"], 16)
                    step.put(dve.tensor_tensor(y[:, :], y[:, :], gate[:, :], ALU.mult))
                    dve.wait_ge(S["turned"], 1)
                    dve.tensor_copy(oT[:, 4:8, rows], K.bank[1][:, :].rearrange("p (k t) -> p k t", t=P))\
                        .then_inc(S["out_b"], 1)

                @block.scalar
                def _(act):
                    act.wait_ge(S["v_step"], 4)
                    act.activation(sq[:, :], y[:, :], ACT.Square).then_inc(S["sq_done"], 1)
                    act.wait_ge(S["v_step"], 5)
                    act.activation(st[:, 2, :], st[:, 1, :], ACT.Sqrt, bias=K.gneps[:, :], scale=1.0 / HD)\
                        .then_inc(S["rms_done"], 1)
                    act.wait_ge(S["turned"], 1)
                    act.activation(oT[:, 0:4, rows], K.bank[0][:, :].rearrange("p (k t) -> p k t", t=P), ACT.Copy)\
                        .then_inc(S["out_a"], 1)

                @block.tensor
                def _(pe):
                    pe.wait_ge(S["v_step"], 11)
                    for k in range(KD):
                        t = pe.transpose(K.bank[k // 4][:, (k % 4) * P:(k % 4 + 1) * P], y[:, k * P:(k + 1) * P], K.ident)
                    t.then_inc(S["turned"], 1)


def load_context(K, src):
    with phase(K.nc, "x_in") as (block, S):
        @block.sync
        def _(sp):
            sp.dma_start(K.X[:, 0:JC, :], src.rearrange("(j p) n -> p j n", p=P)).then_inc(S["x_in"], 16)
            sp.wait_ge(S["x_in"], 16)


def second_modulation(K, I, layer):
    nc = K.nc
    gain = K.colA[:, WHERE_A["norm_g_2"] + layer * KD:WHERE_A["norm_g_2"] + (layer + 1) * KD]
    with ExitStack() as c:
        K.wring = c.enter_context(sbuf(nc, "weights", [P, RING, KD, WCH], F32))
        row = c.enter_context(sbuf(nc, "mod_row", [2, 3 * D], F32))
        modulation(K, (I["c_2"][0], I["c_ctx_2"]), I["mod_w_2"][layer], I["mod_b_2"][layer], 3 * D, row)
        spread(K, row, [(0, None, K.mods[:, 0, 1, :, :]), (D, gain, K.mods[:, 0, 0, :, :])],
               [(0, 2 * D, K.gate[:, 0, :]), (1, 2 * D, K.gate[:, 1, :])])


def rwkv_layer(K, I, scratch, dbg):
    nc = K.nc
    rw, Y = scratch["rwkv"], scratch["y"]
    load_context(K, I["ctx_2"][0])
    second_modulation(K, I, 0)
    with ExitStack() as c:
        sb = lambda name, shape, s=c: s.enter_context(sbuf(nc, name, shape, F32))
        tw, ta = sb("rwkv_tw", [P, TT]), sb("rwkv_ta", [P, TT])
        with ExitStack() as c2:
            K.hT = sb("hT", [P, KD, TT], c2)
            norm_turn(K, range(NT), K.mods[:, 0, 0, :, :], K.mods[:, 0, 1, :, :])
            dump(K, dbg, "hh0", K.hT[:, :, :])
            rwkv_projections(K, I, rw, tw, ta)
        rwkv_prepare(K, I, rw, tw, ta)
    for n, a in (("p_r", R_), ("p_v", V_), ("p_gate", GATE_)):
        dump(K, dbg, n, rw[a])
    for n, a in (("p_kdir", KD_), ("p_b", B_), ("p_logw", LW_)):
        dump(K, dbg, n, rw[a:a + 2])
    with ExitStack() as c:
        St = [c.enter_context(sbuf(nc, "rwkv_state", [P, 2, P], F32)) for _ in range(2)]
        with nc.Fori(0, H2 // 4) as g:
            with phase(nc, "zeroed") as (block, S):
                @block.vector
                def _(dve):
                    for t in St:
                        dve.memset(t[:, :, :], 0.0).then_inc(S["zeroed"], 1)
            with nc.Fori(0, JC) as i:
                rwkv_step(K, rw, Y, St, g, (i, JC - 1 - i))
            with nc.Fori(0, JX) as i:
                rwkv_step(K, rw, Y, St, g, (i + JC, NT - 1 - i))
    with ExitStack() as c:
        oT = c.enter_context(sbuf(nc, "rwkv_oT", [P, KD, TT], F32))
        rwkv_readout(K, I, rw, Y, oT)
        output_projection(K, oT, I["rwkv_w_out_2"][0], lambda j: K.gate[:, 0 if j >= JC else 1, :], range(NT), 0)
    dump(K, dbg, "xx0", K.X[:, :, :])

NOPE, ROPE = 64, 32
QK = NOPE + ROPE
QL, KVL = 384, 256
NQ, NKV = QL // P, KVL // P
SMALL = QL + KVL + ROPE


def mla_inputs(K, I, qc, kvc, ssq, gT, kT):
    nc = K.nc
    w = I["mla_w_in_2"][0].rearrange("(k p) n -> p k n", p=P)
    units = [(0, j) for j in range(JC, NT)] + [(1, j) for j in range(NT)]
    names = "w_in g_in0 g_in1 rot lat_mm copied squared pe_mm rope1 rope2 pe_out gate_mm gate_out"
    with ExitStack() as c, phase(nc, names) as (block, S):
        ws = c.enter_context(sbuf(nc, "ml_w", [P, KD, SMALL], F32))
        wr = c.enter_context(sbuf(nc, "ml_wrot", [P, KD, ROPE], F32))
        wg = c.enter_context(sbuf(nc, "ml_wg", [P, 2, KD, 512], F32))
        junk = c.enter_context(sbuf(nc, "ml_junk", [P, QL], F32))
        t = c.enter_context(sbuf(nc, "ml_rope", [P, 2, TX], F32))
        g_in = (S["g_in0"], S["g_in1"])

        @block.sync
        def _(sp):
            sp.dma_start(ws[:, :, :], w[:, :, 0:SMALL]).then_inc(S["w_in"], 16)
            for h in range(2):
                sp.dma_start(wg[:, h, :, :], w[:, :, SMALL + h * 512:SMALL + (h + 1) * 512]).then_inc(g_in[h], 16)

        @block.tensor
        def _(pe):
            pe.wait_ge(S["w_in"], 16)
            for u, (which, j) in enumerate(units):
                if u >= 2:
                    pe.wait_ge(S["squared"], u - 1)
                off, n = ((0, QL), (QL, KVL))[which]
                for k in range(KD):
                    mm = pe.matmul(K.bank[u % 2][:, 0:n], K.hT[:, k, j * P:(j + 1) * P], ws[:, k, off:off + n],
                                   start=(k == 0), stop=(k == KD - 1))
                mm.then_inc(S["lat_mm"], 1)
            pe.wait_ge(S["rot"], 1)
            for b, (wt, t0, t1) in enumerate(((ws, 0, TC), (ws, TC, TT), (wr, TC, TT))):
                off = QL + KVL if wt is ws else 0
                for k in range(KD):
                    mm = pe.matmul(K.bank[2 + b][NOPE:QK, 0:t1 - t0], wt[:, k, off:off + ROPE], K.hT[:, k, t0:t1],
                                   start=(k == 0), stop=(k == KD - 1))
            mm.then_inc(S["pe_mm"], 1)
            for m in range(KD):
                if m % 4 == 0:
                    pe.wait_ge(g_in[m // 4], 16)
                if m >= 2:
                    pe.wait_ge(S["gate_out"], m - 1)
                for k in range(KD):
                    mm = pe.matmul(K.bank[6 + m % 2][:, :], wg[:, m // 4, k, (m % 4) * P:(m % 4 + 1) * P],
                                   K.hT[:, k, TC:TT], start=(k == 0), stop=(k == KD - 1))
                mm.then_inc(S["gate_mm"], 1)

        @block.scalar
        def _(act):
            for u, (which, j) in enumerate(units):
                n = (QL, KVL)[which]
                dst = qc[:, j - JC, :] if which == 0 else kvc[:, j, :]
                act.wait_ge(S["lat_mm"], u + 1)
                act.activation(dst, K.bank[u % 2][:, 0:n], ACT.Copy).then_inc(S["copied"], 1)
                if u:
                    act.wait_ge(S["squared"], u)
                act.activation(junk[:, 0:n], K.bank[u % 2][:, 0:n], ACT.Square, accum_out=ssq[:, u:u + 1])\
                    .then_inc(S["squared"], 1)
            for m in range(KD):
                act.wait_ge(S["gate_mm"], m + 1)
                act.activation(gT[:, m, :], K.bank[6 + m % 2][:, :], ACT.Silu).then_inc(S["gate_out"], 1)

        @block.vector
        def _(dve):
            dve.wait_ge(S["w_in"], 16)
            half = ROPE // 2
            pe0 = QL + KVL
            dve.tensor_copy(wr[:, :, 0:half], ws[:, :, pe0 + half:pe0 + ROPE])
            dve.tensor_copy(wr[:, :, half:ROPE], ws[:, :, pe0:pe0 + half]).then_inc(S["rot"], 1)
            dve.wait_ge(S["pe_mm"], 1)
            r = slice(NOPE, QK)
            for s in range(2):
                dve.tensor_copy(kT[r, s, 0:TC], K.bank[2][r, 0:TC]).then_inc(S["pe_out"], 1)
            dve.tensor_tensor(t[r, 0, :], K.bank[3][r, :], K.cos, ALU.mult).then_inc(S["rope1"], 1)
            dve.tensor_tensor(t[r, 1, :], K.bank[4][r, :], K.sin, ALU.mult).then_inc(S["rope1"], 1)
            dve.wait_ge(S["rope1"], 2)
            for s in range(2):
                dve.tensor_tensor(kT[r, s, TC:TT], t[r, 0, :], t[r, 1, :], ALU.add).then_inc(S["pe_out"], 1)


def mla_latents(K, qc, kvc, ssq, qcT, kvT):
    nc = K.nc
    units = [(0, j) for j in range(JX)] + [(1, j) for j in range(NT)]
    NU = len(units)
    with ExitStack() as c, phase(nc, "mean rms_done inv_done normed turned out") as (block, S):
        st = c.enter_context(sbuf(nc, "mn_stats", [P, 2, NU], F32))
        gain = lambda n, k: K.colB[:, WHERE_B[n] + k:WHERE_B[n] + k + 1]

        @block.scalar
        def _(act):
            act.activation(st[:, 0, 0:JX], ssq[:, 0:JX], ACT.Sqrt, bias=K.eps[:, :], scale=1.0 / QL)\
                .then_inc(S["rms_done"], 1)
            act.activation(st[:, 0, JX:NU], ssq[:, JX:NU], ACT.Sqrt, bias=K.eps[:, :], scale=1.0 / KVL)\
                .then_inc(S["rms_done"], 1)

        @block.vector
        def _(dve):
            dve.wait_ge(S["rms_done"], 2)
            dve.reciprocal(st[:, 1, :], st[:, 0, :]).then_inc(S["inv_done"], 1)
            dve.wait_ge(S["inv_done"], 1)
            for u, (which, j) in enumerate(units):
                x = (qc, kvc)[which][:, j, :]
                dve.tensor_scalar(x, x, st[:, 1, u:u + 1], None, ALU.mult).then_inc(S["normed"], 1)
            for u, (which, j) in enumerate(units):
                dve.wait_ge(S["turned"], u + 1)
                dst, name, n = ((qcT, "q_norm", NQ), (kvT, "kv_norm", NKV))[which]
                for k in range(n):
                    ins = dve.tensor_scalar(dst[:, k, j * P:(j + 1) * P], K.bank[u % 4][:, k * P:(k + 1) * P],
                                            gain(name, k), None, ALU.mult)
                ins.then_inc(S["out"], 1)

        @block.tensor
        def _(pe):
            for u, (which, j) in enumerate(units):
                pe.wait_ge(S["normed"], u + 1)
                if u >= 4:
                    pe.wait_ge(S["out"], u - 3)
                for k in range((NQ, NKV)[which]):
                    tr = pe.transpose(K.bank[u % 4][:, k * P:(k + 1) * P], (qc, kvc)[which][:, j, k * P:(k + 1) * P],
                                      K.ident)
                tr.then_inc(S["turned"], 1)


def attention_pair(K, I, pair, qcT, kvT, gT, kT, oT):
    nc = K.nc
    SCALE = float(QK) ** -0.5
    names = ("wq_in wkv_in rot q_mm k_mm v_mm q_out rope k_out v_out sc_mm max_done nb_done exp_done inv_done "
             "norm_done turned pt_a pt_b o_mm o_out")
    with ExitStack() as c, phase(nc, names) as (block, S):
        buf = lambda name, shape: c.enter_context(sbuf(nc, "at_" + name, shape, F32))
        wq = buf("wq", [P, NQ, 2, QK])
        wr = buf("wr", [P, NQ, 2, ROPE])
        wkv = buf("wkv", [P, NKV, 2, 2 * HD])
        qT = buf("qT", [P, 2, TX])
        t = buf("rope", [P, 2, 2, TX])
        V = buf("v", [P, NT, P])
        Pm = buf("p", [P, 8, TT])
        PT = buf("pT", [P, 2, NT, TX])
        st = buf("stats", [P, 4, 8])
        r = slice(NOPE, QK)

        @block.sync
        def _(sp):
            sp.dma_start(wq[:, :, :, :], I["mla_w_qb_2"][0].rearrange("(k p) n -> p k n", p=P)
                         [:, :, bass.ds(pair * 2 * QK, 2 * QK)].rearrange("p k (h n) -> p k h n", h=2))\
                .then_inc(S["wq_in"], 16)
            sp.dma_start(wkv[:, :, :, :], I["mla_w_kvb_2"][0].rearrange("(k p) n -> p k n", p=P)
                         [:, :, bass.ds(pair * 4 * HD, 4 * HD)].rearrange("p k (h n) -> p k h n", h=2))\
                .then_inc(S["wkv_in"], 16)

        @block.tensor
        def _(pe):
            pe.wait_ge(S["wkv_in"], 16)
            for s in range(2):
                for b, (t0, t1) in enumerate(((0, 512), (512, TT))):
                    for k in range(NKV):
                        mm = pe.matmul(K.bank[4 * s + 2 + b][0:NOPE, 0:t1 - t0], wkv[:, k, s, 0:HD], kvT[:, k, t0:t1],
                                       start=(k == 0), stop=(k == NKV - 1))
                mm.then_inc(S["k_mm"], 1)
            pe.wait_ge(S["wq_in"], 16)
            pe.wait_ge(S["rot"], 1)
            for s in range(2):
                for k in range(NQ):
                    pe.matmul(K.bank[4 * s][0:QK, :], wq[:, k, s, :], qcT[:, k, :], start=(k == 0), stop=(k == NQ - 1))
                for k in range(NQ):
                    mm = pe.matmul(K.bank[4 * s + 1][r, :], wr[:, k, s, :], qcT[:, k, :],
                                   start=(k == 0), stop=(k == NQ - 1))
                mm.then_inc(S["q_mm"], 1)
            pe.wait_ge(S["k_out"], 4)
            for j in range(NT):
                for k in range(NKV):
                    mm = pe.matmul(K.bank[2 + j // 4][:, (j % 4) * P:(j % 4 + 1) * P].rearrange("p (h n) -> p h n", h=2),
                                   kvT[:, k, j * P:(j + 1) * P], wkv[:, k, :, HD:2 * HD],
                                   start=(k == 0), stop=(k == NKV - 1))
            mm.then_inc(S["v_mm"], 1)
            for u in range(8):
                s, qt = divmod(u, 4)
                if qt == 0:
                    pe.wait_ge(S["q_out"], 4 if s == 0 else 4)
                    pe.wait_ge(S["v_out"], 2)
                if u >= 4:
                    pe.wait_ge(S["exp_done"], u - 3)
                for b, (t0, t1) in enumerate(((0, 512), (512, TT))):
                    mm = pe.matmul(K.bank[2 * (u % 4) + b][:, 0:t1 - t0], qT[0:QK, s, qt * P:(qt + 1) * P],
                                   kT[0:QK, s, t0:t1], start=True, stop=True)
                mm.then_inc(S["sc_mm"], 1)
            for s in range(2):
                pe.wait_ge(S["exp_done"], 8)
                pe.wait_ge(S["norm_done"], 4 * s + 4)
                for kt in range(NT):
                    n = NT * s + kt
                    if n >= 4:
                        pe.wait_ge((S["pt_a"], S["pt_b"])[n % 2], (n - 4) // 2 + 1)
                    for qt in range(4):
                        tr = pe.transpose(K.bank[n % 4][:, qt * P:(qt + 1) * P], Pm[:, 4 * s + qt, kt * P:(kt + 1) * P],
                                          K.ident)
                    tr.then_inc(S["turned"], 1)
                pe.wait_ge(S["pt_a"], 3 * (s + 1))
                pe.wait_ge(S["pt_b"], 3 * (s + 1))
                for kt in range(NT):
                    mm = pe.matmul(K.bank[4][s * HD:(s + 1) * HD, :], V[:, kt, s * HD:(s + 1) * HD], PT[:, s, kt, :],
                                   start=(kt == 0), stop=(kt == NT - 1))
                mm.then_inc(S["o_mm"], 1)

        @block.scalar
        def _(act):
            for s in range(2):
                act.wait_ge(S["k_mm"], s + 1)
                for b, (t0, t1) in enumerate(((0, 512), (512, TT))):
                    act.activation(kT[0:NOPE, s, t0:t1], K.bank[4 * s + 2 + b][0:NOPE, 0:t1 - t0], ACT.Copy)\
                        .then_inc(S["k_out"], 1)
            act.wait_ge(S["v_mm"], 1)
            act.activation(V[:, 0:4, :], K.bank[2][:, :].rearrange("p (j n) -> p j n", n=P), ACT.Copy)\
                .then_inc(S["v_out"], 1)
            act.activation(V[:, 4:NT, :], K.bank[3][:, 0:(NT - 4) * P].rearrange("p (j n) -> p j n", n=P), ACT.Copy)\
                .then_inc(S["v_out"], 1)
            for u in range(8):
                act.wait_ge(S["nb_done"], u + 1)
                b = 2 * (u % 4)
                act.activation(Pm[:, u, :], K.psum[:, b * 512:b * 512 + TT], ACT.Exp, bias=st[:, 1, u:u + 1],
                               scale=SCALE, accum_out=st[:, 2, u:u + 1]).then_inc(S["exp_done"], 1)
            for n in range(0, 2 * NT, 2):
                s, kt = divmod(n, NT)
                act.wait_ge(S["turned"], n + 1)
                act.activation(PT[:, s, kt, :], K.bank[n % 4][:, :], ACT.Copy).then_inc(S["pt_a"], 1)

        @block.gpsimd
        def _(pool):
            for u in range(8):
                pool.wait_ge(S["inv_done"], u + 1)
                pool.tensor_scalar(Pm[:, u, :], Pm[:, u, :], st[:, 3, u:u + 1], None, ALU.mult).then_inc(S["norm_done"], 1)

        @block.vector
        def _(dve):
            half = ROPE // 2
            dve.wait_ge(S["wq_in"], 16)
            dve.tensor_copy(wr[:, :, :, 0:half], wq[:, :, :, NOPE + half:QK])
            dve.tensor_copy(wr[:, :, :, half:ROPE], wq[:, :, :, NOPE:NOPE + half]).then_inc(S["rot"], 1)
            for s in range(2):
                dve.wait_ge(S["q_mm"], s + 1)
                dve.tensor_copy(qT[0:NOPE, s, :], K.bank[4 * s][0:NOPE, :]).then_inc(S["q_out"], 1)
                dve.tensor_tensor(t[r, s, 0, :], K.bank[4 * s][r, :], K.cos, ALU.mult).then_inc(S["rope"], 1)
                dve.tensor_tensor(t[r, s, 1, :], K.bank[4 * s + 1][r, :], K.sin, ALU.mult).then_inc(S["rope"], 1)
                dve.wait_ge(S["rope"], 2 * s + 2)
                dve.tensor_tensor(qT[r, s, :], t[r, s, 0, :], t[r, s, 1, :], ALU.add).then_inc(S["q_out"], 1)

            def inverse(u):
                dve.wait_ge(S["exp_done"], u + 1)
                dve.reciprocal(st[:, 3, u:u + 1], st[:, 2, u:u + 1]).then_inc(S["inv_done"], 1)

            for u in range(8):
                b = 2 * (u % 4)
                dve.wait_ge(S["sc_mm"], u + 1)
                dve.tensor_reduce(st[:, 0, u:u + 1], K.psum[:, b * 512:b * 512 + TT], AX.X, ALU.max)\
                    .then_inc(S["max_done"], 1)
                dve.wait_ge(S["max_done"], u + 1)
                dve.tensor_scalar(st[:, 1, u:u + 1], st[:, 0, u:u + 1], -SCALE, None, ALU.mult).then_inc(S["nb_done"], 1)
                if u:
                    inverse(u - 1)
            inverse(7)
            for n in range(1, 2 * NT, 2):
                s, kt = divmod(n, NT)
                dve.wait_ge(S["turned"], n + 1)
                dve.tensor_copy(PT[:, s, kt, :], K.bank[n % 4][:, :]).then_inc(S["pt_b"], 1)
            dve.wait_ge(S["o_mm"], 2)
            at = bass.ds(pair, 1)
            dve.tensor_tensor(oT[:, at, :].rearrange("p o n -> p (o n)"), K.bank[4][:, :],
                              gT[:, at, :].rearrange("p o n -> p (o n)"), ALU.mult).then_inc(S["o_out"], 1)


def mla_layer(K, I, dbg):
    nc = K.nc
    second_modulation(K, I, 1)
    with ExitStack() as c:
        sb = lambda name, shape, s=c: s.enter_context(sbuf(nc, name, shape, F32))
        oT, gT = sb("mla_oT", [P, KD, TX]), sb("mla_gate", [P, KD, TX])
        with ExitStack() as c2:
            qcT, kvT = sb("mla_qcT", [P, NQ, TX], c2), sb("mla_kvT", [P, NKV, TT], c2)
            kT = sb("mla_kT", [P, 2, TT], c2)
            with ExitStack() as c3:
                K.hT = sb("hT", [P, KD, TT], c3)
                norm_turn(K, range(NT), K.mods[:, 0, 0, :, :], K.mods[:, 0, 1, :, :])
                dump(K, dbg, "hh1", K.hT[:, :, :])
                qc, kvc = sb("mla_qc", [P, JX, QL], c3), sb("mla_kvc", [P, NT, KVL], c3)
                ssq = sb("mla_ssq", [P, JX + NT], c3)
                mla_inputs(K, I, qc, kvc, ssq, gT, kT)
                mla_latents(K, qc, kvc, ssq, qcT, kvT)
            with nc.Fori(0, H2 // 2) as pair:
                attention_pair(K, I, pair, qcT, kvT, gT, kT, oT)
        output_projection(K, oT, I["mla_w_out_2"][0], lambda j: K.gate[:, 0, :], range(JC, NT), JC)
    dump(K, dbg, "xx1", K.X[:, :, :])

def build(nc, I, out, scratch, dbg=None, stop=None):
    USED.clear()
    K = Kernel()
    K.nc = nc
    with ExitStack() as c:
        def sb(name, shape, stack=c):
            return stack.enter_context(sbuf(nc, name, shape, F32))

        K.const = sb("const", [P, CONST_COLS])
        K.colA, K.colB = sb("param_cols_a", [P, N_A]), sb("param_cols_b", [P, N_B])
        K.colC = sb("param_cols_c", [P, N_C])
        K.eps, K.one, K.gneps = sb("eps", [P, 1]), sb("one", [P, 1]), sb("gneps", [P, 1])
        K.X = sb("tokens", [P, NT, D])
        K.mods = sb("mod_cols", [P, 2, 2, KD, 2])
        K.gate = sb("mod_gate", [P, 2, D])
        K.psum = c.enter_context(nc.psum_tensor("psum", [P, 8 * 512], F32))
        K.bank = [K.psum[:, i * 512:(i + 1) * 512] for i in range(8)]
        part = lambda n: K.const[:, n * P:(n + 1) * P]
        K.ident, K.ones = part(0), part(1)
        K.inc, K.cum = (part(3), part(5)), (part(6), part(7))
        by4 = lambda ap: ap.unsqueeze(1).broadcast_to([P, 4, P])
        K.ident4 = by4(K.ident)
        K.incl4, K.strict4 = (by4(part(3)), by4(part(5))), (by4(part(2)), by4(part(4)))
        K.mask2 = [K.const[:, n * P:(n + 2) * P].rearrange("p (b t) -> p b t", b=2) for n in (2, 4)]
        K.cos = K.const[64:96, ROPE_COL:ROPE_COL + TX]
        K.sin = K.const[64:96, ROPE_COL + TX:ROPE_COL + 2 * TX]
        K.same_head = K.const[:, MIX_COL + 4:].unsqueeze(1).broadcast_to([P, 2, P])
        K.cross = [[by4(K.const[:, CROSS_COL + (d * LEVELS + n) * P:CROSS_COL + (d * LEVELS + n + 1) * P])
                    for n in range(LEVELS)] for d in range(2)]

        load_parameters(K, I)
        if stop != "skip_first":
            first_model(K, I, scratch, dbg, stop)
        if stop == "first":
            with phase(nc, "out_done") as (block, S):
                @block.sync
                def _(sp):
                    sp.dma_start(out.rearrange("o (j p) n -> (o p) j n", p=P), K.X[:, JC:NT, :]).then_inc(S["out_done"], 16)
                    sp.wait_ge(S["out_done"], 16)
            return
        if stop in ("mix", "delta"):
            return
        rwkv_layer(K, I, scratch, dbg)
        mla_layer(K, I, dbg)
        final_norm(K, I["final_g_2"], range(JC, NT), out.rearrange("o t n -> (o t) n"))


def dump(K, dbg, name, ap):
    if dbg is None or name not in dbg:
        return
    with phase(K.nc, "dumped") as (block, S):
        @block.sync
        def _(sp):
            sp.dma_start(dbg[name], ap).then_inc(S["dumped"], 16)
            sp.wait_ge(S["dumped"], 16)


def first_model(K, I, scratch, dbg, stop):
    nc = K.nc
    cols = lambda name, n, off=0: K.colA[:, WHERE_A[name] + off:WHERE_A[name] + off + n]
    with ExitStack() as c1:
        sb = lambda name, shape, stack=c1: stack.enter_context(sbuf(nc, name, shape, F32))
        with ExitStack() as c:
            K.wring = sb("weights", [P, RING, KD, WCH], c)
            row = sb("mod_row", [2, 6 * D], c)
            modulation(K, (I["c"][0], I["c_ctx"]), I["w_mod"][0], I["b_mod"][0], 6 * D, row)
            spread(K, row,
                   [(0, None, K.mods[:, 0, 1, :, :]), (D, cols("g_mix", KD), K.mods[:, 0, 0, :, :]),
                    (3 * D, None, K.mods[:, 1, 1, :, :]), (4 * D, cols("g_ffn", KD), K.mods[:, 1, 0, :, :])],
                   [(0, 2 * D, K.gate[:, 0, :]), (0, 5 * D, K.gate[:, 1, :])])
        headsT = sb("mix_heads", [P, H1 + NCF, TX])
        zT = headsT[:, 0:H1, :]
        cfT = headsT[:, H1:H1 + NCF, :]
        with ExitStack() as c:
            C = sb("conv_out", [P, NQKV, TT], c)
            ba = sb("ba", [P, NT, 16], c)
            with ExitStack() as c2:
                cfa, cfs = sb("cf_a", [P, NCF, TX], c2), sb("cf_s", [P, NCF, TX], c2)
                with ExitStack() as c3:
                    K.hT = sb("hT", [P, KD, TT], c3)
                    K.wring = sb("weights2", [P, RING, KD, WCH], c3)
                    norm_turn(K, range(NT), K.mods[:, 0, 0, :, :], K.mods[:, 0, 1, :, :])
                    dump(K, dbg, "hT", K.hT[:, :, :])
                    mixer_inputs(K, I, C, zT, cfa, cfs, ba[:, :, :])
                conformer(K, cfa, cfs, cfT)
            qk_norm(K, C)
            dump(K, dbg, "C", C[:, :, :])
            dump(K, dbg, "headsT0", headsT[:, :, :])
            Ktok, Vtok = sb("k_tokens", [P, H1, NT, P], c), sb("v_tokens", [P, H1, NT, P], c)
            turn_back(K, [C[:, H1 + n, :] for n in range(2 * H1)],
                      [Ktok[:, h, :, :] for h in range(H1)] + [Vtok[:, h, :, :] for h in range(H1)])
            O = sb("delta_out", [P, JX, H1 * DK], c)
            G = {n: sb("gates_" + n, [P, 2, NT, H1], c) for n in ("cumg", "beta", "egc", "ekd", "egl")}
            delta_gates(K, I, ba, G)
            St = [sb(f"delta_state{d}", [P, H1, P], c) for d in range(2)]
            with phase(nc, "zeroed") as (block, S):
                @block.vector
                def _(dve):
                    for t in (*St, O):
                        dve.memset(t[:, :, :], 0.0).then_inc(S["zeroed"], 1)
            with nc.Fori(0, JC) as i:
                delta_step(K, C, Ktok, Vtok, G, O, St, (i, JC - 1 - i), False)
            with nc.Fori(0, JX) as i:
                delta_step(K, C, Ktok, Vtok, G, O, St, (i + JC, NT - 1 - i), True)
            dump(K, dbg, "O", O[:, :, :])
            if stop == "delta":
                return
            delta_readout(K, O, headsT)
        dump(K, dbg, "headsT", headsT[:, :, :])
        output_projection(K, headsT, I["w_out"][0], lambda j: K.gate[:, 0, :], range(JC, NT), JC)
        dump(K, dbg, "x1", K.X[:, JC:NT, :])
    if stop == "mix":
        return
    with ExitStack() as c:
        K.hT = c.enter_context(sbuf(nc, "hT", [P, KD, TT], F32))
        norm_turn(K, range(JC, NT), K.mods[:, 1, 0, :, :], K.mods[:, 1, 1, :, :])
        mixture(K, I)
    final_norm(K, I["g_final"], range(JC, NT))



INPUTS = ['x', 'c', 'ctx', 'c_ctx', 'w_mod', 'b_mod', 'g_mix', 'g_ffn', 'w_in', 'w_out', 'dn_conv_w', 'dn_a_log',
          'dn_dt_bias', 'dn_norm_g', 'cf_dw_w', 'cf_dw_b', 'cf_ln_g', 'cf_ln_b', 'router_w', 'router_bias',
          'exp_w_gate', 'exp_w_up', 'exp_w_down', 'sh_w_gate', 'sh_w_up', 'sh_w_down', 'g_final', 'c_2', 'ctx_2',
          'c_ctx_2', 'norm_g_2', 'mod_w_2', 'mod_b_2', 'rwkv_mu_2', 'rwkv_w_in_2', 'rwkv_w0_2', 'rwkv_w1_2',
          'rwkv_w2_2', 'rwkv_a0_2', 'rwkv_a1_2', 'rwkv_a2_2', 'rwkv_k_k_2', 'rwkv_k_a_2', 'rwkv_r_k_2',
          'rwkv_lnx_g_2', 'rwkv_lnx_b_2', 'rwkv_w_out_2', 'mla_w_in_2', 'mla_q_norm_g_2', 'mla_w_qb_2',
          'mla_kv_norm_g_2', 'mla_w_kvb_2', 'mla_w_out_2', 'final_g_2']
SCRATCH = {"rwkv": (N_RW, TT, D), "y": (2, TT, D)}


def kernel(**inputs):
    import numpy as np
    import concourse.bacc as bacc
    from concourse.bass_utils import run_bass_kernel_spmd

    nc = bacc.Bacc("TRN2", target_bir_lowering=False, num_devices=1)
    arrays, aps = {}, {}
    for name in INPUTS:
        a = np.ascontiguousarray(inputs[name])
        arrays[f"in_{name}"] = a
        aps[name] = nc.dram_tensor(f"in_{name}", a.shape, mybir.dt.from_np(a.dtype), kind="ExternalInput").ap()
    arrays["in_consts"] = constants()
    aps["consts"] = nc.dram_tensor("in_consts", (P, CONST_COLS), F32, kind="ExternalInput").ap()
    out = nc.dram_tensor("out", (1, TX, D), F32, kind="ExternalOutput").ap()
    scratch = {n: nc.dram_tensor("scratch_" + n, shape, F32, kind="Internal").ap() for n, shape in SCRATCH.items()}
    build(nc, aps, out, scratch)
    r = run_bass_kernel_spmd(nc, [arrays], core_ids=[0])
    return r.results[0]["out"]
```

```python
from contextlib import ExitStack, contextmanager

import concourse.bass as bass
from concourse import mybir

F32 = mybir.dt.float32
ALU = mybir.AluOpType
ACT = mybir.ActivationFunctionType
AX = mybir.AxisListType

P = 128
D = 1024
KD = D // P
TC, TX = 256, 512
NT = (TC + TX) // P
JC = TC // P
JX = TX // P
TT = TC + TX
H1, DK = 4, 128
QKV = 3 * H1 * DK
NQKV = QKV // P
CFC = 512
NCF = CFC // P
TAPS = 7
GRID_W = 64
ROWS = TX // GRID_W
EPS = 1e-6
LEVELS = 7
NE = 64
GROUPS = 8
DE = 256
H2 = 16
HD = 64
LORA = 64


USED = {}


def sbuf(nc, name, shape, dtype):
    USED[name] = USED.get(name, 0) + 1
    return nc.sbuf_tensor(f"{name}_{USED[name]}", shape, dtype)


@contextmanager
def phase(nc, names):
    with ExitStack() as held:
        by_name = {n: held.enter_context(nc.semaphore(n)) for n in names.split()}
        handles = list(by_name.values())
        signals = by_name
        with nc.Block(no_gpsimd_drain=True) as block:
            yield block, signals
        with nc.Block(no_gpsimd_drain=True) as clearing:
            @clearing.sync
            def _(sp):
                nums = sorted(h.num for h in handles)
                if nums[-1] - nums[0] + 1 == len(nums):
                    sp.sem_clear(range(nums[0], nums[-1] + 1))
                else:
                    for h in handles:
                        sp.sem_clear(h)


class Chain:

    def __init__(self, eng, sem):
        self.eng, self.sem, self.n = eng, sem, 0

    def __call__(self, ins):
        self.put(ins)
        self.wait()

    def put(self, ins):
        self.n += 1
        ins.then_inc(self.sem, 1)

    def wait(self, back=0):
        if self.n - back > 0:
            self.eng.wait_ge(self.sem, self.n - back)


class Kernel:
    pass



MASK_NAMES = ["ident", "ones", "strF", "incF", "strB", "incB", "cumF", "cumB"]
ROPE_COL = len(MASK_NAMES) * P
CROSS_COL = ROPE_COL + 2 * TX
MIX_COL = CROSS_COL + 2 * LEVELS * P
SLOT_COL = MIX_COL + 4 + P
TOKEN_COL = SLOT_COL + NE
CONST_COLS = TOKEN_COL + JX


def constants():
    import numpy as np

    t = np.arange(P)
    s_, t_ = t[:, None], t[None, :]
    out = np.zeros((P, CONST_COLS), np.float32)

    def put(n, m):
        out[:, n * P:(n + 1) * P] = m

    put(0, s_ == t_)
    put(1, 1)
    put(2, s_ < t_)
    put(3, s_ <= t_)
    put(4, s_ > t_)
    put(5, s_ >= t_)
    put(6, (s_ <= t_).astype(np.float32) - (s_ < P // 2))
    put(7, (s_ >= t_).astype(np.float32) - (s_ >= P // 2))
    out[:, MIX_COL + 0] = t < P // 2
    out[:, MIX_COL + 1] = t >= P // 2
    out[:, MIX_COL + 2] = t >= P // 2
    out[:, MIX_COL + 3] = t < P // 2
    out[:, MIX_COL + 4:SLOT_COL] = (s_ // HD == t_ // HD)
    out[:, SLOT_COL:TOKEN_COL] = np.arange(NE) * P
    out[:, TOKEN_COL:] = np.arange(JX) * P + t[:, None]
    for d in range(2):
        for level in range(LEVELS):
            b = 1 << level
            m = (s_ // b == t_ // b + 1) & (s_ // (2 * b) == t_ // (2 * b))
            if d:
                m = m.T
            at = CROSS_COL + (d * LEVELS + level) * P
            out[:, at:at + P] = -1.0 * m
    half = 16
    pos = np.arange(TX)
    inv = 1.0 / (10000.0 ** (np.arange(0, half, 2, dtype=np.float32) / half))
    ang = np.concatenate([(pos // GRID_W)[:, None] * inv, (pos % GRID_W)[:, None] * inv], -1)
    cos, sin = np.cos(ang.astype(np.float32)).T, np.sin(ang.astype(np.float32)).T
    out[64:96, ROPE_COL:ROPE_COL + TX] = np.concatenate([cos, cos])
    out[64:96, ROPE_COL + TX:ROPE_COL + 2 * TX] = np.concatenate([-sin, sin])
    return out


def rows_of(spec):
    at, where = 0, {}
    for name, n in spec:
        where[name] = at
        at += n
    return where, at


HALO = ROWS - 1
CF_USED = 2 * HALO + 1
SPEC_A = [("g_mix", KD), ("g_ffn", KD), ("norm_g_2", 2 * KD), ("cf_dw_b", NCF), ("cf_ln_g", NCF),
          ("cf_ln_b", NCF), ("dn_norm_g", 1), ("cf_dw_w", CF_USED * NCF)]
SPEC_B = [("dn_conv_w", TAPS * NQKV), ("q_norm", 3), ("kv_norm", 2)]
WHERE_A, N_A = rows_of(SPEC_A)
WHERE_B, N_B = rows_of(SPEC_B)
N_C = 6 * KD


def load_parameters(K, I):
    nc = K.nc
    cf_used = I["cf_dw_w"][0][15 - HALO:15 + HALO + 1, :].rearrange("j (f p) -> (j f) p", p=P)
    rows_a = {
        "g_mix": I["g_mix"][0].rearrange("(k p) -> k p", p=P),
        "g_ffn": I["g_ffn"][0].rearrange("(k p) -> k p", p=P),
        "norm_g_2": I["norm_g_2"].rearrange("l (k p) -> (l k) p", p=P),
        "cf_dw_b": I["cf_dw_b"][0].rearrange("(k p) -> k p", p=P),
        "cf_ln_g": I["cf_ln_g"][0].rearrange("(k p) -> k p", p=P),
        "cf_ln_b": I["cf_ln_b"][0].rearrange("(k p) -> k p", p=P),
        "dn_norm_g": I["dn_norm_g"],
        "cf_dw_w": cf_used,
    }
    rows_b = {
        "dn_conv_w": I["dn_conv_w"][0].rearrange("j (f p) -> (j f) p", p=P),
        "q_norm": I["mla_q_norm_g_2"][0].rearrange("(k p) -> k p", p=P),
        "kv_norm": I["mla_kv_norm_g_2"][0].rearrange("(k p) -> k p", p=P),
    }
    with ExitStack() as c, phase(nc, "consts_in rows_in turned cols_done x_in eps_set") as (block, S):
        ra = c.enter_context(sbuf(nc, "param_rows_a", [N_A, P], F32))
        rb = c.enter_context(sbuf(nc, "param_rows_b", [N_B, P], F32))
        rc = c.enter_context(sbuf(nc, "param_rows_c", [N_C, P], F32))

        @block.sync
        def _(sp):
            sp.dma_start(K.const[:, :], I["consts"]).then_inc(S["consts_in"], 16)
            sp.dma_start(rc[:, :], I["rwkv_mu_2"][0].rearrange("j (k p) -> (j k) p", p=P)).then_inc(S["rows_in"], 16)
            n = 1
            for where, rows, dst in ((WHERE_A, rows_a, ra), (WHERE_B, rows_b, rb)):
                for name, src in rows.items():
                    sp.dma_start(dst[where[name]:where[name] + src.shape[0], :], src).then_inc(S["rows_in"], 16)
                    n += 1
            sp.dma_start(K.X[:, 0:JC, :], I["ctx"][0].rearrange("(j p) n -> p j n", p=P)).then_inc(S["x_in"], 16)
            sp.dma_start(K.X[:, JC:NT, :], I["x"][0].rearrange("(j p) n -> p j n", p=P)).then_inc(S["x_in"], 16)
            sp.wait_ge(S["x_in"], 32)
            sp.wait_ge(S["rows_in"], 16 * n)

        @block.tensor
        def _(pe):
            pe.wait_ge(S["consts_in"], 16)
            pe.wait_ge(S["rows_in"], 16 * (1 + len(rows_a) + len(rows_b)))
            pe.transpose(K.bank[0][:, 0:N_A], ra[:, :], K.ident[0:N_A, 0:N_A])
            pe.transpose(K.bank[2][:, 0:N_C], rc[:, :], K.ident[0:N_C, 0:N_C])
            pe.transpose(K.bank[1][:, 0:N_B], rb[:, :], K.ident[0:N_B, 0:N_B]).then_inc(S["turned"], 1)

        @block.vector
        def _(dve):
            dve.memset(K.eps[:, :], EPS).then_inc(S["eps_set"], 1)
            dve.memset(K.one[:, :], 1.0).then_inc(S["eps_set"], 1)
            dve.memset(K.zeros[:, :], 0.0).then_inc(S["eps_set"], 1)
            dve.memset(K.gneps[:, :], 64e-5).then_inc(S["eps_set"], 1)
            dve.wait_ge(S["turned"], 1)
            dve.tensor_copy(K.colA[:, :], K.bank[0][:, 0:N_A]).then_inc(S["cols_done"], 1)
            dve.tensor_copy(K.colB[:, :], K.bank[1][:, 0:N_B]).then_inc(S["cols_done"], 1)
            dve.tensor_copy(K.colC[:, :], K.bank[2][:, 0:N_C]).then_inc(S["cols_done"], 1)



WCH = 512
RING = 3


def modulation(K, vectors, w, b, N, row, rows_needed=None):
    nc = K.nc
    n_chunks = N // WCH
    names = "vec_in bias_in silu_done mm_done sum_done " + " ".join(f"w_in{i}" for i in range(RING))
    with ExitStack() as c, phase(nc, names) as (block, S):
        vec = c.enter_context(sbuf(nc, "mod_vec", [P, 2, KD], F32))
        act_vec = c.enter_context(sbuf(nc, "mod_silu", [P, 2, KD], F32))
        w_in = (S["w_in0"], S["w_in1"], S["w_in2"])
        w_rows = w.rearrange("(p k) n -> p k n", k=KD)

        @block.sync
        def _(sp):
            for r in range(2):
                sp.dma_start(vec[:, r, :], vectors[r].rearrange("(p k) -> p k", k=KD)).then_inc(S["vec_in"], 16)
                sp.dma_start(row[r:r + 1, 0:N], b.rearrange("(a n) -> a n", a=1)).then_inc(S["bias_in"], 16)
            for n in range(n_chunks):
                if n >= RING:
                    sp.wait_ge(S["mm_done"], n - RING + 1)
                sp.dma_start(K.wring[:, n % RING, :, :], w_rows[:, :, n * WCH:(n + 1) * WCH])\
                    .then_inc(w_in[n % RING], 16)

        @block.scalar
        def _(act):
            act.wait_ge(S["vec_in"], 32)
            act.activation(act_vec[:, :, :], vec[:, :, :], ACT.Silu).then_inc(S["silu_done"], 1)

        @block.tensor
        def _(pe):
            pe.wait_ge(S["silu_done"], 1)
            for n in range(n_chunks):
                pe.wait_ge(w_in[n % RING], 16 * (n // RING + 1))
                if n >= 2:
                    pe.wait_ge(S["sum_done"], n - 1)
                for k in range(KD):
                    mm = pe.matmul(K.bank[n % 2][0:2, :], act_vec[:, :, k], K.wring[:, n % RING, k, :],
                                   start=(k == 0), stop=(k == KD - 1))
                mm.then_inc(S["mm_done"], 1)

        @block.vector
        def _(dve):
            dve.wait_ge(S["bias_in"], 32)
            for n in range(n_chunks):
                part = row[0:2, n * WCH:(n + 1) * WCH]
                dve.wait_ge(S["mm_done"], n + 1)
                dve.tensor_tensor(part, K.bank[n % 2][0:2, :], part, ALU.add).then_inc(S["sum_done"], 1)


def spread(K, row, columns, broadcasts):
    nc = K.nc
    with ExitStack() as c, phase(nc, "sel_a sel_set turned cols_done spread_done copied") as (block, S):
        sel = c.enter_context(sbuf(nc, "row_selector", [2, 2, P], F32))

        @block.gpsimd
        def _(pool):
            pool.memset(sel[:, :, :], 1.0).then_inc(S["sel_a"], 1)
            pool.wait_ge(S["sel_a"], 1)
            pool.affine_select(out=sel[:, :, :], in_=sel[:, :, :], compare_op=ALU.is_equal, fill=0.0, base=0,
                               pattern=[[-1, 2], [0, P]], channel_multiplier=1).then_inc(S["sel_set"], 1)

        @block.tensor
        def _(pe):
            for n, (off, _, _) in enumerate(columns):
                for k in range(KD):
                    mm = pe.matmul(K.bank[0][:, (n * KD + k) * 2:(n * KD + k) * 2 + 2],
                                   row[0:2, off + k * P:off + (k + 1) * P], K.ident[0:2, 0:2],
                                   start=True, stop=True)
            mm.then_inc(S["turned"], 1)
            pe.wait_ge(S["sel_set"], 1)
            m = 0
            for r, off, _ in broadcasts:
                for h in range(D // 512):
                    if m >= 2:
                        pe.wait_ge(S["copied"], m - 1)
                    pe.matmul(K.bank[1 + m % 2][:, :], sel[:, r, :], row[0:2, off + h * 512:off + (h + 1) * 512],
                              start=True, stop=True).then_inc(S["spread_done"], 1)
                    m += 1

        @block.vector
        def _(dve):
            dve.wait_ge(S["turned"], 1)
            for n, (_, gain, dst) in enumerate(columns):
                src = K.bank[0][:, n * KD * 2:(n + 1) * KD * 2].rearrange("p (k r) -> p k r", r=2)
                if gain is None:
                    dve.tensor_copy(dst, src).then_inc(S["cols_done"], 1)
                else:
                    for r in range(2):
                        dve.scalar_tensor_tensor(out=dst[:, :, r], in0=src[:, :, r], scalar=1.0, in1=gain,
                                                 op0=ALU.add, op1=ALU.mult).then_inc(S["cols_done"], 1)

        @block.scalar
        def _(act):
            m = 0
            for _, _, dst in broadcasts:
                for h in range(D // 512):
                    act.wait_ge(S["spread_done"], m + 1)
                    act.activation(dst[:, h * 512:(h + 1) * 512], K.bank[1 + m % 2][:, :], ACT.Copy)\
                        .then_inc(S["copied"], 1)
                    m += 1



def norm_turn(K, tiles, gain, shift, zero_gain_cols=None):
    nc = K.nc
    names = "sq_done rms_done inv_done xn_done turned evac_a evac_b"
    with ExitStack() as c, phase(nc, names) as (block, S):
        junk = c.enter_context(sbuf(nc, "norm_junk", [P, D], F32))
        ssq = c.enter_context(sbuf(nc, "norm_ssq", [P, NT], F32))
        rms = c.enter_context(sbuf(nc, "norm_rms", [P, NT], F32))
        inv = c.enter_context(sbuf(nc, "norm_inv", [P, NT], F32))
        xn = c.enter_context(sbuf(nc, "norm_xn", [P, 2, D], F32))
        N = len(tiles)

        def bank(n, half):
            return K.bank[2 * (n % 2) + half]

        @block.scalar
        def _(act):
            for n, j in enumerate(tiles):
                if n:
                    act.wait_ge(S["sq_done"], n)
                act.activation(junk[:, :], K.X[:, j, :], ACT.Square, accum_out=ssq[:, n:n + 1]).then_inc(S["sq_done"], 1)
            act.wait_ge(S["sq_done"], N)
            act.activation(rms[:, 0:N], ssq[:, 0:N], ACT.Sqrt, bias=K.eps[:, :], scale=1.0 / D).then_inc(S["rms_done"], 1)
            for n, j in enumerate(tiles):
                r = int(j < JC)
                act.wait_ge(S["turned"], n + 1)
                for k in range(KD // 2):
                    last = act.activation(K.hT[:, k, j * P:(j + 1) * P], bank(n, 0)[:, k * P:(k + 1) * P],
                                          ACT.Identity, bias=shift[:, k, r:r + 1], scale=gain[:, k, r:r + 1])
                last.then_inc(S["evac_a"], 1)

        @block.vector
        def _(dve):
            dve.wait_ge(S["rms_done"], 1)
            dve.reciprocal(inv[:, 0:N], rms[:, 0:N]).then_inc(S["inv_done"], 1)
            dve.wait_ge(S["inv_done"], 1)

            def scale(n):
                if n >= 2:
                    dve.wait_ge(S["turned"], n - 1)
                dve.tensor_scalar(xn[:, n % 2, :], K.X[:, tiles[n], :], inv[:, n:n + 1], None, ALU.mult)\
                    .then_inc(S["xn_done"], 1)

            scale(0)
            for n, j in enumerate(tiles):
                if n + 1 < N:
                    scale(n + 1)
                r = int(j < JC)
                dve.wait_ge(S["turned"], n + 1)
                for k in range(KD // 2, KD):
                    q = k - KD // 2
                    last = dve.tensor_scalar(K.hT[:, k, j * P:(j + 1) * P], bank(n, 1)[:, q * P:(q + 1) * P],
                                             gain[:, k, r:r + 1], shift[:, k, r:r + 1], ALU.mult, ALU.add)
                last.then_inc(S["evac_b"], 1)

        @block.tensor
        def _(pe):
            for n in range(N):
                pe.wait_ge(S["xn_done"], n + 1)
                if n >= 2:
                    pe.wait_ge(S["evac_a"], n - 1)
                    pe.wait_ge(S["evac_b"], n - 1)
                for k in range(KD):
                    half, q = divmod(k, KD // 2)
                    tr = pe.transpose(bank(n, half)[:, q * P:(q + 1) * P], xn[:, n % 2, k * P:(k + 1) * P], K.ident)
                tr.then_inc(S["turned"], 1)



UC, UX = TC + 2 * (TAPS // 2), TX + 2 * (TAPS // 2)


def mixer_inputs(K, I, C, zT, cfa, cfs, ba):
    nc = K.nc
    w = I["w_in"][0].rearrange("(k p) n -> p k n", p=P)
    off_z, off_ba = QKV, QKV + H1 * DK
    off_cf = off_ba + 16
    loads = [(0, 512), (512, 512), (1024, 512), (off_z, 512), (off_cf, 512), (off_cf + 512, 512), (off_ba, 16)]
    names = ("pads mm_x mm_c qkv_out conv_x conv_c silu_done plain_out ba_turned ba_out "
             + " ".join(f"w_in{i}" for i in range(RING)) + " tap_c tap_x")
    NU = 3
    with ExitStack() as c, phase(nc, names) as (block, S):
        w_in = (S["w_in0"], S["w_in1"], S["w_in2"])
        U = c.enter_context(sbuf(nc, "conv_in", [P, NU, UC + UX], F32))
        baT = c.enter_context(sbuf(nc, "baT", [16, TT], F32))
        PAD = TAPS // 2
        n_plain = NCF * 3

        @block.sync
        def _(sp):
            for n, (off, cols) in enumerate(loads):
                if n >= RING:
                    sp.wait_ge(S["mm_x"], 4 * (n - RING + 1))
                sp.dma_start(K.wring[:, n % RING, :, 0:cols], w[:, :, off:off + cols]).then_inc(w_in[n % RING], 16)

        @block.tensor
        def _(pe):
            for f in range(NQKV + n_plain):
                n, m = divmod(f, 4)
                if m == 0:
                    pe.wait_ge(w_in[n % RING], 16 * (n // RING + 1))
                if f >= 4:
                    if f - 4 < NQKV:
                        pe.wait_ge(S["qkv_out"], f - 3)
                    else:
                        pe.wait_ge(S["plain_out"], f - 3 - NQKV)
                if f < NQKV:
                    for k in range(KD):
                        mm = pe.matmul(K.bank[2 * (f % 4) + 1][:, 0:TC], K.wring[:, n % RING, k, m * P:(m + 1) * P],
                                       K.hT[:, k, 0:TC], start=(k == 0), stop=(k == KD - 1))
                    mm.then_inc(S["mm_c"], 1)
                for k in range(KD):
                    mm = pe.matmul(K.bank[2 * (f % 4)][:, :], K.wring[:, n % RING, k, m * P:(m + 1) * P],
                                   K.hT[:, k, TC:TT], start=(k == 0), stop=(k == KD - 1))
                mm.then_inc(S["mm_x"], 1)
            n = len(loads) - 1
            pe.wait_ge(w_in[n % RING], 16 * (n // RING + 1))
            pe.wait_ge(S["plain_out"], n_plain)
            for b0, t0, t1 in ((0, 0, TC), (1, TC, TT)):
                for k in range(KD):
                    mm = pe.matmul(K.bank[b0][0:16, 0:t1 - t0], K.wring[:, n % RING, k, 0:16], K.hT[:, k, t0:t1],
                                   start=(k == 0), stop=(k == KD - 1))
            mm.then_inc(S["mm_x"], 1)
            pe.wait_ge(S["plain_out"], n_plain + 2)
            for j in range(NT):
                tr = pe.transpose(K.bank[2][:, j * 16:(j + 1) * 16], baT[:, j * P:(j + 1) * P], K.ident[0:16, 0:16])
            tr.then_inc(S["ba_turned"], 1)

        @block.gpsimd
        def _(pool):
            for a, b in ((0, PAD), (PAD + TC, UC), (UC, UC + PAD), (UC + PAD + TX, UC + UX)):
                pool.memset(U[:, :, a:b], 0.0).then_inc(S["pads"], 1)

        @block.scalar
        def _(act):
            def silu(f):
                act.wait_ge(S["conv_c"], f + 1)
                act.wait_ge(S["conv_x"], f + 1)
                act.activation(C[:, f, :], C[:, f, :], ACT.Silu).then_inc(S["silu_done"], 1)

            for f in range(NQKV):
                if f >= NU:
                    act.wait_ge(S["conv_c"], f - NU + 1)
                    act.wait_ge(S["conv_x"], f - NU + 1)
                act.wait_ge(S["mm_c"], f + 1)
                act.wait_ge(S["mm_x"], f + 1)
                act.activation(U[:, f % NU, PAD:PAD + TC], K.bank[2 * (f % 4) + 1][:, 0:TC], ACT.Copy)
                act.activation(U[:, f % NU, UC + PAD:UC + PAD + TX], K.bank[2 * (f % 4)][:, :], ACT.Copy)\
                    .then_inc(S["qkv_out"], 1)
                if f >= 2:
                    silu(f - 2)
            for f in range(NQKV - 2, NQKV):
                silu(f)
            for m in range(n_plain):
                f = NQKV + m
                act.wait_ge(S["mm_x"], f + 1)
                which, q = divmod(m, NCF)
                dst, func = ((zT, ACT.Silu), (cfa, ACT.Copy), (cfs, ACT.Sigmoid))[which]
                act.activation(dst[:, q, :], K.bank[2 * (f % 4)][:, :], func).then_inc(S["plain_out"], 1)
            act.wait_ge(S["mm_x"], NQKV + n_plain + 1)
            act.activation(baT[:, 0:TC], K.bank[0][0:16, 0:TC], ACT.Copy).then_inc(S["plain_out"], 1)
            act.activation(baT[:, TC:TT], K.bank[1][0:16, :], ACT.Copy).then_inc(S["plain_out"], 1)

        @block.vector
        def _(dve):
            dve.wait_ge(S["pads"], 4)
            tap_done = (S["tap_c"], S["tap_x"])
            for f in range(NQKV):
                dve.wait_ge(S["qkv_out"], f + 1)
                for tap in range(TAPS):
                    col = WHERE_B["dn_conv_w"] + tap * NQKV + f
                    wt = K.colB[:, col:col + 1]
                    for seg, (u0, c0, n, done) in enumerate(((0, 0, TC, S["conv_c"]), (UC, TC, TX, S["conv_x"]))):
                        src, dst = U[:, f % NU, u0 + tap:u0 + tap + n], C[:, f, c0:c0 + n]
                        if tap == 0:
                            ins = dve.tensor_scalar(dst, src, wt, None, ALU.mult)
                        else:
                            dve.wait_ge(tap_done[seg], f * (TAPS - 1) + tap)
                            ins = dve.scalar_tensor_tensor(out=dst, in0=src, scalar=wt, in1=dst,
                                                           op0=ALU.mult, op1=ALU.add)
                        ins.then_inc(done if tap == TAPS - 1 else tap_done[seg], 1)
            dve.wait_ge(S["ba_turned"], 1)
            dve.tensor_copy(ba, K.bank[2][:, 0:NT * 16].rearrange("p (j n) -> p j n", n=16)).then_inc(S["ba_out"], 1)

def qk_norm(K, C):
    nc = K.nc
    N = 2 * H1
    with ExitStack() as c, phase(nc, "sq_done sum_done len_done inv_done scaled") as (block, S):
        sq = c.enter_context(sbuf(nc, "qk_sq", [P, 2, TT], F32))
        ln = c.enter_context(sbuf(nc, "qk_len", [P, 2, TT], F32))
        inv = c.enter_context(sbuf(nc, "qk_inv", [P, 2, TT], F32))
        parts = ((0, 0, 512), (1, 512, TT))

        @block.scalar
        def _(act):
            def square(f):
                if f >= 2:
                    act.wait_ge(S["sum_done"], f - 1)
                act.activation(sq[:, f % 2, :], C[:, f, :], ACT.Square).then_inc(S["sq_done"], 1)

            square(0)
            for f in range(N):
                if f + 1 < N:
                    square(f + 1)
                act.wait_ge(S["sum_done"], f + 1)
                if f >= 2:
                    act.wait_ge(S["inv_done"], f - 1)
                for b, t0, t1 in parts:
                    last = act.activation(ln[:, f % 2, t0:t1], K.bank[2 * (f % 2) + b][:, 0:t1 - t0], ACT.Sqrt,
                                          bias=K.eps[:, :])
                last.then_inc(S["len_done"], 1)

        @block.tensor
        def _(pe):
            for f in range(N):
                pe.wait_ge(S["sq_done"], f + 1)
                if f >= 2:
                    pe.wait_ge(S["len_done"], f - 1)
                for b, t0, t1 in parts:
                    mm = pe.matmul(K.bank[2 * (f % 2) + b][:, 0:t1 - t0], K.ones, sq[:, f % 2, t0:t1],
                                   start=True, stop=True)
                mm.then_inc(S["sum_done"], 1)

        @block.vector
        def _(dve):
            for f in range(N):
                dve.wait_ge(S["len_done"], f + 1)
                if f >= 2:
                    dve.wait_ge(S["scaled"], f - 1)
                dve.reciprocal(inv[:, f % 2, :], ln[:, f % 2, :]).then_inc(S["inv_done"], 1)
                dve.wait_ge(S["inv_done"], f + 1)
                dve.scalar_tensor_tensor(out=C[:, f, :], in0=inv[:, f % 2, :],
                                         scalar=DK ** -0.5 if f < H1 else 1.0, in1=C[:, f, :],
                                         op0=ALU.mult, op1=ALU.mult).then_inc(S["scaled"], 1)


def turn_back(K, sources, destinations):
    nc = K.nc
    with phase(nc, "turned_a turned_b out_a out_b") as (block, S):
        @block.tensor
        def _(pe):
            for n, src in enumerate(sources):
                for lo, hi, b, turned, out in ((0, 4, 0, S["turned_a"], S["out_a"]), (4, NT, 1, S["turned_b"], S["out_b"])):
                    if n >= 2:
                        pe.wait_ge(out, n - 1)
                    for j in range(lo, hi):
                        tr = pe.transpose(K.bank[2 * (n % 2) + b][:, (j - lo) * P:(j - lo + 1) * P],
                                          src[:, j * P:(j + 1) * P], K.ident)
                    tr.then_inc(turned, 1)

        @block.scalar
        def _(act):
            for n, dst in enumerate(destinations):
                act.wait_ge(S["turned_a"], n + 1)
                act.activation(dst[:, 0:4, :], K.bank[2 * (n % 2)][:, :].rearrange("p (j n) -> p j n", n=P),
                               ACT.Copy).then_inc(S["out_a"], 1)

        @block.vector
        def _(dve):
            for n, dst in enumerate(destinations):
                dve.wait_ge(S["turned_b"], n + 1)
                dve.tensor_copy(dst[:, 4:NT, :], K.bank[2 * (n % 2) + 1][:, 0:(NT - 4) * P]
                                .rearrange("p (j n) -> p j n", n=P)).then_inc(S["out_b"], 1)


def conformer(K, cfa, cfs, cfT):
    nc = K.nc
    names = "glu tap conv_done sum1 centred sq_done sum2 rms_done inv_done normed out_done"
    with ExitStack() as c, phase(nc, names) as (block, S):
        y = c.enter_context(sbuf(nc, "cf_glu", [P, NCF, TX], F32))
        z = c.enter_context(sbuf(nc, "cf_conv", [P, NCF, TX], F32))
        rms = c.enter_context(sbuf(nc, "cf_rms", [P, TX], F32))
        inv = c.enter_context(sbuf(nc, "cf_inv", [P, TX], F32))

        def col(name, n):
            return K.colA[:, WHERE_A[name] + n:WHERE_A[name] + n + 1]

        @block.vector
        def _(dve):
            step = Chain(dve, S["tap"])
            for m in range(NCF):
                dve.tensor_tensor(y[:, m, :], cfa[:, m, :], cfs[:, m, :], ALU.mult).then_inc(S["glu"], 1)
                dve.wait_ge(S["glu"], m + 1)
                step(dve.tensor_scalar(z[:, m, :], y[:, m, :], col("cf_dw_w", HALO * NCF + m), col("cf_dw_b", m),
                                       ALU.mult, ALU.add))
                for d in range(-HALO, HALO + 1):
                    if d == 0:
                        continue
                    lo, hi = max(0, -d) * GRID_W, (ROWS - max(0, d)) * GRID_W
                    ins = dve.scalar_tensor_tensor(
                        out=z[:, m, lo:hi], in0=y[:, m, lo + d * GRID_W:hi + d * GRID_W],
                        scalar=col("cf_dw_w", (HALO + d) * NCF + m), in1=z[:, m, lo:hi], op0=ALU.mult, op1=ALU.add)
                    if d == HALO:
                        ins.then_inc(S["conv_done"], 1)
                    else:
                        step(ins)
            dve.wait_ge(S["conv_done"], NCF)
            dve.wait_ge(S["sum1"], 1)
            for m in range(NCF):
                dve.scalar_tensor_tensor(out=z[:, m, :], in0=K.bank[0][:, :], scalar=-1.0 / CFC, in1=z[:, m, :],
                                         op0=ALU.mult, op1=ALU.add).then_inc(S["centred"], 1)
            dve.wait_ge(S["rms_done"], 1)
            dve.reciprocal(inv[:, :], rms[:, :]).then_inc(S["inv_done"], 1)
            dve.wait_ge(S["inv_done"], 1)
            for m in range(NCF):
                dve.tensor_tensor(z[:, m, :], z[:, m, :], inv[:, :], ALU.mult).then_inc(S["normed"], 1)

        @block.tensor
        def _(pe):
            for m in range(NCF):
                pe.wait_ge(S["conv_done"], m + 1)
                mm = pe.matmul(K.bank[0][:, :], K.ones, z[:, m, :], start=(m == 0), stop=(m == NCF - 1))
            mm.then_inc(S["sum1"], 1)
            for m in range(NCF):
                pe.wait_ge(S["sq_done"], m + 1)
                mm = pe.matmul(K.bank[1][:, :], K.ones, y[:, m, :], start=(m == 0), stop=(m == NCF - 1))
            mm.then_inc(S["sum2"], 1)

        @block.scalar
        def _(act):
            for m in range(NCF):
                act.wait_ge(S["centred"], m + 1)
                act.activation(y[:, m, :], z[:, m, :], ACT.Square).then_inc(S["sq_done"], 1)
            act.wait_ge(S["sum2"], 1)
            act.activation(rms[:, :], K.bank[1][:, :], ACT.Sqrt, bias=K.eps[:, :], scale=1.0 / CFC)\
                .then_inc(S["rms_done"], 1)
            for m in range(NCF):
                act.wait_ge(S["normed"], m + 1)
                act.activation(cfT[:, m, :], z[:, m, :], ACT.Silu, bias=col("cf_ln_b", m), scale=col("cf_ln_g", m))\
                    .then_inc(S["out_done"], 1)



def delta_gates(K, I, ba, G):
    nc = K.nc
    with ExitStack() as c, phase(nc, "par_in a_step d_step sums gl_out") as (block, S):
        def buf(name):
            return c.enter_context(sbuf(nc, name, [P, 2, NT, H1], F32))

        par = c.enter_context(sbuf(nc, "gate_par", [P, 2, 2, H1], F32))
        ea = c.enter_context(sbuf(nc, "gate_ea", [P, 2, H1], F32))
        a, b, r, g, gl, t = (buf("gate_" + n) for n in ("a", "b", "r", "g", "gl", "t"))
        W = NT * H1

        @block.sync
        def _(sp):
            for n, src in enumerate((I["dn_a_log"], I["dn_dt_bias"])):
                sp.dma_start(par[:, n, :, :], src[0].partition_broadcast(P)).then_inc(S["par_in"], 16)
            sp.wait_ge(S["par_in"], 32)

        @block.vector
        def _(dve):
            step = Chain(dve, S["d_step"])
            dve.wait_ge(S["par_in"], 32)
            for d in range(2):
                dt = par[:, 1, d:d + 1, :].broadcast_to([P, NT, H1])
                ins = dve.tensor_tensor(a[:, d, :, :], ba[:, :, d * 8 + 4:d * 8 + 8], dt, ALU.add)
                step(ins)
            step(dve.tensor_scalar(b[:, :, :, :], a[:, :, :, :], 0.0, None, ALU.max))
            dve.wait_ge(S["a_step"], 5)
            step(dve.tensor_tensor(b[:, :, :, :], b[:, :, :, :], r[:, :, :, :], ALU.add))
            for d in range(2):
                e = ea[:, d:d + 1, :].broadcast_to([P, NT, H1])
                step(dve.scalar_tensor_tensor(out=g[:, d, :, :], in0=b[:, d, :, :], scalar=-1.0, in1=e,
                                              op0=ALU.mult, op1=ALU.mult))
            dve.wait_ge(S["sums"], 1)
            for d in range(2):
                step(dve.tensor_copy(G["cumg"][:, d, :, :], K.bank[0][:, d * W:(d + 1) * W]
                                     .rearrange("p (j h) -> p j h", h=H1)))
            step(dve.tensor_copy(gl[:, :, :, :], K.bank[1][:, 0:2 * W]
                                 .rearrange("p (d j h) -> p d j h", d=2, h=H1)))
            step(dve.tensor_tensor(t[:, :, :, :], gl[:, :, :, :], G["cumg"][:, :, :, :], ALU.subtract))

        @block.scalar
        def _(act):
            step = Chain(act, S["a_step"])
            act.wait_ge(S["par_in"], 32)
            step(act.activation(ea[:, :, :], par[:, 0, :, :], ACT.Exp))
            act.wait_ge(S["d_step"], 2)
            step(act.activation(r[:, :, :, :], a[:, :, :, :], ACT.Abs))
            step(act.activation(r[:, :, :, :], r[:, :, :, :], ACT.Exp, scale=-1.0))
            step(act.activation(t[:, :, :, :], r[:, :, :, :], ACT.Ln, bias=K.one[:, :]))
            step(act.activation(r[:, :, :, :], t[:, :, :, :], ACT.Copy))
            act.wait_ge(S["d_step"], 9)
            step(act.activation(G["egc"][:, :, :, :], G["cumg"][:, :, :, :], ACT.Exp))
            step(act.activation(G["egl"][:, :, :, :], gl[:, :, :, :], ACT.Exp))
            act.wait_ge(S["d_step"], 10)
            step(act.activation(G["ekd"][:, :, :, :], t[:, :, :, :], ACT.Exp))
            for d in range(2):
                step(act.activation(G["beta"][:, d, :, :], ba[:, :, d * 8:d * 8 + 4], ACT.Sigmoid))

        @block.tensor
        def _(pe):
            pe.wait_ge(S["d_step"], 6)
            for d in range(2):
                gd = g[:, d, :, :].rearrange("p j h -> p (j h)")
                pe.matmul(K.bank[0][:, d * W:(d + 1) * W], K.inc[d], gd, start=True, stop=True)
                mm = pe.matmul(K.bank[1][:, d * W:(d + 1) * W], K.ones, gd, start=True, stop=True)
            mm.then_inc(S["sums"], 1)


class Inverse:

    @staticmethod
    def buffers(K, c, d):
        def buf(name):
            return c.enter_context(sbuf(K.nc, f"inv_{name}{d}", [P, 4, P], F32))
        return buf("X"), buf("Z"), buf("Y")

    MM_COUNT = 1 + 3 * (LEVELS - 2) + 2
    STEP_COUNT = 3 + 3 * (LEVELS - 2) + 2


def tensor_inverses(pe, K, As, bufs, banks, steps, base, mms):
    dirs = range(len(As))
    for d in dirs:
        pe.wait_ge(steps[d], base + 2)
        for h in range(4):
            tr = pe.transpose(banks[d][0][:, h * P:(h + 1) * P], bufs[d][1][:, h, :], K.ident)
        tr.then_inc(mms[d], 1)
    n = base + 3
    for level in range(1, LEVELS):
        for d in dirs:
            pe.wait_ge(steps[d], n)
            for h in range(4):
                m = pe.matmul(banks[d][0][:, h * P:(h + 1) * P], As[d](h), bufs[d][0][:, h, :], start=True, stop=True)
            m.then_inc(mms[d], 1)
        for d in dirs:
            _, Z, Y = bufs[d]
            pe.wait_ge(steps[d], n + 1)
            if level < LEVELS - 1:
                for h in range(4):
                    m = pe.matmul(banks[d][1][:, h * P:(h + 1) * P], Z[:, h, :], Y[:, h, :], start=True, stop=True)
                m.then_inc(mms[d], 1)
            for h in range(4):
                m = pe.matmul(banks[d][2][:, h * P:(h + 1) * P], Y[:, h, :], Z[:, h, :], start=True, stop=True)
            m.then_inc(mms[d], 1)
        n += 3


def vector_inverses(dve, K, As, bufs, banks, steps, mms, before):
    dirs = range(len(As))

    def four(bank):
        return bank[:, :].rearrange("p (h t) -> p h t", h=4)

    for d in dirs:
        steps[d].put(dve.tensor_tensor(bufs[d][1][:, :, :], As[d], K.cross[1 - d % 2][0], ALU.mult))
    for d in dirs:
        Z = bufs[d][1]
        steps[d].wait()
        steps[d].put(dve.tensor_tensor(Z[:, :, :], Z[:, :, :], K.ident4, ALU.add))
    n = before + 1
    for d in dirs:
        dve.wait_ge(mms[d], n)
        steps[d].put(dve.tensor_copy(bufs[d][0][:, :, :], four(banks[d][0])))
    for level in range(1, LEVELS):
        last = level == LEVELS - 1
        for d in dirs:
            dve.wait_ge(mms[d], n + 1)
            steps[d].put(dve.tensor_tensor(bufs[d][2][:, :, :], four(banks[d][0]), K.cross[d % 2][level], ALU.mult))
        for d in dirs:
            X, Z, _ = bufs[d]
            if not last:
                dve.wait_ge(mms[d], n + 2)
                steps[d].put(dve.tensor_tensor(X[:, :, :], four(banks[d][1]), X[:, :, :], ALU.add))
            dve.wait_ge(mms[d], n + (2 if last else 3))
            steps[d].put(dve.tensor_tensor(Z[:, :, :], four(banks[d][2]), Z[:, :, :], ALU.add))
        n += 3
    for d in dirs:
        steps[d].wait()


def delta_step(K, C, Ktok, Vtok, G, O, St, tile_of, with_output):
    nc = K.nc
    names = "st_f st_b mm_f mm_b v_f v_b a_f a_b p_f p_b"
    with ExitStack() as c, phase(nc, names) as (block, S):
        def buf(name, d):
            return c.enter_context(sbuf(nc, f"{name}{d}", [P, 4, P], F32))

        dirs = (0, 1)
        kT, qT, Kd, Bv, Kb = ([buf(n, d) for d in dirs] for n in ("kT", "qT", "kd", "bv", "kb"))
        Dg, Db, Em, BE, QE, LT, IT = ([buf(n, d) for d in dirs] for n in
                                      ("diag_g", "diag_b", "decay", "bdecay", "qdecay", "LT", "intra"))
        inv = [Inverse.buffers(K, c, d) for d in dirs]
        nW, Vn = Dg, Db
        gcj = [c.enter_context(sbuf(nc, f"gates{d}", [P, 5, H1], F32)) for d in dirs]
        bank = [K.bank[4 * d:4 * d + 4] for d in dirs]
        mm = (S["mm_f"], S["mm_b"])
        vs = (S["v_f"], S["v_b"])
        as_ = (S["a_f"], S["a_b"])
        ps = (S["p_f"], S["p_b"])
        GC, BETA, EGC, EKD, EGL = range(5)
        four = lambda b: b[:, :].rearrange("p (h t) -> p h t", h=4)
        wide = lambda d, q: gcj[d][:, q, :].unsqueeze(2).broadcast_to([P, H1, P])

        @block.gpsimd
        def _(pool):
            for d in dirs:
                j = tile_of[d]
                step = Chain(pool, ps[d])
                for q, src in ((GC, G["cumg"]), (BETA, G["beta"]), (EGC, G["egc"]), (EKD, G["ekd"]), (EGL, G["egl"])):
                    step.put(pool.tensor_copy(gcj[d][:, q, :], src[:, d, bass.ds(j, 1), :]
                                              .rearrange("p o h -> p (o h)")))
            for d in dirs:
                pool.wait_ge(ps[d], 5)
                pool.tensor_tensor(Dg[d][:, :, :], K.ident4, wide(d, GC), ALU.mult).then_inc(ps[d], 1)
                pool.tensor_tensor(Db[d][:, :, :], K.ident4, wide(d, BETA), ALU.mult).then_inc(ps[d], 1)
            for d in dirs:
                j = tile_of[d]
                kt = Ktok[:, :, bass.ds(j, 1), :].rearrange("p h o n -> p (h o) n")
                vt = Vtok[:, :, bass.ds(j, 1), :].rearrange("p h o n -> p (h o) n")
                pool.tensor_tensor(Kb[d][:, :, :], kt, wide(d, BETA), ALU.mult).then_inc(ps[d], 1)
                pool.tensor_tensor(Bv[d][:, :, :], vt, wide(d, BETA), ALU.mult).then_inc(ps[d], 1)
                pool.tensor_tensor(Kd[d][:, :, :], kt, wide(d, EKD), ALU.mult).then_inc(ps[d], 1)
                pool.wait_ge(ps[d], 8)
                pool.tensor_tensor(Kb[d][:, :, :], Kb[d][:, :, :], wide(d, EGC), ALU.mult).then_inc(ps[d], 1)
            if with_output:
                for d in dirs:
                    pool.wait_ge(as_[d], 4)
                    pool.tensor_tensor(QE[d][:, :, :], QE[d][:, :, :], qT[d][:, :, :], ALU.mult).then_inc(ps[d], 1)

        @block.scalar
        def _(act):
            for d in dirs:
                j = tile_of[d]
                ts = bass.ds(j * P, P)
                act.activation(kT[d][:, :, :], C[:, H1:2 * H1, ts], ACT.Copy).then_inc(as_[d], 1)
                act.activation(qT[d][:, :, :], C[:, 0:H1, ts], ACT.Copy).then_inc(as_[d], 1)
            for d in dirs:
                act.wait_ge(vs[d], 1)
                act.activation(Em[d][:, :, :], Em[d][:, :, :], ACT.Exp).then_inc(as_[d], 1)
                act.activation(QE[d][:, :, :], four(bank[d][0]), ACT.Exp).then_inc(as_[d], 1)
            for d in dirs:
                act.wait_ge(mm[d], 3 + Inverse.MM_COUNT + 1)
                act.activation(nW[d][:, :, :], four(bank[d][3]), ACT.Copy, scale=-1.0).then_inc(as_[d], 1)

        @block.tensor
        def _(pe):
            for d in dirs:
                pe.wait_ge(ps[d], 7)
                pe.matmul(bank[d][0][:, :], K.ones, Dg[d][:, :, :], start=True, stop=True).then_inc(mm[d], 1)
                pe.matmul(bank[d][1][:, :], K.ones, Db[d][:, :, :], start=True, stop=True).then_inc(mm[d], 1)
                pe.wait_ge(as_[d], 2)
                for h in range(H1):
                    pe.matmul(bank[d][2][:, h * P:(h + 1) * P], kT[d][:, h, :], kT[d][:, h, :], start=True, stop=True)
                for h in range(H1):
                    m = pe.matmul(bank[d][3][:, h * P:(h + 1) * P], kT[d][:, h, :], qT[d][:, h, :],
                                  start=True, stop=True)
                m.then_inc(mm[d], 1)
            for d in dirs:
                pe.wait_ge(as_[d], 4)
            tensor_inverses(pe, K, [lambda h, d=d: LT[d][:, h, :] for d in dirs], inv, bank, vs, 6, mm)
            n = 6 + Inverse.STEP_COUNT
            for d in dirs:
                Z = inv[d][1]
                pe.wait_ge(ps[d], 11)
                pe.wait_ge(vs[d], n)
                for h in range(H1):
                    m = pe.matmul(bank[d][3][:, h * P:(h + 1) * P], Kb[d][:, h, :], Z[:, h, :], start=True, stop=True)
                m.then_inc(mm[d], 1)
                pe.wait_ge(as_[d], 5)
                for h in range(H1):
                    sl = bank[d][0][:, h * P:(h + 1) * P]
                    pe.matmul(sl, Z[:, h, :], Bv[d][:, h, :], start=True, stop=False)
                    m = pe.matmul(sl, nW[d][:, h, :], St[d][:, h, :], start=False, stop=True)
                m.then_inc(mm[d], 1)
                pe.wait_ge(vs[d], n + 1)
                for h in range(H1):
                    m = pe.matmul(bank[d][2][:, h * P:(h + 1) * P], Kd[d][:, h, :], Vn[d][:, h, :],
                                  start=True, stop=True)
                m.then_inc(mm[d], 1)
                if with_output:
                    pe.wait_ge(ps[d], 12)
                    for h in range(H1):
                        sl = bank[d][1][:, h * P:(h + 1) * P]
                        pe.matmul(sl, QE[d][:, h, :], St[d][:, h, :], start=True, stop=False)
                        m = pe.matmul(sl, IT[d][:, h, :], Vn[d][:, h, :], start=False, stop=True)
                    m.then_inc(mm[d], 1)

        @block.vector
        def _(dve):
            steps = [Chain(dve, vs[d]) for d in dirs]
            for d in dirs:
                dve.wait_ge(mm[d], 1)
                dve.wait_ge(ps[d], 5)
                for h in range(H1):
                    ins = dve.tensor_scalar(Em[d][:, h, :], bank[d][0][:, h * P:(h + 1) * P],
                                            gcj[d][:, GC, h:h + 1], 0.0, ALU.subtract, ALU.min)
                steps[d].put(ins)
            for d in dirs:
                step = steps[d]
                dve.wait_ge(as_[d], 4)
                step(dve.tensor_tensor(Em[d][:, :, :], Em[d][:, :, :], K.incl4[d], ALU.mult))
                dve.wait_ge(mm[d], 3)
                step(dve.tensor_tensor(IT[d][:, :, :], four(bank[d][3]), Em[d][:, :, :], ALU.mult))
                step(dve.tensor_tensor(BE[d][:, :, :], four(bank[d][1]), Em[d][:, :, :], ALU.mult))
                step(dve.tensor_tensor(BE[d][:, :, :], BE[d][:, :, :], K.strict4[d], ALU.mult))
                step(dve.tensor_tensor(LT[d][:, :, :], four(bank[d][2]), BE[d][:, :, :], ALU.mult))
            vector_inverses(dve, K, [LT[d][:, :, :] for d in dirs], inv, bank, steps, mm, 3)
            n = 3 + Inverse.MM_COUNT
            for d in dirs:
                step = steps[d]
                dve.wait_ge(mm[d], n + 2)
                step.put(dve.tensor_copy(Vn[d][:, :, :], four(bank[d][0])))
                dve.wait_ge(mm[d], n + 3 + with_output)
                for h in range(H1):
                    ins = dve.scalar_tensor_tensor(out=St[d][:, h, :], in0=St[d][:, h, :],
                                                   scalar=gcj[d][:, EGL, h:h + 1],
                                                   in1=bank[d][2][:, h * P:(h + 1) * P], op0=ALU.mult, op1=ALU.add)
                if with_output:
                    j = tile_of[d] - JC
                    o = O[:, bass.ds(j, 1), :].rearrange("p o n -> p (o n)")
                    ins = dve.tensor_tensor(o, bank[d][1][:, :], o, ALU.add)
                step.put(ins)

def delta_readout(K, O, headsT):
    nc = K.nc
    with ExitStack() as c, phase(nc, "sq_done v_step rms_done turned gated") as (block, S):
        sq = c.enter_context(sbuf(nc, "dr_sq", [P, JX, H1 * DK], F32))
        st = c.enter_context(sbuf(nc, "dr_stats", [P, 3, JX * H1], F32))

        @block.scalar
        def _(act):
            act.activation(sq[:, :, :], O[:, :, :], ACT.Square).then_inc(S["sq_done"], 1)
            act.wait_ge(S["v_step"], 1)
            act.activation(st[:, 1, :], st[:, 0, :], ACT.Sqrt, bias=K.eps[:, :], scale=1.0 / DK).then_inc(S["rms_done"], 1)

        @block.vector
        def _(dve):
            step = Chain(dve, S["v_step"])
            heads = lambda t: t[:, :, :].rearrange("p j (h n) -> p (j h) n", n=DK)
            dve.wait_ge(S["sq_done"], 1)
            step.put(dve.tensor_reduce(st[:, 0, :], heads(sq), AX.X, ALU.add))
            dve.wait_ge(S["rms_done"], 1)
            step(dve.reciprocal(st[:, 2, :], st[:, 1, :]))
            step.put(dve.tensor_tensor(heads(O), heads(O),
                                       st[:, 2, :].unsqueeze(2).broadcast_to([P, JX * H1, DK]), ALU.mult))
            g = K.colA[:, WHERE_A["dn_norm_g"]:WHERE_A["dn_norm_g"] + 1]
            for h in range(H1):
                dve.wait_ge(S["turned"], h + 1)
                dve.scalar_tensor_tensor(out=headsT[:, h, :], in0=K.bank[h][:, :], scalar=g, in1=headsT[:, h, :],
                                         op0=ALU.mult, op1=ALU.mult).then_inc(S["gated"], 1)

        @block.tensor
        def _(pe):
            pe.wait_ge(S["v_step"], 3)
            for h in range(H1):
                for j in range(JX):
                    tr = pe.transpose(K.bank[h][:, j * P:(j + 1) * P], O[:, j, h * DK:(h + 1) * DK], K.ident)
                tr.then_inc(S["turned"], 1)


def output_projection(K, srcT, w, gates, tiles, first_col):
    nc = K.nc
    with ExitStack() as c, phase(nc, "w_in0 w_in1 mm_done gated added") as (block, S):
        wb = c.enter_context(sbuf(nc, "wo", [P, 2, KD, 512], F32))
        t = c.enter_context(sbuf(nc, "wo_gated", [P, 2, 512], F32))
        w_in = (S["w_in0"], S["w_in1"])
        units = [(n, j) for n in range(2) for j in tiles]

        @block.sync
        def _(sp):
            for n in range(2):
                sp.dma_start(wb[:, n, :, :], w.rearrange("(k p) n -> p k n", p=P)[:, :, n * 512:(n + 1) * 512])\
                    .then_inc(w_in[n], 16)

        @block.tensor
        def _(pe):
            for u, (n, j) in enumerate(units):
                pe.wait_ge(w_in[n], 16)
                if u >= 4:
                    pe.wait_ge(S["gated"], u - 3)
                for k in range(KD):
                    mm = pe.matmul(K.bank[u % 4][:, :], srcT[:, k, (j - first_col) * P:(j - first_col + 1) * P],
                                   wb[:, n, k, :], start=(k == 0), stop=(k == KD - 1))
                mm.then_inc(S["mm_done"], 1)

        @block.vector
        def _(dve):
            for u, (n, j) in enumerate(units):
                dve.wait_ge(S["mm_done"], u + 1)
                if u >= 2:
                    dve.wait_ge(S["added"], u - 1)
                x = K.X[:, j, n * 512:(n + 1) * 512]
                dve.tensor_tensor(t[:, u % 2, :], K.bank[u % 4][:, :], gates(j)[:, n * 512:(n + 1) * 512], ALU.mult)\
                    .then_inc(S["gated"], 1)
                dve.wait_ge(S["gated"], u + 1)
                dve.tensor_tensor(x, x, t[:, u % 2, :], ALU.add).then_inc(S["added"], 1)


def final_norm(K, g, tiles, out=None):
    nc = K.nc
    N = len(tiles)
    with ExitStack() as c, phase(nc, "g_in sq_done rms_done v_step normed stored") as (block, S):
        gb = c.enter_context(sbuf(nc, "fn_gain", [P, D], F32))
        junk = c.enter_context(sbuf(nc, "fn_junk", [P, D], F32))
        st = c.enter_context(sbuf(nc, "fn_stats", [P, 3, NT], F32))

        @block.sync
        def _(sp):
            sp.dma_start(gb[:, :], g.partition_broadcast(P)).then_inc(S["g_in"], 16)
            sp.wait_ge(S["g_in"], 16)
            if out is not None:
                for n, j in enumerate(tiles):
                    sp.wait_ge(S["normed"], n + 1)
                    sp.dma_start(out[n * P:(n + 1) * P, :], K.X[:, j, :]).then_inc(S["stored"], 16)
                sp.wait_ge(S["stored"], 16 * N)

        @block.scalar
        def _(act):
            for n, j in enumerate(tiles):
                if n:
                    act.wait_ge(S["sq_done"], n)
                act.activation(junk[:, :], K.X[:, j, :], ACT.Square, accum_out=st[:, 0, n:n + 1]).then_inc(S["sq_done"], 1)
            act.wait_ge(S["sq_done"], N)
            act.activation(st[:, 1, 0:N], st[:, 0, 0:N], ACT.Sqrt, bias=K.eps[:, :], scale=1.0 / D)\
                .then_inc(S["rms_done"], 1)

        @block.vector
        def _(dve):
            step = Chain(dve, S["v_step"])
            dve.wait_ge(S["rms_done"], 1)
            step(dve.reciprocal(st[:, 2, 0:N], st[:, 1, 0:N]))
            dve.wait_ge(S["g_in"], 16)
            for n, j in enumerate(tiles):
                dve.scalar_tensor_tensor(out=K.X[:, j, :], in0=K.X[:, j, :], scalar=st[:, 2, n:n + 1],
                                         in1=gb[:, :], op0=ALU.mult, op1=ALU.mult).then_inc(S["normed"], 1)



def pick(dve, step, values, keep, k, n, bufs):
    top, eq, cnt, run, zero = bufs
    bc = lambda ap: ap.broadcast_to([P, JX, n])
    for j in range(JX):
        step.put(dve.max(top[:, j, :], values[:, j, :]))
    step.wait()
    least = bc(top[:, :, k - 1:k])
    step.put(dve.tensor_tensor(keep, values, least, ALU.is_gt))
    step(dve.tensor_tensor(eq, values, least, ALU.is_equal))
    step.put(dve.tensor_reduce(cnt[:, :], keep, AX.X, ALU.add))
    for j in range(JX):
        step.put(dve.tensor_tensor_scan(run[:, j, :], eq[:, j, :], zero[:, 0:n], 0.0, ALU.add, ALU.add))
    step.wait()
    step(dve.tensor_tensor(run, run, cnt[:, :].unsqueeze(2).broadcast_to([P, JX, n]), ALU.add))
    step(dve.scalar_tensor_tensor(out=eq, in0=run, scalar=k + 0.5, in1=eq, op0=ALU.is_le, op1=ALU.mult))
    step(dve.tensor_tensor(keep, keep, eq, ALU.add))


def router(K, I, wt, kept):
    nc = K.nc
    with ExitStack() as c, phase(nc, "in_done mm_done sig_done v_step") as (block, S):
        buf = lambda name, shape: c.enter_context(sbuf(nc, "rt_" + name, shape, F32))
        rw = buf("w", [P, KD, NE])
        bias = buf("bias", [P, NE])
        kp = kept
        sc, sel, eq, run = (buf(n, [P, JX, NE]) for n in ("scores", "sel", "eq", "run"))
        top2, top = buf("top2", [P, JX * GROUPS, 8]), buf("top", [P, JX, 8])
        gs, gk, geq, grun = (buf(n, [P, JX, GROUPS]) for n in ("gs", "gk", "geq", "grun"))
        cnt, zero, tot = buf("cnt", [P, JX]), buf("zero", [P, NE]), buf("tot", [P, 2, JX])

        @block.sync
        def _(sp):
            sp.dma_start(rw[:, :, :], I["router_w"][0].rearrange("(k p) n -> p k n", p=P)).then_inc(S["in_done"], 16)
            sp.dma_start(bias[:, :], I["router_bias"][0].partition_broadcast(P)).then_inc(S["in_done"], 16)
            sp.wait_ge(S["in_done"], 32)

        @block.tensor
        def _(pe):
            pe.wait_ge(S["in_done"], 32)
            for j in range(JX):
                for k in range(KD):
                    mm = pe.matmul(K.bank[0][:, j * NE:(j + 1) * NE], K.hT[:, k, TC + j * P:TC + (j + 1) * P],
                                   rw[:, k, :], start=(k == 0), stop=(k == KD - 1))
            mm.then_inc(S["mm_done"], 1)

        @block.scalar
        def _(act):
            act.wait_ge(S["mm_done"], 1)
            act.activation(sc[:, :, :], K.bank[0][:, 0:JX * NE].rearrange("p (j e) -> p j e", e=NE), ACT.Sigmoid)\
                .then_inc(S["sig_done"], 1)

        @block.vector
        def _(dve):
            step = Chain(dve, S["v_step"])
            step.put(dve.memset(zero[:, :], 0.0))
            dve.wait_ge(S["sig_done"], 1)
            dve.wait_ge(S["in_done"], 32)
            step(dve.tensor_tensor(sel[:, :, :], sc[:, :, :], bias[:, :].unsqueeze(1).broadcast_to([P, JX, NE]), ALU.add))
            n = NE // GROUPS
            for j in range(JX):
                for g in range(GROUPS):
                    step.put(dve.max(top2[:, j * GROUPS + g, :], sel[:, j, g * n:(g + 1) * n]))
            step.wait()
            t2 = top2[:, :, :].rearrange("p (j g) e -> p j g e", g=GROUPS)
            step(dve.tensor_tensor(gs[:, :, :], t2[:, :, :, 0], t2[:, :, :, 1], ALU.add))
            pick(dve, step, gs[:, :, :], gk[:, :, :], 4, GROUPS, (top, geq[:, :, :], cnt, grun[:, :, :], zero))
            step(dve.tensor_scalar(geq[:, :, :], gk[:, :, :], 1e30, -1e30, ALU.mult, ALU.add))
            for g in range(GROUPS):
                part = sel[:, :, g * n:(g + 1) * n]
                step.put(dve.tensor_tensor(part, part, geq[:, :, g:g + 1].broadcast_to([P, JX, n]), ALU.add))
            step.wait()
            pick(dve, step, sel[:, :, :], kp[:, :, :], 6, NE, (top, eq[:, :, :], cnt, run[:, :, :], zero))
            step(dve.tensor_tensor(sc[:, :, :], sc[:, :, :], kp[:, :, :], ALU.mult))
            step(dve.tensor_reduce(tot[:, 0, :], sc[:, :, :], AX.X, ALU.add))
            step(dve.reciprocal(tot[:, 1, :], tot[:, 0, :]))
            step(dve.scalar_tensor_tensor(out=wt[:, :, :], in0=sc[:, :, :], scalar=2.5,
                                          in1=tot[:, 1, :].unsqueeze(2).broadcast_to([P, JX, NE]),
                                          op0=ALU.mult, op1=ALU.mult))


def load_expert(eng, Wb, s, srcs, sem):
    gate, up, down = srcs
    eng.dma_start(Wb[:, s, 0, :].rearrange("p (k n) -> p k n", n=DE), gate.rearrange("(k p) n -> p k n", p=P))\
        .then_inc(sem, 16)
    eng.dma_start(Wb[:, s, 1, :].rearrange("p (k n) -> p k n", n=DE), up.rearrange("(k p) n -> p k n", p=P))\
        .then_inc(sem, 16)
    eng.dma_start(Wb[:, s, 2, :].rearrange("p (k n) -> p k n", n=D), down.rearrange("(k p) n -> p k n", p=P))\
        .then_inc(sem, 16)


def experts(K, Wb, acc, weights, following):
    nc = K.nc
    N = len(weights)
    names = "in0 in1 up_done silu_done act_done down_done acc_done"
    with ExitStack() as c, phase(nc, names) as (block, S):
        sg = c.enter_context(sbuf(nc, "ex_silu", [P, 2, TX], F32))
        aT = c.enter_context(sbuf(nc, "ex_act", [P, 2, 2, TX], F32))

        @block.sync
        def _(sp):
            if N > 1:
                load_expert(sp, Wb, 1, following[1], S["in1"])
            if following[0] is not None:
                sp.wait_ge(S["down_done"], 8)
                load_expert(sp, Wb, 0, following[0], S["in0"])
                sp.wait_ge(S["in0"], 48)
            if N > 1:
                sp.wait_ge(S["in1"], 48)

        @block.tensor
        def _(pe):
            for s in range(N):
                if s:
                    pe.wait_ge(S["in1"], 48)
                for m in range(2):
                    for which in range(2):
                        if s:
                            pe.wait_ge(S["act_done"], 2 * (s - 1) + m + 1)
                        for k in range(KD):
                            mm = pe.matmul(K.bank[2 * m + which][:, :],
                                           Wb[:, s, which, k * DE + m * P:k * DE + (m + 1) * P],
                                           K.hT[:, k, TC:TT], start=(k == 0), stop=(k == KD - 1))
                        mm.then_inc(S["up_done"], 1)
            for s in range(N):
                pe.wait_ge(S["act_done"], 2 * s + 2)
                for j in range(JX):
                    for n in range(2):
                        u = 8 * s + 2 * j + n
                        if u >= 4:
                            pe.wait_ge(S["acc_done"], u - 3)
                        for m in range(2):
                            mm = pe.matmul(K.bank[4 + u % 4][:, :], aT[:, s, m, j * P:(j + 1) * P],
                                           Wb[:, s, 2, m * D + n * 512:m * D + (n + 1) * 512],
                                           start=(m == 0), stop=(m == 1))
                        mm.then_inc(S["down_done"], 1)

        @block.scalar
        def _(act):
            for s in range(N):
                for m in range(2):
                    if s:
                        act.wait_ge(S["act_done"], 2 * (s - 1) + m + 1)
                    act.wait_ge(S["up_done"], 4 * s + 2 * m + 1)
                    act.activation(sg[:, m, :], K.bank[2 * m][:, :], ACT.Silu).then_inc(S["silu_done"], 1)

        @block.vector
        def _(dve):
            def gated(s):
                for m in range(2):
                    dve.wait_ge(S["silu_done"], 2 * s + m + 1)
                    dve.wait_ge(S["up_done"], 4 * s + 2 * m + 2)
                    dve.tensor_tensor(aT[:, s, m, :], sg[:, m, :], K.bank[2 * m + 1][:, :], ALU.mult)\
                        .then_inc(S["act_done"], 1)

            for s in range(N):
                gated(s)
            for s in range(N):
                for j in range(JX):
                    for n in range(2):
                        u = 8 * s + 2 * j + n
                        if s:
                            dve.wait_ge(S["acc_done"], u - 7)
                        dve.wait_ge(S["down_done"], u + 1)
                        part = acc[:, j, n * 512:(n + 1) * 512]
                        dve.scalar_tensor_tensor(out=part, in0=K.bank[4 + u % 4][:, :], scalar=weights[s](j),
                                                 in1=part, op0=ALU.mult, op1=ALU.add).then_inc(S["acc_done"], 1)


def experts_start(K, I, Wb):
    with phase(K.nc, "in0") as (block, S):
        @block.sync
        def _(sp):
            load_expert(sp, Wb, 0, (I["exp_w_gate"][0, 0], I["exp_w_up"][0, 0], I["exp_w_down"][0, 0]), S["in0"])
            sp.wait_ge(S["in0"], 48)


def add_experts(K, acc, gate):
    nc = K.nc
    with phase(nc, "gated added") as (block, S):
        @block.vector
        def _(dve):
            for j in range(JX):
                dve.tensor_tensor(acc[:, j, :], acc[:, j, :], gate, ALU.mult).then_inc(S["gated"], 1)
            for j in range(JX):
                dve.wait_ge(S["gated"], j + 1)
                dve.tensor_tensor(K.X[:, JC + j, :], K.X[:, JC + j, :], acc[:, j, :], ALU.add).then_inc(S["added"], 1)

TOP_K = 6
SLOTS = P
FURTHER = TX * TOP_K // SLOTS
TILES = NE + FURTHER
UNUSED = 1e6


def forget(pool, sems):
    for sem in sems:
        pool.dma_reset(range(sem.num, sem.num + 1))


def dispatch(K, wt, kept, slot_of, w_of, extra, h_rows, slot_tokens, ys, idx):
    nc = K.nc
    U32 = mybir.dt.uint32
    names = ("pos_mm copied v_step fill_set filled slots_set sc0 sc1 sc2 sc3 sc4 sc5 sc6 sc7 scattered back idx_mm idx_out "
             "h_mm h_a h_b h_st0 h_st1 blank_set blanked")
    with ExitStack() as c, phase(nc, names) as (block, S):
        buf = lambda name, shape, dt=F32: c.enter_context(sbuf(nc, "dp_" + name, shape, dt))
        pos, fits, run, m, pr, slot = (buf(n, [P, JX, NE]) for n in ("pos", "fits", "run", "m", "pr", "slot"))
        to_f = buf("to", [P, TOP_K, JX])
        cnt, more, upto, away, near = (buf(n, [P, NE]) for n in ("cnt", "more", "upto", "away", "near"))
        which, ext = buf("which", [P, FURTHER, NE]), buf("ext", [P, 1 + FURTHER])
        fill, back = buf("fill", [TILES, SLOTS]), buf("back", [TILES, SLOTS])
        rows, blank = buf("rows", [P, 2, D]), buf("blank", [P, D])
        first = K.const[:, SLOT_COL:SLOT_COL + NE]
        every = lambda ap: ap.unsqueeze(1).broadcast_to([P, JX, NE])
        table = slot_tokens.rearrange("(e s) o -> e (s o)", s=SLOTS)

        @block.tensor
        def _(pe):
            for j in range(JX):
                out = K.bank[0][:, j * NE:(j + 1) * NE]
                pe.matmul(out, K.before, kept[:, j, :], start=True, stop=(j == 0))
                for i in range(j):
                    pe.matmul(out, K.ones, kept[:, i, :], start=False, stop=(i == j - 1))
            for j in range(JX):
                mm = pe.matmul(K.bank[0][:, JX * NE:(JX + 1) * NE], K.ones, kept[:, j, :],
                               start=(j == 0), stop=(j == JX - 1))
            mm.then_inc(S["pos_mm"], 1)
            for j in range(JX):
                if j >= 2:
                    pe.wait_ge(S["h_a"], j - 1)
                    pe.wait_ge(S["h_b"], j - 1)
                for k in range(KD):
                    tr = pe.transpose(K.bank[2 + 2 * (j % 2) + k // 4][:, (k % 4) * P:(k % 4 + 1) * P],
                                      K.hT[:, k, TC + j * P:TC + (j + 1) * P], K.ident)
                tr.then_inc(S["h_mm"], 1)
            pe.wait_ge(S["back"], 16)
            pe.transpose(K.bank[1][:, 0:TILES], back[:, :], K.ident[0:TILES, 0:TILES]).then_inc(S["idx_mm"], 1)

        @block.scalar
        def _(act):
            act.wait_ge(S["blank_set"], 1)
            for n in range(NE, TILES + 1):
                act.dma_start(ys[n * SLOTS:(n + 1) * SLOTS, :], blank[:, :]).then_inc(S["blanked"], 16)
            for j in range(JX):
                act.wait_ge(S["h_mm"], j + 1)
                if j >= 2:
                    act.wait_ge((S["h_st0"], S["h_st1"])[j % 2], 16)
                act.activation(rows[:, j % 2, 0:512], K.bank[2 + 2 * (j % 2)][:, :], ACT.Copy).then_inc(S["h_a"], 1)
                act.activation(rows[:, j % 2, 512:D], K.bank[3 + 2 * (j % 2)][:, :], ACT.Copy).then_inc(S["h_b"], 1)
            act.wait_ge(S["blanked"], 16 * (TILES + 1 - NE))

        @block.sync
        def _(sp):
            sp.wait_ge(S["fill_set"], 1)
            sp.dma_start(table, fill[:, :]).then_inc(S["filled"], 16)
            for j in range(JX):
                sp.wait_ge(S["h_a"], j + 1)
                sp.wait_ge(S["h_b"], j + 1)
                sp.dma_start(h_rows[j * P:(j + 1) * P, :], rows[:, j % 2, :]).then_inc((S["h_st0"], S["h_st1"])[j % 2], 16)
            sp.wait_ge(S["scattered"], 1)
            sp.dma_start(back[:, :], table).then_inc(S["back"], 16)
            sp.wait_ge(S["h_st0"], 32)
            sp.wait_ge(S["h_st1"], 32)

        @block.gpsimd
        def _(pool):
            pool.wait_ge(S["filled"], 16)
            pool.wait_ge(S["slots_set"], 1)
            sc = [S[f"sc{n}"] for n in range(8)]
            for k in range(TOP_K):
                for j in range(JX):
                    u = k * JX + j
                    if u >= 8:
                        pool.wait_ge(sc[u % 8], 16 * (u // 8))
                    pool.indirect_dma_start(
                        out=slot_tokens, out_offset=bass.IndirectOffsetOnAxis(ap=slot_of[:, k, j:j + 1], axis=0),
                        in_=K.const[:, TOKEN_COL + j:TOKEN_COL + j + 1], in_offset=None,
                        bounds_check=TILES * SLOTS - 1, oob_is_err=False).then_inc(sc[u % 8], 16)
            for n in range(8):
                pool.wait_ge(sc[n], 16 * (TOP_K * JX // 8))
            forget(pool, sc)
            pool.sem_inc(S["scattered"], 1)

        @block.vector
        def _(dve):
            step = Chain(dve, S["v_step"])
            dve.memset(fill[:, :], UNUSED).then_inc(S["fill_set"], 1)
            dve.memset(blank[:, :], 0.0).then_inc(S["blank_set"], 1)
            dve.wait_ge(S["pos_mm"], 1)
            step.put(dve.tensor_copy(pos[:, :, :], K.bank[0][:, 0:JX * NE].rearrange("p (j e) -> p j e", e=NE)))
            step(dve.tensor_copy(cnt[:, :], K.bank[0][:, JX * NE:(JX + 1) * NE]))
            step(dve.tensor_scalar(more[:, :], cnt[:, :], float(SLOTS), None, ALU.is_gt))
            for n in range(2, TX // SLOTS):
                step(dve.scalar_tensor_tensor(out=more[:, :], in0=cnt[:, :], scalar=float(n * SLOTS), in1=more[:, :],
                                              op0=ALU.is_gt, op1=ALU.add))
            step(dve.tensor_tensor_scan(upto[:, :], more[:, :], K.zeros[:, 0:NE], 0.0, ALU.add, ALU.add))
            step(dve.tensor_tensor(away[:, :], upto[:, :], more[:, :], ALU.subtract))
            step(dve.tensor_scalar(away[:, :], away[:, :], float(NE - 1), float(SLOTS), ALU.add, ALU.mult))
            step(dve.tensor_tensor(near[:, :], first, away[:, :], ALU.subtract))
            step(dve.tensor_scalar(fits[:, :, :], pos[:, :, :], float(SLOTS), None, ALU.is_lt))
            step.put(dve.tensor_tensor(slot[:, :, :], pos[:, :, :], every(away[:, :]), ALU.add))
            step(dve.tensor_tensor(fits[:, :, :], fits[:, :, :], every(near[:, :]), ALU.mult))
            step(dve.tensor_tensor(slot[:, :, :], slot[:, :, :], fits[:, :, :], ALU.add))
            for j in range(JX):
                step.put(dve.tensor_tensor_scan(run[:, j, :], kept[:, j, :], K.zeros[:, 0:NE], 0.0, ALU.add, ALU.add))
            step.wait()
            for k in range(TOP_K):
                step(dve.scalar_tensor_tensor(out=m[:, :, :], in0=run[:, :, :], scalar=k + 1.0, in1=kept[:, :, :],
                                              op0=ALU.is_equal, op1=ALU.mult))
                step(dve.tensor_tensor(pr[:, :, :], m[:, :, :], slot[:, :, :], ALU.mult))
                step.put(dve.tensor_reduce(to_f[:, k, :], pr[:, :, :], AX.X, ALU.add))
                step(dve.tensor_tensor(m[:, :, :], m[:, :, :], wt[:, :, :], ALU.mult))
                step(dve.tensor_reduce(w_of[:, k, :], m[:, :, :], AX.X, ALU.add))
            dve.tensor_copy(slot_of[:, :, :], to_f[:, :, :]).then_inc(S["slots_set"], 1)
            step(dve.tensor_scalar(near[:, :], upto[:, :], float(SLOTS), None, ALU.mult))
            step(dve.tensor_tensor(which[:, :, :], near[:, :].unsqueeze(1).broadcast_to([P, FURTHER, NE]),
                                   first[:, 0:FURTHER].unsqueeze(2).broadcast_to([P, FURTHER, NE]), ALU.is_le))
            step.put(dve.tensor_copy(ext[:, 0:1], upto[:, NE - 1:NE]))
            step(dve.tensor_reduce(ext[:, 1:1 + FURTHER], which[:, :, :], AX.X, ALU.add))
            step(dve.tensor_scalar(ext[:, 1:1 + FURTHER], ext[:, 1:1 + FURTHER], float(NE - 1), None, ALU.min))
            step.put(dve.tensor_copy(extra[:, 0:1 + FURTHER], ext[:, :]))
            dve.wait_ge(S["idx_mm"], 1)
            dve.tensor_copy(idx[:, 0:TILES], K.bank[1][:, 0:TILES]).then_inc(S["idx_out"], 1)


def gather_rows(pool, Hg, col, h_rows, sem):
    pool.indirect_dma_start(out=Hg, out_offset=None, in_=h_rows,
                            in_offset=bass.IndirectOffsetOnAxis(ap=col, axis=0),
                            bounds_check=TX - 1, oob_is_err=False).then_inc(sem, 16)


def slots_start(K, Wb, Hg, h_rows, idx, cols, tile, weights):
    with phase(K.nc, "in0 zeroed copied got0 got1") as (block, S):
        @block.sync
        def _(sp):
            load_expert(sp, Wb, 0, weights, S["in0"])
            sp.wait_ge(S["in0"], 48)

        @block.vector
        def _(dve):
            dve.memset(Hg[:, :, :], 0.0).then_inc(S["zeroed"], 1)

        @block.tensor
        def _(pe):
            pe.wait_ge(S["zeroed"], 1)

        @block.scalar
        def _(act):
            act.wait_ge(S["zeroed"], 1)

        @block.gpsimd
        def _(pool):
            pool.tensor_copy(cols[:, :], idx[:, bass.ds(tile, 2)]).then_inc(S["copied"], 1)
            pool.wait_ge(S["copied"], 1)
            pool.wait_ge(S["zeroed"], 1)
            for s in range(2):
                gather_rows(pool, Hg[:, s, :], cols[:, s:s + 1], h_rows, S[f"got{s}"])
            for s in range(2):
                pool.wait_ge(S[f"got{s}"], 16)
            forget(pool, (S["got0"], S["got1"]))


def slot_experts(K, Wb, Hg, cols, XT, aT, sg, yb, idx, h_rows, ys, e, following, more):
    nc = K.nc
    names = "in0 in1 turned xt_a xt_b up_done silu_done act_done down_done y_a y_b st0 st1 cols_set got0 got1"
    with phase(nc, names) as (block, S):
        banks_t = ((0, 1), (2, 3))
        banks_y = ((6, 7), (0, 1))
        st = (S["st0"], S["st1"])
        got = (S["got0"], S["got1"])

        @block.sync
        def _(sp):
            load_expert(sp, Wb, 1, following[1], S["in1"])
            if following[0] is not None:
                sp.wait_ge(S["down_done"], 2)
                load_expert(sp, Wb, 0, following[0], S["in0"])
            for s in range(2):
                sp.wait_ge(S["y_a"], s + 1)
                sp.wait_ge(S["y_b"], s + 1)
                sp.dma_start(ys[bass.ds((e + s) * SLOTS, SLOTS), :], yb[:, s, :]).then_inc(st[s], 16)
            if following[0] is not None:
                sp.wait_ge(S["in0"], 48)
            for s in range(2):
                sp.wait_ge(st[s], 16)

        @block.gpsimd
        def _(pool):
            if more:
                pool.tensor_copy(cols[:, :], idx[:, bass.ds(e + 2, 2)]).then_inc(S["cols_set"], 1)
                pool.wait_ge(S["cols_set"], 1)
                for s in range(2):
                    pool.wait_ge(S["turned"], s + 1)
                    gather_rows(pool, Hg[:, s, :], cols[:, s:s + 1], h_rows, got[s])
                for s in range(2):
                    pool.wait_ge(got[s], 16)
                forget(pool, got)
            else:
                pool.wait_ge(S["turned"], 2)

        @block.tensor
        def _(pe):
            def turn(s):
                for k in range(KD):
                    tr = pe.transpose(K.bank[banks_t[s][k // 4]][:, (k % 4) * P:(k % 4 + 1) * P],
                                      Hg[:, s, k * P:(k + 1) * P], K.ident)
                tr.then_inc(S["turned"], 1)

            def up(s):
                pe.wait_ge(S["xt_a"], s + 1)
                pe.wait_ge(S["xt_b"], s + 1)
                if s:
                    pe.wait_ge(S["in1"], 48)
                for m in range(2):
                    for which in range(2):
                        q = 2 * which + m
                        for k in range(KD):
                            mm = pe.matmul(K.bank[4 + s][:, q * P:(q + 1) * P],
                                           Wb[:, s, which, k * DE + m * P:k * DE + (m + 1) * P],
                                           XT[:, s, k, :], start=(k == 0), stop=(k == KD - 1))
                mm.then_inc(S["up_done"], 1)

            def down(s):
                pe.wait_ge(S["act_done"], s + 1)
                for n in range(2):
                    for m in range(2):
                        mm = pe.matmul(K.bank[banks_y[s][n]][:, :], aT[:, s, m, :],
                                       Wb[:, s, 2, m * D + n * 512:m * D + (n + 1) * 512],
                                       start=(m == 0), stop=(m == 1))
                    mm.then_inc(S["down_done"], 1)

            turn(0)
            turn(1)
            up(0)
            up(1)
            down(0)
            down(1)

        @block.scalar
        def _(act):
            for s in range(2):
                act.wait_ge(S["turned"], s + 1)
                act.activation(XT[:, s, 0:4, :], K.bank[banks_t[s][0]].rearrange("p (k t) -> p k t", k=4), ACT.Copy)\
                    .then_inc(S["xt_a"], 1)
            for s in range(2):
                act.wait_ge(S["up_done"], s + 1)
                act.activation(sg[:, s, :, :], K.bank[4 + s][:, 0:2 * P].rearrange("p (m t) -> p m t", m=2), ACT.Silu)\
                    .then_inc(S["silu_done"], 1)
            for s in range(2):
                act.wait_ge(S["down_done"], 2 * s + 1)
                act.activation(yb[:, s, 0:512], K.bank[banks_y[s][0]], ACT.Copy).then_inc(S["y_a"], 1)

        @block.vector
        def _(dve):
            for s in range(2):
                dve.wait_ge(S["turned"], s + 1)
                dve.tensor_copy(XT[:, s, 4:8, :], K.bank[banks_t[s][1]].rearrange("p (k t) -> p k t", k=4))\
                    .then_inc(S["xt_b"], 1)
            for s in range(2):
                dve.wait_ge(S["silu_done"], s + 1)
                dve.tensor_tensor(aT[:, s, :, :], sg[:, s, :, :],
                                  K.bank[4 + s][:, 2 * P:4 * P].rearrange("p (m t) -> p m t", m=2), ALU.mult)\
                    .then_inc(S["act_done"], 1)
            for s in range(2):
                dve.wait_ge(S["down_done"], 2 * s + 2)
                dve.tensor_copy(yb[:, s, 512:D], K.bank[banks_y[s][1]]).then_inc(S["y_b"], 1)


def combine(K, acc, ys, slot_of, w_of):
    nc = K.nc
    RINGN = 4
    units = [(j, k) for k in range(TOP_K) for j in range(JX)]
    with ExitStack() as c, phase(nc, "g0 g1 g2 g3 added") as (block, S):
        rows = c.enter_context(sbuf(nc, "cb_rows", [P, RINGN, D], F32))
        g = (S["g0"], S["g1"], S["g2"], S["g3"])

        @block.gpsimd
        def _(pool):
            for u, (j, k) in enumerate(units):
                if u >= RINGN:
                    pool.wait_ge(S["added"], u - RINGN + 1)
                pool.indirect_dma_start(out=rows[:, u % RINGN, :], out_offset=None, in_=ys,
                                        in_offset=bass.IndirectOffsetOnAxis(ap=slot_of[:, k, j:j + 1], axis=0),
                                        bounds_check=TILES * SLOTS - 1, oob_is_err=False).then_inc(g[u % RINGN], 16)
            for n in range(RINGN):
                pool.wait_ge(g[n], 16 * (len(units) // RINGN))
            forget(pool, g)

        @block.vector
        def _(dve):
            for u, (j, k) in enumerate(units):
                dve.wait_ge(g[u % RINGN], 16 * (u // RINGN + 1))
                if k:
                    dve.wait_ge(S["added"], u - JX + 1)
                dve.scalar_tensor_tensor(out=acc[:, j, :], in0=rows[:, u % RINGN, :], scalar=w_of[:, k, j:j + 1],
                                         in1=acc[:, j, :], op0=ALU.mult, op1=ALU.add).then_inc(S["added"], 1)


def mixture(K, I, scratch):
    nc = K.nc
    h_rows, slot_tokens, ys = scratch["h_rows"], scratch["slot_tokens"], scratch["ys"]
    U32 = mybir.dt.uint32
    src = lambda e: tuple(a[0][bass.ds(e, 1)].rearrange("o k n -> (o k) n")
                          for a in (I["exp_w_gate"], I["exp_w_up"], I["exp_w_down"]))
    shared = (I["sh_w_gate"][0], I["sh_w_up"][0], I["sh_w_down"][0])
    with ExitStack() as c:
        sb = lambda name, shape, dt=F32, s=c: s.enter_context(sbuf(nc, name, shape, dt))
        wt, kept = (sb("expert_" + n, [P, JX, NE]) for n in ("weights", "kept"))
        slot_of, w_of = sb("slot_of", [P, TOP_K, JX], U32), sb("w_of", [P, TOP_K, JX])
        extra, idx = sb("extra", [P, 2 + FURTHER], mybir.dt.int32), sb("slot_idx", [P, TILES + 1], U32)
        router(K, I, wt, kept)
        dispatch(K, wt, kept, slot_of, w_of, extra, h_rows, slot_tokens, ys, idx)
        Wb = sb("ex_w", [P, 2, 3, KD * DE])
        with ExitStack() as c2:
            Hg, yb = sb("slot_rows", [P, 2, D], F32, c2), sb("slot_out", [P, 2, D], F32, c2)
            XT = sb("slot_x", [P, 2, KD, P], F32, c2)
            aT, sg = sb("slot_act", [P, 2, 2, P], F32, c2), sb("slot_silu", [P, 2, 2, P], F32, c2)
            cols = sb("slot_cols", [P, 2], U32, c2)
            step = lambda e, following, more: slot_experts(K, Wb, Hg, cols, XT, aT, sg, yb, idx, h_rows, ys, e,
                                                           following, more)
            in_use = nc.values_load(extra[0:1, 0:1], min_val=0, max_val=FURTHER)
            with nc.Fori(0, FURTHER, 2) as u:
                with nc.If(in_use > u):
                    owner = [nc.values_load(extra[0:1, bass.ds(u + 1 + s, 1)], engines=(mybir.EngineType.SP,),
                                            min_val=0, max_val=NE - 1) for s in range(2)]
                    slots_start(K, Wb, Hg, h_rows, idx, cols, u + NE, src(owner[0]))
                    step(u + NE, (None, src(owner[1])), False)
            slots_start(K, Wb, Hg, h_rows, idx, cols, 0, src(0))
            with nc.Fori(0, NE - 2, 2) as e:
                step(e, (src(e + 2), src(e + 1)), True)
            step(NE - 2, (shared, src(NE - 1)), False)
        acc = sb("ex_acc", [P, JX, D])
        with phase(nc, "zeroed") as (block, S):
            @block.vector
            def _(dve):
                dve.memset(acc[:, :, :], 0.0).then_inc(S["zeroed"], 1)
        experts(K, Wb, acc, ((lambda j: K.one[:, :]),), (None,))
        combine(K, acc, ys, slot_of, w_of)
        add_experts(K, acc, K.gate[:, 1, :])

(R_, V_, KK_, K_, GATE_, BONUS_, KD_, B_, LW_) = (0, 1, 2, 3, 4, 5, 6, 8, 10)
N_RW = 12
DECAY = float(2.718281828459045 ** -0.5)


def rwkv_projections(K, I, rw, tw, ta):
    nc = K.nc
    names = ("edges xx_sum xx_done lerped w_in0 w_in1 w1_in mm_done lora_done evac lora_out "
             "st0 st1 st2 st3")
    dest = (R_, K_, V_, GATE_)
    with ExitStack() as c, phase(nc, names) as (block, S):
        xx = c.enter_context(sbuf(nc, "rp_xx", [P, KD, TT], F32))
        lerp = c.enter_context(sbuf(nc, "rp_lerp", [P, 2, KD, TT], F32))
        wb = c.enter_context(sbuf(nc, "rp_w", [P, 2, KD, 512], F32))
        w1 = c.enter_context(sbuf(nc, "rp_w1", [P, 2, KD, 2 * LORA], F32))
        stage = c.enter_context(sbuf(nc, "rp_stage", [P, 4, 512], F32))
        w_in = (S["w_in0"], S["w_in1"])
        st = (S["st0"], S["st1"], S["st2"], S["st3"])
        units = [(n, half, j) for n in range(4) for half in range(2) for j in range(NT)]

        @block.sync
        def _(sp):
            for a, w in enumerate((I["rwkv_w1_2"], I["rwkv_a1_2"])):
                for d in range(2):
                    sp.dma_start(w1[:, a, :, d * LORA:(d + 1) * LORA], w[0, d].rearrange("(k p) r -> p k r", p=P))\
                        .then_inc(S["w1_in"], 16)
            for u in range(8):
                if u >= 2:
                    sp.wait_ge(S["mm_done"], NT * (u - 1))
                n, half = divmod(u, 2)
                w = I["rwkv_w_in_2"][0, n].rearrange("(k p) n -> p k n", p=P)
                sp.dma_start(wb[:, u % 2, :, :], w[:, :, half * 512:(half + 1) * 512]).then_inc(w_in[u % 2], 16)

        @block.vector
        def _(dve):
            h = K.hT
            for t0, t1 in ((0, TC), (TC, TT)):
                dve.tensor_tensor(xx[:, :, t0 + 1:t1 - 1], h[:, :, t0:t1 - 2], h[:, :, t0 + 2:t1], ALU.add)
                dve.tensor_copy(xx[:, :, t0:t0 + 1], h[:, :, t0 + 1:t0 + 2])
                dve.tensor_copy(xx[:, :, t1 - 1:t1], h[:, :, t1 - 2:t1 - 1]).then_inc(S["xx_sum"], 1)
            dve.wait_ge(S["xx_sum"], 2)
            dve.scalar_tensor_tensor(out=xx[:, :, :], in0=xx[:, :, :], scalar=0.5, in1=h[:, :, :],
                                     op0=ALU.mult, op1=ALU.subtract).then_inc(S["xx_done"], 1)
            dve.wait_ge(S["xx_done"], 1)
            for n in range(6):
                if n in (2, 3, 4):
                    dve.wait_ge(S["mm_done"], 2 * NT * (n - 1))
                if n == 5:
                    dve.wait_ge(S["mm_done"], 2 * NT * 4)
                for k in range(KD):
                    ins = dve.scalar_tensor_tensor(out=lerp[:, n % 2, k, :], in0=xx[:, k, :],
                                                   scalar=K.colC[:, n * KD + k:n * KD + k + 1], in1=h[:, k, :],
                                                   op0=ALU.mult, op1=ALU.add)
                ins.then_inc(S["lerped"], 1)

        @block.tensor
        def _(pe):
            for u, (n, half, j) in enumerate(units):
                if j == 0:
                    pe.wait_ge(S["lerped"], n + 1)
                    pe.wait_ge(w_in[half], 16 * (n + 1))
                if u >= 4:
                    pe.wait_ge(S["evac"], u - 3)
                for k in range(KD):
                    mm = pe.matmul(K.bank[u % 4][:, :], lerp[:, n % 2, k, j * P:(j + 1) * P], wb[:, half, k, :],
                                   start=(k == 0), stop=(k == KD - 1))
                mm.then_inc(S["mm_done"], 1)
            pe.wait_ge(S["w1_in"], 64)
            for a in range(2):
                pe.wait_ge(S["lerped"], 5 + a)
                for b, (t0, t1) in enumerate(((0, TC), (TC, TT))):
                    for k in range(KD):
                        mm = pe.matmul(K.bank[4 + 2 * a + b][:, 0:t1 - t0], w1[:, a, k, :], lerp[:, a, k, t0:t1],
                                       start=(k == 0), stop=(k == KD - 1))
                    mm.then_inc(S["lora_done"], 1)

        @block.scalar
        def _(act):
            def store(u):
                n, half, j = units[u]
                act.wait_ge(S["evac"], u + 1)
                act.dma_start(rw[dest[n], j * P:(j + 1) * P, half * 512:(half + 1) * 512], stage[:, u % 4, :])\
                    .then_inc(st[u % 4], 16)

            for u, (n, half, j) in enumerate(units):
                act.wait_ge(S["mm_done"], u + 1)
                if u >= 4:
                    act.wait_ge(st[u % 4], 16 * (u // 4))
                act.activation(stage[:, u % 4, :], K.bank[u % 4][:, :], ACT.Silu if n == 3 else ACT.Copy)\
                    .then_inc(S["evac"], 1)
                if u:
                    store(u - 1)
            store(len(units) - 1)
            for a in range(2):
                for b, (t0, t1) in enumerate(((0, TC), (TC, TT))):
                    act.wait_ge(S["lora_done"], 2 * a + b + 1)
                    act.activation((tw, ta)[a][:, t0:t1], K.bank[4 + 2 * a + b][:, 0:t1 - t0],
                                   (ACT.Tanh, ACT.Copy)[a]).then_inc(S["lora_out"], 1)
            for q in range(4):
                act.wait_ge(st[q], 16 * (len(units) // 4))


def rwkv_prepare(K, I, rw, tw, ta):
    nc = K.nc
    with ExitStack() as c0:
        sb = lambda name, shape, c: c.enter_context(sbuf(nc, "rq_" + name, shape, F32))
        w0, a0, w2 = sb("w0", [P, 2, D], c0), sb("a0", [P, 2, D], c0), sb("w2", [P, 2, D], c0)
        kk_p, ka_p, rk_p = sb("k_k", [P, D], c0), sb("k_a", [P, D], c0), sb("r_k", [P, D], c0)
        with phase(nc, "in_done") as (block, S):
            @block.sync
            def _(sp):
                for d in range(2):
                    sp.dma_start(w0[:, d, :], I["rwkv_w0_2"][0, d].partition_broadcast(P)).then_inc(S["in_done"], 16)
                    sp.dma_start(a0[:, d, :], I["rwkv_a0_2"][0, d].partition_broadcast(P)).then_inc(S["in_done"], 16)
                sp.dma_start(w2[:, 0, :], I["rwkv_w2_2"][0].rearrange("d r n -> (d r) n")).then_inc(S["in_done"], 16)
                sp.dma_start(w2[:, 1, :], I["rwkv_a2_2"][0].rearrange("d r n -> (d r) n")).then_inc(S["in_done"], 16)
                sp.dma_start(kk_p[:, :], I["rwkv_k_k_2"][0].partition_broadcast(P)).then_inc(S["in_done"], 16)
                sp.dma_start(ka_p[:, :], I["rwkv_k_a_2"][0].partition_broadcast(P)).then_inc(S["in_done"], 16)
                sp.dma_start(rk_p[:, :], I["rwkv_r_k_2"][0].rearrange("h n -> (h n)").partition_broadcast(P))\
                    .then_inc(S["in_done"], 16)
                sp.wait_ge(S["in_done"], 16 * 9)
        kin, rin, vin = sb("k", [P, D], c0), sb("r", [P, D], c0), sb("v", [P, D], c0)
        kk, sq, bon = sb("kk", [P, D], c0), sb("sq", [P, D], c0), sb("bonus", [P, D], c0)
        lw, aa, kd, bb = (sb(n, [P, 2, D], c0) for n in ("lw", "a", "kd", "b"))
        st = sb("stats", [P, 4, H2], c0)
        low = sb("low", [P, 2, P], c0)
        heads = lambda t: t.rearrange("p (h n) -> p h n", n=HD)
        wide = lambda ap: ap.unsqueeze(2).broadcast_to([P, H2, HD])
        with nc.Fori(0, NT) as j:
            with phase(nc, "in_k in_r in_v lowered mm_done v_step a_step p_step stored") as (block, S):
                rows = bass.ds(j * P, P)

                @block.sync
                def _(sp):
                    sp.dma_start(kin[:, :], rw[K_, rows, :]).then_inc(S["in_k"], 16)
                    sp.dma_start(rin[:, :], rw[R_, rows, :]).then_inc(S["in_r"], 16)
                    sp.dma_start(vin[:, :], rw[V_, rows, :]).then_inc(S["in_v"], 16)
                    sp.wait_ge(S["v_step"], 13)
                    sp.dma_start(rw[KK_, rows, :], kk[:, :]).then_inc(S["stored"], 16)
                    for d in range(2):
                        sp.dma_start(rw[LW_ + d, rows, :], lw[:, d, :]).then_inc(S["stored"], 16)
                        sp.dma_start(rw[KD_ + d, rows, :], kd[:, d, :]).then_inc(S["stored"], 16)
                    sp.wait_ge(S["p_step"], 2)
                    for d in range(2):
                        sp.dma_start(rw[B_ + d, rows, :], bb[:, d, :]).then_inc(S["stored"], 16)
                    sp.wait_ge(S["v_step"], 18)
                    sp.dma_start(rw[BONUS_, rows, :], bon[:, :]).then_inc(S["stored"], 16)
                    sp.wait_ge(S["stored"], 16 * 8)

                @block.tensor
                def _(pe):
                    pe.wait_ge(S["lowered"], 2)
                    for a in range(2):
                        for d in range(2):
                            for half in range(2):
                                pe.matmul(K.bank[4 * a + 2 * d + half][:, :], low[d * LORA:(d + 1) * LORA, a, :],
                                          w2[d * LORA:(d + 1) * LORA, a, half * 512:(half + 1) * 512],
                                          start=True, stop=True).then_inc(S["mm_done"], 1)

                @block.scalar
                def _(act):
                    act.activation(low[:, 0, :], tw[:, rows], ACT.Copy).then_inc(S["lowered"], 1)
                    act.activation(low[:, 1, :], ta[:, rows], ACT.Copy).then_inc(S["lowered"], 1)
                    step = Chain(act, S["a_step"])
                    act.wait_ge(S["v_step"], 1)
                    step.put(act.activation(sq[:, :], kk[:, :], ACT.Square))
                    act.wait_ge(S["v_step"], 2)
                    step.put(act.activation(st[:, 1, :], st[:, 0, :], ACT.Sqrt))
                    act.wait_ge(S["v_step"], 4)
                    step.put(act.activation(lw[:, :, :], lw[:, :, :], ACT.Sigmoid))
                    act.wait_ge(S["v_step"], 5)
                    step.put(act.activation(aa[:, :, :], aa[:, :, :], ACT.Sigmoid))

                @block.gpsimd
                def _(pool):
                    for d in range(2):
                        pool.wait_ge(S["v_step"], 8)
                        pool.wait_ge(S["a_step"], 4)
                        pool.tensor_tensor(bb[:, d, :], kk[:, :], aa[:, d, :], ALU.mult).then_inc(S["p_step"], 1)

                @block.vector
                def _(dve):
                    step = Chain(dve, S["v_step"])
                    dve.wait_ge(S["in_k"], 16)
                    step.put(dve.tensor_tensor(kk[:, :], kin[:, :], kk_p[:, :], ALU.mult))
                    dve.wait_ge(S["a_step"], 1)
                    step.put(dve.tensor_reduce(st[:, 0, :], heads(sq[:, :]), AX.X, ALU.add))
                    for a, (dst, base) in enumerate(((lw, w0), (aa, a0))):
                        dve.wait_ge(S["mm_done"], 4 * a + 4)
                        for d in range(2):
                            for half in range(2):
                                part = slice(half * 512, (half + 1) * 512)
                                ins = dve.tensor_tensor(dst[:, d, part], K.bank[4 * a + 2 * d + half][:, :],
                                                        base[:, d, part], ALU.add)
                        step.put(ins)
                        if a == 0:
                            step.put(dve.memset(st[:, 3, :], 0.0))
                    dve.wait_ge(S["a_step"], 2)
                    step(dve.tensor_scalar(st[:, 1, :], st[:, 1, :], 1e-12, None, ALU.max))
                    step(dve.reciprocal(st[:, 2, :], st[:, 1, :]))
                    step.put(dve.tensor_tensor(heads(kk[:, :]), heads(kk[:, :]), wide(st[:, 2, :]), ALU.mult))
                    dve.wait_ge(S["a_step"], 4)
                    step.put(dve.tensor_scalar(lw[:, :, :], lw[:, :, :], -DECAY, None, ALU.mult))
                    for d in range(2):
                        step(dve.scalar_tensor_tensor(out=kd[:, d, :], in0=aa[:, d, :], scalar=1.0, in1=ka_p[:, :],
                                                      op0=ALU.subtract, op1=ALU.mult))
                        step(dve.scalar_tensor_tensor(out=kd[:, d, :], in0=kd[:, d, :], scalar=1.0, in1=kin[:, :],
                                                      op0=ALU.add, op1=ALU.mult))
                    dve.wait_ge(S["in_r"], 16)
                    step(dve.tensor_tensor(bon[:, :], kd[:, 0, :], kd[:, 1, :], ALU.add))
                    step(dve.tensor_tensor(bon[:, :], bon[:, :], rin[:, :], ALU.mult))
                    step(dve.tensor_tensor(bon[:, :], bon[:, :], rk_p[:, :], ALU.mult))
                    step(dve.tensor_reduce(st[:, 3, :], heads(bon[:, :]), AX.X, ALU.add))
                    dve.wait_ge(S["in_v"], 16)
                    step.put(dve.tensor_tensor(heads(bon[:, :]), heads(vin[:, :]), wide(st[:, 3, :]), ALU.mult))


UNITS = 4
UNIT_DIR = (0, 1, 0, 1)


def rwkv_step(K, rw, Y, St, FA, pair, tile_of):
    nc = K.nc
    names = " ".join(f"{n}{u}" for n in ("in", "mm", "v", "a", "p", "st") for u in range(UNITS))
    W = 4 * HD
    units = range(UNITS)
    with ExitStack() as c, phase(nc, names) as (block, S):
        def buf(name, shape):
            return [c.enter_context(sbuf(nc, f"rs_{name}", shape, F32)) for _ in units]

        IN = buf("in", [P, 6, W])
        E = buf("exps", [P, 3, W])
        TM = buf("tokens", [P, 4, W])
        FM = buf("features", [P, 2, 2, P])
        SC = buf("scores", [P, 4, 4, P])
        em = buf("em", [P, 2, 2])
        S0 = buf("s0", [P, 2, P])
        RH, yb, SA = ([E[u][:, n, :] for u in units] for n in range(3))
        inv = [Inverse.buffers(K, c, u) for u in units]
        bank = [K.bank[2 * u:2 * u + 2] for u in units]
        inv_bank = [(b[0], b[1], b[0]) for b in bank]
        ins_, mm, vs, as_, ps, sts = ([S[f"{n}{u}"] for u in units] for n in ("in", "mm", "v", "a", "p", "st"))
        M0 = 5 + Inverse.MM_COUNT
        V0 = 7 + Inverse.STEP_COUNT
        pairs = lambda t: t.rearrange("p (q n) -> p q n", q=2)
        rows = [bass.ds(tile_of[d] * P, P) for d in UNIT_DIR]
        cols = [bass.ds((pair * 2 + u // 2) * W, W) for u in units]

        @block.sync
        def _(sp):
            for u in units:
                d = UNIT_DIR[u]
                for n, src in enumerate((R_, V_, KK_, KD_ + d, B_ + d, LW_ + d)):
                    sp.dma_start(IN[u][:, n, :], rw[src, rows[u], cols[u]]).then_inc(ins_[u], 16)
            for u in units:
                sp.wait_ge(as_[u], 13)
                sp.dma_start(Y[UNIT_DIR[u], rows[u], cols[u]], yb[u]).then_inc(sts[u], 16)
            for u in units:
                sp.wait_ge(sts[u], 16)

        @block.scalar
        def _(act):
            for u in units:
                act.wait_ge(mm[u], 1)
                act.activation(E[u][:, 0, :], bank[u][0][:, 0:W], ACT.Exp).then_inc(as_[u], 1)
                act.activation(E[u][:, 1, :], bank[u][0][:, 0:W], ACT.Exp, scale=-1.0).then_inc(as_[u], 1)
                act.activation(em[u][:, :, :], bank[u][0][:, W:W + 4].rearrange("p (q n) -> p q n", q=2), ACT.Exp)\
                    .then_inc(as_[u], 1)
                act.wait_ge(vs[u], 1)
                act.activation(E[u][:, 2, :], E[u][:, 2, :], ACT.Exp).then_inc(as_[u], 1)
            for u in units:
                act.wait_ge(mm[u], 2)
                for p in range(2):
                    four = bank[u][p][:, :].rearrange("p (a t) -> p a t", a=4)
                    act.activation(FM[u][:, p, :, :], four[:, 0:2, :], ACT.Copy).then_inc(as_[u], 1)
                    for q in range(2):
                        own = slice(q * HD, (q + 1) * HD)
                        act.activation(FA[u][own, p, q, :, :], four[own, 2:4, :], ACT.Copy)\
                            .then_inc(as_[u], 1)
            for u in units:
                act.wait_ge(mm[u], 5)
                act.activation(RH[u], bank[u][1][:, 0:W], ACT.Copy).then_inc(as_[u], 1)
            for u in units:
                act.wait_ge(mm[u], M0 + 1)
                act.activation(SA[u], bank[u][0][:, 0:W], ACT.Copy, scale=-1.0).then_inc(as_[u], 1)
            for u in units:
                act.wait_ge(mm[u], M0 + 3)
                act.activation(yb[u], bank[u][0][:, W:2 * W], ACT.Copy).then_inc(as_[u], 1)

        @block.gpsimd
        def _(pool):
            for u in units:
                pool.wait_ge(ins_[u], 96)
                pool.wait_ge(as_[u], 2)
                for dst, src, e in ((0, 4, 1), (1, 3, 1), (3, 0, 0)):
                    pool.tensor_tensor(TM[u][:, dst, :], IN[u][:, src, :], E[u][:, e, :], ALU.mult).then_inc(ps[u], 1)

        @block.tensor
        def _(pe):
            def scores(u, p):
                for q in range(2):
                    for a in range(2):
                        m = pe.matmul(bank[u][q][:, a * 2 * P:(a + 1) * 2 * P], FM[u][:, p, a, :], FA[u][:, p, q, :, :],
                                      start=True, stop=True)
                m.then_inc(mm[u], 1)

            for u in units:
                pe.wait_ge(ins_[u], 96)
                lw = IN[u][:, 5, :]
                d = UNIT_DIR[u]
                pe.matmul(bank[u][0][:, 0:W], K.cum[d], lw, start=True, stop=True)
                for p in range(2):
                    m = pe.matmul(bank[u][0][:, W + 2 * p:W + 2 * p + 2], lw[:, p * P:(p + 1) * P],
                                  K.const[:, MIX_COL + 2 * d:MIX_COL + 2 * d + 2], start=True, stop=True)
                m.then_inc(mm[u], 1)
            for u in units:
                pe.wait_ge(ps[u], 3)
                pe.wait_ge(vs[u], 3)
                for p in range(2):
                    for a in range(4):
                        t = pe.transpose(bank[u][p][:, a * P:(a + 1) * P], TM[u][:, a, p * P:(p + 1) * P], K.ident)
                t.then_inc(mm[u], 1)
            for u in units:
                pe.wait_ge(as_[u], 10)
                scores(u, 0)
            for u in units:
                pe.wait_ge(vs[u], 5)
                scores(u, 1)
            for u in units:
                V = IN[u][:, 1, :]
                pe.wait_ge(vs[u], 7)
                for h in range(4):
                    p, q = divmod(h, 2)
                    hc = slice(h * HD, (h + 1) * HD)
                    pe.matmul(bank[u][1][:, hc], FA[u][:, p, q, 0, :], S0[u][:, p, q * HD:(q + 1) * HD],
                              start=True, stop=False)
                    m = pe.matmul(bank[u][1][:, hc], SC[u][:, h, 2, :], V[:, hc], start=False, stop=True)
                m.then_inc(mm[u], 1)
            for u in units:
                pe.wait_ge(as_[u], 11)
            tensor_inverses(pe, K, [lambda h, u=u: SC[u][:, h, 0, :] for u in units], inv, inv_bank, vs, 7, mm)
            for u in units:
                Z = inv[u][1]
                pe.wait_ge(vs[u], V0)
                for h in range(4):
                    m = pe.matmul(bank[u][0][:, h * HD:(h + 1) * HD], Z[:, h, :], RH[u][:, h * HD:(h + 1) * HD],
                                  start=True, stop=True)
                m.then_inc(mm[u], 1)
            for u in units:
                V = IN[u][:, 1, :]
                pe.wait_ge(as_[u], 12)
                for p in range(2):
                    pc = slice(p * P, (p + 1) * P)
                    pe.matmul(bank[u][1][:, pc], TM[u][:, 1, pc], V[:, pc], start=True, stop=False)
                    m = pe.matmul(bank[u][1][:, pc], TM[u][:, 0, pc], SA[u][:, pc], start=False, stop=True)
                m.then_inc(mm[u], 1)
                for h in range(4):
                    p, q = divmod(h, 2)
                    hc, out = slice(h * HD, (h + 1) * HD), bank[u][0][:, W + h * HD:W + (h + 1) * HD]
                    pe.matmul(out, FA[u][:, p, q, 1, :], S0[u][:, p, q * HD:(q + 1) * HD], start=True, stop=False)
                    pe.matmul(out, SC[u][:, h, 3, :], V[:, hc], start=False, stop=False)
                    m = pe.matmul(out, SC[u][:, h, 1, :], SA[u][:, hc], start=False, stop=True)
                m.then_inc(mm[u], 1)

        @block.vector
        def _(dve):
            steps = [Chain(dve, vs[u]) for u in units]

            def masks(u, p):
                for q in range(2):
                    steps[u].put(dve.tensor_tensor(
                        SC[u][:, 2 * p + q, :, :].rearrange("p (a b) t -> p a b t", a=2),
                        bank[u][q][:, :].rearrange("p (a b t) -> p a b t", a=2, b=2),
                        K.mask2[UNIT_DIR[u]].unsqueeze(1).broadcast_to([P, 2, 2, P]), ALU.mult))

            for u in units:
                step = steps[u]
                dve.wait_ge(ins_[u], 96)
                dve.wait_ge(as_[u], 3)
                step.put(dve.tensor_tensor(E[u][:, 2, :], bank[u][0][:, 0:W], IN[u][:, 5, :], ALU.subtract))
                for p in range(2):
                    ins = dve.tensor_scalar(S0[u][:, p, :], St[u][:, p, :], em[u][:, p, 0:1], None, ALU.mult)
                step.put(ins)
                dve.wait_ge(as_[u], 4)
                step.put(dve.tensor_tensor(TM[u][:, 2, :], IN[u][:, 2, :], E[u][:, 2, :], ALU.mult))
            for p in range(2):
                for u in units:
                    dve.wait_ge(mm[u], 3 + p)
                    masks(u, p)
            for u in units:
                steps[u].wait()
            vector_inverses(dve, K, [SC[u][:, :, 0, :] for u in units], inv, inv_bank, steps, mm, 5)
            for u in units:
                step = steps[u]
                dve.wait_ge(mm[u], M0 + 2)
                step(dve.tensor_tensor(pairs(RH[u]), pairs(bank[u][1][:, 0:W]), S0[u][:, :, :], ALU.add))
                for p in range(2):
                    ins = dve.tensor_scalar(St[u][:, p, :], RH[u][:, p * P:(p + 1) * P], em[u][:, p, 1:2], None, ALU.mult)
                step.put(ins)


def rwkv_readout(K, I, rw, Y, oT):
    nc = K.nc
    with ExitStack() as c0:
        sb = lambda name, shape: c0.enter_context(sbuf(nc, "ro_" + name, shape, F32))
        g, b = sb("g", [P, D]), sb("b", [P, D])
        with phase(nc, "in_done") as (block, S):
            @block.sync
            def _(sp):
                sp.dma_start(g[:, :], I["rwkv_lnx_g_2"][0].partition_broadcast(P)).then_inc(S["in_done"], 16)
                sp.dma_start(b[:, :], I["rwkv_lnx_b_2"][0].partition_broadcast(P)).then_inc(S["in_done"], 16)
                sp.wait_ge(S["in_done"], 32)
        y, y2, bon, gate, sq = (sb(n, [P, D]) for n in ("y", "y2", "bonus", "gate", "sq"))
        st = sb("stats", [P, 4, H2])
        heads = lambda t: t[:, :].rearrange("p (h n) -> p h n", n=HD)
        wide = lambda ap: ap.unsqueeze(2).broadcast_to([P, H2, HD])
        with nc.Fori(0, NT) as j:
            with phase(nc, "in_y in_bonus in_gate v_step sq_done rms_done turned out_a out_b") as (block, S):
                rows = bass.ds(j * P, P)

                @block.sync
                def _(sp):
                    sp.dma_start(y[:, :], Y[0, rows, :]).then_inc(S["in_y"], 16)
                    sp.dma_start(y2[:, :], Y[1, rows, :]).then_inc(S["in_y"], 16)
                    sp.dma_start(bon[:, :], rw[BONUS_, rows, :]).then_inc(S["in_bonus"], 16)
                    sp.dma_start(gate[:, :], rw[GATE_, rows, :]).then_inc(S["in_gate"], 16)
                    sp.wait_ge(S["in_gate"], 16)

                @block.vector
                def _(dve):
                    step = Chain(dve, S["v_step"])
                    dve.wait_ge(S["in_y"], 32)
                    step(dve.tensor_tensor(y[:, :], y[:, :], y2[:, :], ALU.add))
                    step(dve.tensor_reduce(st[:, 0, :], heads(y), AX.X, ALU.add))
                    step(dve.tensor_scalar(st[:, 0, :], st[:, 0, :], 1.0 / HD, None, ALU.mult))
                    step.put(dve.tensor_tensor(heads(y), heads(y), wide(st[:, 0, :]), ALU.subtract))
                    dve.wait_ge(S["sq_done"], 1)
                    step.put(dve.tensor_reduce(st[:, 1, :], heads(sq), AX.X, ALU.add))
                    dve.wait_ge(S["rms_done"], 1)
                    step(dve.reciprocal(st[:, 3, :], st[:, 2, :]))
                    step(dve.tensor_tensor(heads(y), heads(y), wide(st[:, 3, :]), ALU.mult))
                    step(dve.tensor_tensor(y[:, :], y[:, :], g[:, :], ALU.mult))
                    step(dve.tensor_tensor(y[:, :], y[:, :], b[:, :], ALU.add))
                    dve.wait_ge(S["in_bonus"], 16)
                    step(dve.tensor_tensor(y[:, :], y[:, :], bon[:, :], ALU.add))
                    dve.wait_ge(S["in_gate"], 16)
                    step.put(dve.tensor_tensor(y[:, :], y[:, :], gate[:, :], ALU.mult))
                    dve.wait_ge(S["turned"], 1)
                    dve.tensor_copy(oT[:, 4:8, rows], K.bank[1][:, :].rearrange("p (k t) -> p k t", t=P))\
                        .then_inc(S["out_b"], 1)

                @block.scalar
                def _(act):
                    act.wait_ge(S["v_step"], 4)
                    act.activation(sq[:, :], y[:, :], ACT.Square).then_inc(S["sq_done"], 1)
                    act.wait_ge(S["v_step"], 5)
                    act.activation(st[:, 2, :], st[:, 1, :], ACT.Sqrt, bias=K.gneps[:, :], scale=1.0 / HD)\
                        .then_inc(S["rms_done"], 1)
                    act.wait_ge(S["turned"], 1)
                    act.activation(oT[:, 0:4, rows], K.bank[0][:, :].rearrange("p (k t) -> p k t", t=P), ACT.Copy)\
                        .then_inc(S["out_a"], 1)

                @block.tensor
                def _(pe):
                    pe.wait_ge(S["v_step"], 11)
                    for k in range(KD):
                        t = pe.transpose(K.bank[k // 4][:, (k % 4) * P:(k % 4 + 1) * P], y[:, k * P:(k + 1) * P], K.ident)
                    t.then_inc(S["turned"], 1)


def load_context(K, src):
    with phase(K.nc, "x_in") as (block, S):
        @block.sync
        def _(sp):
            sp.dma_start(K.X[:, 0:JC, :], src.rearrange("(j p) n -> p j n", p=P)).then_inc(S["x_in"], 16)
            sp.wait_ge(S["x_in"], 16)


def second_modulation(K, I, layer):
    nc = K.nc
    gain = K.colA[:, WHERE_A["norm_g_2"] + layer * KD:WHERE_A["norm_g_2"] + (layer + 1) * KD]
    with ExitStack() as c:
        K.wring = c.enter_context(sbuf(nc, "weights", [P, RING, KD, WCH], F32))
        row = c.enter_context(sbuf(nc, "mod_row", [2, 3 * D], F32))
        modulation(K, (I["c_2"][0], I["c_ctx_2"]), I["mod_w_2"][layer], I["mod_b_2"][layer], 3 * D, row)
        spread(K, row, [(0, None, K.mods[:, 0, 1, :, :]), (D, gain, K.mods[:, 0, 0, :, :])],
               [(0, 2 * D, K.gate[:, 0, :]), (1, 2 * D, K.gate[:, 1, :])])


def rwkv_layer(K, I, scratch, dbg):
    nc = K.nc
    rw, Y = scratch["rwkv"], scratch["y"]
    load_context(K, I["ctx_2"][0])
    second_modulation(K, I, 0)
    with ExitStack() as c:
        sb = lambda name, shape, s=c: s.enter_context(sbuf(nc, name, shape, F32))
        tw, ta = sb("rwkv_tw", [P, TT]), sb("rwkv_ta", [P, TT])
        with ExitStack() as c2:
            K.hT = sb("hT", [P, KD, TT], c2)
            norm_turn(K, range(NT), K.mods[:, 0, 0, :, :], K.mods[:, 0, 1, :, :])
            dump(K, dbg, "hh0", K.hT[:, :, :])
            rwkv_projections(K, I, rw, tw, ta)
        rwkv_prepare(K, I, rw, tw, ta)
    for n, a in (("p_r", R_), ("p_v", V_), ("p_gate", GATE_)):
        dump(K, dbg, n, rw[a])
    for n, a in (("p_kdir", KD_), ("p_b", B_), ("p_logw", LW_)):
        dump(K, dbg, n, rw[a:a + 2])
    with ExitStack() as c:
        St = [c.enter_context(sbuf(nc, "rwkv_state", [P, 2, P], F32)) for _ in range(UNITS)]
        FA = [c.enter_context(sbuf(nc, "rwkv_own", [P, 2, 2, 2, P], F32)) for _ in range(UNITS)]
        with nc.Fori(0, H2 // 8) as pair:
            with phase(nc, "zeroed") as (block, S):
                @block.vector
                def _(dve):
                    for t in St:
                        dve.memset(t[:, :, :], 0.0).then_inc(S["zeroed"], 1)
                    for t in FA:
                        dve.memset(t.rearrange("p a b c t -> p (a b c t)"), 0.0).then_inc(S["zeroed"], 1)
            with nc.Fori(0, JC) as i:
                rwkv_step(K, rw, Y, St, FA, pair, (i, JC - 1 - i))
            with nc.Fori(0, JX) as i:
                rwkv_step(K, rw, Y, St, FA, pair, (i + JC, NT - 1 - i))
    with ExitStack() as c:
        oT = c.enter_context(sbuf(nc, "rwkv_oT", [P, KD, TT], F32))
        rwkv_readout(K, I, rw, Y, oT)
        output_projection(K, oT, I["rwkv_w_out_2"][0], lambda j: K.gate[:, 0 if j >= JC else 1, :], range(NT), 0)
    dump(K, dbg, "xx0", K.X[:, :, :])

NOPE, ROPE = 64, 32
QK = NOPE + ROPE
QL, KVL = 384, 256
NQ, NKV = QL // P, KVL // P
SMALL = QL + KVL + ROPE


def mla_inputs(K, I, qc, kvc, ssq, gT, kT):
    nc = K.nc
    w = I["mla_w_in_2"][0].rearrange("(k p) n -> p k n", p=P)
    units = [(0, j) for j in range(JC, NT)] + [(1, j) for j in range(NT)]
    names = "w_in g_in0 g_in1 rot lat_mm copied squared pe_mm rope1 rope2 pe_out gate_mm gate_out"
    with ExitStack() as c, phase(nc, names) as (block, S):
        ws = c.enter_context(sbuf(nc, "ml_w", [P, KD, SMALL], F32))
        wr = c.enter_context(sbuf(nc, "ml_wrot", [P, KD, ROPE], F32))
        wg = c.enter_context(sbuf(nc, "ml_wg", [P, 2, KD, 512], F32))
        junk = c.enter_context(sbuf(nc, "ml_junk", [P, QL], F32))
        t = c.enter_context(sbuf(nc, "ml_rope", [P, 2, TX], F32))
        g_in = (S["g_in0"], S["g_in1"])

        @block.sync
        def _(sp):
            sp.dma_start(ws[:, :, :], w[:, :, 0:SMALL]).then_inc(S["w_in"], 16)
            for h in range(2):
                sp.dma_start(wg[:, h, :, :], w[:, :, SMALL + h * 512:SMALL + (h + 1) * 512]).then_inc(g_in[h], 16)

        @block.tensor
        def _(pe):
            pe.wait_ge(S["w_in"], 16)
            for u, (which, j) in enumerate(units):
                if u >= 2:
                    pe.wait_ge(S["squared"], u - 1)
                off, n = ((0, QL), (QL, KVL))[which]
                for k in range(KD):
                    mm = pe.matmul(K.bank[u % 2][:, 0:n], K.hT[:, k, j * P:(j + 1) * P], ws[:, k, off:off + n],
                                   start=(k == 0), stop=(k == KD - 1))
                mm.then_inc(S["lat_mm"], 1)
            pe.wait_ge(S["rot"], 1)
            for b, (wt, t0, t1) in enumerate(((ws, 0, TC), (ws, TC, TT), (wr, TC, TT))):
                off = QL + KVL if wt is ws else 0
                for k in range(KD):
                    mm = pe.matmul(K.bank[2 + b][NOPE:QK, 0:t1 - t0], wt[:, k, off:off + ROPE], K.hT[:, k, t0:t1],
                                   start=(k == 0), stop=(k == KD - 1))
            mm.then_inc(S["pe_mm"], 1)
            for m in range(KD):
                if m % 4 == 0:
                    pe.wait_ge(g_in[m // 4], 16)
                if m >= 2:
                    pe.wait_ge(S["gate_out"], m - 1)
                for k in range(KD):
                    mm = pe.matmul(K.bank[6 + m % 2][:, :], wg[:, m // 4, k, (m % 4) * P:(m % 4 + 1) * P],
                                   K.hT[:, k, TC:TT], start=(k == 0), stop=(k == KD - 1))
                mm.then_inc(S["gate_mm"], 1)

        @block.scalar
        def _(act):
            for u, (which, j) in enumerate(units):
                n = (QL, KVL)[which]
                dst = qc[:, j - JC, :] if which == 0 else kvc[:, j, :]
                act.wait_ge(S["lat_mm"], u + 1)
                act.activation(dst, K.bank[u % 2][:, 0:n], ACT.Copy).then_inc(S["copied"], 1)
                if u:
                    act.wait_ge(S["squared"], u)
                act.activation(junk[:, 0:n], K.bank[u % 2][:, 0:n], ACT.Square, accum_out=ssq[:, u:u + 1])\
                    .then_inc(S["squared"], 1)
            for m in range(KD):
                act.wait_ge(S["gate_mm"], m + 1)
                act.activation(gT[:, m, :], K.bank[6 + m % 2][:, :], ACT.Silu).then_inc(S["gate_out"], 1)

        @block.vector
        def _(dve):
            dve.wait_ge(S["w_in"], 16)
            half = ROPE // 2
            pe0 = QL + KVL
            dve.tensor_copy(wr[:, :, 0:half], ws[:, :, pe0 + half:pe0 + ROPE])
            dve.tensor_copy(wr[:, :, half:ROPE], ws[:, :, pe0:pe0 + half]).then_inc(S["rot"], 1)
            dve.wait_ge(S["pe_mm"], 1)
            r = slice(NOPE, QK)
            for s in range(2):
                dve.tensor_copy(kT[r, s, 0:TC], K.bank[2][r, 0:TC]).then_inc(S["pe_out"], 1)
            dve.tensor_tensor(t[r, 0, :], K.bank[3][r, :], K.cos, ALU.mult).then_inc(S["rope1"], 1)
            dve.tensor_tensor(t[r, 1, :], K.bank[4][r, :], K.sin, ALU.mult).then_inc(S["rope1"], 1)
            dve.wait_ge(S["rope1"], 2)
            for s in range(2):
                dve.tensor_tensor(kT[r, s, TC:TT], t[r, 0, :], t[r, 1, :], ALU.add).then_inc(S["pe_out"], 1)


def mla_latents(K, qc, kvc, ssq, qcT, kvT):
    nc = K.nc
    units = [(0, j) for j in range(JX)] + [(1, j) for j in range(NT)]
    NU = len(units)
    with ExitStack() as c, phase(nc, "mean rms_done inv_done normed turned out") as (block, S):
        st = c.enter_context(sbuf(nc, "mn_stats", [P, 2, NU], F32))
        gain = lambda n, k: K.colB[:, WHERE_B[n] + k:WHERE_B[n] + k + 1]

        @block.scalar
        def _(act):
            act.activation(st[:, 0, 0:JX], ssq[:, 0:JX], ACT.Sqrt, bias=K.eps[:, :], scale=1.0 / QL)\
                .then_inc(S["rms_done"], 1)
            act.activation(st[:, 0, JX:NU], ssq[:, JX:NU], ACT.Sqrt, bias=K.eps[:, :], scale=1.0 / KVL)\
                .then_inc(S["rms_done"], 1)

        @block.vector
        def _(dve):
            dve.wait_ge(S["rms_done"], 2)
            dve.reciprocal(st[:, 1, :], st[:, 0, :]).then_inc(S["inv_done"], 1)
            dve.wait_ge(S["inv_done"], 1)
            for u, (which, j) in enumerate(units):
                x = (qc, kvc)[which][:, j, :]
                dve.tensor_scalar(x, x, st[:, 1, u:u + 1], None, ALU.mult).then_inc(S["normed"], 1)
            for u, (which, j) in enumerate(units):
                dve.wait_ge(S["turned"], u + 1)
                dst, name, n = ((qcT, "q_norm", NQ), (kvT, "kv_norm", NKV))[which]
                for k in range(n):
                    ins = dve.tensor_scalar(dst[:, k, j * P:(j + 1) * P], K.bank[u % 4][:, k * P:(k + 1) * P],
                                            gain(name, k), None, ALU.mult)
                ins.then_inc(S["out"], 1)

        @block.tensor
        def _(pe):
            for u, (which, j) in enumerate(units):
                pe.wait_ge(S["normed"], u + 1)
                if u >= 4:
                    pe.wait_ge(S["out"], u - 3)
                for k in range((NQ, NKV)[which]):
                    tr = pe.transpose(K.bank[u % 4][:, k * P:(k + 1) * P], (qc, kvc)[which][:, j, k * P:(k + 1) * P],
                                      K.ident)
                tr.then_inc(S["turned"], 1)


def attention_pair(K, I, pair, qcT, kvT, gT, kT, oT):
    nc = K.nc
    SCALE = float(QK) ** -0.5
    names = ("wq_in wkv_in rot q_mm k_mm v_mm q_out rope k_out v_out sc_mm max_done nb_done exp_done inv_done "
             "norm_done turned pt_a pt_b o_mm o_out")
    with ExitStack() as c, phase(nc, names) as (block, S):
        buf = lambda name, shape: c.enter_context(sbuf(nc, "at_" + name, shape, F32))
        wq = buf("wq", [P, NQ, 2, QK])
        wr = buf("wr", [P, NQ, 2, ROPE])
        wkv = buf("wkv", [P, NKV, 2, 2 * HD])
        qT = buf("qT", [P, 2, TX])
        t = buf("rope", [P, 2, 2, TX])
        V = buf("v", [P, NT, P])
        Pm = buf("p", [P, 8, TT])
        PT = buf("pT", [P, 2, NT, TX])
        st = buf("stats", [P, 4, 8])
        r = slice(NOPE, QK)

        @block.sync
        def _(sp):
            sp.dma_start(wq[:, :, :, :], I["mla_w_qb_2"][0].rearrange("(k p) n -> p k n", p=P)
                         [:, :, bass.ds(pair * 2 * QK, 2 * QK)].rearrange("p k (h n) -> p k h n", h=2))\
                .then_inc(S["wq_in"], 16)
            sp.dma_start(wkv[:, :, :, :], I["mla_w_kvb_2"][0].rearrange("(k p) n -> p k n", p=P)
                         [:, :, bass.ds(pair * 4 * HD, 4 * HD)].rearrange("p k (h n) -> p k h n", h=2))\
                .then_inc(S["wkv_in"], 16)

        @block.tensor
        def _(pe):
            pe.wait_ge(S["wkv_in"], 16)
            for s in range(2):
                for b, (t0, t1) in enumerate(((0, 512), (512, TT))):
                    for k in range(NKV):
                        mm = pe.matmul(K.bank[4 * s + 2 + b][0:NOPE, 0:t1 - t0], wkv[:, k, s, 0:HD], kvT[:, k, t0:t1],
                                       start=(k == 0), stop=(k == NKV - 1))
                mm.then_inc(S["k_mm"], 1)
            pe.wait_ge(S["wq_in"], 16)
            pe.wait_ge(S["rot"], 1)
            for s in range(2):
                for k in range(NQ):
                    pe.matmul(K.bank[4 * s][0:QK, :], wq[:, k, s, :], qcT[:, k, :], start=(k == 0), stop=(k == NQ - 1))
                for k in range(NQ):
                    mm = pe.matmul(K.bank[4 * s + 1][r, :], wr[:, k, s, :], qcT[:, k, :],
                                   start=(k == 0), stop=(k == NQ - 1))
                mm.then_inc(S["q_mm"], 1)
            pe.wait_ge(S["k_out"], 4)
            for j in range(NT):
                for k in range(NKV):
                    mm = pe.matmul(K.bank[2 + j // 4][:, (j % 4) * P:(j % 4 + 1) * P].rearrange("p (h n) -> p h n", h=2),
                                   kvT[:, k, j * P:(j + 1) * P], wkv[:, k, :, HD:2 * HD],
                                   start=(k == 0), stop=(k == NKV - 1))
            mm.then_inc(S["v_mm"], 1)
            for u in range(8):
                s, qt = divmod(u, 4)
                if qt == 0:
                    pe.wait_ge(S["q_out"], 4 if s == 0 else 4)
                    pe.wait_ge(S["v_out"], 2)
                if u >= 4:
                    pe.wait_ge(S["exp_done"], u - 3)
                for b, (t0, t1) in enumerate(((0, 512), (512, TT))):
                    mm = pe.matmul(K.bank[2 * (u % 4) + b][:, 0:t1 - t0], qT[0:QK, s, qt * P:(qt + 1) * P],
                                   kT[0:QK, s, t0:t1], start=True, stop=True)
                mm.then_inc(S["sc_mm"], 1)
            for s in range(2):
                pe.wait_ge(S["exp_done"], 8)
                pe.wait_ge(S["norm_done"], 4 * s + 4)
                for kt in range(NT):
                    n = NT * s + kt
                    if n >= 4:
                        pe.wait_ge((S["pt_a"], S["pt_b"])[n % 2], (n - 4) // 2 + 1)
                    for qt in range(4):
                        tr = pe.transpose(K.bank[n % 4][:, qt * P:(qt + 1) * P], Pm[:, 4 * s + qt, kt * P:(kt + 1) * P],
                                          K.ident)
                    tr.then_inc(S["turned"], 1)
                pe.wait_ge(S["pt_a"], 3 * (s + 1))
                pe.wait_ge(S["pt_b"], 3 * (s + 1))
                for kt in range(NT):
                    mm = pe.matmul(K.bank[4][s * HD:(s + 1) * HD, :], V[:, kt, s * HD:(s + 1) * HD], PT[:, s, kt, :],
                                   start=(kt == 0), stop=(kt == NT - 1))
                mm.then_inc(S["o_mm"], 1)

        @block.scalar
        def _(act):
            for s in range(2):
                act.wait_ge(S["k_mm"], s + 1)
                for b, (t0, t1) in enumerate(((0, 512), (512, TT))):
                    act.activation(kT[0:NOPE, s, t0:t1], K.bank[4 * s + 2 + b][0:NOPE, 0:t1 - t0], ACT.Copy)\
                        .then_inc(S["k_out"], 1)
            act.wait_ge(S["v_mm"], 1)
            act.activation(V[:, 0:4, :], K.bank[2][:, :].rearrange("p (j n) -> p j n", n=P), ACT.Copy)\
                .then_inc(S["v_out"], 1)
            act.activation(V[:, 4:NT, :], K.bank[3][:, 0:(NT - 4) * P].rearrange("p (j n) -> p j n", n=P), ACT.Copy)\
                .then_inc(S["v_out"], 1)
            for u in range(8):
                act.wait_ge(S["nb_done"], u + 1)
                b = 2 * (u % 4)
                act.activation(Pm[:, u, :], K.psum[:, b * 512:b * 512 + TT], ACT.Exp, bias=st[:, 1, u:u + 1],
                               scale=SCALE, accum_out=st[:, 2, u:u + 1]).then_inc(S["exp_done"], 1)
            for n in range(0, 2 * NT, 2):
                s, kt = divmod(n, NT)
                act.wait_ge(S["turned"], n + 1)
                act.activation(PT[:, s, kt, :], K.bank[n % 4][:, :], ACT.Copy).then_inc(S["pt_a"], 1)

        @block.gpsimd
        def _(pool):
            for u in range(8):
                pool.wait_ge(S["inv_done"], u + 1)
                pool.tensor_scalar(Pm[:, u, :], Pm[:, u, :], st[:, 3, u:u + 1], None, ALU.mult).then_inc(S["norm_done"], 1)

        @block.vector
        def _(dve):
            half = ROPE // 2
            dve.wait_ge(S["wq_in"], 16)
            dve.tensor_copy(wr[:, :, :, 0:half], wq[:, :, :, NOPE + half:QK])
            dve.tensor_copy(wr[:, :, :, half:ROPE], wq[:, :, :, NOPE:NOPE + half]).then_inc(S["rot"], 1)
            for s in range(2):
                dve.wait_ge(S["q_mm"], s + 1)
                dve.tensor_copy(qT[0:NOPE, s, :], K.bank[4 * s][0:NOPE, :]).then_inc(S["q_out"], 1)
                dve.tensor_tensor(t[r, s, 0, :], K.bank[4 * s][r, :], K.cos, ALU.mult).then_inc(S["rope"], 1)
                dve.tensor_tensor(t[r, s, 1, :], K.bank[4 * s + 1][r, :], K.sin, ALU.mult).then_inc(S["rope"], 1)
                dve.wait_ge(S["rope"], 2 * s + 2)
                dve.tensor_tensor(qT[r, s, :], t[r, s, 0, :], t[r, s, 1, :], ALU.add).then_inc(S["q_out"], 1)

            def inverse(u):
                dve.wait_ge(S["exp_done"], u + 1)
                dve.reciprocal(st[:, 3, u:u + 1], st[:, 2, u:u + 1]).then_inc(S["inv_done"], 1)

            for u in range(8):
                b = 2 * (u % 4)
                dve.wait_ge(S["sc_mm"], u + 1)
                dve.tensor_reduce(st[:, 0, u:u + 1], K.psum[:, b * 512:b * 512 + TT], AX.X, ALU.max)\
                    .then_inc(S["max_done"], 1)
                dve.wait_ge(S["max_done"], u + 1)
                dve.tensor_scalar(st[:, 1, u:u + 1], st[:, 0, u:u + 1], -SCALE, None, ALU.mult).then_inc(S["nb_done"], 1)
                if u:
                    inverse(u - 1)
            inverse(7)
            for n in range(1, 2 * NT, 2):
                s, kt = divmod(n, NT)
                dve.wait_ge(S["turned"], n + 1)
                dve.tensor_copy(PT[:, s, kt, :], K.bank[n % 4][:, :]).then_inc(S["pt_b"], 1)
            dve.wait_ge(S["o_mm"], 2)
            at = bass.ds(pair, 1)
            dve.tensor_tensor(oT[:, at, :].rearrange("p o n -> p (o n)"), K.bank[4][:, :],
                              gT[:, at, :].rearrange("p o n -> p (o n)"), ALU.mult).then_inc(S["o_out"], 1)


def mla_layer(K, I, dbg):
    nc = K.nc
    second_modulation(K, I, 1)
    with ExitStack() as c:
        sb = lambda name, shape, s=c: s.enter_context(sbuf(nc, name, shape, F32))
        oT, gT = sb("mla_oT", [P, KD, TX]), sb("mla_gate", [P, KD, TX])
        with ExitStack() as c2:
            qcT, kvT = sb("mla_qcT", [P, NQ, TX], c2), sb("mla_kvT", [P, NKV, TT], c2)
            kT = sb("mla_kT", [P, 2, TT], c2)
            with ExitStack() as c3:
                K.hT = sb("hT", [P, KD, TT], c3)
                norm_turn(K, range(NT), K.mods[:, 0, 0, :, :], K.mods[:, 0, 1, :, :])
                dump(K, dbg, "hh1", K.hT[:, :, :])
                qc, kvc = sb("mla_qc", [P, JX, QL], c3), sb("mla_kvc", [P, NT, KVL], c3)
                ssq = sb("mla_ssq", [P, JX + NT], c3)
                mla_inputs(K, I, qc, kvc, ssq, gT, kT)
                mla_latents(K, qc, kvc, ssq, qcT, kvT)
            with nc.Fori(0, H2 // 2) as pair:
                attention_pair(K, I, pair, qcT, kvT, gT, kT, oT)
        output_projection(K, oT, I["mla_w_out_2"][0], lambda j: K.gate[:, 0, :], range(JC, NT), JC)
    dump(K, dbg, "xx1", K.X[:, :, :])

def build(nc, I, out, scratch, dbg=None, stop=None):
    USED.clear()
    K = Kernel()
    K.nc = nc
    with ExitStack() as c:
        def sb(name, shape, stack=c):
            return stack.enter_context(sbuf(nc, name, shape, F32))

        K.const = sb("const", [P, CONST_COLS])
        K.colA, K.colB = sb("param_cols_a", [P, N_A]), sb("param_cols_b", [P, N_B])
        K.colC = sb("param_cols_c", [P, N_C])
        K.eps, K.one, K.gneps = sb("eps", [P, 1]), sb("one", [P, 1]), sb("gneps", [P, 1])
        K.X = sb("tokens", [P, NT, D])
        K.mods = sb("mod_cols", [P, 2, 2, KD, 2])
        K.gate = sb("mod_gate", [P, 2, D])
        K.psum = c.enter_context(nc.psum_tensor("psum", [P, 8 * 512], F32))
        K.bank = [K.psum[:, i * 512:(i + 1) * 512] for i in range(8)]
        part = lambda n: K.const[:, n * P:(n + 1) * P]
        K.ident, K.ones = part(0), part(1)
        K.inc, K.cum = (part(3), part(5)), (part(6), part(7))
        by4 = lambda ap: ap.unsqueeze(1).broadcast_to([P, 4, P])
        K.ident4 = by4(K.ident)
        K.incl4, K.strict4 = (by4(part(3)), by4(part(5))), (by4(part(2)), by4(part(4)))
        K.mask2 = [K.const[:, n * P:(n + 2) * P].rearrange("p (b t) -> p b t", b=2) for n in (2, 4)]
        K.before = part(2)
        K.zeros = sb("zeros", [P, NE])
        K.cos = K.const[64:96, ROPE_COL:ROPE_COL + TX]
        K.sin = K.const[64:96, ROPE_COL + TX:ROPE_COL + 2 * TX]
        K.same_head = K.const[:, MIX_COL + 4:SLOT_COL].unsqueeze(1).broadcast_to([P, 2, P])
        K.cross = [[by4(K.const[:, CROSS_COL + (d * LEVELS + n) * P:CROSS_COL + (d * LEVELS + n + 1) * P])
                    for n in range(LEVELS)] for d in range(2)]

        load_parameters(K, I)
        if stop != "skip_first":
            first_model(K, I, scratch, dbg, stop)
        if stop == "first":
            with phase(nc, "out_done") as (block, S):
                @block.sync
                def _(sp):
                    sp.dma_start(out.rearrange("o (j p) n -> (o p) j n", p=P), K.X[:, JC:NT, :]).then_inc(S["out_done"], 16)
                    sp.wait_ge(S["out_done"], 16)
            return
        if stop in ("mix", "delta"):
            return
        rwkv_layer(K, I, scratch, dbg)
        mla_layer(K, I, dbg)
        final_norm(K, I["final_g_2"], range(JC, NT), out.rearrange("o t n -> (o t) n"))


def dump(K, dbg, name, ap):
    if dbg is None or name not in dbg:
        return
    with phase(K.nc, "dumped") as (block, S):
        @block.sync
        def _(sp):
            sp.dma_start(dbg[name], ap).then_inc(S["dumped"], 16)
            sp.wait_ge(S["dumped"], 16)


def first_model(K, I, scratch, dbg, stop):
    nc = K.nc
    cols = lambda name, n, off=0: K.colA[:, WHERE_A[name] + off:WHERE_A[name] + off + n]
    with ExitStack() as c1:
        sb = lambda name, shape, stack=c1: stack.enter_context(sbuf(nc, name, shape, F32))
        with ExitStack() as c:
            K.wring = sb("weights", [P, RING, KD, WCH], c)
            row = sb("mod_row", [2, 6 * D], c)
            modulation(K, (I["c"][0], I["c_ctx"]), I["w_mod"][0], I["b_mod"][0], 6 * D, row)
            spread(K, row,
                   [(0, None, K.mods[:, 0, 1, :, :]), (D, cols("g_mix", KD), K.mods[:, 0, 0, :, :]),
                    (3 * D, None, K.mods[:, 1, 1, :, :]), (4 * D, cols("g_ffn", KD), K.mods[:, 1, 0, :, :])],
                   [(0, 2 * D, K.gate[:, 0, :]), (0, 5 * D, K.gate[:, 1, :])])
        headsT = sb("mix_heads", [P, H1 + NCF, TX])
        zT = headsT[:, 0:H1, :]
        cfT = headsT[:, H1:H1 + NCF, :]
        with ExitStack() as c:
            C = sb("conv_out", [P, NQKV, TT], c)
            ba = sb("ba", [P, NT, 16], c)
            with ExitStack() as c2:
                cfa, cfs = sb("cf_a", [P, NCF, TX], c2), sb("cf_s", [P, NCF, TX], c2)
                with ExitStack() as c3:
                    K.hT = sb("hT", [P, KD, TT], c3)
                    K.wring = sb("weights2", [P, RING, KD, WCH], c3)
                    norm_turn(K, range(NT), K.mods[:, 0, 0, :, :], K.mods[:, 0, 1, :, :])
                    dump(K, dbg, "hT", K.hT[:, :, :])
                    mixer_inputs(K, I, C, zT, cfa, cfs, ba[:, :, :])
                conformer(K, cfa, cfs, cfT)
            qk_norm(K, C)
            dump(K, dbg, "C", C[:, :, :])
            dump(K, dbg, "headsT0", headsT[:, :, :])
            Ktok, Vtok = sb("k_tokens", [P, H1, NT, P], c), sb("v_tokens", [P, H1, NT, P], c)
            turn_back(K, [C[:, H1 + n, :] for n in range(2 * H1)],
                      [Ktok[:, h, :, :] for h in range(H1)] + [Vtok[:, h, :, :] for h in range(H1)])
            O = sb("delta_out", [P, JX, H1 * DK], c)
            G = {n: sb("gates_" + n, [P, 2, NT, H1], c) for n in ("cumg", "beta", "egc", "ekd", "egl")}
            delta_gates(K, I, ba, G)
            St = [sb(f"delta_state{d}", [P, H1, P], c) for d in range(2)]
            with phase(nc, "zeroed") as (block, S):
                @block.vector
                def _(dve):
                    for t in (*St, O):
                        dve.memset(t[:, :, :], 0.0).then_inc(S["zeroed"], 1)
            with nc.Fori(0, JC) as i:
                delta_step(K, C, Ktok, Vtok, G, O, St, (i, JC - 1 - i), False)
            with nc.Fori(0, JX) as i:
                delta_step(K, C, Ktok, Vtok, G, O, St, (i + JC, NT - 1 - i), True)
            dump(K, dbg, "O", O[:, :, :])
            if stop == "delta":
                return
            delta_readout(K, O, headsT)
        dump(K, dbg, "headsT", headsT[:, :, :])
        output_projection(K, headsT, I["w_out"][0], lambda j: K.gate[:, 0, :], range(JC, NT), JC)
        dump(K, dbg, "x1", K.X[:, JC:NT, :])
    if stop == "mix":
        return
    with ExitStack() as c:
        K.hT = c.enter_context(sbuf(nc, "hT", [P, KD, TT], F32))
        norm_turn(K, range(JC, NT), K.mods[:, 1, 0, :, :], K.mods[:, 1, 1, :, :])
        mixture(K, I, scratch)
    final_norm(K, I["g_final"], range(JC, NT))



INPUTS = ['x', 'c', 'ctx', 'c_ctx', 'w_mod', 'b_mod', 'g_mix', 'g_ffn', 'w_in', 'w_out', 'dn_conv_w', 'dn_a_log',
          'dn_dt_bias', 'dn_norm_g', 'cf_dw_w', 'cf_dw_b', 'cf_ln_g', 'cf_ln_b', 'router_w', 'router_bias',
          'exp_w_gate', 'exp_w_up', 'exp_w_down', 'sh_w_gate', 'sh_w_up', 'sh_w_down', 'g_final', 'c_2', 'ctx_2',
          'c_ctx_2', 'norm_g_2', 'mod_w_2', 'mod_b_2', 'rwkv_mu_2', 'rwkv_w_in_2', 'rwkv_w0_2', 'rwkv_w1_2',
          'rwkv_w2_2', 'rwkv_a0_2', 'rwkv_a1_2', 'rwkv_a2_2', 'rwkv_k_k_2', 'rwkv_k_a_2', 'rwkv_r_k_2',
          'rwkv_lnx_g_2', 'rwkv_lnx_b_2', 'rwkv_w_out_2', 'mla_w_in_2', 'mla_q_norm_g_2', 'mla_w_qb_2',
          'mla_kv_norm_g_2', 'mla_w_kvb_2', 'mla_w_out_2', 'final_g_2']
SCRATCH = {"rwkv": (N_RW, TT, D), "y": (2, TT, D), "h_rows": (TX, D), "slot_tokens": (TILES * SLOTS, 1),
           "ys": ((TILES + 1) * SLOTS, D)}


def kernel(**inputs):
    import numpy as np
    import concourse.bacc as bacc
    from concourse.bass_utils import run_bass_kernel_spmd

    nc = bacc.Bacc("TRN2", target_bir_lowering=False, num_devices=1)
    arrays, aps = {}, {}
    for name in INPUTS:
        a = np.ascontiguousarray(inputs[name])
        arrays[f"in_{name}"] = a
        aps[name] = nc.dram_tensor(f"in_{name}", a.shape, mybir.dt.from_np(a.dtype), kind="ExternalInput").ap()
    arrays["in_consts"] = constants()
    aps["consts"] = nc.dram_tensor("in_consts", (P, CONST_COLS), F32, kind="ExternalInput").ap()
    out = nc.dram_tensor("out", (1, TX, D), F32, kind="ExternalOutput").ap()
    scratch = {n: nc.dram_tensor("scratch_" + n, shape, F32, kind="Internal").ap() for n, shape in SCRATCH.items()}
    build(nc, aps, out, scratch)
    r = run_bass_kernel_spmd(nc, [arrays], core_ids=[0])
    return r.results[0]["out"]
```

```python
from contextlib import ExitStack, contextmanager

import concourse.bass as bass
from concourse import mybir

F32 = mybir.dt.float32
ALU = mybir.AluOpType
ACT = mybir.ActivationFunctionType
AX = mybir.AxisListType

P = 128
D = 1024
KD = D // P
TC, TX = 256, 512
NT = (TC + TX) // P
JC = TC // P
JX = TX // P
TT = TC + TX
H1, DK = 4, 128
QKV = 3 * H1 * DK
NQKV = QKV // P
CFC = 512
NCF = CFC // P
TAPS = 7
GRID_W = 64
ROWS = TX // GRID_W
EPS = 1e-6
LEVELS = 7
NE = 64
GROUPS = 8
DE = 256
H2 = 16
HD = 64
LORA = 64


USED = {}


def sbuf(nc, name, shape, dtype):
    USED[name] = USED.get(name, 0) + 1
    return nc.sbuf_tensor(f"{name}_{USED[name]}", shape, dtype)


@contextmanager
def phase(nc, names):
    with ExitStack() as held:
        by_name = {n: held.enter_context(nc.semaphore(n)) for n in names.split()}
        handles = list(by_name.values())
        signals = by_name
        with nc.Block(no_gpsimd_drain=True) as block:
            yield block, signals
        with nc.Block(no_gpsimd_drain=True) as clearing:
            @clearing.sync
            def _(sp):
                nums = sorted(h.num for h in handles)
                if nums[-1] - nums[0] + 1 == len(nums):
                    sp.sem_clear(range(nums[0], nums[-1] + 1))
                else:
                    for h in handles:
                        sp.sem_clear(h)


class Chain:

    def __init__(self, eng, sem):
        self.eng, self.sem, self.n = eng, sem, 0

    def __call__(self, ins):
        self.put(ins)
        self.wait()

    def put(self, ins):
        self.n += 1
        ins.then_inc(self.sem, 1)

    def wait(self, back=0):
        if self.n - back > 0:
            self.eng.wait_ge(self.sem, self.n - back)


class Kernel:
    pass



MASK_NAMES = ["ident", "ones", "strF", "incF", "strB", "incB", "cumF", "cumB"]
ROPE_COL = len(MASK_NAMES) * P
CROSS_COL = ROPE_COL + 2 * TX
MIX_COL = CROSS_COL + 2 * LEVELS * P
SLOT_COL = MIX_COL + 4 + P
TOKEN_COL = SLOT_COL + NE
CONST_COLS = TOKEN_COL + JX


def constants():
    import numpy as np

    t = np.arange(P)
    s_, t_ = t[:, None], t[None, :]
    out = np.zeros((P, CONST_COLS), np.float32)

    def put(n, m):
        out[:, n * P:(n + 1) * P] = m

    put(0, s_ == t_)
    put(1, 1)
    put(2, s_ < t_)
    put(3, s_ <= t_)
    put(4, s_ > t_)
    put(5, s_ >= t_)
    put(6, (s_ <= t_).astype(np.float32) - (s_ < P // 2))
    put(7, (s_ >= t_).astype(np.float32) - (s_ >= P // 2))
    out[:, MIX_COL + 0] = t < P // 2
    out[:, MIX_COL + 1] = t >= P // 2
    out[:, MIX_COL + 2] = t >= P // 2
    out[:, MIX_COL + 3] = t < P // 2
    out[:, MIX_COL + 4:SLOT_COL] = (s_ // HD == t_ // HD)
    out[:, SLOT_COL:TOKEN_COL] = np.arange(NE) * P
    out[:, TOKEN_COL:] = np.arange(JX) * P + t[:, None]
    for d in range(2):
        for level in range(LEVELS):
            b = 1 << level
            m = (s_ // b == t_ // b + 1) & (s_ // (2 * b) == t_ // (2 * b))
            if d:
                m = m.T
            at = CROSS_COL + (d * LEVELS + level) * P
            out[:, at:at + P] = -1.0 * m
    half = 16
    pos = np.arange(TX)
    inv = 1.0 / (10000.0 ** (np.arange(0, half, 2, dtype=np.float32) / half))
    ang = np.concatenate([(pos // GRID_W)[:, None] * inv, (pos % GRID_W)[:, None] * inv], -1)
    cos, sin = np.cos(ang.astype(np.float32)).T, np.sin(ang.astype(np.float32)).T
    out[64:96, ROPE_COL:ROPE_COL + TX] = np.concatenate([cos, cos])
    out[64:96, ROPE_COL + TX:ROPE_COL + 2 * TX] = np.concatenate([-sin, sin])
    return out


def rows_of(spec):
    at, where = 0, {}
    for name, n in spec:
        where[name] = at
        at += n
    return where, at


HALO = ROWS - 1
CF_USED = 2 * HALO + 1
SPEC_A = [("g_mix", KD), ("g_ffn", KD), ("norm_g_2", 2 * KD), ("cf_dw_b", NCF), ("cf_ln_g", NCF),
          ("cf_ln_b", NCF), ("dn_norm_g", 1), ("cf_dw_w", CF_USED * NCF)]
SPEC_B = [("dn_conv_w", TAPS * NQKV), ("q_norm", 3), ("kv_norm", 2)]
WHERE_A, N_A = rows_of(SPEC_A)
WHERE_B, N_B = rows_of(SPEC_B)
N_C = 6 * KD


def load_parameters(K, I):
    nc = K.nc
    cf_used = I["cf_dw_w"][0][15 - HALO:15 + HALO + 1, :].rearrange("j (f p) -> (j f) p", p=P)
    rows_a = {
        "g_mix": I["g_mix"][0].rearrange("(k p) -> k p", p=P),
        "g_ffn": I["g_ffn"][0].rearrange("(k p) -> k p", p=P),
        "norm_g_2": I["norm_g_2"].rearrange("l (k p) -> (l k) p", p=P),
        "cf_dw_b": I["cf_dw_b"][0].rearrange("(k p) -> k p", p=P),
        "cf_ln_g": I["cf_ln_g"][0].rearrange("(k p) -> k p", p=P),
        "cf_ln_b": I["cf_ln_b"][0].rearrange("(k p) -> k p", p=P),
        "dn_norm_g": I["dn_norm_g"],
        "cf_dw_w": cf_used,
    }
    rows_b = {
        "dn_conv_w": I["dn_conv_w"][0].rearrange("j (f p) -> (j f) p", p=P),
        "q_norm": I["mla_q_norm_g_2"][0].rearrange("(k p) -> k p", p=P),
        "kv_norm": I["mla_kv_norm_g_2"][0].rearrange("(k p) -> k p", p=P),
    }
    with ExitStack() as c, phase(nc, "consts_in rows_in turned cols_done x_in eps_set") as (block, S):
        ra = c.enter_context(sbuf(nc, "param_rows_a", [N_A, P], F32))
        rb = c.enter_context(sbuf(nc, "param_rows_b", [N_B, P], F32))
        rc = c.enter_context(sbuf(nc, "param_rows_c", [N_C, P], F32))

        @block.sync
        def _(sp):
            sp.dma_start(K.const[:, :], I["consts"]).then_inc(S["consts_in"], 16)
            sp.dma_start(rc[:, :], I["rwkv_mu_2"][0].rearrange("j (k p) -> (j k) p", p=P)).then_inc(S["rows_in"], 16)
            n = 1
            for where, rows, dst in ((WHERE_A, rows_a, ra), (WHERE_B, rows_b, rb)):
                for name, src in rows.items():
                    sp.dma_start(dst[where[name]:where[name] + src.shape[0], :], src).then_inc(S["rows_in"], 16)
                    n += 1
            sp.dma_start(K.X[:, 0:JC, :], I["ctx"][0].rearrange("(j p) n -> p j n", p=P)).then_inc(S["x_in"], 16)
            sp.dma_start(K.X[:, JC:NT, :], I["x"][0].rearrange("(j p) n -> p j n", p=P)).then_inc(S["x_in"], 16)
            sp.wait_ge(S["x_in"], 32)
            sp.wait_ge(S["rows_in"], 16 * n)

        @block.tensor
        def _(pe):
            pe.wait_ge(S["consts_in"], 16)
            pe.wait_ge(S["rows_in"], 16 * (1 + len(rows_a) + len(rows_b)))
            pe.transpose(K.bank[0][:, 0:N_A], ra[:, :], K.ident[0:N_A, 0:N_A])
            pe.transpose(K.bank[2][:, 0:N_C], rc[:, :], K.ident[0:N_C, 0:N_C])
            pe.transpose(K.bank[1][:, 0:N_B], rb[:, :], K.ident[0:N_B, 0:N_B]).then_inc(S["turned"], 1)

        @block.vector
        def _(dve):
            dve.memset(K.eps[:, :], EPS).then_inc(S["eps_set"], 1)
            dve.memset(K.one[:, :], 1.0).then_inc(S["eps_set"], 1)
            dve.memset(K.zeros[:, :], 0.0).then_inc(S["eps_set"], 1)
            dve.memset(K.gneps[:, :], 64e-5).then_inc(S["eps_set"], 1)
            dve.wait_ge(S["turned"], 1)
            dve.tensor_copy(K.colA[:, :], K.bank[0][:, 0:N_A]).then_inc(S["cols_done"], 1)
            dve.tensor_copy(K.colB[:, :], K.bank[1][:, 0:N_B]).then_inc(S["cols_done"], 1)
            dve.tensor_copy(K.colC[:, :], K.bank[2][:, 0:N_C]).then_inc(S["cols_done"], 1)



WCH = 512
RING = 3


def modulation(K, vectors, w, b, N, row, rows_needed=None):
    nc = K.nc
    n_chunks = N // WCH
    names = "vec_in bias_in silu_done mm_done sum_done " + " ".join(f"w_in{i}" for i in range(RING))
    with ExitStack() as c, phase(nc, names) as (block, S):
        vec = c.enter_context(sbuf(nc, "mod_vec", [P, 2, KD], F32))
        act_vec = c.enter_context(sbuf(nc, "mod_silu", [P, 2, KD], F32))
        w_in = (S["w_in0"], S["w_in1"], S["w_in2"])
        w_rows = w.rearrange("(p k) n -> p k n", k=KD)

        @block.sync
        def _(sp):
            for r in range(2):
                sp.dma_start(vec[:, r, :], vectors[r].rearrange("(p k) -> p k", k=KD)).then_inc(S["vec_in"], 16)
                sp.dma_start(row[r:r + 1, 0:N], b.rearrange("(a n) -> a n", a=1)).then_inc(S["bias_in"], 16)
            for n in range(n_chunks):
                if n >= RING:
                    sp.wait_ge(S["mm_done"], n - RING + 1)
                sp.dma_start(K.wring[:, n % RING, :, :], w_rows[:, :, n * WCH:(n + 1) * WCH])\
                    .then_inc(w_in[n % RING], 16)

        @block.scalar
        def _(act):
            act.wait_ge(S["vec_in"], 32)
            act.activation(act_vec[:, :, :], vec[:, :, :], ACT.Silu).then_inc(S["silu_done"], 1)

        @block.tensor
        def _(pe):
            pe.wait_ge(S["silu_done"], 1)
            for n in range(n_chunks):
                pe.wait_ge(w_in[n % RING], 16 * (n // RING + 1))
                if n >= 2:
                    pe.wait_ge(S["sum_done"], n - 1)
                for k in range(KD):
                    mm = pe.matmul(K.bank[n % 2][0:2, :], act_vec[:, :, k], K.wring[:, n % RING, k, :],
                                   start=(k == 0), stop=(k == KD - 1))
                mm.then_inc(S["mm_done"], 1)

        @block.vector
        def _(dve):
            dve.wait_ge(S["bias_in"], 32)
            for n in range(n_chunks):
                part = row[0:2, n * WCH:(n + 1) * WCH]
                dve.wait_ge(S["mm_done"], n + 1)
                dve.tensor_tensor(part, K.bank[n % 2][0:2, :], part, ALU.add).then_inc(S["sum_done"], 1)


def spread(K, row, columns, broadcasts):
    nc = K.nc
    with ExitStack() as c, phase(nc, "sel_a sel_set turned cols_done spread_done copied") as (block, S):
        sel = c.enter_context(sbuf(nc, "row_selector", [2, 2, P], F32))

        @block.gpsimd
        def _(pool):
            pool.memset(sel[:, :, :], 1.0).then_inc(S["sel_a"], 1)
            pool.wait_ge(S["sel_a"], 1)
            pool.affine_select(out=sel[:, :, :], in_=sel[:, :, :], compare_op=ALU.is_equal, fill=0.0, base=0,
                               pattern=[[-1, 2], [0, P]], channel_multiplier=1).then_inc(S["sel_set"], 1)

        @block.tensor
        def _(pe):
            for n, (off, _, _) in enumerate(columns):
                for k in range(KD):
                    mm = pe.matmul(K.bank[0][:, (n * KD + k) * 2:(n * KD + k) * 2 + 2],
                                   row[0:2, off + k * P:off + (k + 1) * P], K.ident[0:2, 0:2],
                                   start=True, stop=True)
            mm.then_inc(S["turned"], 1)
            pe.wait_ge(S["sel_set"], 1)
            m = 0
            for r, off, _ in broadcasts:
                for h in range(D // 512):
                    if m >= 2:
                        pe.wait_ge(S["copied"], m - 1)
                    pe.matmul(K.bank[1 + m % 2][:, :], sel[:, r, :], row[0:2, off + h * 512:off + (h + 1) * 512],
                              start=True, stop=True).then_inc(S["spread_done"], 1)
                    m += 1

        @block.vector
        def _(dve):
            dve.wait_ge(S["turned"], 1)
            for n, (_, gain, dst) in enumerate(columns):
                src = K.bank[0][:, n * KD * 2:(n + 1) * KD * 2].rearrange("p (k r) -> p k r", r=2)
                if gain is None:
                    dve.tensor_copy(dst, src).then_inc(S["cols_done"], 1)
                else:
                    for r in range(2):
                        dve.scalar_tensor_tensor(out=dst[:, :, r], in0=src[:, :, r], scalar=1.0, in1=gain,
                                                 op0=ALU.add, op1=ALU.mult).then_inc(S["cols_done"], 1)

        @block.scalar
        def _(act):
            m = 0
            for _, _, dst in broadcasts:
                for h in range(D // 512):
                    act.wait_ge(S["spread_done"], m + 1)
                    act.activation(dst[:, h * 512:(h + 1) * 512], K.bank[1 + m % 2][:, :], ACT.Copy)\
                        .then_inc(S["copied"], 1)
                    m += 1



def norm_turn(K, tiles, gain, shift, zero_gain_cols=None):
    nc = K.nc
    names = "sq_done rms_done inv_done xn_done turned evac_a evac_b"
    with ExitStack() as c, phase(nc, names) as (block, S):
        junk = c.enter_context(sbuf(nc, "norm_junk", [P, D], F32))
        ssq = c.enter_context(sbuf(nc, "norm_ssq", [P, NT], F32))
        rms = c.enter_context(sbuf(nc, "norm_rms", [P, NT], F32))
        inv = c.enter_context(sbuf(nc, "norm_inv", [P, NT], F32))
        xn = c.enter_context(sbuf(nc, "norm_xn", [P, 2, D], F32))
        N = len(tiles)

        def bank(n, half):
            return K.bank[2 * (n % 2) + half]

        @block.scalar
        def _(act):
            for n, j in enumerate(tiles):
                if n:
                    act.wait_ge(S["sq_done"], n)
                act.activation(junk[:, :], K.X[:, j, :], ACT.Square, accum_out=ssq[:, n:n + 1]).then_inc(S["sq_done"], 1)
            act.wait_ge(S["sq_done"], N)
            act.activation(rms[:, 0:N], ssq[:, 0:N], ACT.Sqrt, bias=K.eps[:, :], scale=1.0 / D).then_inc(S["rms_done"], 1)
            for n, j in enumerate(tiles):
                r = int(j < JC)
                act.wait_ge(S["turned"], n + 1)
                for k in range(KD // 2):
                    last = act.activation(K.hT[:, k, j * P:(j + 1) * P], bank(n, 0)[:, k * P:(k + 1) * P],
                                          ACT.Identity, bias=shift[:, k, r:r + 1], scale=gain[:, k, r:r + 1])
                last.then_inc(S["evac_a"], 1)

        @block.vector
        def _(dve):
            dve.wait_ge(S["rms_done"], 1)
            dve.reciprocal(inv[:, 0:N], rms[:, 0:N]).then_inc(S["inv_done"], 1)
            dve.wait_ge(S["inv_done"], 1)

            def scale(n):
                if n >= 2:
                    dve.wait_ge(S["turned"], n - 1)
                dve.tensor_scalar(xn[:, n % 2, :], K.X[:, tiles[n], :], inv[:, n:n + 1], None, ALU.mult)\
                    .then_inc(S["xn_done"], 1)

            scale(0)
            for n, j in enumerate(tiles):
                if n + 1 < N:
                    scale(n + 1)
                r = int(j < JC)
                dve.wait_ge(S["turned"], n + 1)
                for k in range(KD // 2, KD):
                    q = k - KD // 2
                    last = dve.tensor_scalar(K.hT[:, k, j * P:(j + 1) * P], bank(n, 1)[:, q * P:(q + 1) * P],
                                             gain[:, k, r:r + 1], shift[:, k, r:r + 1], ALU.mult, ALU.add)
                last.then_inc(S["evac_b"], 1)

        @block.tensor
        def _(pe):
            for n in range(N):
                pe.wait_ge(S["xn_done"], n + 1)
                if n >= 2:
                    pe.wait_ge(S["evac_a"], n - 1)
                    pe.wait_ge(S["evac_b"], n - 1)
                for k in range(KD):
                    half, q = divmod(k, KD // 2)
                    tr = pe.transpose(bank(n, half)[:, q * P:(q + 1) * P], xn[:, n % 2, k * P:(k + 1) * P], K.ident)
                tr.then_inc(S["turned"], 1)



UC, UX = TC + 2 * (TAPS // 2), TX + 2 * (TAPS // 2)


def mixer_inputs(K, I, C, zT, cfa, cfs, ba):
    nc = K.nc
    w = I["w_in"][0].rearrange("(k p) n -> p k n", p=P)
    off_z, off_ba = QKV, QKV + H1 * DK
    off_cf = off_ba + 16
    loads = [(0, 512), (512, 512), (1024, 512), (off_z, 512), (off_cf, 512), (off_cf + 512, 512), (off_ba, 16)]
    names = ("pads mm_x mm_c qkv_out conv_x conv_c silu_done plain_out ba_turned ba_out "
             + " ".join(f"w_in{i}" for i in range(RING)) + " tap_c tap_x")
    NU = 3
    with ExitStack() as c, phase(nc, names) as (block, S):
        w_in = (S["w_in0"], S["w_in1"], S["w_in2"])
        U = c.enter_context(sbuf(nc, "conv_in", [P, NU, UC + UX], F32))
        baT = c.enter_context(sbuf(nc, "baT", [16, TT], F32))
        PAD = TAPS // 2
        n_plain = NCF * 3

        @block.sync
        def _(sp):
            for n, (off, cols) in enumerate(loads):
                if n >= RING:
                    sp.wait_ge(S["mm_x"], 4 * (n - RING + 1))
                sp.dma_start(K.wring[:, n % RING, :, 0:cols], w[:, :, off:off + cols]).then_inc(w_in[n % RING], 16)

        @block.tensor
        def _(pe):
            for f in range(NQKV + n_plain):
                n, m = divmod(f, 4)
                if m == 0:
                    pe.wait_ge(w_in[n % RING], 16 * (n // RING + 1))
                if f >= 4:
                    if f - 4 < NQKV:
                        pe.wait_ge(S["qkv_out"], f - 3)
                    else:
                        pe.wait_ge(S["plain_out"], f - 3 - NQKV)
                if f < NQKV:
                    for k in range(KD):
                        mm = pe.matmul(K.bank[2 * (f % 4) + 1][:, 0:TC], K.wring[:, n % RING, k, m * P:(m + 1) * P],
                                       K.hT[:, k, 0:TC], start=(k == 0), stop=(k == KD - 1))
                    mm.then_inc(S["mm_c"], 1)
                for k in range(KD):
                    mm = pe.matmul(K.bank[2 * (f % 4)][:, :], K.wring[:, n % RING, k, m * P:(m + 1) * P],
                                   K.hT[:, k, TC:TT], start=(k == 0), stop=(k == KD - 1))
                mm.then_inc(S["mm_x"], 1)
            n = len(loads) - 1
            pe.wait_ge(w_in[n % RING], 16 * (n // RING + 1))
            pe.wait_ge(S["plain_out"], n_plain)
            for b0, t0, t1 in ((0, 0, TC), (1, TC, TT)):
                for k in range(KD):
                    mm = pe.matmul(K.bank[b0][0:16, 0:t1 - t0], K.wring[:, n % RING, k, 0:16], K.hT[:, k, t0:t1],
                                   start=(k == 0), stop=(k == KD - 1))
            mm.then_inc(S["mm_x"], 1)
            pe.wait_ge(S["plain_out"], n_plain + 2)
            for j in range(NT):
                tr = pe.transpose(K.bank[2][:, j * 16:(j + 1) * 16], baT[:, j * P:(j + 1) * P], K.ident[0:16, 0:16])
            tr.then_inc(S["ba_turned"], 1)

        @block.gpsimd
        def _(pool):
            for a, b in ((0, PAD), (PAD + TC, UC), (UC, UC + PAD), (UC + PAD + TX, UC + UX)):
                pool.memset(U[:, :, a:b], 0.0).then_inc(S["pads"], 1)

        @block.scalar
        def _(act):
            def silu(f):
                act.wait_ge(S["conv_c"], f + 1)
                act.wait_ge(S["conv_x"], f + 1)
                act.activation(C[:, f, :], C[:, f, :], ACT.Silu).then_inc(S["silu_done"], 1)

            for f in range(NQKV):
                if f >= NU:
                    act.wait_ge(S["conv_c"], f - NU + 1)
                    act.wait_ge(S["conv_x"], f - NU + 1)
                act.wait_ge(S["mm_c"], f + 1)
                act.wait_ge(S["mm_x"], f + 1)
                act.activation(U[:, f % NU, PAD:PAD + TC], K.bank[2 * (f % 4) + 1][:, 0:TC], ACT.Copy)
                act.activation(U[:, f % NU, UC + PAD:UC + PAD + TX], K.bank[2 * (f % 4)][:, :], ACT.Copy)\
                    .then_inc(S["qkv_out"], 1)
                if f >= 2:
                    silu(f - 2)
            for f in range(NQKV - 2, NQKV):
                silu(f)
            for m in range(n_plain):
                f = NQKV + m
                act.wait_ge(S["mm_x"], f + 1)
                which, q = divmod(m, NCF)
                dst, func = ((zT, ACT.Silu), (cfa, ACT.Copy), (cfs, ACT.Sigmoid))[which]
                act.activation(dst[:, q, :], K.bank[2 * (f % 4)][:, :], func).then_inc(S["plain_out"], 1)
            act.wait_ge(S["mm_x"], NQKV + n_plain + 1)
            act.activation(baT[:, 0:TC], K.bank[0][0:16, 0:TC], ACT.Copy).then_inc(S["plain_out"], 1)
            act.activation(baT[:, TC:TT], K.bank[1][0:16, :], ACT.Copy).then_inc(S["plain_out"], 1)

        @block.vector
        def _(dve):
            dve.wait_ge(S["pads"], 4)
            tap_done = (S["tap_c"], S["tap_x"])
            for f in range(NQKV):
                dve.wait_ge(S["qkv_out"], f + 1)
                for tap in range(TAPS):
                    col = WHERE_B["dn_conv_w"] + tap * NQKV + f
                    wt = K.colB[:, col:col + 1]
                    for seg, (u0, c0, n, done) in enumerate(((0, 0, TC, S["conv_c"]), (UC, TC, TX, S["conv_x"]))):
                        src, dst = U[:, f % NU, u0 + tap:u0 + tap + n], C[:, f, c0:c0 + n]
                        if tap == 0:
                            ins = dve.tensor_scalar(dst, src, wt, None, ALU.mult)
                        else:
                            dve.wait_ge(tap_done[seg], f * (TAPS - 1) + tap)
                            ins = dve.scalar_tensor_tensor(out=dst, in0=src, scalar=wt, in1=dst,
                                                           op0=ALU.mult, op1=ALU.add)
                        ins.then_inc(done if tap == TAPS - 1 else tap_done[seg], 1)
            dve.wait_ge(S["ba_turned"], 1)
            dve.tensor_copy(ba, K.bank[2][:, 0:NT * 16].rearrange("p (j n) -> p j n", n=16)).then_inc(S["ba_out"], 1)

def qk_norm(K, C):
    nc = K.nc
    N = 2 * H1
    with ExitStack() as c, phase(nc, "sq_done sum_done len_done inv_done scaled") as (block, S):
        sq = c.enter_context(sbuf(nc, "qk_sq", [P, 2, TT], F32))
        ln = c.enter_context(sbuf(nc, "qk_len", [P, 2, TT], F32))
        inv = c.enter_context(sbuf(nc, "qk_inv", [P, 2, TT], F32))
        parts = ((0, 0, 512), (1, 512, TT))

        @block.scalar
        def _(act):
            def square(f):
                if f >= 2:
                    act.wait_ge(S["sum_done"], f - 1)
                act.activation(sq[:, f % 2, :], C[:, f, :], ACT.Square).then_inc(S["sq_done"], 1)

            square(0)
            for f in range(N):
                if f + 1 < N:
                    square(f + 1)
                act.wait_ge(S["sum_done"], f + 1)
                if f >= 2:
                    act.wait_ge(S["inv_done"], f - 1)
                for b, t0, t1 in parts:
                    last = act.activation(ln[:, f % 2, t0:t1], K.bank[2 * (f % 2) + b][:, 0:t1 - t0], ACT.Sqrt,
                                          bias=K.eps[:, :])
                last.then_inc(S["len_done"], 1)

        @block.tensor
        def _(pe):
            for f in range(N):
                pe.wait_ge(S["sq_done"], f + 1)
                if f >= 2:
                    pe.wait_ge(S["len_done"], f - 1)
                for b, t0, t1 in parts:
                    mm = pe.matmul(K.bank[2 * (f % 2) + b][:, 0:t1 - t0], K.ones, sq[:, f % 2, t0:t1],
                                   start=True, stop=True)
                mm.then_inc(S["sum_done"], 1)

        @block.vector
        def _(dve):
            for f in range(N):
                dve.wait_ge(S["len_done"], f + 1)
                if f >= 2:
                    dve.wait_ge(S["scaled"], f - 1)
                dve.reciprocal(inv[:, f % 2, :], ln[:, f % 2, :]).then_inc(S["inv_done"], 1)
                dve.wait_ge(S["inv_done"], f + 1)
                dve.scalar_tensor_tensor(out=C[:, f, :], in0=inv[:, f % 2, :],
                                         scalar=DK ** -0.5 if f < H1 else 1.0, in1=C[:, f, :],
                                         op0=ALU.mult, op1=ALU.mult).then_inc(S["scaled"], 1)


def turn_back(K, sources, destinations):
    nc = K.nc
    with phase(nc, "turned_a turned_b out_a out_b") as (block, S):
        @block.tensor
        def _(pe):
            for n, src in enumerate(sources):
                for lo, hi, b, turned, out in ((0, 4, 0, S["turned_a"], S["out_a"]), (4, NT, 1, S["turned_b"], S["out_b"])):
                    if n >= 2:
                        pe.wait_ge(out, n - 1)
                    for j in range(lo, hi):
                        tr = pe.transpose(K.bank[2 * (n % 2) + b][:, (j - lo) * P:(j - lo + 1) * P],
                                          src[:, j * P:(j + 1) * P], K.ident)
                    tr.then_inc(turned, 1)

        @block.scalar
        def _(act):
            for n, dst in enumerate(destinations):
                act.wait_ge(S["turned_a"], n + 1)
                act.activation(dst[:, 0:4, :], K.bank[2 * (n % 2)][:, :].rearrange("p (j n) -> p j n", n=P),
                               ACT.Copy).then_inc(S["out_a"], 1)

        @block.vector
        def _(dve):
            for n, dst in enumerate(destinations):
                dve.wait_ge(S["turned_b"], n + 1)
                dve.tensor_copy(dst[:, 4:NT, :], K.bank[2 * (n % 2) + 1][:, 0:(NT - 4) * P]
                                .rearrange("p (j n) -> p j n", n=P)).then_inc(S["out_b"], 1)


def conformer(K, cfa, cfs, cfT):
    nc = K.nc
    names = "glu tap conv_done sum1 centred sq_done sum2 rms_done inv_done normed out_done"
    with ExitStack() as c, phase(nc, names) as (block, S):
        y = c.enter_context(sbuf(nc, "cf_glu", [P, NCF, TX], F32))
        z = c.enter_context(sbuf(nc, "cf_conv", [P, NCF, TX], F32))
        rms = c.enter_context(sbuf(nc, "cf_rms", [P, TX], F32))
        inv = c.enter_context(sbuf(nc, "cf_inv", [P, TX], F32))

        def col(name, n):
            return K.colA[:, WHERE_A[name] + n:WHERE_A[name] + n + 1]

        @block.vector
        def _(dve):
            step = Chain(dve, S["tap"])
            for m in range(NCF):
                dve.tensor_tensor(y[:, m, :], cfa[:, m, :], cfs[:, m, :], ALU.mult).then_inc(S["glu"], 1)
                dve.wait_ge(S["glu"], m + 1)
                step(dve.tensor_scalar(z[:, m, :], y[:, m, :], col("cf_dw_w", HALO * NCF + m), col("cf_dw_b", m),
                                       ALU.mult, ALU.add))
                for d in range(-HALO, HALO + 1):
                    if d == 0:
                        continue
                    lo, hi = max(0, -d) * GRID_W, (ROWS - max(0, d)) * GRID_W
                    ins = dve.scalar_tensor_tensor(
                        out=z[:, m, lo:hi], in0=y[:, m, lo + d * GRID_W:hi + d * GRID_W],
                        scalar=col("cf_dw_w", (HALO + d) * NCF + m), in1=z[:, m, lo:hi], op0=ALU.mult, op1=ALU.add)
                    if d == HALO:
                        ins.then_inc(S["conv_done"], 1)
                    else:
                        step(ins)
            dve.wait_ge(S["conv_done"], NCF)
            dve.wait_ge(S["sum1"], 1)
            for m in range(NCF):
                dve.scalar_tensor_tensor(out=z[:, m, :], in0=K.bank[0][:, :], scalar=-1.0 / CFC, in1=z[:, m, :],
                                         op0=ALU.mult, op1=ALU.add).then_inc(S["centred"], 1)
            dve.wait_ge(S["rms_done"], 1)
            dve.reciprocal(inv[:, :], rms[:, :]).then_inc(S["inv_done"], 1)
            dve.wait_ge(S["inv_done"], 1)
            for m in range(NCF):
                dve.tensor_tensor(z[:, m, :], z[:, m, :], inv[:, :], ALU.mult).then_inc(S["normed"], 1)

        @block.tensor
        def _(pe):
            for m in range(NCF):
                pe.wait_ge(S["conv_done"], m + 1)
                mm = pe.matmul(K.bank[0][:, :], K.ones, z[:, m, :], start=(m == 0), stop=(m == NCF - 1))
            mm.then_inc(S["sum1"], 1)
            for m in range(NCF):
                pe.wait_ge(S["sq_done"], m + 1)
                mm = pe.matmul(K.bank[1][:, :], K.ones, y[:, m, :], start=(m == 0), stop=(m == NCF - 1))
            mm.then_inc(S["sum2"], 1)

        @block.scalar
        def _(act):
            for m in range(NCF):
                act.wait_ge(S["centred"], m + 1)
                act.activation(y[:, m, :], z[:, m, :], ACT.Square).then_inc(S["sq_done"], 1)
            act.wait_ge(S["sum2"], 1)
            act.activation(rms[:, :], K.bank[1][:, :], ACT.Sqrt, bias=K.eps[:, :], scale=1.0 / CFC)\
                .then_inc(S["rms_done"], 1)
            for m in range(NCF):
                act.wait_ge(S["normed"], m + 1)
                act.activation(cfT[:, m, :], z[:, m, :], ACT.Silu, bias=col("cf_ln_b", m), scale=col("cf_ln_g", m))\
                    .then_inc(S["out_done"], 1)



def delta_gates(K, I, ba, G):
    nc = K.nc
    with ExitStack() as c, phase(nc, "par_in a_step d_step sums gl_out") as (block, S):
        def buf(name):
            return c.enter_context(sbuf(nc, name, [P, 2, NT, H1], F32))

        par = c.enter_context(sbuf(nc, "gate_par", [P, 2, 2, H1], F32))
        ea = c.enter_context(sbuf(nc, "gate_ea", [P, 2, H1], F32))
        a, b, r, g, gl, t = (buf("gate_" + n) for n in ("a", "b", "r", "g", "gl", "t"))
        W = NT * H1

        @block.sync
        def _(sp):
            for n, src in enumerate((I["dn_a_log"], I["dn_dt_bias"])):
                sp.dma_start(par[:, n, :, :], src[0].partition_broadcast(P)).then_inc(S["par_in"], 16)
            sp.wait_ge(S["par_in"], 32)

        @block.vector
        def _(dve):
            step = Chain(dve, S["d_step"])
            dve.wait_ge(S["par_in"], 32)
            for d in range(2):
                dt = par[:, 1, d:d + 1, :].broadcast_to([P, NT, H1])
                ins = dve.tensor_tensor(a[:, d, :, :], ba[:, :, d * 8 + 4:d * 8 + 8], dt, ALU.add)
                step(ins)
            step(dve.tensor_scalar(b[:, :, :, :], a[:, :, :, :], 0.0, None, ALU.max))
            dve.wait_ge(S["a_step"], 5)
            step(dve.tensor_tensor(b[:, :, :, :], b[:, :, :, :], r[:, :, :, :], ALU.add))
            for d in range(2):
                e = ea[:, d:d + 1, :].broadcast_to([P, NT, H1])
                step(dve.scalar_tensor_tensor(out=g[:, d, :, :], in0=b[:, d, :, :], scalar=-1.0, in1=e,
                                              op0=ALU.mult, op1=ALU.mult))
            dve.wait_ge(S["sums"], 1)
            for d in range(2):
                step(dve.tensor_copy(G["cumg"][:, d, :, :], K.bank[0][:, d * W:(d + 1) * W]
                                     .rearrange("p (j h) -> p j h", h=H1)))
            step(dve.tensor_copy(gl[:, :, :, :], K.bank[1][:, 0:2 * W]
                                 .rearrange("p (d j h) -> p d j h", d=2, h=H1)))
            step(dve.tensor_tensor(t[:, :, :, :], gl[:, :, :, :], G["cumg"][:, :, :, :], ALU.subtract))

        @block.scalar
        def _(act):
            step = Chain(act, S["a_step"])
            act.wait_ge(S["par_in"], 32)
            step(act.activation(ea[:, :, :], par[:, 0, :, :], ACT.Exp))
            act.wait_ge(S["d_step"], 2)
            step(act.activation(r[:, :, :, :], a[:, :, :, :], ACT.Abs))
            step(act.activation(r[:, :, :, :], r[:, :, :, :], ACT.Exp, scale=-1.0))
            step(act.activation(t[:, :, :, :], r[:, :, :, :], ACT.Ln, bias=K.one[:, :]))
            step(act.activation(r[:, :, :, :], t[:, :, :, :], ACT.Copy))
            act.wait_ge(S["d_step"], 9)
            step(act.activation(G["egc"][:, :, :, :], G["cumg"][:, :, :, :], ACT.Exp))
            step(act.activation(G["egl"][:, :, :, :], gl[:, :, :, :], ACT.Exp))
            act.wait_ge(S["d_step"], 10)
            step(act.activation(G["ekd"][:, :, :, :], t[:, :, :, :], ACT.Exp))
            for d in range(2):
                step(act.activation(G["beta"][:, d, :, :], ba[:, :, d * 8:d * 8 + 4], ACT.Sigmoid))

        @block.tensor
        def _(pe):
            pe.wait_ge(S["d_step"], 6)
            for d in range(2):
                gd = g[:, d, :, :].rearrange("p j h -> p (j h)")
                pe.matmul(K.bank[0][:, d * W:(d + 1) * W], K.inc[d], gd, start=True, stop=True)
                mm = pe.matmul(K.bank[1][:, d * W:(d + 1) * W], K.ones, gd, start=True, stop=True)
            mm.then_inc(S["sums"], 1)


class Inverse:

    @staticmethod
    def buffers(K, c, d):
        def buf(name):
            return c.enter_context(sbuf(K.nc, f"inv_{name}{d}", [P, 4, P], F32))
        return buf("X"), buf("Z"), buf("Y")

    MM_COUNT = 1 + 3 * (LEVELS - 2) + 2
    STEP_COUNT = 3 + 3 * (LEVELS - 2) + 2


def tensor_inverses(pe, K, As, bufs, banks, steps, base, mms):
    dirs = range(len(As))
    for d in dirs:
        pe.wait_ge(steps[d], base + 2)
        for h in range(4):
            tr = pe.transpose(banks[d][0][:, h * P:(h + 1) * P], bufs[d][1][:, h, :], K.ident)
        tr.then_inc(mms[d], 1)
    n = base + 3
    for level in range(1, LEVELS):
        for d in dirs:
            pe.wait_ge(steps[d], n)
            for h in range(4):
                m = pe.matmul(banks[d][0][:, h * P:(h + 1) * P], As[d](h), bufs[d][0][:, h, :], start=True, stop=True)
            m.then_inc(mms[d], 1)
        for d in dirs:
            _, Z, Y = bufs[d]
            pe.wait_ge(steps[d], n + 1)
            if level < LEVELS - 1:
                for h in range(4):
                    m = pe.matmul(banks[d][1][:, h * P:(h + 1) * P], Z[:, h, :], Y[:, h, :], start=True, stop=True)
                m.then_inc(mms[d], 1)
            for h in range(4):
                m = pe.matmul(banks[d][2][:, h * P:(h + 1) * P], Y[:, h, :], Z[:, h, :], start=True, stop=True)
            m.then_inc(mms[d], 1)
        n += 3


def vector_inverses(dve, K, As, bufs, banks, steps, mms, before):
    dirs = range(len(As))

    def four(bank):
        return bank[:, :].rearrange("p (h t) -> p h t", h=4)

    for d in dirs:
        steps[d].put(dve.tensor_tensor(bufs[d][1][:, :, :], As[d], K.cross[1 - d % 2][0], ALU.mult))
    for d in dirs:
        Z = bufs[d][1]
        steps[d].wait()
        steps[d].put(dve.tensor_tensor(Z[:, :, :], Z[:, :, :], K.ident4, ALU.add))
    n = before + 1
    for d in dirs:
        dve.wait_ge(mms[d], n)
        steps[d].put(dve.tensor_copy(bufs[d][0][:, :, :], four(banks[d][0])))
    for level in range(1, LEVELS):
        last = level == LEVELS - 1
        for d in dirs:
            dve.wait_ge(mms[d], n + 1)
            steps[d].put(dve.tensor_tensor(bufs[d][2][:, :, :], four(banks[d][0]), K.cross[d % 2][level], ALU.mult))
        for d in dirs:
            X, Z, _ = bufs[d]
            if not last:
                dve.wait_ge(mms[d], n + 2)
                steps[d].put(dve.tensor_tensor(X[:, :, :], four(banks[d][1]), X[:, :, :], ALU.add))
            dve.wait_ge(mms[d], n + (2 if last else 3))
            steps[d].put(dve.tensor_tensor(Z[:, :, :], four(banks[d][2]), Z[:, :, :], ALU.add))
        n += 3
    for d in dirs:
        steps[d].wait()


def delta_step(K, C, Ktok, Vtok, G, O, St, tile_of, with_output):
    nc = K.nc
    names = "st_f st_b mm_f mm_b v_f v_b a_f a_b p_f p_b"
    with ExitStack() as c, phase(nc, names) as (block, S):
        def buf(name, d):
            return c.enter_context(sbuf(nc, f"{name}{d}", [P, 4, P], F32))

        dirs = (0, 1)
        kT, qT, Kd, Bv, Kb = ([buf(n, d) for d in dirs] for n in ("kT", "qT", "kd", "bv", "kb"))
        Dg, Db, Em, BE, QE, LT, IT = ([buf(n, d) for d in dirs] for n in
                                      ("diag_g", "diag_b", "decay", "bdecay", "qdecay", "LT", "intra"))
        inv = [Inverse.buffers(K, c, d) for d in dirs]
        nW, Vn = Dg, Db
        gcj = [c.enter_context(sbuf(nc, f"gates{d}", [P, 5, H1], F32)) for d in dirs]
        bank = [K.bank[4 * d:4 * d + 4] for d in dirs]
        mm = (S["mm_f"], S["mm_b"])
        vs = (S["v_f"], S["v_b"])
        as_ = (S["a_f"], S["a_b"])
        ps = (S["p_f"], S["p_b"])
        GC, BETA, EGC, EKD, EGL = range(5)
        four = lambda b: b[:, :].rearrange("p (h t) -> p h t", h=4)
        wide = lambda d, q: gcj[d][:, q, :].unsqueeze(2).broadcast_to([P, H1, P])

        @block.gpsimd
        def _(pool):
            for d in dirs:
                j = tile_of[d]
                step = Chain(pool, ps[d])
                for q, src in ((GC, G["cumg"]), (BETA, G["beta"]), (EGC, G["egc"]), (EKD, G["ekd"]), (EGL, G["egl"])):
                    step.put(pool.tensor_copy(gcj[d][:, q, :], src[:, d, bass.ds(j, 1), :]
                                              .rearrange("p o h -> p (o h)")))
            for d in dirs:
                pool.wait_ge(ps[d], 5)
                pool.tensor_tensor(Dg[d][:, :, :], K.ident4, wide(d, GC), ALU.mult).then_inc(ps[d], 1)
                pool.tensor_tensor(Db[d][:, :, :], K.ident4, wide(d, BETA), ALU.mult).then_inc(ps[d], 1)
            for d in dirs:
                j = tile_of[d]
                kt = Ktok[:, :, bass.ds(j, 1), :].rearrange("p h o n -> p (h o) n")
                vt = Vtok[:, :, bass.ds(j, 1), :].rearrange("p h o n -> p (h o) n")
                pool.tensor_tensor(Kb[d][:, :, :], kt, wide(d, BETA), ALU.mult).then_inc(ps[d], 1)
                pool.tensor_tensor(Bv[d][:, :, :], vt, wide(d, BETA), ALU.mult).then_inc(ps[d], 1)
                pool.tensor_tensor(Kd[d][:, :, :], kt, wide(d, EKD), ALU.mult).then_inc(ps[d], 1)
                pool.wait_ge(ps[d], 8)
                pool.tensor_tensor(Kb[d][:, :, :], Kb[d][:, :, :], wide(d, EGC), ALU.mult).then_inc(ps[d], 1)
            if with_output:
                for d in dirs:
                    pool.wait_ge(as_[d], 4)
                    pool.tensor_tensor(QE[d][:, :, :], QE[d][:, :, :], qT[d][:, :, :], ALU.mult).then_inc(ps[d], 1)

        @block.scalar
        def _(act):
            for d in dirs:
                j = tile_of[d]
                ts = bass.ds(j * P, P)
                act.activation(kT[d][:, :, :], C[:, H1:2 * H1, ts], ACT.Copy).then_inc(as_[d], 1)
                act.activation(qT[d][:, :, :], C[:, 0:H1, ts], ACT.Copy).then_inc(as_[d], 1)
            for d in dirs:
                act.wait_ge(vs[d], 1)
                act.activation(Em[d][:, :, :], Em[d][:, :, :], ACT.Exp).then_inc(as_[d], 1)
                act.activation(QE[d][:, :, :], four(bank[d][0]), ACT.Exp).then_inc(as_[d], 1)
            for d in dirs:
                act.wait_ge(mm[d], 3 + Inverse.MM_COUNT + 1)
                act.activation(nW[d][:, :, :], four(bank[d][3]), ACT.Copy, scale=-1.0).then_inc(as_[d], 1)

        @block.tensor
        def _(pe):
            for d in dirs:
                pe.wait_ge(ps[d], 7)
                pe.matmul(bank[d][0][:, :], K.ones, Dg[d][:, :, :], start=True, stop=True).then_inc(mm[d], 1)
                pe.matmul(bank[d][1][:, :], K.ones, Db[d][:, :, :], start=True, stop=True).then_inc(mm[d], 1)
                pe.wait_ge(as_[d], 2)
                for h in range(H1):
                    pe.matmul(bank[d][2][:, h * P:(h + 1) * P], kT[d][:, h, :], kT[d][:, h, :], start=True, stop=True)
                for h in range(H1):
                    m = pe.matmul(bank[d][3][:, h * P:(h + 1) * P], kT[d][:, h, :], qT[d][:, h, :],
                                  start=True, stop=True)
                m.then_inc(mm[d], 1)
            for d in dirs:
                pe.wait_ge(as_[d], 4)
            tensor_inverses(pe, K, [lambda h, d=d: LT[d][:, h, :] for d in dirs], inv, bank, vs, 6, mm)
            n = 6 + Inverse.STEP_COUNT
            for d in dirs:
                Z = inv[d][1]
                pe.wait_ge(ps[d], 11)
                pe.wait_ge(vs[d], n)
                for h in range(H1):
                    m = pe.matmul(bank[d][3][:, h * P:(h + 1) * P], Kb[d][:, h, :], Z[:, h, :], start=True, stop=True)
                m.then_inc(mm[d], 1)
                pe.wait_ge(as_[d], 5)
                for h in range(H1):
                    sl = bank[d][0][:, h * P:(h + 1) * P]
                    pe.matmul(sl, Z[:, h, :], Bv[d][:, h, :], start=True, stop=False)
                    m = pe.matmul(sl, nW[d][:, h, :], St[d][:, h, :], start=False, stop=True)
                m.then_inc(mm[d], 1)
                pe.wait_ge(vs[d], n + 1)
                for h in range(H1):
                    m = pe.matmul(bank[d][2][:, h * P:(h + 1) * P], Kd[d][:, h, :], Vn[d][:, h, :],
                                  start=True, stop=True)
                m.then_inc(mm[d], 1)
                if with_output:
                    pe.wait_ge(ps[d], 12)
                    for h in range(H1):
                        sl = bank[d][1][:, h * P:(h + 1) * P]
                        pe.matmul(sl, QE[d][:, h, :], St[d][:, h, :], start=True, stop=False)
                        m = pe.matmul(sl, IT[d][:, h, :], Vn[d][:, h, :], start=False, stop=True)
                    m.then_inc(mm[d], 1)

        @block.vector
        def _(dve):
            steps = [Chain(dve, vs[d]) for d in dirs]
            for d in dirs:
                dve.wait_ge(mm[d], 1)
                dve.wait_ge(ps[d], 5)
                for h in range(H1):
                    ins = dve.tensor_scalar(Em[d][:, h, :], bank[d][0][:, h * P:(h + 1) * P],
                                            gcj[d][:, GC, h:h + 1], 0.0, ALU.subtract, ALU.min)
                steps[d].put(ins)
            for d in dirs:
                step = steps[d]
                dve.wait_ge(as_[d], 4)
                step(dve.tensor_tensor(Em[d][:, :, :], Em[d][:, :, :], K.incl4[d], ALU.mult))
                dve.wait_ge(mm[d], 3)
                step(dve.tensor_tensor(IT[d][:, :, :], four(bank[d][3]), Em[d][:, :, :], ALU.mult))
                step(dve.tensor_tensor(BE[d][:, :, :], four(bank[d][1]), Em[d][:, :, :], ALU.mult))
                step(dve.tensor_tensor(BE[d][:, :, :], BE[d][:, :, :], K.strict4[d], ALU.mult))
                step(dve.tensor_tensor(LT[d][:, :, :], four(bank[d][2]), BE[d][:, :, :], ALU.mult))
            vector_inverses(dve, K, [LT[d][:, :, :] for d in dirs], inv, bank, steps, mm, 3)
            n = 3 + Inverse.MM_COUNT
            for d in dirs:
                step = steps[d]
                dve.wait_ge(mm[d], n + 2)
                step.put(dve.tensor_copy(Vn[d][:, :, :], four(bank[d][0])))
                dve.wait_ge(mm[d], n + 3 + with_output)
                for h in range(H1):
                    ins = dve.scalar_tensor_tensor(out=St[d][:, h, :], in0=St[d][:, h, :],
                                                   scalar=gcj[d][:, EGL, h:h + 1],
                                                   in1=bank[d][2][:, h * P:(h + 1) * P], op0=ALU.mult, op1=ALU.add)
                if with_output:
                    j = tile_of[d] - JC
                    o = O[:, bass.ds(j, 1), :].rearrange("p o n -> p (o n)")
                    ins = dve.tensor_tensor(o, bank[d][1][:, :], o, ALU.add)
                step.put(ins)

def delta_readout(K, O, headsT):
    nc = K.nc
    with ExitStack() as c, phase(nc, "sq_done v_step rms_done turned gated") as (block, S):
        sq = c.enter_context(sbuf(nc, "dr_sq", [P, JX, H1 * DK], F32))
        st = c.enter_context(sbuf(nc, "dr_stats", [P, 3, JX * H1], F32))

        @block.scalar
        def _(act):
            act.activation(sq[:, :, :], O[:, :, :], ACT.Square).then_inc(S["sq_done"], 1)
            act.wait_ge(S["v_step"], 1)
            act.activation(st[:, 1, :], st[:, 0, :], ACT.Sqrt, bias=K.eps[:, :], scale=1.0 / DK).then_inc(S["rms_done"], 1)

        @block.vector
        def _(dve):
            step = Chain(dve, S["v_step"])
            heads = lambda t: t[:, :, :].rearrange("p j (h n) -> p (j h) n", n=DK)
            dve.wait_ge(S["sq_done"], 1)
            step.put(dve.tensor_reduce(st[:, 0, :], heads(sq), AX.X, ALU.add))
            dve.wait_ge(S["rms_done"], 1)
            step(dve.reciprocal(st[:, 2, :], st[:, 1, :]))
            step.put(dve.tensor_tensor(heads(O), heads(O),
                                       st[:, 2, :].unsqueeze(2).broadcast_to([P, JX * H1, DK]), ALU.mult))
            g = K.colA[:, WHERE_A["dn_norm_g"]:WHERE_A["dn_norm_g"] + 1]
            for h in range(H1):
                dve.wait_ge(S["turned"], h + 1)
                dve.scalar_tensor_tensor(out=headsT[:, h, :], in0=K.bank[h][:, :], scalar=g, in1=headsT[:, h, :],
                                         op0=ALU.mult, op1=ALU.mult).then_inc(S["gated"], 1)

        @block.tensor
        def _(pe):
            pe.wait_ge(S["v_step"], 3)
            for h in range(H1):
                for j in range(JX):
                    tr = pe.transpose(K.bank[h][:, j * P:(j + 1) * P], O[:, j, h * DK:(h + 1) * DK], K.ident)
                tr.then_inc(S["turned"], 1)


def output_projection(K, srcT, w, gates, tiles, first_col):
    nc = K.nc
    with ExitStack() as c, phase(nc, "w_in0 w_in1 mm_done gated added") as (block, S):
        wb = c.enter_context(sbuf(nc, "wo", [P, 2, KD, 512], F32))
        t = c.enter_context(sbuf(nc, "wo_gated", [P, 2, 512], F32))
        w_in = (S["w_in0"], S["w_in1"])
        units = [(n, j) for n in range(2) for j in tiles]

        @block.sync
        def _(sp):
            for n in range(2):
                sp.dma_start(wb[:, n, :, :], w.rearrange("(k p) n -> p k n", p=P)[:, :, n * 512:(n + 1) * 512])\
                    .then_inc(w_in[n], 16)

        @block.tensor
        def _(pe):
            for u, (n, j) in enumerate(units):
                pe.wait_ge(w_in[n], 16)
                if u >= 4:
                    pe.wait_ge(S["gated"], u - 3)
                for k in range(KD):
                    mm = pe.matmul(K.bank[u % 4][:, :], srcT[:, k, (j - first_col) * P:(j - first_col + 1) * P],
                                   wb[:, n, k, :], start=(k == 0), stop=(k == KD - 1))
                mm.then_inc(S["mm_done"], 1)

        @block.vector
        def _(dve):
            for u, (n, j) in enumerate(units):
                dve.wait_ge(S["mm_done"], u + 1)
                if u >= 2:
                    dve.wait_ge(S["added"], u - 1)
                x = K.X[:, j, n * 512:(n + 1) * 512]
                dve.tensor_tensor(t[:, u % 2, :], K.bank[u % 4][:, :], gates(j)[:, n * 512:(n + 1) * 512], ALU.mult)\
                    .then_inc(S["gated"], 1)
                dve.wait_ge(S["gated"], u + 1)
                dve.tensor_tensor(x, x, t[:, u % 2, :], ALU.add).then_inc(S["added"], 1)


def final_norm(K, g, tiles, out=None):
    nc = K.nc
    N = len(tiles)
    with ExitStack() as c, phase(nc, "g_in sq_done rms_done v_step normed stored") as (block, S):
        gb = c.enter_context(sbuf(nc, "fn_gain", [P, D], F32))
        junk = c.enter_context(sbuf(nc, "fn_junk", [P, D], F32))
        st = c.enter_context(sbuf(nc, "fn_stats", [P, 3, NT], F32))

        @block.sync
        def _(sp):
            sp.dma_start(gb[:, :], g.partition_broadcast(P)).then_inc(S["g_in"], 16)
            sp.wait_ge(S["g_in"], 16)
            if out is not None:
                for n, j in enumerate(tiles):
                    sp.wait_ge(S["normed"], n + 1)
                    sp.dma_start(out[n * P:(n + 1) * P, :], K.X[:, j, :]).then_inc(S["stored"], 16)
                sp.wait_ge(S["stored"], 16 * N)

        @block.scalar
        def _(act):
            for n, j in enumerate(tiles):
                if n:
                    act.wait_ge(S["sq_done"], n)
                act.activation(junk[:, :], K.X[:, j, :], ACT.Square, accum_out=st[:, 0, n:n + 1]).then_inc(S["sq_done"], 1)
            act.wait_ge(S["sq_done"], N)
            act.activation(st[:, 1, 0:N], st[:, 0, 0:N], ACT.Sqrt, bias=K.eps[:, :], scale=1.0 / D)\
                .then_inc(S["rms_done"], 1)

        @block.vector
        def _(dve):
            step = Chain(dve, S["v_step"])
            dve.wait_ge(S["rms_done"], 1)
            step(dve.reciprocal(st[:, 2, 0:N], st[:, 1, 0:N]))
            dve.wait_ge(S["g_in"], 16)
            for n, j in enumerate(tiles):
                dve.scalar_tensor_tensor(out=K.X[:, j, :], in0=K.X[:, j, :], scalar=st[:, 2, n:n + 1],
                                         in1=gb[:, :], op0=ALU.mult, op1=ALU.mult).then_inc(S["normed"], 1)



def pick(dve, step, values, keep, k, n, bufs):
    top, eq, cnt, run, zero = bufs
    bc = lambda ap: ap.broadcast_to([P, JX, n])
    for j in range(JX):
        step.put(dve.max(top[:, j, :], values[:, j, :]))
    step.wait()
    least = bc(top[:, :, k - 1:k])
    step.put(dve.tensor_tensor(keep, values, least, ALU.is_gt))
    step(dve.tensor_tensor(eq, values, least, ALU.is_equal))
    step.put(dve.tensor_reduce(cnt[:, :], keep, AX.X, ALU.add))
    for j in range(JX):
        step.put(dve.tensor_tensor_scan(run[:, j, :], eq[:, j, :], zero[:, 0:n], 0.0, ALU.add, ALU.add))
    step.wait()
    step(dve.tensor_tensor(run, run, cnt[:, :].unsqueeze(2).broadcast_to([P, JX, n]), ALU.add))
    step(dve.scalar_tensor_tensor(out=eq, in0=run, scalar=k + 0.5, in1=eq, op0=ALU.is_le, op1=ALU.mult))
    step(dve.tensor_tensor(keep, keep, eq, ALU.add))


def router(K, I, wt, kept):
    nc = K.nc
    with ExitStack() as c, phase(nc, "in_done mm_done sig_done v_step") as (block, S):
        buf = lambda name, shape: c.enter_context(sbuf(nc, "rt_" + name, shape, F32))
        rw = buf("w", [P, KD, NE])
        bias = buf("bias", [P, NE])
        kp = kept
        sc, sel, eq, run = (buf(n, [P, JX, NE]) for n in ("scores", "sel", "eq", "run"))
        top2, top = buf("top2", [P, JX * GROUPS, 8]), buf("top", [P, JX, 8])
        gs, gk, geq, grun = (buf(n, [P, JX, GROUPS]) for n in ("gs", "gk", "geq", "grun"))
        cnt, zero, tot = buf("cnt", [P, JX]), buf("zero", [P, NE]), buf("tot", [P, 2, JX])

        @block.sync
        def _(sp):
            sp.dma_start(rw[:, :, :], I["router_w"][0].rearrange("(k p) n -> p k n", p=P)).then_inc(S["in_done"], 16)
            sp.dma_start(bias[:, :], I["router_bias"][0].partition_broadcast(P)).then_inc(S["in_done"], 16)
            sp.wait_ge(S["in_done"], 32)

        @block.tensor
        def _(pe):
            pe.wait_ge(S["in_done"], 32)
            for j in range(JX):
                for k in range(KD):
                    mm = pe.matmul(K.bank[0][:, j * NE:(j + 1) * NE], K.hT[:, k, TC + j * P:TC + (j + 1) * P],
                                   rw[:, k, :], start=(k == 0), stop=(k == KD - 1))
            mm.then_inc(S["mm_done"], 1)

        @block.scalar
        def _(act):
            act.wait_ge(S["mm_done"], 1)
            act.activation(sc[:, :, :], K.bank[0][:, 0:JX * NE].rearrange("p (j e) -> p j e", e=NE), ACT.Sigmoid)\
                .then_inc(S["sig_done"], 1)

        @block.vector
        def _(dve):
            step = Chain(dve, S["v_step"])
            step.put(dve.memset(zero[:, :], 0.0))
            dve.wait_ge(S["sig_done"], 1)
            dve.wait_ge(S["in_done"], 32)
            step(dve.tensor_tensor(sel[:, :, :], sc[:, :, :], bias[:, :].unsqueeze(1).broadcast_to([P, JX, NE]), ALU.add))
            n = NE // GROUPS
            for j in range(JX):
                for g in range(GROUPS):
                    step.put(dve.max(top2[:, j * GROUPS + g, :], sel[:, j, g * n:(g + 1) * n]))
            step.wait()
            t2 = top2[:, :, :].rearrange("p (j g) e -> p j g e", g=GROUPS)
            step(dve.tensor_tensor(gs[:, :, :], t2[:, :, :, 0], t2[:, :, :, 1], ALU.add))
            pick(dve, step, gs[:, :, :], gk[:, :, :], 4, GROUPS, (top, geq[:, :, :], cnt, grun[:, :, :], zero))
            step(dve.tensor_scalar(geq[:, :, :], gk[:, :, :], 1e30, -1e30, ALU.mult, ALU.add))
            for g in range(GROUPS):
                part = sel[:, :, g * n:(g + 1) * n]
                step.put(dve.tensor_tensor(part, part, geq[:, :, g:g + 1].broadcast_to([P, JX, n]), ALU.add))
            step.wait()
            pick(dve, step, sel[:, :, :], kp[:, :, :], 6, NE, (top, eq[:, :, :], cnt, run[:, :, :], zero))
            step(dve.tensor_tensor(sc[:, :, :], sc[:, :, :], kp[:, :, :], ALU.mult))
            step(dve.tensor_reduce(tot[:, 0, :], sc[:, :, :], AX.X, ALU.add))
            step(dve.reciprocal(tot[:, 1, :], tot[:, 0, :]))
            step(dve.scalar_tensor_tensor(out=wt[:, :, :], in0=sc[:, :, :], scalar=2.5,
                                          in1=tot[:, 1, :].unsqueeze(2).broadcast_to([P, JX, NE]),
                                          op0=ALU.mult, op1=ALU.mult))


def load_expert(eng, Wb, s, srcs, sem, which=(0, 1, 2)):
    for w in which:
        eng.dma_start(Wb[:, s, w, :].rearrange("p (k n) -> p k n", n=(DE, DE, D)[w]),
                      srcs[w].rearrange("(k p) n -> p k n", p=P)).then_inc(sem, 16)


def experts(K, Wb, acc, weights, following):
    nc = K.nc
    N = len(weights)
    names = "in0 in1 up_done silu_done act_done down_done acc_done"
    with ExitStack() as c, phase(nc, names) as (block, S):
        sg = c.enter_context(sbuf(nc, "ex_silu", [P, 2, TX], F32))
        aT = c.enter_context(sbuf(nc, "ex_act", [P, 2, 2, TX], F32))

        @block.sync
        def _(sp):
            if N > 1:
                load_expert(sp, Wb, 1, following[1], S["in1"])
            if following[0] is not None:
                sp.wait_ge(S["down_done"], 8)
                load_expert(sp, Wb, 0, following[0], S["in0"])
                sp.wait_ge(S["in0"], 48)
            if N > 1:
                sp.wait_ge(S["in1"], 48)

        @block.tensor
        def _(pe):
            for s in range(N):
                if s:
                    pe.wait_ge(S["in1"], 48)
                for m in range(2):
                    for which in range(2):
                        if s:
                            pe.wait_ge(S["act_done"], 2 * (s - 1) + m + 1)
                        for k in range(KD):
                            mm = pe.matmul(K.bank[2 * m + which][:, :],
                                           Wb[:, s, which, k * DE + m * P:k * DE + (m + 1) * P],
                                           K.hT[:, k, TC:TT], start=(k == 0), stop=(k == KD - 1))
                        mm.then_inc(S["up_done"], 1)
            for s in range(N):
                pe.wait_ge(S["act_done"], 2 * s + 2)
                for j in range(JX):
                    for n in range(2):
                        u = 8 * s + 2 * j + n
                        if u >= 4:
                            pe.wait_ge(S["acc_done"], u - 3)
                        for m in range(2):
                            mm = pe.matmul(K.bank[4 + u % 4][:, :], aT[:, s, m, j * P:(j + 1) * P],
                                           Wb[:, s, 2, m * D + n * 512:m * D + (n + 1) * 512],
                                           start=(m == 0), stop=(m == 1))
                        mm.then_inc(S["down_done"], 1)

        @block.scalar
        def _(act):
            for s in range(N):
                for m in range(2):
                    if s:
                        act.wait_ge(S["act_done"], 2 * (s - 1) + m + 1)
                    act.wait_ge(S["up_done"], 4 * s + 2 * m + 1)
                    act.activation(sg[:, m, :], K.bank[2 * m][:, :], ACT.Silu).then_inc(S["silu_done"], 1)

        @block.vector
        def _(dve):
            def gated(s):
                for m in range(2):
                    dve.wait_ge(S["silu_done"], 2 * s + m + 1)
                    dve.wait_ge(S["up_done"], 4 * s + 2 * m + 2)
                    dve.tensor_tensor(aT[:, s, m, :], sg[:, m, :], K.bank[2 * m + 1][:, :], ALU.mult)\
                        .then_inc(S["act_done"], 1)

            for s in range(N):
                gated(s)
            for s in range(N):
                for j in range(JX):
                    for n in range(2):
                        u = 8 * s + 2 * j + n
                        if s:
                            dve.wait_ge(S["acc_done"], u - 7)
                        dve.wait_ge(S["down_done"], u + 1)
                        part = acc[:, j, n * 512:(n + 1) * 512]
                        dve.scalar_tensor_tensor(out=part, in0=K.bank[4 + u % 4][:, :], scalar=weights[s](j),
                                                 in1=part, op0=ALU.mult, op1=ALU.add).then_inc(S["acc_done"], 1)


def experts_start(K, I, Wb, weights):
    with phase(K.nc, "in0") as (block, S):
        @block.sync
        def _(sp):
            load_expert(sp, Wb, 0, weights, S["in0"])
            sp.wait_ge(S["in0"], 48)


def add_experts(K, acc, gate):
    nc = K.nc
    with phase(nc, "gated added") as (block, S):
        @block.vector
        def _(dve):
            for j in range(JX):
                dve.tensor_tensor(acc[:, j, :], acc[:, j, :], gate, ALU.mult).then_inc(S["gated"], 1)
            for j in range(JX):
                dve.wait_ge(S["gated"], j + 1)
                dve.tensor_tensor(K.X[:, JC + j, :], K.X[:, JC + j, :], acc[:, j, :], ALU.add).then_inc(S["added"], 1)

TOP_K = 6
SLOTS = P
FURTHER = TX * TOP_K // SLOTS
TILES = NE + FURTHER
AT_ONCE = 4
AHEAD = 4
UNUSED = 1e6


def forget(pool, sems):
    for sem in sems:
        pool.dma_reset(range(sem.num, sem.num + 1))


def dispatch(K, wt, kept, slot_of, w_of, extra, h_rows, slot_tokens, ys, idx):
    nc = K.nc
    U32 = mybir.dt.uint32
    names = ("pos_mm copied v_step fill_set filled slots_set sc0 sc1 sc2 sc3 sc4 sc5 sc6 sc7 scattered back idx_mm idx_out "
             "h_mm h_a h_b h_st0 h_st1 blank_set blanked")
    with ExitStack() as c, phase(nc, names) as (block, S):
        buf = lambda name, shape, dt=F32: c.enter_context(sbuf(nc, "dp_" + name, shape, dt))
        pos, fits, run, m, pr, slot = (buf(n, [P, JX, NE]) for n in ("pos", "fits", "run", "m", "pr", "slot"))
        to_f = buf("to", [P, TOP_K, JX])
        cnt, more, upto, away, near = (buf(n, [P, NE]) for n in ("cnt", "more", "upto", "away", "near"))
        which, ext = buf("which", [P, FURTHER, NE]), buf("ext", [P, 1 + FURTHER + AHEAD])
        none = buf("none", [P, AHEAD])
        fill, back = buf("fill", [TILES, SLOTS]), buf("back", [TILES, SLOTS])
        rows, blank = buf("rows", [P, 2, D]), buf("blank", [P, D])
        first = K.const[:, SLOT_COL:SLOT_COL + NE]
        every = lambda ap: ap.unsqueeze(1).broadcast_to([P, JX, NE])
        table = slot_tokens.rearrange("(e s) o -> e (s o)", s=SLOTS)

        @block.tensor
        def _(pe):
            for j in range(JX):
                out = K.bank[0][:, j * NE:(j + 1) * NE]
                pe.matmul(out, K.before, kept[:, j, :], start=True, stop=(j == 0))
                for i in range(j):
                    pe.matmul(out, K.ones, kept[:, i, :], start=False, stop=(i == j - 1))
            for j in range(JX):
                mm = pe.matmul(K.bank[0][:, JX * NE:(JX + 1) * NE], K.ones, kept[:, j, :],
                               start=(j == 0), stop=(j == JX - 1))
            mm.then_inc(S["pos_mm"], 1)
            for j in range(JX):
                if j >= 2:
                    pe.wait_ge(S["h_a"], j - 1)
                    pe.wait_ge(S["h_b"], j - 1)
                for k in range(KD):
                    tr = pe.transpose(K.bank[2 + 2 * (j % 2) + k // 4][:, (k % 4) * P:(k % 4 + 1) * P],
                                      K.hT[:, k, TC + j * P:TC + (j + 1) * P], K.ident)
                tr.then_inc(S["h_mm"], 1)
            pe.wait_ge(S["back"], 16)
            pe.transpose(K.bank[1][:, 0:TILES], back[:, :], K.ident[0:TILES, 0:TILES]).then_inc(S["idx_mm"], 1)

        @block.scalar
        def _(act):
            act.wait_ge(S["blank_set"], 1)
            for n in range(NE, TILES + 1):
                act.dma_start(ys[n * SLOTS:(n + 1) * SLOTS, :], blank[:, :]).then_inc(S["blanked"], 16)
            for j in range(JX):
                act.wait_ge(S["h_mm"], j + 1)
                if j >= 2:
                    act.wait_ge((S["h_st0"], S["h_st1"])[j % 2], 16)
                act.activation(rows[:, j % 2, 0:512], K.bank[2 + 2 * (j % 2)][:, :], ACT.Copy).then_inc(S["h_a"], 1)
                act.activation(rows[:, j % 2, 512:D], K.bank[3 + 2 * (j % 2)][:, :], ACT.Copy).then_inc(S["h_b"], 1)
            act.wait_ge(S["blanked"], 16 * (TILES + 1 - NE))

        @block.sync
        def _(sp):
            sp.wait_ge(S["fill_set"], 1)
            sp.dma_start(table, fill[:, :]).then_inc(S["filled"], 16)
            for j in range(JX):
                sp.wait_ge(S["h_a"], j + 1)
                sp.wait_ge(S["h_b"], j + 1)
                sp.dma_start(h_rows[j * P:(j + 1) * P, :], rows[:, j % 2, :]).then_inc((S["h_st0"], S["h_st1"])[j % 2], 16)
            sp.wait_ge(S["scattered"], 1)
            sp.dma_start(back[:, :], table).then_inc(S["back"], 16)
            sp.wait_ge(S["h_st0"], 32)
            sp.wait_ge(S["h_st1"], 32)

        @block.gpsimd
        def _(pool):
            pool.wait_ge(S["filled"], 16)
            pool.wait_ge(S["slots_set"], 1)
            sc = [S[f"sc{n}"] for n in range(8)]
            for k in range(TOP_K):
                for j in range(JX):
                    u = k * JX + j
                    if u >= 8:
                        pool.wait_ge(sc[u % 8], 16 * (u // 8))
                    pool.indirect_dma_start(
                        out=slot_tokens, out_offset=bass.IndirectOffsetOnAxis(ap=slot_of[:, k, j:j + 1], axis=0),
                        in_=K.const[:, TOKEN_COL + j:TOKEN_COL + j + 1], in_offset=None,
                        bounds_check=TILES * SLOTS - 1, oob_is_err=False).then_inc(sc[u % 8], 16)
            for n in range(8):
                pool.wait_ge(sc[n], 16 * (TOP_K * JX // 8))
            forget(pool, sc)
            pool.sem_inc(S["scattered"], 1)

        @block.vector
        def _(dve):
            step = Chain(dve, S["v_step"])
            dve.memset(fill[:, :], UNUSED).then_inc(S["fill_set"], 1)
            dve.memset(blank[:, :], 0.0).then_inc(S["blank_set"], 1)
            step.put(dve.memset(ext[:, :], 0.0))
            step(dve.memset(none[:, :], UNUSED))
            dve.wait_ge(S["pos_mm"], 1)
            step.put(dve.tensor_copy(pos[:, :, :], K.bank[0][:, 0:JX * NE].rearrange("p (j e) -> p j e", e=NE)))
            step(dve.tensor_copy(cnt[:, :], K.bank[0][:, JX * NE:(JX + 1) * NE]))
            step(dve.tensor_scalar(more[:, :], cnt[:, :], float(SLOTS), None, ALU.is_gt))
            for n in range(2, TX // SLOTS):
                step(dve.scalar_tensor_tensor(out=more[:, :], in0=cnt[:, :], scalar=float(n * SLOTS), in1=more[:, :],
                                              op0=ALU.is_gt, op1=ALU.add))
            step(dve.tensor_tensor_scan(upto[:, :], more[:, :], K.zeros[:, 0:NE], 0.0, ALU.add, ALU.add))
            step(dve.tensor_tensor(away[:, :], upto[:, :], more[:, :], ALU.subtract))
            step(dve.tensor_scalar(away[:, :], away[:, :], float(NE - 1), float(SLOTS), ALU.add, ALU.mult))
            step(dve.tensor_tensor(near[:, :], first, away[:, :], ALU.subtract))
            step(dve.tensor_scalar(fits[:, :, :], pos[:, :, :], float(SLOTS), None, ALU.is_lt))
            step.put(dve.tensor_tensor(slot[:, :, :], pos[:, :, :], every(away[:, :]), ALU.add))
            step(dve.tensor_tensor(fits[:, :, :], fits[:, :, :], every(near[:, :]), ALU.mult))
            step(dve.tensor_tensor(slot[:, :, :], slot[:, :, :], fits[:, :, :], ALU.add))
            for j in range(JX):
                step.put(dve.tensor_tensor_scan(run[:, j, :], kept[:, j, :], K.zeros[:, 0:NE], 0.0, ALU.add, ALU.add))
            step.wait()
            for k in range(TOP_K):
                step(dve.scalar_tensor_tensor(out=m[:, :, :], in0=run[:, :, :], scalar=k + 1.0, in1=kept[:, :, :],
                                              op0=ALU.is_equal, op1=ALU.mult))
                step(dve.tensor_tensor(pr[:, :, :], m[:, :, :], slot[:, :, :], ALU.mult))
                step.put(dve.tensor_reduce(to_f[:, k, :], pr[:, :, :], AX.X, ALU.add))
                step(dve.tensor_tensor(m[:, :, :], m[:, :, :], wt[:, :, :], ALU.mult))
                step(dve.tensor_reduce(w_of[:, k, :], m[:, :, :], AX.X, ALU.add))
            dve.tensor_copy(slot_of[:, :, :], to_f[:, :, :]).then_inc(S["slots_set"], 1)
            step(dve.tensor_scalar(near[:, :], upto[:, :], float(SLOTS), None, ALU.mult))
            step(dve.tensor_tensor(which[:, :, :], near[:, :].unsqueeze(1).broadcast_to([P, FURTHER, NE]),
                                   first[:, 0:FURTHER].unsqueeze(2).broadcast_to([P, FURTHER, NE]), ALU.is_le))
            step.put(dve.tensor_copy(ext[:, 0:1], upto[:, NE - 1:NE]))
            step(dve.tensor_reduce(ext[:, 1:1 + FURTHER], which[:, :, :], AX.X, ALU.add))
            step(dve.tensor_scalar(ext[:, 1:1 + FURTHER], ext[:, 1:1 + FURTHER], float(NE - 1), None, ALU.min))
            step.put(dve.tensor_copy(extra[:, :], ext[:, :]))
            step.put(dve.tensor_copy(idx[:, TILES:TILES + AHEAD], none[:, :]))
            dve.wait_ge(S["idx_mm"], 1)
            dve.tensor_copy(idx[:, 0:TILES], K.bank[1][:, 0:TILES]).then_inc(S["idx_out"], 1)


def gather_rows(pool, Hg, col, h_rows, sem):
    pool.indirect_dma_start(out=Hg, out_offset=None, in_=h_rows,
                            in_offset=bass.IndirectOffsetOnAxis(ap=col, axis=0),
                            bounds_check=TX - 1, oob_is_err=False).then_inc(sem, 16)


def slots_start(K, Wb, Hg, h_rows, idx, cols, tile, weights):
    with phase(K.nc, "in0 in1 zeroed copied got0 got1") as (block, S):
        @block.sync
        def _(sp):
            for s in range(2):
                load_expert(sp, Wb, s, weights[s], S[f"in{s}"])
            for s in range(2):
                sp.wait_ge(S[f"in{s}"], 48)

        @block.vector
        def _(dve):
            dve.memset(Hg[:, :, :], 0.0).then_inc(S["zeroed"], 1)

        @block.tensor
        def _(pe):
            pe.wait_ge(S["zeroed"], 1)

        @block.scalar
        def _(act):
            act.wait_ge(S["zeroed"], 1)

        @block.gpsimd
        def _(pool):
            pool.tensor_copy(cols[:, 0:2], idx[:, bass.ds(tile, 2)]).then_inc(S["copied"], 1)
            pool.wait_ge(S["copied"], 1)
            pool.wait_ge(S["zeroed"], 1)
            for s in range(2):
                gather_rows(pool, Hg[:, s, :], cols[:, s:s + 1], h_rows, S[f"got{s}"])
            for s in range(2):
                pool.wait_ge(S[f"got{s}"], 16)
            forget(pool, (S["got0"], S["got1"]))


def slot_experts(K, Wb, Hg, cols, XT, aT, sg, yb, idx, h_rows, ys, e, weights, following, more):
    nc = K.nc
    T = 2 + len(weights)
    gathers = range(2, T + 2 if more else T)
    names = "in0 in1 in2 in3 turned xt_a xt_b up_done silu_done act_done down_done y_a y_b st0 st1 cols_set got0 got1"
    with phase(nc, names) as (block, S):
        banks_t = ((0, 1), (2, 3))
        st, got, in_ = (S["st0"], S["st1"]), (S["got0"], S["got1"]), [S[f"in{n}"] for n in range(AT_ONCE)]

        @block.sync
        def _(sp):
            def store(t):
                sp.wait_ge(S["y_a"], t + 1)
                sp.wait_ge(S["y_b"], t + 1)
                sp.dma_start(ys[bass.ds((e + t) * SLOTS, SLOTS), :], yb[:, t % 2, :]).then_inc(st[t % 2], 16)

            for t in range(2, T):
                load_expert(sp, Wb, t, weights[t - 2], in_[t])
            for t in range(T):
                if t < len(following):
                    sp.wait_ge(S["up_done"], t + 1)
                    load_expert(sp, Wb, t, following[t], in_[t], (0, 1))
                    sp.wait_ge(S["down_done"], 2 * (t + 1))
                    load_expert(sp, Wb, t, following[t], in_[t], (2,))
                store(t)
            for t in range(len(following)):
                sp.wait_ge(in_[t], 48)
            for s in range(2):
                sp.wait_ge(st[s], 16 * (T // 2))

        @block.gpsimd
        def _(pool):
            if gathers:
                pool.tensor_copy(cols[:, 0:len(gathers)], idx[:, bass.ds(e + 2, len(gathers))]).then_inc(S["cols_set"], 1)
                pool.wait_ge(S["cols_set"], 1)
                for t in gathers:
                    s = t % 2
                    pool.wait_ge(S["turned"], t - 1)
                    if t >= 4:
                        pool.wait_ge(got[s], 16 * (t // 2 - 1))
                    gather_rows(pool, Hg[:, s, :], cols[:, t - 2:t - 1], h_rows, got[s])
                for s in range(2):
                    pool.wait_ge(got[s], 16 * (len(gathers) // 2))
                forget(pool, got)
            else:
                pool.wait_ge(S["turned"], T)

        @block.tensor
        def _(pe):
            def turn(t):
                s = t % 2
                if t >= 2:
                    pe.wait_ge(got[s], 16 * (t // 2))
                for k in range(KD):
                    tr = pe.transpose(K.bank[banks_t[s][k // 4]][:, (k % 4) * P:(k % 4 + 1) * P],
                                      Hg[:, s, k * P:(k + 1) * P], K.ident)
                tr.then_inc(S["turned"], 1)

            def up(t):
                s = t % 2
                pe.wait_ge(S["xt_a"], t + 1)
                pe.wait_ge(S["xt_b"], t + 1)
                if t >= 2:
                    pe.wait_ge(in_[t], 48)
                for m in range(2):
                    for which in range(2):
                        q = 2 * which + m
                        for k in range(KD):
                            mm = pe.matmul(K.bank[4 + s][:, q * P:(q + 1) * P],
                                           Wb[:, t, which, k * DE + m * P:k * DE + (m + 1) * P],
                                           XT[:, s, k, :], start=(k == 0), stop=(k == KD - 1))
                mm.then_inc(S["up_done"], 1)

            def down(t):
                s = t % 2
                pe.wait_ge(S["act_done"], t + 1)
                if t:
                    pe.wait_ge(S["y_a"], t)
                    pe.wait_ge(S["y_b"], t)
                for n in range(2):
                    for m in range(2):
                        mm = pe.matmul(K.bank[6 + n][:, :], aT[:, s, m, :],
                                       Wb[:, t, 2, m * D + n * 512:m * D + (n + 1) * 512],
                                       start=(m == 0), stop=(m == 1))
                    mm.then_inc(S["down_done"], 1)

            turn(0)
            turn(1)
            up(0)
            for t in range(1, T):
                up(t)
                down(t - 1)
                if t + 1 < T:
                    turn(t + 1)
            down(T - 1)

        def steps(copy_in, activate, copy_out):
            copy_in(0)
            copy_in(1)
            activate(0)
            for t in range(1, T):
                activate(t)
                copy_out(t - 1)
                if t + 1 < T:
                    copy_in(t + 1)
            copy_out(T - 1)

        @block.scalar
        def _(act):
            def copy_in(t):
                s = t % 2
                act.wait_ge(S["turned"], t + 1)
                if t >= 2:
                    act.wait_ge(S["up_done"], t - 1)
                act.activation(XT[:, s, 0:4, :], K.bank[banks_t[s][0]].rearrange("p (k t) -> p k t", k=4), ACT.Copy)\
                    .then_inc(S["xt_a"], 1)

            def activate(t):
                s = t % 2
                act.wait_ge(S["up_done"], t + 1)
                if t >= 2:
                    act.wait_ge(S["act_done"], t - 1)
                act.activation(sg[:, s, :, :], K.bank[4 + s][:, 0:2 * P].rearrange("p (m t) -> p m t", m=2), ACT.Silu)\
                    .then_inc(S["silu_done"], 1)

            def copy_out(t):
                act.wait_ge(S["down_done"], 2 * t + 1)
                if t >= 2:
                    act.wait_ge(st[t % 2], 16 * (t // 2))
                act.activation(yb[:, t % 2, 0:512], K.bank[6], ACT.Copy).then_inc(S["y_a"], 1)

            steps(copy_in, activate, copy_out)

        @block.vector
        def _(dve):
            def copy_in(t):
                s = t % 2
                dve.wait_ge(S["turned"], t + 1)
                if t >= 2:
                    dve.wait_ge(S["up_done"], t - 1)
                dve.tensor_copy(XT[:, s, 4:8, :], K.bank[banks_t[s][1]].rearrange("p (k t) -> p k t", k=4))\
                    .then_inc(S["xt_b"], 1)

            def activate(t):
                s = t % 2
                dve.wait_ge(S["silu_done"], t + 1)
                if t >= 2:
                    dve.wait_ge(S["down_done"], 2 * (t - 1))
                dve.tensor_tensor(aT[:, s, :, :], sg[:, s, :, :],
                                  K.bank[4 + s][:, 2 * P:4 * P].rearrange("p (m t) -> p m t", m=2), ALU.mult)\
                    .then_inc(S["act_done"], 1)

            def copy_out(t):
                dve.wait_ge(S["down_done"], 2 * t + 2)
                if t >= 2:
                    dve.wait_ge(st[t % 2], 16 * (t // 2))
                dve.tensor_copy(yb[:, t % 2, 512:D], K.bank[7]).then_inc(S["y_b"], 1)

            steps(copy_in, activate, copy_out)


def combine(K, acc, ys, slot_of, w_of):
    nc = K.nc
    RINGN = 4
    units = [(j, k) for k in range(TOP_K) for j in range(JX)]
    with ExitStack() as c, phase(nc, "g0 g1 g2 g3 added") as (block, S):
        rows = c.enter_context(sbuf(nc, "cb_rows", [P, RINGN, D], F32))
        g = (S["g0"], S["g1"], S["g2"], S["g3"])

        @block.gpsimd
        def _(pool):
            for u, (j, k) in enumerate(units):
                if u >= RINGN:
                    pool.wait_ge(S["added"], u - RINGN + 1)
                pool.indirect_dma_start(out=rows[:, u % RINGN, :], out_offset=None, in_=ys,
                                        in_offset=bass.IndirectOffsetOnAxis(ap=slot_of[:, k, j:j + 1], axis=0),
                                        bounds_check=TILES * SLOTS - 1, oob_is_err=False).then_inc(g[u % RINGN], 16)
            for n in range(RINGN):
                pool.wait_ge(g[n], 16 * (len(units) // RINGN))
            forget(pool, g)

        @block.vector
        def _(dve):
            for u, (j, k) in enumerate(units):
                dve.wait_ge(g[u % RINGN], 16 * (u // RINGN + 1))
                if k:
                    dve.wait_ge(S["added"], u - JX + 1)
                dve.scalar_tensor_tensor(out=acc[:, j, :], in0=rows[:, u % RINGN, :], scalar=w_of[:, k, j:j + 1],
                                         in1=acc[:, j, :], op0=ALU.mult, op1=ALU.add).then_inc(S["added"], 1)


def mixture(K, I, scratch):
    nc = K.nc
    h_rows, slot_tokens, ys = scratch["h_rows"], scratch["slot_tokens"], scratch["ys"]
    U32 = mybir.dt.uint32
    src = lambda e: tuple(a[0][bass.ds(e, 1)].rearrange("o k n -> (o k) n")
                          for a in (I["exp_w_gate"], I["exp_w_up"], I["exp_w_down"]))
    shared = (I["sh_w_gate"][0], I["sh_w_up"][0], I["sh_w_down"][0])
    with ExitStack() as c:
        sb = lambda name, shape, dt=F32, s=c: s.enter_context(sbuf(nc, name, shape, dt))
        wt, kept = (sb("expert_" + n, [P, JX, NE]) for n in ("weights", "kept"))
        slot_of, w_of = sb("slot_of", [P, TOP_K, JX], U32), sb("w_of", [P, TOP_K, JX])
        extra, idx = sb("extra", [P, 1 + FURTHER + AHEAD], mybir.dt.int32), sb("slot_idx", [P, TILES + AHEAD], U32)
        router(K, I, wt, kept)
        dispatch(K, wt, kept, slot_of, w_of, extra, h_rows, slot_tokens, ys, idx)
        Wb = sb("ex_w", [P, AT_ONCE, 3, KD * DE])
        with ExitStack() as c2:
            Hg, yb = sb("slot_rows", [P, 2, D], F32, c2), sb("slot_out", [P, 2, D], F32, c2)
            XT = sb("slot_x", [P, 2, KD, P], F32, c2)
            aT, sg = sb("slot_act", [P, 2, 2, P], F32, c2), sb("slot_silu", [P, 2, 2, P], F32, c2)
            cols = sb("slot_cols", [P, AT_ONCE], U32, c2)
            step = lambda e, weights, following, more: slot_experts(
                K, Wb, Hg, cols, XT, aT, sg, yb, idx, h_rows, ys, e, weights, following, more)
            owner = lambda u: src(nc.values_load(extra[0:1, bass.ds(u + 1, 1)], engines=(mybir.EngineType.SP,),
                                                 min_val=0, max_val=NE - 1))
            in_use = nc.values_load(extra[0:1, 0:1], min_val=0, max_val=FURTHER)
            slots_start(K, Wb, Hg, h_rows, idx, cols, 0, (src(0), src(1)))
            with nc.Fori(0, NE // AT_ONCE - 1) as n:
                e = n * AT_ONCE
                step(e, [src(e + t) for t in range(2, AT_ONCE)], [src(e + AT_ONCE), src(e + AT_ONCE + 1)], True)
            step(NE - AT_ONCE, [src(n) for n in range(NE - AT_ONCE + 2, NE)], [owner(0), owner(1)], True)
            with nc.Fori(0, FURTHER, 2) as u:
                with nc.If(in_use > u):
                    step(u + NE, (), [owner(u + 2), owner(u + 3)], True)
            experts_start(K, I, Wb, shared)
        acc = sb("ex_acc", [P, JX, D])
        with phase(nc, "zeroed") as (block, S):
            @block.vector
            def _(dve):
                dve.memset(acc[:, :, :], 0.0).then_inc(S["zeroed"], 1)
        experts(K, Wb, acc, ((lambda j: K.one[:, :]),), (None,))
        combine(K, acc, ys, slot_of, w_of)
        add_experts(K, acc, K.gate[:, 1, :])

(R_, V_, KK_, K_, GATE_, BONUS_, KD_, B_, LW_) = (0, 1, 2, 3, 4, 5, 6, 8, 10)
N_RW = 12
DECAY = float(2.718281828459045 ** -0.5)


def rwkv_projections(K, I, rw, tw, ta):
    nc = K.nc
    names = ("edges xx_sum xx_done lerped w_in0 w_in1 w1_in mm_done lora_done evac lora_out "
             "st0 st1 st2 st3")
    dest = (R_, K_, V_, GATE_)
    with ExitStack() as c, phase(nc, names) as (block, S):
        xx = c.enter_context(sbuf(nc, "rp_xx", [P, KD, TT], F32))
        lerp = c.enter_context(sbuf(nc, "rp_lerp", [P, 2, KD, TT], F32))
        wb = c.enter_context(sbuf(nc, "rp_w", [P, 2, KD, 512], F32))
        w1 = c.enter_context(sbuf(nc, "rp_w1", [P, 2, KD, 2 * LORA], F32))
        stage = c.enter_context(sbuf(nc, "rp_stage", [P, 4, 512], F32))
        w_in = (S["w_in0"], S["w_in1"])
        st = (S["st0"], S["st1"], S["st2"], S["st3"])
        units = [(n, half, j) for n in range(4) for half in range(2) for j in range(NT)]

        @block.sync
        def _(sp):
            for a, w in enumerate((I["rwkv_w1_2"], I["rwkv_a1_2"])):
                for d in range(2):
                    sp.dma_start(w1[:, a, :, d * LORA:(d + 1) * LORA], w[0, d].rearrange("(k p) r -> p k r", p=P))\
                        .then_inc(S["w1_in"], 16)
            for u in range(8):
                if u >= 2:
                    sp.wait_ge(S["mm_done"], NT * (u - 1))
                n, half = divmod(u, 2)
                w = I["rwkv_w_in_2"][0, n].rearrange("(k p) n -> p k n", p=P)
                sp.dma_start(wb[:, u % 2, :, :], w[:, :, half * 512:(half + 1) * 512]).then_inc(w_in[u % 2], 16)

        @block.vector
        def _(dve):
            h = K.hT
            for t0, t1 in ((0, TC), (TC, TT)):
                dve.tensor_tensor(xx[:, :, t0 + 1:t1 - 1], h[:, :, t0:t1 - 2], h[:, :, t0 + 2:t1], ALU.add)
                dve.tensor_copy(xx[:, :, t0:t0 + 1], h[:, :, t0 + 1:t0 + 2])
                dve.tensor_copy(xx[:, :, t1 - 1:t1], h[:, :, t1 - 2:t1 - 1]).then_inc(S["xx_sum"], 1)
            dve.wait_ge(S["xx_sum"], 2)
            dve.scalar_tensor_tensor(out=xx[:, :, :], in0=xx[:, :, :], scalar=0.5, in1=h[:, :, :],
                                     op0=ALU.mult, op1=ALU.subtract).then_inc(S["xx_done"], 1)
            dve.wait_ge(S["xx_done"], 1)
            for n in range(6):
                if n in (2, 3, 4):
                    dve.wait_ge(S["mm_done"], 2 * NT * (n - 1))
                if n == 5:
                    dve.wait_ge(S["mm_done"], 2 * NT * 4)
                for k in range(KD):
                    ins = dve.scalar_tensor_tensor(out=lerp[:, n % 2, k, :], in0=xx[:, k, :],
                                                   scalar=K.colC[:, n * KD + k:n * KD + k + 1], in1=h[:, k, :],
                                                   op0=ALU.mult, op1=ALU.add)
                ins.then_inc(S["lerped"], 1)

        @block.tensor
        def _(pe):
            for u, (n, half, j) in enumerate(units):
                if j == 0:
                    pe.wait_ge(S["lerped"], n + 1)
                    pe.wait_ge(w_in[half], 16 * (n + 1))
                if u >= 4:
                    pe.wait_ge(S["evac"], u - 3)
                for k in range(KD):
                    mm = pe.matmul(K.bank[u % 4][:, :], lerp[:, n % 2, k, j * P:(j + 1) * P], wb[:, half, k, :],
                                   start=(k == 0), stop=(k == KD - 1))
                mm.then_inc(S["mm_done"], 1)
            pe.wait_ge(S["w1_in"], 64)
            for a in range(2):
                pe.wait_ge(S["lerped"], 5 + a)
                for b, (t0, t1) in enumerate(((0, TC), (TC, TT))):
                    for k in range(KD):
                        mm = pe.matmul(K.bank[4 + 2 * a + b][:, 0:t1 - t0], w1[:, a, k, :], lerp[:, a, k, t0:t1],
                                       start=(k == 0), stop=(k == KD - 1))
                    mm.then_inc(S["lora_done"], 1)

        @block.scalar
        def _(act):
            def store(u):
                n, half, j = units[u]
                act.wait_ge(S["evac"], u + 1)
                act.dma_start(rw[dest[n], j * P:(j + 1) * P, half * 512:(half + 1) * 512], stage[:, u % 4, :])\
                    .then_inc(st[u % 4], 16)

            for u, (n, half, j) in enumerate(units):
                act.wait_ge(S["mm_done"], u + 1)
                if u >= 4:
                    act.wait_ge(st[u % 4], 16 * (u // 4))
                act.activation(stage[:, u % 4, :], K.bank[u % 4][:, :], ACT.Silu if n == 3 else ACT.Copy)\
                    .then_inc(S["evac"], 1)
                if u:
                    store(u - 1)
            store(len(units) - 1)
            for a in range(2):
                for b, (t0, t1) in enumerate(((0, TC), (TC, TT))):
                    act.wait_ge(S["lora_done"], 2 * a + b + 1)
                    act.activation((tw, ta)[a][:, t0:t1], K.bank[4 + 2 * a + b][:, 0:t1 - t0],
                                   (ACT.Tanh, ACT.Copy)[a]).then_inc(S["lora_out"], 1)
            for q in range(4):
                act.wait_ge(st[q], 16 * (len(units) // 4))


def rwkv_prepare(K, I, rw, tw, ta):
    nc = K.nc
    with ExitStack() as c0:
        sb = lambda name, shape, c: c.enter_context(sbuf(nc, "rq_" + name, shape, F32))
        w0, a0, w2 = sb("w0", [P, 2, D], c0), sb("a0", [P, 2, D], c0), sb("w2", [P, 2, D], c0)
        kk_p, ka_p, rk_p = sb("k_k", [P, D], c0), sb("k_a", [P, D], c0), sb("r_k", [P, D], c0)
        with phase(nc, "in_done") as (block, S):
            @block.sync
            def _(sp):
                for d in range(2):
                    sp.dma_start(w0[:, d, :], I["rwkv_w0_2"][0, d].partition_broadcast(P)).then_inc(S["in_done"], 16)
                    sp.dma_start(a0[:, d, :], I["rwkv_a0_2"][0, d].partition_broadcast(P)).then_inc(S["in_done"], 16)
                sp.dma_start(w2[:, 0, :], I["rwkv_w2_2"][0].rearrange("d r n -> (d r) n")).then_inc(S["in_done"], 16)
                sp.dma_start(w2[:, 1, :], I["rwkv_a2_2"][0].rearrange("d r n -> (d r) n")).then_inc(S["in_done"], 16)
                sp.dma_start(kk_p[:, :], I["rwkv_k_k_2"][0].partition_broadcast(P)).then_inc(S["in_done"], 16)
                sp.dma_start(ka_p[:, :], I["rwkv_k_a_2"][0].partition_broadcast(P)).then_inc(S["in_done"], 16)
                sp.dma_start(rk_p[:, :], I["rwkv_r_k_2"][0].rearrange("h n -> (h n)").partition_broadcast(P))\
                    .then_inc(S["in_done"], 16)
                sp.wait_ge(S["in_done"], 16 * 9)
        two = (0, 1)
        kin, rin, vin, kk, bon = ([sb(n, [P, D], c0) for _ in two] for n in ("k", "r", "v", "kk", "bonus"))
        sq = bon
        lw, aa, kd, bb = ([sb(n, [P, 2, D], c0) for _ in two] for n in ("lw", "a", "kd", "b"))
        st, low = ([sb(n, shape, c0) for _ in two] for n, shape in (("stats", [P, 4, H2]), ("low", [P, 2, P])))
        heads = lambda t: t.rearrange("p (h n) -> p h n", n=HD)
        wide = lambda ap: ap.unsqueeze(2).broadcast_to([P, H2, HD])
        names = " ".join(f"{n}{s}" for n in ("in_k", "in_rv", "lowered", "mm", "v", "a", "p", "stored") for s in two)
        with nc.Fori(0, NT // 2) as pair:
            with phase(nc, names) as (block, S):
                rows = [bass.ds((pair * 2 + s) * P, P) for s in two]
                in_k, in_rv, lowered, mm, vs, as_, ps, stored = (
                    [S[f"{n}{s}"] for s in two] for n in ("in_k", "in_rv", "lowered", "mm", "v", "a", "p", "stored"))

                @block.sync
                def _(sp):
                    for s in two:
                        sp.dma_start(kin[s][:, :], rw[K_, rows[s], :]).then_inc(in_k[s], 16)
                    for s in two:
                        sp.dma_start(rin[s][:, :], rw[R_, rows[s], :]).then_inc(in_rv[s], 16)
                        sp.dma_start(vin[s][:, :], rw[V_, rows[s], :]).then_inc(in_rv[s], 16)
                    for s in two:
                        sp.wait_ge(vs[s], 13)
                        sp.dma_start(rw[KK_, rows[s], :], kk[s][:, :]).then_inc(stored[s], 16)
                        for d in range(2):
                            sp.dma_start(rw[LW_ + d, rows[s], :], lw[s][:, d, :]).then_inc(stored[s], 16)
                            sp.dma_start(rw[KD_ + d, rows[s], :], kd[s][:, d, :]).then_inc(stored[s], 16)
                        sp.wait_ge(ps[s], 5)
                        for d in range(2):
                            sp.dma_start(rw[B_ + d, rows[s], :], bb[s][:, d, :]).then_inc(stored[s], 16)
                    for s in two:
                        sp.wait_ge(ps[s], 6)
                        sp.dma_start(rw[BONUS_, rows[s], :], bon[s][:, :]).then_inc(stored[s], 16)
                    for s in two:
                        sp.wait_ge(stored[s], 16 * 8)

                @block.tensor
                def _(pe):
                    for s in two:
                        pe.wait_ge(lowered[s], 2)
                        for a in range(2):
                            if s:
                                pe.wait_ge(vs[0], (4, 5)[a])
                            for d in range(2):
                                for half in range(2):
                                    m = pe.matmul(K.bank[4 * a + 2 * d + half][:, :], low[s][d * LORA:(d + 1) * LORA, a, :],
                                                  w2[d * LORA:(d + 1) * LORA, a, half * 512:(half + 1) * 512],
                                                  start=True, stop=True)
                            m.then_inc(mm[s], 1)

                @block.scalar
                def _(act):
                    for s in two:
                        act.activation(low[s][:, 0, :], tw[:, rows[s]], ACT.Copy).then_inc(lowered[s], 1)
                        act.activation(low[s][:, 1, :], ta[:, rows[s]], ACT.Copy).then_inc(lowered[s], 1)
                    for s in two:
                        act.wait_ge(vs[s], 1)
                        act.activation(sq[s][:, :], kk[s][:, :], ACT.Square).then_inc(as_[s], 1)
                    for s in two:
                        act.wait_ge(vs[s], 2)
                        act.activation(st[s][:, 1, :], st[s][:, 0, :], ACT.Sqrt).then_inc(as_[s], 1)
                    for s in two:
                        act.wait_ge(vs[s], 4)
                        act.activation(lw[s][:, :, :], lw[s][:, :, :], ACT.Sigmoid).then_inc(as_[s], 1)
                        act.wait_ge(vs[s], 5)
                        act.activation(aa[s][:, :, :], aa[s][:, :, :], ACT.Sigmoid).then_inc(as_[s], 1)

                @block.gpsimd
                def _(pool):
                    steps = [Chain(pool, ps[s]) for s in two]
                    for s in two:
                        step = steps[s]
                        pool.wait_ge(vs[s], 11)
                        pool.wait_ge(in_rv[s], 32)
                        step(pool.tensor_tensor(bon[s][:, :], kd[s][:, 0, :], kd[s][:, 1, :], ALU.add))
                        step(pool.tensor_tensor(bon[s][:, :], bon[s][:, :], rin[s][:, :], ALU.mult))
                        step.put(pool.tensor_tensor(bon[s][:, :], bon[s][:, :], rk_p[:, :], ALU.mult))
                        pool.wait_ge(as_[s], 4)
                        pool.wait_ge(vs[s], 12)
                        for d in range(2):
                            step.put(pool.tensor_tensor(bb[s][:, d, :], kk[s][:, :], aa[s][:, d, :], ALU.mult))
                    for s in two:
                        pool.wait_ge(vs[s], 14)
                        steps[s].put(pool.tensor_tensor(heads(bon[s][:, :]), heads(vin[s][:, :]),
                                                        wide(st[s][:, 3, :]), ALU.mult))

                @block.vector
                def _(dve):
                    steps = [Chain(dve, vs[s]) for s in two]
                    for s in two:
                        dve.wait_ge(in_k[s], 16)
                        steps[s].put(dve.tensor_tensor(kk[s][:, :], kin[s][:, :], kk_p[:, :], ALU.mult))
                    for s in two:
                        dve.wait_ge(as_[s], 1)
                        steps[s].put(dve.tensor_reduce(st[s][:, 0, :], heads(sq[s][:, :]), AX.X, ALU.add))
                    for s in two:
                        step = steps[s]
                        step.put(dve.memset(st[s][:, 3, :], 0.0))
                        for a, (dst, base) in enumerate(((lw[s], w0), (aa[s], a0))):
                            dve.wait_ge(mm[s], a + 1)
                            for d in range(2):
                                for half in range(2):
                                    part = slice(half * 512, (half + 1) * 512)
                                    ins = dve.tensor_tensor(dst[:, d, part], K.bank[4 * a + 2 * d + half][:, :],
                                                            base[:, d, part], ALU.add)
                            step.put(ins)
                    for s in two:
                        step = steps[s]
                        dve.wait_ge(as_[s], 2)
                        step(dve.tensor_scalar(st[s][:, 1, :], st[s][:, 1, :], 1e-12, None, ALU.max))
                        step(dve.reciprocal(st[s][:, 2, :], st[s][:, 1, :]))
                        dve.wait_ge(as_[s], 4)
                        for d in range(2):
                            step.put(dve.scalar_tensor_tensor(out=kd[s][:, d, :], in0=aa[s][:, d, :], scalar=1.0,
                                                              in1=ka_p[:, :], op0=ALU.subtract, op1=ALU.mult))
                        step.wait()
                        for d in range(2):
                            step.put(dve.scalar_tensor_tensor(out=kd[s][:, d, :], in0=kd[s][:, d, :], scalar=1.0,
                                                              in1=kin[s][:, :], op0=ALU.add, op1=ALU.mult))
                        step.put(dve.tensor_tensor(heads(kk[s][:, :]), heads(kk[s][:, :]), wide(st[s][:, 2, :]),
                                                   ALU.mult))
                        step.put(dve.tensor_scalar(lw[s][:, :, :], lw[s][:, :, :], -DECAY, None, ALU.mult))
                    for s in two:
                        dve.wait_ge(ps[s], 3)
                        steps[s].put(dve.tensor_reduce(st[s][:, 3, :], heads(bon[s][:, :]), AX.X, ALU.add))


UNITS = 4
UNIT_DIR = (0, 1, 0, 1)


def rwkv_step(K, rw, Y, St, FA, pair, tile_of):
    nc = K.nc
    names = " ".join(f"{n}{u}" for n in ("lw", "in", "mm", "v", "a", "p", "st") for u in range(UNITS))
    W = 4 * HD
    units = range(UNITS)
    with ExitStack() as c, phase(nc, names) as (block, S):
        def buf(name, shape):
            return [c.enter_context(sbuf(nc, f"rs_{name}", shape, F32)) for _ in units]

        IN = buf("in", [P, 6, W])
        E = buf("exps", [P, 3, W])
        TM = buf("tokens", [P, 4, W])
        FM = buf("features", [P, 2, 2, P])
        SC = buf("scores", [P, 4, 4, P])
        em = buf("em", [P, 2, 2])
        S0 = buf("s0", [P, 2, P])
        RH, yb, SA = ([E[u][:, n, :] for u in units] for n in range(3))
        inv = [Inverse.buffers(K, c, u) for u in units]
        bank = [K.bank[2 * u:2 * u + 2] for u in units]
        inv_bank = [(b[0], b[1], b[0]) for b in bank]
        lws, ins_, mm, vs, as_, ps, sts = ([S[f"{n}{u}"] for u in units]
                                           for n in ("lw", "in", "mm", "v", "a", "p", "st"))
        M0 = 5 + Inverse.MM_COUNT
        V0 = 7 + Inverse.STEP_COUNT
        pairs = lambda t: t.rearrange("p (q n) -> p q n", q=2)
        rows = [bass.ds(tile_of[d] * P, P) for d in UNIT_DIR]
        cols = [bass.ds((pair * 2 + u // 2) * W, W) for u in units]

        @block.sync
        def _(sp):
            for u in units:
                sp.dma_start(IN[u][:, 5, :], rw[LW_ + UNIT_DIR[u], rows[u], cols[u]]).then_inc(lws[u], 16)
            for u in units:
                d = UNIT_DIR[u]
                sp.dma_start(IN[u][:, 3:5, :], rw[KD_ + d:KD_ + d + 3:2, rows[u], cols[u]].rearrange("a p c -> p a c"))\
                    .then_inc(ins_[u], 16)
            for u in units:
                sp.wait_ge(as_[u], 13)
                sp.dma_start(Y[UNIT_DIR[u], rows[u], cols[u]], yb[u]).then_inc(sts[u], 16)
            for u in units:
                sp.wait_ge(sts[u], 16)

        @block.scalar
        def _(act):
            for u in units:
                act.dma_start(IN[u][:, 0:3, :], rw[R_:KK_ + 1, rows[u], cols[u]].rearrange("a p c -> p a c"))\
                    .then_inc(ins_[u], 16)
            for u in units:
                act.wait_ge(mm[u], 1)
                act.activation(E[u][:, 0, :], bank[u][0][:, 0:W], ACT.Exp).then_inc(as_[u], 1)
                act.activation(E[u][:, 1, :], bank[u][0][:, 0:W], ACT.Exp, scale=-1.0).then_inc(as_[u], 1)
                act.activation(em[u][:, :, :], bank[u][0][:, W:W + 4].rearrange("p (q n) -> p q n", q=2), ACT.Exp)\
                    .then_inc(as_[u], 1)
                act.wait_ge(vs[u], 1)
                act.activation(E[u][:, 2, :], E[u][:, 2, :], ACT.Exp).then_inc(as_[u], 1)
            for u in units:
                act.wait_ge(mm[u], 2)
                for p in range(2):
                    four = bank[u][p][:, :].rearrange("p (a t) -> p a t", a=4)
                    act.activation(FM[u][:, p, :, :], four[:, 0:2, :], ACT.Copy).then_inc(as_[u], 1)
                    for q in range(2):
                        own = slice(q * HD, (q + 1) * HD)
                        act.activation(FA[u][own, p, q, :, :], four[own, 2:4, :], ACT.Copy)\
                            .then_inc(as_[u], 1)
            for u in units:
                act.wait_ge(mm[u], 5)
                act.activation(RH[u], bank[u][1][:, 0:W], ACT.Copy).then_inc(as_[u], 1)
            for u in units:
                act.wait_ge(mm[u], M0 + 1)
                act.activation(SA[u], bank[u][0][:, 0:W], ACT.Copy, scale=-1.0).then_inc(as_[u], 1)
            for u in units:
                act.wait_ge(mm[u], M0 + 3)
                act.activation(yb[u], bank[u][0][:, W:2 * W], ACT.Copy).then_inc(as_[u], 1)

        @block.gpsimd
        def _(pool):
            for u in units:
                pool.wait_ge(ins_[u], 32)
                pool.wait_ge(as_[u], 2)
                for dst, src, e in ((0, 4, 1), (1, 3, 1), (3, 0, 0)):
                    pool.tensor_tensor(TM[u][:, dst, :], IN[u][:, src, :], E[u][:, e, :], ALU.mult).then_inc(ps[u], 1)

        @block.tensor
        def _(pe):
            def scores(u, p):
                for q in range(2):
                    for a in range(2):
                        m = pe.matmul(bank[u][q][:, a * 2 * P:(a + 1) * 2 * P], FM[u][:, p, a, :], FA[u][:, p, q, :, :],
                                      start=True, stop=True)
                m.then_inc(mm[u], 1)

            for u in units:
                pe.wait_ge(lws[u], 16)
                lw = IN[u][:, 5, :]
                d = UNIT_DIR[u]
                pe.matmul(bank[u][0][:, 0:W], K.cum[d], lw, start=True, stop=True)
                for p in range(2):
                    m = pe.matmul(bank[u][0][:, W + 2 * p:W + 2 * p + 2], lw[:, p * P:(p + 1) * P],
                                  K.const[:, MIX_COL + 2 * d:MIX_COL + 2 * d + 2], start=True, stop=True)
                m.then_inc(mm[u], 1)
            for u in units:
                pe.wait_ge(ps[u], 3)
                pe.wait_ge(vs[u], 3)
                for p in range(2):
                    for a in range(4):
                        t = pe.transpose(bank[u][p][:, a * P:(a + 1) * P], TM[u][:, a, p * P:(p + 1) * P], K.ident)
                t.then_inc(mm[u], 1)
            for u in units:
                pe.wait_ge(as_[u], 10)
                scores(u, 0)
            for u in units:
                pe.wait_ge(vs[u], 5)
                scores(u, 1)
            for u in units:
                V = IN[u][:, 1, :]
                pe.wait_ge(ins_[u], 32)
                pe.wait_ge(vs[u], 7)
                for h in range(4):
                    p, q = divmod(h, 2)
                    hc = slice(h * HD, (h + 1) * HD)
                    pe.matmul(bank[u][1][:, hc], FA[u][:, p, q, 0, :], S0[u][:, p, q * HD:(q + 1) * HD],
                              start=True, stop=False)
                    m = pe.matmul(bank[u][1][:, hc], SC[u][:, h, 2, :], V[:, hc], start=False, stop=True)
                m.then_inc(mm[u], 1)
            for u in units:
                pe.wait_ge(as_[u], 11)
            tensor_inverses(pe, K, [lambda h, u=u: SC[u][:, h, 0, :] for u in units], inv, inv_bank, vs, 7, mm)
            for u in units:
                Z = inv[u][1]
                pe.wait_ge(vs[u], V0)
                for h in range(4):
                    m = pe.matmul(bank[u][0][:, h * HD:(h + 1) * HD], Z[:, h, :], RH[u][:, h * HD:(h + 1) * HD],
                                  start=True, stop=True)
                m.then_inc(mm[u], 1)
            for u in units:
                V = IN[u][:, 1, :]
                pe.wait_ge(as_[u], 12)
                for p in range(2):
                    pc = slice(p * P, (p + 1) * P)
                    pe.matmul(bank[u][1][:, pc], TM[u][:, 1, pc], V[:, pc], start=True, stop=False)
                    m = pe.matmul(bank[u][1][:, pc], TM[u][:, 0, pc], SA[u][:, pc], start=False, stop=True)
                m.then_inc(mm[u], 1)
                for h in range(4):
                    p, q = divmod(h, 2)
                    hc, out = slice(h * HD, (h + 1) * HD), bank[u][0][:, W + h * HD:W + (h + 1) * HD]
                    pe.matmul(out, FA[u][:, p, q, 1, :], S0[u][:, p, q * HD:(q + 1) * HD], start=True, stop=False)
                    pe.matmul(out, SC[u][:, h, 3, :], V[:, hc], start=False, stop=False)
                    m = pe.matmul(out, SC[u][:, h, 1, :], SA[u][:, hc], start=False, stop=True)
                m.then_inc(mm[u], 1)

        @block.vector
        def _(dve):
            steps = [Chain(dve, vs[u]) for u in units]

            def masks(u, p):
                for q in range(2):
                    steps[u].put(dve.tensor_tensor(
                        SC[u][:, 2 * p + q, :, :].rearrange("p (a b) t -> p a b t", a=2),
                        bank[u][q][:, :].rearrange("p (a b t) -> p a b t", a=2, b=2),
                        K.mask2[UNIT_DIR[u]].unsqueeze(1).broadcast_to([P, 2, 2, P]), ALU.mult))

            for u in units:
                step = steps[u]
                dve.wait_ge(lws[u], 16)
                dve.wait_ge(as_[u], 3)
                step.put(dve.tensor_tensor(E[u][:, 2, :], bank[u][0][:, 0:W], IN[u][:, 5, :], ALU.subtract))
                for p in range(2):
                    ins = dve.tensor_scalar(S0[u][:, p, :], St[u][:, p, :], em[u][:, p, 0:1], None, ALU.mult)
                step.put(ins)
                dve.wait_ge(as_[u], 4)
                dve.wait_ge(ins_[u], 32)
                step.put(dve.tensor_tensor(TM[u][:, 2, :], IN[u][:, 2, :], E[u][:, 2, :], ALU.mult))
            for p in range(2):
                for u in units:
                    dve.wait_ge(mm[u], 3 + p)
                    masks(u, p)
            for u in units:
                steps[u].wait()
            vector_inverses(dve, K, [SC[u][:, :, 0, :] for u in units], inv, inv_bank, steps, mm, 5)
            for u in units:
                step = steps[u]
                dve.wait_ge(mm[u], M0 + 2)
                step(dve.tensor_tensor(pairs(RH[u]), pairs(bank[u][1][:, 0:W]), S0[u][:, :, :], ALU.add))
                for p in range(2):
                    ins = dve.tensor_scalar(St[u][:, p, :], RH[u][:, p * P:(p + 1) * P], em[u][:, p, 1:2], None, ALU.mult)
                step.put(ins)


def rwkv_readout(K, I, rw, Y, oT):
    nc = K.nc
    with ExitStack() as c0:
        sb = lambda name, shape: c0.enter_context(sbuf(nc, "ro_" + name, shape, F32))
        g, b = sb("g", [P, D]), sb("b", [P, D])
        with phase(nc, "in_done") as (block, S):
            @block.sync
            def _(sp):
                sp.dma_start(g[:, :], I["rwkv_lnx_g_2"][0].partition_broadcast(P)).then_inc(S["in_done"], 16)
                sp.dma_start(b[:, :], I["rwkv_lnx_b_2"][0].partition_broadcast(P)).then_inc(S["in_done"], 16)
                sp.wait_ge(S["in_done"], 32)
        two = (0, 1)
        y, y2, bon, gate = ([sb(n, [P, D]) for _ in two] for n in ("y", "y2", "bonus", "gate"))
        sq = y2
        st = [sb("stats", [P, 4, H2]) for _ in two]
        heads = lambda t: t[:, :].rearrange("p (h n) -> p h n", n=HD)
        wide = lambda ap: ap.unsqueeze(2).broadcast_to([P, H2, HD])
        names = " ".join(f"{n}{s}" for n in ("in_y", "in_bonus", "in_gate", "v", "shifted", "sq_done", "rms_done",
                                             "turned", "out_a", "out_b") for s in two)
        with nc.Fori(0, NT // 2) as pair:
            with phase(nc, names) as (block, S):
                rows = [bass.ds((pair * 2 + s) * P, P) for s in two]

                @block.sync
                def _(sp):
                    for s in two:
                        sp.dma_start(y[s][:, :], Y[0, rows[s], :]).then_inc(S[f"in_y{s}"], 16)
                        sp.dma_start(y2[s][:, :], Y[1, rows[s], :]).then_inc(S[f"in_y{s}"], 16)
                    for s in two:
                        sp.dma_start(bon[s][:, :], rw[BONUS_, rows[s], :]).then_inc(S[f"in_bonus{s}"], 16)
                        sp.dma_start(gate[s][:, :], rw[GATE_, rows[s], :]).then_inc(S[f"in_gate{s}"], 16)
                    for s in two:
                        sp.wait_ge(S[f"in_gate{s}"], 16)

                @block.gpsimd
                def _(pool):
                    for s in two:
                        pool.wait_ge(S[f"in_bonus{s}"], 16)
                        pool.tensor_tensor(bon[s][:, :], bon[s][:, :], b[:, :], ALU.add).then_inc(S[f"shifted{s}"], 1)

                @block.vector
                def _(dve):
                    steps = [Chain(dve, S[f"v{s}"]) for s in two]
                    for s in two:
                        step = steps[s]
                        dve.wait_ge(S[f"in_y{s}"], 32)
                        step(dve.tensor_tensor(y[s][:, :], y[s][:, :], y2[s][:, :], ALU.add))
                        step(dve.tensor_reduce(st[s][:, 0, :], heads(y[s]), AX.X, ALU.add))
                        step(dve.tensor_scalar(st[s][:, 0, :], st[s][:, 0, :], 1.0 / HD, None, ALU.mult))
                        step.put(dve.tensor_tensor(heads(y[s]), heads(y[s]), wide(st[s][:, 0, :]), ALU.subtract))
                    for s in two:
                        dve.wait_ge(S[f"sq_done{s}"], 1)
                        steps[s].put(dve.tensor_reduce(st[s][:, 1, :], heads(sq[s]), AX.X, ALU.add))
                    for s in two:
                        step = steps[s]
                        dve.wait_ge(S[f"rms_done{s}"], 1)
                        step(dve.reciprocal(st[s][:, 3, :], st[s][:, 2, :]))
                        step(dve.tensor_tensor(heads(y[s]), heads(y[s]), wide(st[s][:, 3, :]), ALU.mult))
                        step(dve.tensor_tensor(y[s][:, :], y[s][:, :], g[:, :], ALU.mult))
                        dve.wait_ge(S[f"shifted{s}"], 1)
                        step(dve.tensor_tensor(y[s][:, :], y[s][:, :], bon[s][:, :], ALU.add))
                        dve.wait_ge(S[f"in_gate{s}"], 16)
                        step.put(dve.tensor_tensor(y[s][:, :], y[s][:, :], gate[s][:, :], ALU.mult))
                    for s in two:
                        dve.wait_ge(S[f"turned{s}"], 1)
                        dve.tensor_copy(oT[:, 4:8, rows[s]], K.bank[2 * s + 1][:, :].rearrange("p (k t) -> p k t", t=P))\
                            .then_inc(S[f"out_b{s}"], 1)

                @block.scalar
                def _(act):
                    for s in two:
                        act.wait_ge(S[f"v{s}"], 4)
                        act.activation(sq[s][:, :], y[s][:, :], ACT.Square).then_inc(S[f"sq_done{s}"], 1)
                    for s in two:
                        act.wait_ge(S[f"v{s}"], 5)
                        act.activation(st[s][:, 2, :], st[s][:, 1, :], ACT.Sqrt, bias=K.gneps[:, :], scale=1.0 / HD)\
                            .then_inc(S[f"rms_done{s}"], 1)
                    for s in two:
                        act.wait_ge(S[f"turned{s}"], 1)
                        act.activation(oT[:, 0:4, rows[s]], K.bank[2 * s][:, :].rearrange("p (k t) -> p k t", t=P), ACT.Copy)\
                            .then_inc(S[f"out_a{s}"], 1)

                @block.tensor
                def _(pe):
                    for s in two:
                        pe.wait_ge(S[f"v{s}"], 10)
                        for k in range(KD):
                            t = pe.transpose(K.bank[2 * s + k // 4][:, (k % 4) * P:(k % 4 + 1) * P],
                                             y[s][:, k * P:(k + 1) * P], K.ident)
                        t.then_inc(S[f"turned{s}"], 1)


def load_context(K, src):
    with phase(K.nc, "x_in") as (block, S):
        @block.sync
        def _(sp):
            sp.dma_start(K.X[:, 0:JC, :], src.rearrange("(j p) n -> p j n", p=P)).then_inc(S["x_in"], 16)
            sp.wait_ge(S["x_in"], 16)


def second_modulation(K, I, layer):
    nc = K.nc
    gain = K.colA[:, WHERE_A["norm_g_2"] + layer * KD:WHERE_A["norm_g_2"] + (layer + 1) * KD]
    with ExitStack() as c:
        K.wring = c.enter_context(sbuf(nc, "weights", [P, RING, KD, WCH], F32))
        row = c.enter_context(sbuf(nc, "mod_row", [2, 3 * D], F32))
        modulation(K, (I["c_2"][0], I["c_ctx_2"]), I["mod_w_2"][layer], I["mod_b_2"][layer], 3 * D, row)
        spread(K, row, [(0, None, K.mods[:, 0, 1, :, :]), (D, gain, K.mods[:, 0, 0, :, :])],
               [(0, 2 * D, K.gate[:, 0, :]), (1, 2 * D, K.gate[:, 1, :])])


def rwkv_layer(K, I, scratch, dbg):
    nc = K.nc
    rw, Y = scratch["rwkv"], scratch["y"]
    load_context(K, I["ctx_2"][0])
    second_modulation(K, I, 0)
    with ExitStack() as c:
        sb = lambda name, shape, s=c: s.enter_context(sbuf(nc, name, shape, F32))
        tw, ta = sb("rwkv_tw", [P, TT]), sb("rwkv_ta", [P, TT])
        with ExitStack() as c2:
            K.hT = sb("hT", [P, KD, TT], c2)
            norm_turn(K, range(NT), K.mods[:, 0, 0, :, :], K.mods[:, 0, 1, :, :])
            dump(K, dbg, "hh0", K.hT[:, :, :])
            rwkv_projections(K, I, rw, tw, ta)
        rwkv_prepare(K, I, rw, tw, ta)
    for n, a in (("p_r", R_), ("p_v", V_), ("p_gate", GATE_)):
        dump(K, dbg, n, rw[a])
    for n, a in (("p_kdir", KD_), ("p_b", B_), ("p_logw", LW_)):
        dump(K, dbg, n, rw[a:a + 2])
    with ExitStack() as c:
        St = [c.enter_context(sbuf(nc, "rwkv_state", [P, 2, P], F32)) for _ in range(UNITS)]
        FA = [c.enter_context(sbuf(nc, "rwkv_own", [P, 2, 2, 2, P], F32)) for _ in range(UNITS)]
        with nc.Fori(0, H2 // 8) as pair:
            with phase(nc, "zeroed") as (block, S):
                @block.vector
                def _(dve):
                    for t in St:
                        dve.memset(t[:, :, :], 0.0).then_inc(S["zeroed"], 1)
                    for t in FA:
                        dve.memset(t.rearrange("p a b c t -> p (a b c t)"), 0.0).then_inc(S["zeroed"], 1)
            with nc.Fori(0, JC) as i:
                rwkv_step(K, rw, Y, St, FA, pair, (i, JC - 1 - i))
            with nc.Fori(0, JX) as i:
                rwkv_step(K, rw, Y, St, FA, pair, (i + JC, NT - 1 - i))
    with ExitStack() as c:
        oT = c.enter_context(sbuf(nc, "rwkv_oT", [P, KD, TT], F32))
        rwkv_readout(K, I, rw, Y, oT)
        output_projection(K, oT, I["rwkv_w_out_2"][0], lambda j: K.gate[:, 0 if j >= JC else 1, :], range(NT), 0)
    dump(K, dbg, "xx0", K.X[:, :, :])

NOPE, ROPE = 64, 32
QK = NOPE + ROPE
QL, KVL = 384, 256
NQ, NKV = QL // P, KVL // P
SMALL = QL + KVL + ROPE


def mla_inputs(K, I, qc, kvc, ssq, gT, kT):
    nc = K.nc
    w = I["mla_w_in_2"][0].rearrange("(k p) n -> p k n", p=P)
    units = [(0, j) for j in range(JC, NT)] + [(1, j) for j in range(NT)]
    names = "w_in g_in0 g_in1 rot lat_mm copied squared pe_mm rope1 rope2 pe_out gate_mm gate_out"
    with ExitStack() as c, phase(nc, names) as (block, S):
        ws = c.enter_context(sbuf(nc, "ml_w", [P, KD, SMALL], F32))
        wr = c.enter_context(sbuf(nc, "ml_wrot", [P, KD, ROPE], F32))
        wg = c.enter_context(sbuf(nc, "ml_wg", [P, 2, KD, 512], F32))
        junk = c.enter_context(sbuf(nc, "ml_junk", [P, QL], F32))
        t = c.enter_context(sbuf(nc, "ml_rope", [P, 2, TX], F32))
        g_in = (S["g_in0"], S["g_in1"])

        @block.sync
        def _(sp):
            sp.dma_start(ws[:, :, :], w[:, :, 0:SMALL]).then_inc(S["w_in"], 16)
            for h in range(2):
                sp.dma_start(wg[:, h, :, :], w[:, :, SMALL + h * 512:SMALL + (h + 1) * 512]).then_inc(g_in[h], 16)

        @block.tensor
        def _(pe):
            pe.wait_ge(S["w_in"], 16)
            for u, (which, j) in enumerate(units):
                if u >= 2:
                    pe.wait_ge(S["squared"], u - 1)
                off, n = ((0, QL), (QL, KVL))[which]
                for k in range(KD):
                    mm = pe.matmul(K.bank[u % 2][:, 0:n], K.hT[:, k, j * P:(j + 1) * P], ws[:, k, off:off + n],
                                   start=(k == 0), stop=(k == KD - 1))
                mm.then_inc(S["lat_mm"], 1)
            pe.wait_ge(S["rot"], 1)
            for b, (wt, t0, t1) in enumerate(((ws, 0, TC), (ws, TC, TT), (wr, TC, TT))):
                off = QL + KVL if wt is ws else 0
                for k in range(KD):
                    mm = pe.matmul(K.bank[2 + b][NOPE:QK, 0:t1 - t0], wt[:, k, off:off + ROPE], K.hT[:, k, t0:t1],
                                   start=(k == 0), stop=(k == KD - 1))
            mm.then_inc(S["pe_mm"], 1)
            for m in range(KD):
                if m % 4 == 0:
                    pe.wait_ge(g_in[m // 4], 16)
                if m >= 2:
                    pe.wait_ge(S["gate_out"], m - 1)
                for k in range(KD):
                    mm = pe.matmul(K.bank[6 + m % 2][:, :], wg[:, m // 4, k, (m % 4) * P:(m % 4 + 1) * P],
                                   K.hT[:, k, TC:TT], start=(k == 0), stop=(k == KD - 1))
                mm.then_inc(S["gate_mm"], 1)

        @block.scalar
        def _(act):
            for u, (which, j) in enumerate(units):
                n = (QL, KVL)[which]
                dst = qc[:, j - JC, :] if which == 0 else kvc[:, j, :]
                act.wait_ge(S["lat_mm"], u + 1)
                act.activation(dst, K.bank[u % 2][:, 0:n], ACT.Copy).then_inc(S["copied"], 1)
                if u:
                    act.wait_ge(S["squared"], u)
                act.activation(junk[:, 0:n], K.bank[u % 2][:, 0:n], ACT.Square, accum_out=ssq[:, u:u + 1])\
                    .then_inc(S["squared"], 1)
            for m in range(KD):
                act.wait_ge(S["gate_mm"], m + 1)
                act.activation(gT[:, m, :], K.bank[6 + m % 2][:, :], ACT.Silu).then_inc(S["gate_out"], 1)

        @block.vector
        def _(dve):
            dve.wait_ge(S["w_in"], 16)
            half = ROPE // 2
            pe0 = QL + KVL
            dve.tensor_copy(wr[:, :, 0:half], ws[:, :, pe0 + half:pe0 + ROPE])
            dve.tensor_copy(wr[:, :, half:ROPE], ws[:, :, pe0:pe0 + half]).then_inc(S["rot"], 1)
            dve.wait_ge(S["pe_mm"], 1)
            r = slice(NOPE, QK)
            for s in range(2):
                dve.tensor_copy(kT[r, s, 0:TC], K.bank[2][r, 0:TC]).then_inc(S["pe_out"], 1)
            dve.tensor_tensor(t[r, 0, :], K.bank[3][r, :], K.cos, ALU.mult).then_inc(S["rope1"], 1)
            dve.tensor_tensor(t[r, 1, :], K.bank[4][r, :], K.sin, ALU.mult).then_inc(S["rope1"], 1)
            dve.wait_ge(S["rope1"], 2)
            for s in range(2):
                dve.tensor_tensor(kT[r, s, TC:TT], t[r, 0, :], t[r, 1, :], ALU.add).then_inc(S["pe_out"], 1)


def mla_latents(K, qc, kvc, ssq, qcT, kvT):
    nc = K.nc
    units = [(0, j) for j in range(JX)] + [(1, j) for j in range(NT)]
    NU = len(units)
    with ExitStack() as c, phase(nc, "mean rms_done inv_done normed turned out") as (block, S):
        st = c.enter_context(sbuf(nc, "mn_stats", [P, 2, NU], F32))
        gain = lambda n, k: K.colB[:, WHERE_B[n] + k:WHERE_B[n] + k + 1]

        @block.scalar
        def _(act):
            act.activation(st[:, 0, 0:JX], ssq[:, 0:JX], ACT.Sqrt, bias=K.eps[:, :], scale=1.0 / QL)\
                .then_inc(S["rms_done"], 1)
            act.activation(st[:, 0, JX:NU], ssq[:, JX:NU], ACT.Sqrt, bias=K.eps[:, :], scale=1.0 / KVL)\
                .then_inc(S["rms_done"], 1)

        @block.vector
        def _(dve):
            dve.wait_ge(S["rms_done"], 2)
            dve.reciprocal(st[:, 1, :], st[:, 0, :]).then_inc(S["inv_done"], 1)
            dve.wait_ge(S["inv_done"], 1)
            for u, (which, j) in enumerate(units):
                x = (qc, kvc)[which][:, j, :]
                dve.tensor_scalar(x, x, st[:, 1, u:u + 1], None, ALU.mult).then_inc(S["normed"], 1)
            for u, (which, j) in enumerate(units):
                dve.wait_ge(S["turned"], u + 1)
                dst, name, n = ((qcT, "q_norm", NQ), (kvT, "kv_norm", NKV))[which]
                for k in range(n):
                    ins = dve.tensor_scalar(dst[:, k, j * P:(j + 1) * P], K.bank[u % 4][:, k * P:(k + 1) * P],
                                            gain(name, k), None, ALU.mult)
                ins.then_inc(S["out"], 1)

        @block.tensor
        def _(pe):
            for u, (which, j) in enumerate(units):
                pe.wait_ge(S["normed"], u + 1)
                if u >= 4:
                    pe.wait_ge(S["out"], u - 3)
                for k in range((NQ, NKV)[which]):
                    tr = pe.transpose(K.bank[u % 4][:, k * P:(k + 1) * P], (qc, kvc)[which][:, j, k * P:(k + 1) * P],
                                      K.ident)
                tr.then_inc(S["turned"], 1)


def attention_pair(K, I, pair, qcT, kvT, gT, kT, oT):
    nc = K.nc
    SCALE = float(QK) ** -0.5
    names = ("wq_in wkv_in rot q_mm k_mm v_mm q_out rope k_out v_out sc_mm max_done nb_done exp_done inv_done "
             "norm_done turned pt_a pt_b o_mm o_out")
    with ExitStack() as c, phase(nc, names) as (block, S):
        buf = lambda name, shape: c.enter_context(sbuf(nc, "at_" + name, shape, F32))
        wq = buf("wq", [P, NQ, 2, QK])
        wr = buf("wr", [P, NQ, 2, ROPE])
        wkv = buf("wkv", [P, NKV, 2, 2 * HD])
        qT = buf("qT", [P, 2, TX])
        t = buf("rope", [P, 2, 2, TX])
        V = buf("v", [P, NT, P])
        Pm = buf("p", [P, 8, TT])
        PT = buf("pT", [P, 2, NT, TX])
        st = buf("stats", [P, 4, 8])
        r = slice(NOPE, QK)

        @block.sync
        def _(sp):
            sp.dma_start(wq[:, :, :, :], I["mla_w_qb_2"][0].rearrange("(k p) n -> p k n", p=P)
                         [:, :, bass.ds(pair * 2 * QK, 2 * QK)].rearrange("p k (h n) -> p k h n", h=2))\
                .then_inc(S["wq_in"], 16)
            sp.dma_start(wkv[:, :, :, :], I["mla_w_kvb_2"][0].rearrange("(k p) n -> p k n", p=P)
                         [:, :, bass.ds(pair * 4 * HD, 4 * HD)].rearrange("p k (h n) -> p k h n", h=2))\
                .then_inc(S["wkv_in"], 16)

        @block.tensor
        def _(pe):
            pe.wait_ge(S["wkv_in"], 16)
            for s in range(2):
                for b, (t0, t1) in enumerate(((0, 512), (512, TT))):
                    for k in range(NKV):
                        mm = pe.matmul(K.bank[4 * s + 2 + b][0:NOPE, 0:t1 - t0], wkv[:, k, s, 0:HD], kvT[:, k, t0:t1],
                                       start=(k == 0), stop=(k == NKV - 1))
                mm.then_inc(S["k_mm"], 1)
            pe.wait_ge(S["wq_in"], 16)
            pe.wait_ge(S["rot"], 1)
            for s in range(2):
                for k in range(NQ):
                    pe.matmul(K.bank[4 * s][0:QK, :], wq[:, k, s, :], qcT[:, k, :], start=(k == 0), stop=(k == NQ - 1))
                for k in range(NQ):
                    mm = pe.matmul(K.bank[4 * s + 1][r, :], wr[:, k, s, :], qcT[:, k, :],
                                   start=(k == 0), stop=(k == NQ - 1))
                mm.then_inc(S["q_mm"], 1)
            pe.wait_ge(S["k_out"], 4)
            for j in range(NT):
                for k in range(NKV):
                    mm = pe.matmul(K.bank[2 + j // 4][:, (j % 4) * P:(j % 4 + 1) * P].rearrange("p (h n) -> p h n", h=2),
                                   kvT[:, k, j * P:(j + 1) * P], wkv[:, k, :, HD:2 * HD],
                                   start=(k == 0), stop=(k == NKV - 1))
            mm.then_inc(S["v_mm"], 1)
            for u in range(8):
                s, qt = divmod(u, 4)
                if qt == 0:
                    pe.wait_ge(S["q_out"], 4 if s == 0 else 4)
                    pe.wait_ge(S["v_out"], 2)
                if u >= 4:
                    pe.wait_ge(S["exp_done"], u - 3)
                for b, (t0, t1) in enumerate(((0, 512), (512, TT))):
                    mm = pe.matmul(K.bank[2 * (u % 4) + b][:, 0:t1 - t0], qT[0:QK, s, qt * P:(qt + 1) * P],
                                   kT[0:QK, s, t0:t1], start=True, stop=True)
                mm.then_inc(S["sc_mm"], 1)
            for s in range(2):
                pe.wait_ge(S["exp_done"], 8)
                pe.wait_ge(S["norm_done"], 4 * s + 4)
                for kt in range(NT):
                    n = NT * s + kt
                    if n >= 4:
                        pe.wait_ge((S["pt_a"], S["pt_b"])[n % 2], (n - 4) // 2 + 1)
                    for qt in range(4):
                        tr = pe.transpose(K.bank[n % 4][:, qt * P:(qt + 1) * P], Pm[:, 4 * s + qt, kt * P:(kt + 1) * P],
                                          K.ident)
                    tr.then_inc(S["turned"], 1)
                pe.wait_ge(S["pt_a"], 3 * (s + 1))
                pe.wait_ge(S["pt_b"], 3 * (s + 1))
                for kt in range(NT):
                    mm = pe.matmul(K.bank[4][s * HD:(s + 1) * HD, :], V[:, kt, s * HD:(s + 1) * HD], PT[:, s, kt, :],
                                   start=(kt == 0), stop=(kt == NT - 1))
                mm.then_inc(S["o_mm"], 1)

        @block.scalar
        def _(act):
            for s in range(2):
                act.wait_ge(S["k_mm"], s + 1)
                for b, (t0, t1) in enumerate(((0, 512), (512, TT))):
                    act.activation(kT[0:NOPE, s, t0:t1], K.bank[4 * s + 2 + b][0:NOPE, 0:t1 - t0], ACT.Copy)\
                        .then_inc(S["k_out"], 1)
            act.wait_ge(S["v_mm"], 1)
            act.activation(V[:, 0:4, :], K.bank[2][:, :].rearrange("p (j n) -> p j n", n=P), ACT.Copy)\
                .then_inc(S["v_out"], 1)
            act.activation(V[:, 4:NT, :], K.bank[3][:, 0:(NT - 4) * P].rearrange("p (j n) -> p j n", n=P), ACT.Copy)\
                .then_inc(S["v_out"], 1)
            for u in range(8):
                act.wait_ge(S["nb_done"], u + 1)
                b = 2 * (u % 4)
                act.activation(Pm[:, u, :], K.psum[:, b * 512:b * 512 + TT], ACT.Exp, bias=st[:, 1, u:u + 1],
                               scale=SCALE, accum_out=st[:, 2, u:u + 1]).then_inc(S["exp_done"], 1)
            for n in range(0, 2 * NT, 2):
                s, kt = divmod(n, NT)
                act.wait_ge(S["turned"], n + 1)
                act.activation(PT[:, s, kt, :], K.bank[n % 4][:, :], ACT.Copy).then_inc(S["pt_a"], 1)

        @block.vector
        def _(dve):
            half = ROPE // 2
            dve.wait_ge(S["wq_in"], 16)
            dve.tensor_copy(wr[:, :, :, 0:half], wq[:, :, :, NOPE + half:QK])
            dve.tensor_copy(wr[:, :, :, half:ROPE], wq[:, :, :, NOPE:NOPE + half]).then_inc(S["rot"], 1)
            for s in range(2):
                dve.wait_ge(S["q_mm"], s + 1)
                dve.tensor_copy(qT[0:NOPE, s, :], K.bank[4 * s][0:NOPE, :]).then_inc(S["q_out"], 1)
                dve.tensor_tensor(t[r, s, 0, :], K.bank[4 * s][r, :], K.cos, ALU.mult).then_inc(S["rope"], 1)
                dve.tensor_tensor(t[r, s, 1, :], K.bank[4 * s + 1][r, :], K.sin, ALU.mult).then_inc(S["rope"], 1)
                dve.wait_ge(S["rope"], 2 * s + 2)
                dve.tensor_tensor(qT[r, s, :], t[r, s, 0, :], t[r, s, 1, :], ALU.add).then_inc(S["q_out"], 1)

            def inverse(u):
                dve.wait_ge(S["exp_done"], u + 1)
                dve.reciprocal(st[:, 3, u:u + 1], st[:, 2, u:u + 1]).then_inc(S["inv_done"], 1)
                dve.wait_ge(S["inv_done"], u + 1)
                dve.tensor_scalar(Pm[:, u, :], Pm[:, u, :], st[:, 3, u:u + 1], None, ALU.mult).then_inc(S["norm_done"], 1)

            for u in range(8):
                b = 2 * (u % 4)
                dve.wait_ge(S["sc_mm"], u + 1)
                dve.tensor_reduce(st[:, 0, u:u + 1], K.psum[:, b * 512:b * 512 + TT], AX.X, ALU.max)\
                    .then_inc(S["max_done"], 1)
                dve.wait_ge(S["max_done"], u + 1)
                dve.tensor_scalar(st[:, 1, u:u + 1], st[:, 0, u:u + 1], -SCALE, None, ALU.mult).then_inc(S["nb_done"], 1)
                if u >= 2:
                    inverse(u - 2)
            inverse(6)
            inverse(7)
            for n in range(1, 2 * NT, 2):
                s, kt = divmod(n, NT)
                dve.wait_ge(S["turned"], n + 1)
                dve.tensor_copy(PT[:, s, kt, :], K.bank[n % 4][:, :]).then_inc(S["pt_b"], 1)
            dve.wait_ge(S["o_mm"], 2)
            at = bass.ds(pair, 1)
            dve.tensor_tensor(oT[:, at, :].rearrange("p o n -> p (o n)"), K.bank[4][:, :],
                              gT[:, at, :].rearrange("p o n -> p (o n)"), ALU.mult).then_inc(S["o_out"], 1)


def mla_layer(K, I, dbg):
    nc = K.nc
    second_modulation(K, I, 1)
    with ExitStack() as c:
        sb = lambda name, shape, s=c: s.enter_context(sbuf(nc, name, shape, F32))
        oT, gT = sb("mla_oT", [P, KD, TX]), sb("mla_gate", [P, KD, TX])
        with ExitStack() as c2:
            qcT, kvT = sb("mla_qcT", [P, NQ, TX], c2), sb("mla_kvT", [P, NKV, TT], c2)
            kT = sb("mla_kT", [P, 2, TT], c2)
            with ExitStack() as c3:
                K.hT = sb("hT", [P, KD, TT], c3)
                norm_turn(K, range(NT), K.mods[:, 0, 0, :, :], K.mods[:, 0, 1, :, :])
                dump(K, dbg, "hh1", K.hT[:, :, :])
                qc, kvc = sb("mla_qc", [P, JX, QL], c3), sb("mla_kvc", [P, NT, KVL], c3)
                ssq = sb("mla_ssq", [P, JX + NT], c3)
                mla_inputs(K, I, qc, kvc, ssq, gT, kT)
                mla_latents(K, qc, kvc, ssq, qcT, kvT)
            with nc.Fori(0, H2 // 2) as pair:
                attention_pair(K, I, pair, qcT, kvT, gT, kT, oT)
        output_projection(K, oT, I["mla_w_out_2"][0], lambda j: K.gate[:, 0, :], range(JC, NT), JC)
    dump(K, dbg, "xx1", K.X[:, :, :])

def build(nc, I, out, scratch, dbg=None, stop=None):
    USED.clear()
    K = Kernel()
    K.nc = nc
    with ExitStack() as c:
        def sb(name, shape, stack=c):
            return stack.enter_context(sbuf(nc, name, shape, F32))

        K.const = sb("const", [P, CONST_COLS])
        K.colA, K.colB = sb("param_cols_a", [P, N_A]), sb("param_cols_b", [P, N_B])
        K.colC = sb("param_cols_c", [P, N_C])
        K.eps, K.one, K.gneps = sb("eps", [P, 1]), sb("one", [P, 1]), sb("gneps", [P, 1])
        K.X = sb("tokens", [P, NT, D])
        K.mods = sb("mod_cols", [P, 2, 2, KD, 2])
        K.gate = sb("mod_gate", [P, 2, D])
        K.psum = c.enter_context(nc.psum_tensor("psum", [P, 8 * 512], F32))
        K.bank = [K.psum[:, i * 512:(i + 1) * 512] for i in range(8)]
        part = lambda n: K.const[:, n * P:(n + 1) * P]
        K.ident, K.ones = part(0), part(1)
        K.inc, K.cum = (part(3), part(5)), (part(6), part(7))
        by4 = lambda ap: ap.unsqueeze(1).broadcast_to([P, 4, P])
        K.ident4 = by4(K.ident)
        K.incl4, K.strict4 = (by4(part(3)), by4(part(5))), (by4(part(2)), by4(part(4)))
        K.mask2 = [K.const[:, n * P:(n + 2) * P].rearrange("p (b t) -> p b t", b=2) for n in (2, 4)]
        K.before = part(2)
        K.zeros = sb("zeros", [P, NE])
        K.cos = K.const[64:96, ROPE_COL:ROPE_COL + TX]
        K.sin = K.const[64:96, ROPE_COL + TX:ROPE_COL + 2 * TX]
        K.same_head = K.const[:, MIX_COL + 4:SLOT_COL].unsqueeze(1).broadcast_to([P, 2, P])
        K.cross = [[by4(K.const[:, CROSS_COL + (d * LEVELS + n) * P:CROSS_COL + (d * LEVELS + n + 1) * P])
                    for n in range(LEVELS)] for d in range(2)]

        load_parameters(K, I)
        if stop != "skip_first":
            first_model(K, I, scratch, dbg, stop)
        if stop == "first":
            with phase(nc, "out_done") as (block, S):
                @block.sync
                def _(sp):
                    sp.dma_start(out.rearrange("o (j p) n -> (o p) j n", p=P), K.X[:, JC:NT, :]).then_inc(S["out_done"], 16)
                    sp.wait_ge(S["out_done"], 16)
            return
        if stop in ("mix", "delta"):
            return
        rwkv_layer(K, I, scratch, dbg)
        mla_layer(K, I, dbg)
        final_norm(K, I["final_g_2"], range(JC, NT), out.rearrange("o t n -> (o t) n"))


def dump(K, dbg, name, ap):
    if dbg is None or name not in dbg:
        return
    with phase(K.nc, "dumped") as (block, S):
        @block.sync
        def _(sp):
            sp.dma_start(dbg[name], ap).then_inc(S["dumped"], 16)
            sp.wait_ge(S["dumped"], 16)


def first_model(K, I, scratch, dbg, stop):
    nc = K.nc
    cols = lambda name, n, off=0: K.colA[:, WHERE_A[name] + off:WHERE_A[name] + off + n]
    with ExitStack() as c1:
        sb = lambda name, shape, stack=c1: stack.enter_context(sbuf(nc, name, shape, F32))
        with ExitStack() as c:
            K.wring = sb("weights", [P, RING, KD, WCH], c)
            row = sb("mod_row", [2, 6 * D], c)
            modulation(K, (I["c"][0], I["c_ctx"]), I["w_mod"][0], I["b_mod"][0], 6 * D, row)
            spread(K, row,
                   [(0, None, K.mods[:, 0, 1, :, :]), (D, cols("g_mix", KD), K.mods[:, 0, 0, :, :]),
                    (3 * D, None, K.mods[:, 1, 1, :, :]), (4 * D, cols("g_ffn", KD), K.mods[:, 1, 0, :, :])],
                   [(0, 2 * D, K.gate[:, 0, :]), (0, 5 * D, K.gate[:, 1, :])])
        headsT = sb("mix_heads", [P, H1 + NCF, TX])
        zT = headsT[:, 0:H1, :]
        cfT = headsT[:, H1:H1 + NCF, :]
        with ExitStack() as c:
            C = sb("conv_out", [P, NQKV, TT], c)
            ba = sb("ba", [P, NT, 16], c)
            with ExitStack() as c2:
                cfa, cfs = sb("cf_a", [P, NCF, TX], c2), sb("cf_s", [P, NCF, TX], c2)
                with ExitStack() as c3:
                    K.hT = sb("hT", [P, KD, TT], c3)
                    K.wring = sb("weights2", [P, RING, KD, WCH], c3)
                    norm_turn(K, range(NT), K.mods[:, 0, 0, :, :], K.mods[:, 0, 1, :, :])
                    dump(K, dbg, "hT", K.hT[:, :, :])
                    mixer_inputs(K, I, C, zT, cfa, cfs, ba[:, :, :])
                conformer(K, cfa, cfs, cfT)
            qk_norm(K, C)
            dump(K, dbg, "C", C[:, :, :])
            dump(K, dbg, "headsT0", headsT[:, :, :])
            Ktok, Vtok = sb("k_tokens", [P, H1, NT, P], c), sb("v_tokens", [P, H1, NT, P], c)
            turn_back(K, [C[:, H1 + n, :] for n in range(2 * H1)],
                      [Ktok[:, h, :, :] for h in range(H1)] + [Vtok[:, h, :, :] for h in range(H1)])
            O = sb("delta_out", [P, JX, H1 * DK], c)
            G = {n: sb("gates_" + n, [P, 2, NT, H1], c) for n in ("cumg", "beta", "egc", "ekd", "egl")}
            delta_gates(K, I, ba, G)
            St = [sb(f"delta_state{d}", [P, H1, P], c) for d in range(2)]
            with phase(nc, "zeroed") as (block, S):
                @block.vector
                def _(dve):
                    for t in (*St, O):
                        dve.memset(t[:, :, :], 0.0).then_inc(S["zeroed"], 1)
            with nc.Fori(0, JC) as i:
                delta_step(K, C, Ktok, Vtok, G, O, St, (i, JC - 1 - i), False)
            with nc.Fori(0, JX) as i:
                delta_step(K, C, Ktok, Vtok, G, O, St, (i + JC, NT - 1 - i), True)
            dump(K, dbg, "O", O[:, :, :])
            if stop == "delta":
                return
            delta_readout(K, O, headsT)
        dump(K, dbg, "headsT", headsT[:, :, :])
        output_projection(K, headsT, I["w_out"][0], lambda j: K.gate[:, 0, :], range(JC, NT), JC)
        dump(K, dbg, "x1", K.X[:, JC:NT, :])
    if stop == "mix":
        return
    with ExitStack() as c:
        K.hT = c.enter_context(sbuf(nc, "hT", [P, KD, TT], F32))
        norm_turn(K, range(JC, NT), K.mods[:, 1, 0, :, :], K.mods[:, 1, 1, :, :])
        mixture(K, I, scratch)
    final_norm(K, I["g_final"], range(JC, NT))



INPUTS = ['x', 'c', 'ctx', 'c_ctx', 'w_mod', 'b_mod', 'g_mix', 'g_ffn', 'w_in', 'w_out', 'dn_conv_w', 'dn_a_log',
          'dn_dt_bias', 'dn_norm_g', 'cf_dw_w', 'cf_dw_b', 'cf_ln_g', 'cf_ln_b', 'router_w', 'router_bias',
          'exp_w_gate', 'exp_w_up', 'exp_w_down', 'sh_w_gate', 'sh_w_up', 'sh_w_down', 'g_final', 'c_2', 'ctx_2',
          'c_ctx_2', 'norm_g_2', 'mod_w_2', 'mod_b_2', 'rwkv_mu_2', 'rwkv_w_in_2', 'rwkv_w0_2', 'rwkv_w1_2',
          'rwkv_w2_2', 'rwkv_a0_2', 'rwkv_a1_2', 'rwkv_a2_2', 'rwkv_k_k_2', 'rwkv_k_a_2', 'rwkv_r_k_2',
          'rwkv_lnx_g_2', 'rwkv_lnx_b_2', 'rwkv_w_out_2', 'mla_w_in_2', 'mla_q_norm_g_2', 'mla_w_qb_2',
          'mla_kv_norm_g_2', 'mla_w_kvb_2', 'mla_w_out_2', 'final_g_2']
SCRATCH = {"rwkv": (N_RW, TT, D), "y": (2, TT, D), "h_rows": (TX, D), "slot_tokens": (TILES * SLOTS, 1),
           "ys": ((TILES + 1) * SLOTS, D)}


def kernel(**inputs):
    import numpy as np
    import concourse.bacc as bacc
    from concourse.bass_utils import run_bass_kernel_spmd

    nc = bacc.Bacc("TRN2", target_bir_lowering=False, num_devices=1)
    arrays, aps = {}, {}
    for name in INPUTS:
        a = np.ascontiguousarray(inputs[name])
        arrays[f"in_{name}"] = a
        aps[name] = nc.dram_tensor(f"in_{name}", a.shape, mybir.dt.from_np(a.dtype), kind="ExternalInput").ap()
    arrays["in_consts"] = constants()
    aps["consts"] = nc.dram_tensor("in_consts", (P, CONST_COLS), F32, kind="ExternalInput").ap()
    out = nc.dram_tensor("out", (1, TX, D), F32, kind="ExternalOutput").ap()
    scratch = {n: nc.dram_tensor("scratch_" + n, shape, F32, kind="Internal").ap() for n, shape in SCRATCH.items()}
    build(nc, aps, out, scratch)
    r = run_bass_kernel_spmd(nc, [arrays], core_ids=[0])
    return r.results[0]["out"]
```
